# Optimizing a Trainium2 kernel written in Bass

```python
import jax, jax.numpy as jnp
from jax import lax
import numpy as np

D_MODEL = 1024
BATCH = 1
SEQ = 512
DEPTH = 1

CTX_LEN = 256
GRID_W = 64

GLA_HEADS = 4
GLA_DK = 128
GLA_DV = 256
GLA_RANK = 16
GLA_TAU = 16.0
GLA_CHUNK = 64
GLA_QK = GLA_HEADS * GLA_DK
GLA_V = GLA_HEADS * GLA_DV

RET_HEADS = 4
RET_DK = 128
RET_DV = 256
RET_CHUNK = 128
RET_QK = RET_HEADS * RET_DK
RET_V = RET_HEADS * RET_DV
ROPE_BASE = 10000.0

N_GROUPS = 4
EXPERTS_PER_GROUP = 8
N_EXPERTS = N_GROUPS * EXPERTS_PER_GROUP
TOP_K = 2
EXPERT_FF = 256
MOE_BLOCK = 128

NORM_EPS = 1e-6

IN_SPLITS = (GLA_QK, GLA_QK, GLA_V, GLA_V, GLA_RANK, GLA_RANK,
             RET_QK, RET_QK, RET_V, RET_V, D_MODEL, D_MODEL)
IN_WIDTH = sum(IN_SPLITS)


def rmsnorm(x, g):
    xf = x.astype(jnp.float32)
    y = xf * lax.rsqrt(jnp.mean(xf * xf, axis=-1, keepdims=True) + NORM_EPS)
    return (y * g.astype(jnp.float32)).astype(x.dtype)

def head_groupnorm(o):
    of = o.astype(jnp.float32)
    mu = jnp.mean(of, axis=-1, keepdims=True)
    var = jnp.mean(jnp.square(of - mu), axis=-1, keepdims=True)
    return ((of - mu) * lax.rsqrt(var + NORM_EPS)).astype(o.dtype)

def modulate(h, shift, scale):
    return h * (1.0 + scale) + shift

def split_columns(proj):
    out = []
    start = 0
    for w in IN_SPLITS:
        out.append(proj[..., start:start + w])
        start += w
    return out

def retention_log_decays():
    h = jnp.arange(RET_HEADS, dtype=jnp.float32)
    fwd = jnp.log1p(-jnp.exp2(-5.0 - h))
    bwd = jnp.log1p(-jnp.exp2(-5.5 - h))
    return fwd, bwd

def axial_rope(t, rows, cols):
    half = t.shape[-1] // 2
    n = half // 2
    inv = ROPE_BASE ** (-jnp.arange(n, dtype=jnp.float32) / n)

    def rot(u, p):
        ang = p[:, None] * inv[None, :]
        cos = jnp.cos(ang)[None, :, None, :].astype(u.dtype)
        sin = jnp.sin(ang)[None, :, None, :].astype(u.dtype)
        u1, u2 = u[..., :n], u[..., n:]
        return jnp.concatenate([u1 * cos - u2 * sin, u1 * sin + u2 * cos], axis=-1)

    return jnp.concatenate([rot(t[..., :half], rows), rot(t[..., half:], cols)], axis=-1)

def to_chunks(t, chunk):
    B, L, H, W = t.shape
    return jnp.moveaxis(t.reshape(B, L // chunk, chunk, H, W), 1, 0)

def from_chunks(o):
    N, B, C, H, W = o.shape
    return jnp.moveaxis(o, 0, 1).reshape(B, N * C, H, W)

def gla_scan(q, k, v, log_a, s0, strict):
    C = GLA_CHUNK
    ti = jnp.arange(C)
    mask = (ti[:, None] > ti[None, :]) if strict else (ti[:, None] >= ti[None, :])
    mask5 = mask[None, :, :, None, None]

    def step(S, inp):
        qc, kc, vc, lac = inp
        b = jnp.cumsum(lac.astype(jnp.float32), axis=1)
        inter = jnp.einsum('bthk,bhkv->bthv', qc * jnp.exp(b), S)
        decay = jnp.exp(jnp.where(mask5, b[:, :, None] - b[:, None, :], -jnp.inf))
        scores = jnp.einsum('bthk,btshk,bshk->btsh', qc, decay, kc)
        intra = jnp.einsum('btsh,bshv->bthv', scores, vc)
        b_last = b[:, -1]
        S_new = jnp.exp(b_last)[..., None] * S + jnp.einsum(
            'bshk,bshv->bhkv', kc * jnp.exp(b_last[:, None] - b), vc)
        return S_new, inter + intra

    S_fin, o = lax.scan(step, s0, (to_chunks(q, C), to_chunks(k, C), to_chunks(v, C), to_chunks(log_a, C)))
    return from_chunks(o).astype(v.dtype), S_fin

def retention_scan(q, k, v, log_gamma, s0, strict):
    C = RET_CHUNK
    pos = jnp.arange(C, dtype=jnp.float32)
    ti = jnp.arange(C)
    mask = (ti[:, None] > ti[None, :]) if strict else (ti[:, None] >= ti[None, :])
    rel = pos[:, None] - pos[None, :]
    dmat = jnp.exp(jnp.where(mask[None], rel[None] * log_gamma[:, None, None], -jnp.inf))
    q_decay = jnp.exp((pos + 1.0)[:, None] * log_gamma[None, :])
    k_decay = jnp.exp((C - 1.0 - pos)[:, None] * log_gamma[None, :])
    c_decay = jnp.exp(C * log_gamma)

    def step(S, inp):
        qc, kc, vc = inp
        inter = jnp.einsum('bthk,bhkv->bthv', qc, S) * q_decay[None, :, :, None]
        scores = jnp.einsum('bthk,bshk->bhts', qc, kc) * dmat[None]
        intra = jnp.einsum('bhts,bshv->bthv', scores, vc)
        S_new = c_decay[None, :, None, None] * S + jnp.einsum(
            'bshk,bshv->bhkv', kc * k_decay[None, :, :, None], vc)
        return S_new, inter + intra

    S_fin, o = lax.scan(step, s0, (to_chunks(q, C), to_chunks(k, C), to_chunks(v, C)))
    return from_chunks(o).astype(v.dtype), S_fin

def mixer_heads(h, w_in, gla_lr_w, gla_lr_b, gla_norm, states, rope):
    B, L, _ = h.shape
    (gq, gk, gv, gg, glr_f, glr_b, rq, rk, rv, rg, m_gla, m_ret) = split_columns(h @ w_in)

    def heads(t, n):
        return t.reshape(B, L, n, -1)

    def flip(t):
        return jnp.flip(t, axis=1)

    gq = heads(gq, GLA_HEADS) * GLA_DK ** -0.5
    gk = heads(gk, GLA_HEADS)
    gv = heads(gv, GLA_HEADS)

    def log_gate(lr, d):
        z = (lr @ gla_lr_w[d] + gla_lr_b[d]).astype(jnp.float32)
        return heads(jax.nn.log_sigmoid(z) / GLA_TAU, GLA_HEADS)

    o_f, s_gf = gla_scan(gq, gk, gv, log_gate(glr_f, 0), states[0], False)
    o_b, s_gb = gla_scan(flip(gq), flip(gk), flip(gv), flip(log_gate(glr_b, 1)), states[1], True)
    o_gla = rmsnorm(o_f + flip(o_b), gla_norm) * jax.nn.silu(heads(gg, GLA_HEADS))
    o_gla = o_gla.reshape(B, L, GLA_V)

    rq = heads(rq, RET_HEADS)
    rk = heads(rk, RET_HEADS) * RET_DK ** -0.5
    rv = heads(rv, RET_HEADS)
    if rope is not None:
        rq = axial_rope(rq, rope[0], rope[1])
        rk = axial_rope(rk, rope[0], rope[1])
    lg_f, lg_b = retention_log_decays()
    r_f, s_rf = retention_scan(rq, rk, rv, lg_f, states[2], False)
    r_b, s_rb = retention_scan(flip(rq), flip(rk), flip(rv), lg_b, states[3], True)
    o_ret = head_groupnorm(r_f + flip(r_b)) * jax.nn.silu(heads(rg, RET_HEADS))
    o_ret = o_ret.reshape(B, L, RET_V)
    return o_gla, o_ret, m_gla, m_ret, (s_gf, s_gb, s_rf, s_rb)

def merge_branches(o_gla, o_ret, m_gla, m_ret, w_branch_gla, w_branch_ret, w_out):
    y = jax.nn.sigmoid(m_gla) * (o_gla @ w_branch_gla) + jax.nn.sigmoid(m_ret) * (o_ret @ w_branch_ret)
    return y @ w_out

def hier_moe(h, w_rg, b_rg, w_re, b_re, w_gate, w_up, w_down):
    B, L, D = h.shape
    T = B * L
    xt = h.reshape(T, D)
    g_logits = (xt @ w_rg + b_rg).astype(jnp.float32)
    g_prob = jax.nn.softmax(g_logits, axis=-1)
    g_sel = jnp.argmax(g_logits, axis=-1).astype(jnp.int32)
    g_w = jnp.take_along_axis(g_prob, g_sel[:, None], axis=-1)[:, 0]
    e_logits = (xt @ w_re + b_re).astype(jnp.float32).reshape(T, N_GROUPS, EXPERTS_PER_GROUP)
    e_logits = jnp.take_along_axis(e_logits, g_sel[:, None, None], axis=1)[:, 0]
    top_v, top_i = lax.top_k(e_logits, TOP_K)
    e_w = jax.nn.softmax(top_v, axis=-1) * g_w[:, None]
    expert_id = g_sel[:, None] * EXPERTS_PER_GROUP + top_i.astype(jnp.int32)

    A = T * TOP_K
    flat_e = expert_id.reshape(A)
    flat_tok = jnp.repeat(jnp.arange(T, dtype=jnp.int32), TOP_K)
    flat_w = e_w.reshape(A)
    order = jnp.argsort(flat_e)
    se, stok, sw = flat_e[order], flat_tok[order], flat_w[order]
    counts = jax.ops.segment_sum(jnp.ones((A,), jnp.int32), flat_e, num_segments=N_EXPERTS)
    starts = jnp.cumsum(counts) - counts
    padded = (counts + MOE_BLOCK - 1) // MOE_BLOCK * MOE_BLOCK
    pends = jnp.cumsum(padded)
    pstarts = pends - padded
    dest = pstarts[se] + jnp.arange(A, dtype=jnp.int32) - starts[se]
    P = A + N_EXPERTS * MOE_BLOCK
    NB = P // MOE_BLOCK
    x_pad = jnp.zeros((P, D), h.dtype).at[dest].set(xt[stok])
    tok_pad = jnp.zeros((P,), jnp.int32).at[dest].set(stok)
    w_pad = jnp.zeros((P,), jnp.float32).at[dest].set(sw)
    block_start = jnp.arange(NB, dtype=jnp.int32) * MOE_BLOCK
    block_e = jnp.minimum(jnp.searchsorted(pends, block_start, side='right'), N_EXPERTS - 1)

    def expert_block(args):
        xb, e = args
        hid = jax.nn.silu(xb @ w_gate[e]) * (xb @ w_up[e])
        return hid @ w_down[e]

    y = lax.map(expert_block, (x_pad.reshape(NB, MOE_BLOCK, D), block_e)).reshape(P, D)
    out = jnp.zeros((T, D), jnp.float32).at[tok_pad].add(y.astype(jnp.float32) * w_pad[:, None])
    return out.astype(h.dtype).reshape(B, L, D)

def first_inputs(seed: int = 0) -> dict:
    key = jax.random.key(seed)
    ks = jax.random.split(key, 24)

    def nrm(k, shape, scale):
        return jax.random.normal(k, shape, jnp.float32) * scale

    D = D_MODEL
    return {
        'x': nrm(ks[0], (BATCH, SEQ, D), 1.0),
        'c': nrm(ks[1], (BATCH, D), 1.0),
        'ctx': nrm(ks[2], (BATCH, CTX_LEN, D), 1.0),
        'c_ctx': nrm(ks[3], (D,), 1.0),
        'w_ada': nrm(ks[4], (DEPTH, D, 6 * D), D ** -0.5),
        'b_ada': nrm(ks[5], (DEPTH, 6 * D), 0.02),
        'norm_mix': 1.0 + nrm(ks[6], (DEPTH, D), 0.05),
        'norm_ffn': 1.0 + nrm(ks[7], (DEPTH, D), 0.05),
        'w_in': nrm(ks[8], (DEPTH, D, IN_WIDTH), D ** -0.5),
        'gla_lr_w': nrm(ks[9], (DEPTH, 2, GLA_RANK, GLA_QK), GLA_RANK ** -0.5),
        'gla_lr_b': nrm(ks[10], (DEPTH, 2, GLA_QK), 0.1),
        'gla_norm': 1.0 + nrm(ks[11], (DEPTH, GLA_DV), 0.05),
        'w_branch_gla': nrm(ks[12], (DEPTH, GLA_V, D), GLA_V ** -0.5),
        'w_branch_ret': nrm(ks[13], (DEPTH, RET_V, D), RET_V ** -0.5),
        'w_out': nrm(ks[14], (DEPTH, D, D), D ** -0.5),
        'w_router_group': nrm(ks[15], (DEPTH, D, N_GROUPS), D ** -0.5),
        'b_router_group': nrm(ks[16], (DEPTH, N_GROUPS), 0.01),
        'w_router_expert': nrm(ks[17], (DEPTH, D, N_EXPERTS), D ** -0.5),
        'b_router_expert': nrm(ks[18], (DEPTH, N_EXPERTS), 0.01),
        'w_expert_gate': nrm(ks[19], (DEPTH, N_EXPERTS, D, EXPERT_FF), D ** -0.5),
        'w_expert_up': nrm(ks[20], (DEPTH, N_EXPERTS, D, EXPERT_FF), D ** -0.5),
        'w_expert_down': nrm(ks[21], (DEPTH, N_EXPERTS, EXPERT_FF, D), EXPERT_FF ** -0.5),
        'norm_final': 1.0 + nrm(ks[22], (D,), 0.05),
    }

def first_block(x, c, ctx, c_ctx, w_ada, b_ada, norm_mix, norm_ffn, w_in, gla_lr_w, gla_lr_b, gla_norm,
              w_branch_gla, w_branch_ret, w_out, w_router_group, b_router_group, w_router_expert,
              b_router_expert, w_expert_gate, w_expert_up, w_expert_down, norm_final):
    B, L, _ = x.shape
    ROWS = L // GRID_W
    rows = jnp.repeat(jnp.arange(ROWS, dtype=jnp.float32), GRID_W)
    cols = jnp.tile(jnp.arange(GRID_W, dtype=jnp.float32), ROWS)
    zero_states = (
        jnp.zeros((B, GLA_HEADS, GLA_DK, GLA_DV), jnp.float32),
        jnp.zeros((B, GLA_HEADS, GLA_DK, GLA_DV), jnp.float32),
        jnp.zeros((B, RET_HEADS, RET_DK, RET_DV), jnp.float32),
        jnp.zeros((B, RET_HEADS, RET_DK, RET_DV), jnp.float32),
    )
    h_lat = x
    h_ctx = ctx
    for layer in range(DEPTH):
        sh1, sc1, g1, sh2, sc2, g2 = jnp.split(
            (jax.nn.silu(c) @ w_ada[layer] + b_ada[layer])[:, None, :], 6, axis=-1)
        csh1, csc1, cg1, csh2, csc2, cg2 = jnp.split(
            (jax.nn.silu(c_ctx) @ w_ada[layer] + b_ada[layer])[None, None, :], 6, axis=-1)
        mix_args = (w_in[layer], gla_lr_w[layer], gla_lr_b[layer], gla_norm[layer])
        merge_args = (w_branch_gla[layer], w_branch_ret[layer], w_out[layer])
        moe_args = (w_router_group[layer], b_router_group[layer], w_router_expert[layer],
                    b_router_expert[layer], w_expert_gate[layer], w_expert_up[layer], w_expert_down[layer])

        hc = modulate(rmsnorm(h_ctx, norm_mix[layer]), csh1, csc1)
        c_gla, c_ret, c_mg, c_mr, ctx_states = mixer_heads(hc, *mix_args, zero_states, None)

        hl = modulate(rmsnorm(h_lat, norm_mix[layer]), sh1, sc1)
        l_gla, l_ret, l_mg, l_mr, _ = mixer_heads(hl, *mix_args, ctx_states, (rows, cols))
        h_lat = h_lat + g1 * merge_branches(l_gla, l_ret, l_mg, l_mr, *merge_args)
        h_lat = h_lat + g2 * hier_moe(modulate(rmsnorm(h_lat, norm_ffn[layer]), sh2, sc2), *moe_args)

        if layer < DEPTH - 1:
            h_ctx = h_ctx + cg1 * merge_branches(c_gla, c_ret, c_mg, c_mr, *merge_args)
            h_ctx = h_ctx + cg2 * hier_moe(modulate(rmsnorm(h_ctx, norm_ffn[layer]), csh2, csc2), *moe_args)
    return rmsnorm(h_lat, norm_final)


PLE_DIM = 256
ROPE_THETA = 500000.0
EPS = 1e-6
NEG_INF = -1e30

MIX_WIDTH = D_MODEL
MLA_V_DIM = 64
MLA_NOPE_DIM = 64
MLA_ROPE_DIM = 32
MLA_QK_DIM = MLA_NOPE_DIM + MLA_ROPE_DIM
MLA_WIDTH = MIX_WIDTH // 2
MLA_HEADS = MLA_WIDTH // MLA_V_DIM
MLA_Q_RANK = 3 * D_MODEL // 8
MLA_KV_RANK = 4 * MLA_V_DIM
Q_BLOCK = 128
DIL_HEAD_DIM = 64
DIL_WIDTH = MIX_WIDTH - MLA_WIDTH
DIL_HEADS = DIL_WIDTH // DIL_HEAD_DIM
DIL_ROT_DIM = DIL_HEAD_DIM // 4
DIL_PATTERNS = ((128, 1), (512, 4), (2048, 16))
IN_SPLITS_2 = (MLA_Q_RANK, MLA_KV_RANK, MLA_ROPE_DIM, DIL_WIDTH, DIL_WIDTH, DIL_WIDTH)
IN_WIDTH_2 = sum(IN_SPLITS_2)
PEER_KEYS = 128
PEER_EXPERTS = PEER_KEYS * PEER_KEYS
PEER_HEADS = 8
PEER_QDIM = 128
PEER_HALF = PEER_QDIM // 2
PEER_TOPK = 16
PEER_CHUNK = 128


def rms_norm(x, g):
    xf = x.astype(jnp.float32)
    y = xf * lax.rsqrt(jnp.mean(xf * xf, axis=-1, keepdims=True) + EPS)
    return (y * g.astype(jnp.float32)).astype(x.dtype)

def rope_tables(seq, rot_dim):
    inv = ROPE_THETA ** (-jnp.arange(0, rot_dim, 2, dtype=jnp.float32) / rot_dim)
    ang = jnp.arange(seq, dtype=jnp.float32)[:, None] * inv[None, :]
    return jnp.cos(ang), jnp.sin(ang)

def apply_rope(x, cos, sin, rot_dim):
    half = rot_dim // 2
    shape = (x.shape[1],) + (1,) * (x.ndim - 3) + (half,)
    c = cos.reshape(shape).astype(x.dtype)
    s = sin.reshape(shape).astype(x.dtype)
    x1 = x[..., :half]
    x2 = x[..., half:rot_dim]
    return jnp.concatenate([x1 * c - x2 * s, x2 * c + x1 * s, x[..., rot_dim:]], axis=-1)

def mla_attention(q_nope, q_rope, k_nope, k_rope, v):
    B, S, H, _ = q_nope.shape
    nq = S // Q_BLOCK
    scale = MLA_QK_DIM ** -0.5

    def blocks(t):
        return jnp.moveaxis(t.reshape((B, nq, Q_BLOCK) + t.shape[2:]), 1, 0)

    def one_block(args):
        qn, qr = args
        s = jnp.einsum('bqhd,bkhd->bhqk', qn, k_nope) + jnp.einsum('bqhr,bkr->bhqk', qr, k_rope)
        w = jax.nn.softmax(s.astype(jnp.float32) * scale, axis=-1).astype(v.dtype)
        return jnp.einsum('bhqk,bkhd->bqhd', w, v)

    out = lax.map(one_block, (blocks(q_nope), blocks(q_rope)))
    return jnp.moveaxis(out, 0, 1).reshape(B, S, H, v.shape[-1])

def banded_attention(q, k, v, radius):
    N, L, hd = q.shape
    blk = radius
    nb = -(-L // blk)
    lp = nb * blk
    qb = jnp.pad(q, ((0, 0), (0, lp - L), (0, 0))).reshape(N, nb, blk, hd)

    def windows(t):
        tp = jnp.pad(t, ((0, 0), (blk, lp - L + blk), (0, 0))).reshape(N, nb + 2, blk, hd)
        return jnp.concatenate([tp[:, :-2], tp[:, 1:-1], tp[:, 2:]], axis=2)

    kw, vw = windows(k), windows(v)
    qpos = jnp.arange(nb)[:, None] * blk + jnp.arange(blk)[None, :]
    kpos = jnp.arange(nb)[:, None] * blk - blk + jnp.arange(3 * blk)[None, :]
    kp = kpos[:, None, :]
    mask = (jnp.abs(qpos[:, :, None] - kp) <= radius) & (kp >= 0) & (kp < L)
    s = jnp.einsum('nbqd,nbkd->nbqk', qb, kw).astype(jnp.float32) * (hd ** -0.5)
    s = jnp.where(mask, s, NEG_INF)
    m = jnp.max(s, axis=-1, keepdims=True)
    e = jnp.exp(s - m)
    den = jnp.sum(e, axis=-1, keepdims=True)
    out = jnp.einsum('nbqk,nbkd->nbqd', (e / den).astype(v.dtype), vw)
    lse = (m + jnp.log(den))[..., 0]
    return out.reshape(N, lp, hd)[:, :L], lse.reshape(N, lp)[:, :L]

def dilated_pattern(q, k, v, window, dil):
    B, S, H, hd = q.shape
    L = S // dil

    def to_sub(t):
        return t.reshape(B, L, dil, H, hd).transpose(0, 2, 3, 1, 4).reshape(B * dil * H, L, hd)

    o, l = banded_attention(to_sub(q), to_sub(k), to_sub(v), window // (2 * dil))
    o = o.reshape(B, dil, H, L, hd).transpose(0, 3, 1, 2, 4).reshape(B, S, H, hd)
    l = l.reshape(B, dil, H, L).transpose(0, 3, 1, 2).reshape(B, S, H)
    return o, l

def dilated_attention(q, k, v):
    outs, lses = [], []
    for window, dil in DIL_PATTERNS:
        o, l = dilated_pattern(q, k, v, window, dil)
        outs.append(o)
        lses.append(l)
    wts = jax.nn.softmax(jnp.stack(lses, axis=0), axis=0).astype(q.dtype)
    return jnp.einsum('pbsh,pbshd->bshd', wts, jnp.stack(outs, axis=0))

def peer_ffn(xn, w_q, keys1, keys2, u_tab, v_tab):
    B, S, D = xn.shape
    T = B * S
    xt = xn.reshape(T, D)
    q = (xt @ w_q).reshape(T, PEER_HEADS, 2, PEER_HALF)
    s1 = jnp.einsum('thd,kd->thk', q[:, :, 0], keys1)
    s2 = jnp.einsum('thd,kd->thk', q[:, :, 1], keys2)
    v1, i1 = lax.top_k(s1, PEER_TOPK)
    v2, i2 = lax.top_k(s2, PEER_TOPK)
    cand = (v1[..., :, None] + v2[..., None, :]).reshape(T, PEER_HEADS, PEER_TOPK * PEER_TOPK)
    cidx = (i1[..., :, None] * PEER_KEYS + i2[..., None, :]).reshape(T, PEER_HEADS, PEER_TOPK * PEER_TOPK)
    top, pos = lax.top_k(cand, PEER_TOPK)
    eidx = jnp.take_along_axis(cidx, pos, axis=-1)
    g = jax.nn.softmax(top.astype(jnp.float32), axis=-1).astype(xn.dtype)
    nc = T // PEER_CHUNK

    def chunk(args):
        xc, ec, gc = args
        a = jax.nn.gelu(jnp.einsum('td,thkd->thk', xc, u_tab[ec]), approximate=False)
        return jnp.einsum('thk,thkd->td', gc * a, v_tab[ec])

    y = lax.map(chunk, (xt.reshape(nc, PEER_CHUNK, D),
                        eidx.reshape(nc, PEER_CHUNK, PEER_HEADS, PEER_TOPK),
                        g.reshape(nc, PEER_CHUNK, PEER_HEADS, PEER_TOPK)))
    return y.reshape(B, S, D)

def second_inputs(seed: int = 0) -> dict:
    key = jax.random.key(seed)
    ks = jax.random.split(key, 24)
    f32 = jnp.float32

    def nrm(k, shape, scale):
        return jax.random.normal(k, shape, f32) * scale

    def gain(k, shape):
        return 1.0 + 0.01 * jax.random.normal(k, shape, f32)

    L = DEPTH
    return {
        "x": nrm(ks[0], (BATCH, SEQ, D_MODEL), 1.0),
        "p": nrm(ks[1], (DEPTH, BATCH, SEQ, PLE_DIM), 1.0),
        "g_mix": gain(ks[2], (L, D_MODEL)),
        "w_in": nrm(ks[3], (L, D_MODEL, IN_WIDTH_2), D_MODEL ** -0.5),
        "g_cq": gain(ks[4], (L, MLA_Q_RANK)),
        "w_uq": nrm(ks[5], (L, MLA_Q_RANK, MLA_HEADS * MLA_QK_DIM), MLA_Q_RANK ** -0.5),
        "g_ckv": gain(ks[6], (L, MLA_KV_RANK)),
        "w_ukv": nrm(ks[7], (L, MLA_KV_RANK, MLA_HEADS * (MLA_NOPE_DIM + MLA_V_DIM)), MLA_KV_RANK ** -0.5),
        "g_out_mla": gain(ks[8], (L, MLA_WIDTH)),
        "g_out_dil": gain(ks[9], (L, DIL_WIDTH)),
        "w_out": nrm(ks[10], (L, MIX_WIDTH, D_MODEL), MIX_WIDTH ** -0.5),
        "g_ffn": gain(ks[11], (L, D_MODEL)),
        "w_peer_q": nrm(ks[12], (L, D_MODEL, PEER_HEADS * PEER_QDIM), D_MODEL ** -0.5),
        "peer_keys1": nrm(ks[13], (L, PEER_KEYS, PEER_HALF), PEER_HALF ** -0.5),
        "peer_keys2": nrm(ks[14], (L, PEER_KEYS, PEER_HALF), PEER_HALF ** -0.5),
        "peer_u": nrm(ks[15], (L, PEER_EXPERTS, D_MODEL), D_MODEL ** -0.5),
        "peer_v": nrm(ks[16], (L, PEER_EXPERTS, D_MODEL), 0.5),
        "g_ple": gain(ks[17], (L, D_MODEL)),
        "w_ple_gate": nrm(ks[18], (L, D_MODEL, D_MODEL), D_MODEL ** -0.5),
        "w_ple_proj": nrm(ks[19], (L, PLE_DIM, D_MODEL), PLE_DIM ** -0.5),
        "g_final": gain(ks[20], (D_MODEL,)),
    }

def second_block(x, p, g_mix, w_in, g_cq, w_uq, g_ckv, w_ukv, g_out_mla, g_out_dil, w_out,
              g_ffn, w_peer_q, peer_keys1, peer_keys2, peer_u, peer_v,
              g_ple, w_ple_gate, w_ple_proj, g_final):
    B, S, _ = x.shape
    cos_m, sin_m = rope_tables(S, MLA_ROPE_DIM)
    cos_d, sin_d = rope_tables(S, DIL_ROT_DIM)
    offs = np.cumsum(IN_SPLITS_2)[:-1].tolist()
    h = x
    for i in range(DEPTH):
        hn = rms_norm(h, g_mix[i])
        c_q, c_kv, k_r, q_d, k_d, v_d = jnp.split(hn @ w_in[i], offs, axis=-1)
        q = (rms_norm(c_q, g_cq[i]) @ w_uq[i]).reshape(B, S, MLA_HEADS, MLA_QK_DIM)
        q_nope = q[..., :MLA_NOPE_DIM]
        q_rope = apply_rope(q[..., MLA_NOPE_DIM:], cos_m, sin_m, MLA_ROPE_DIM)
        kv = (rms_norm(c_kv, g_ckv[i]) @ w_ukv[i]).reshape(B, S, MLA_HEADS, MLA_NOPE_DIM + MLA_V_DIM)
        k_nope = kv[..., :MLA_NOPE_DIM]
        v_m = kv[..., MLA_NOPE_DIM:]
        k_rope = apply_rope(k_r, cos_m, sin_m, MLA_ROPE_DIM)
        o_mla = mla_attention(q_nope, q_rope, k_nope, k_rope, v_m).reshape(B, S, MLA_WIDTH)
        qd = apply_rope(q_d.reshape(B, S, DIL_HEADS, DIL_HEAD_DIM), cos_d, sin_d, DIL_ROT_DIM)
        kd = apply_rope(k_d.reshape(B, S, DIL_HEADS, DIL_HEAD_DIM), cos_d, sin_d, DIL_ROT_DIM)
        vd = v_d.reshape(B, S, DIL_HEADS, DIL_HEAD_DIM)
        o_dil = dilated_attention(qd, kd, vd).reshape(B, S, DIL_WIDTH)
        mixed = jnp.concatenate([rms_norm(o_mla, g_out_mla[i]), rms_norm(o_dil, g_out_dil[i])], axis=-1)
        h = h + mixed @ w_out[i]
        h = h + peer_ffn(rms_norm(h, g_ffn[i]), w_peer_q[i], peer_keys1[i], peer_keys2[i],
                         peer_u[i], peer_v[i])
        gate = jax.nn.sigmoid(rms_norm(h, g_ple[i]) @ w_ple_gate[i])
        h = h + gate * (p[i] @ w_ple_proj[i])
    return rms_norm(h, g_final)


_first_inputs = second_inputs


def second_inputs(seed=0):
    import zlib

    import numpy as np

    out = dict(_first_inputs(seed))
    spreads = {}
    factors = {'g_cq': 4.061,
     'g_ckv': 3.209,
     'g_out_mla': 20.425,
     'g_out_dil': 19.89,
     'g_ffn': 13.693,
     'g_ple': 64.0,
     'g_final': 34.918}
    for name, (base, spread) in spreads.items():
        noise = np.random.default_rng([zlib.crc32(name.encode()), seed]).standard_normal(out[name].shape)
        drawn = base * np.exp(spread * noise) if base else spread * noise
        out[name] = __import__('jax').numpy.asarray(drawn.astype(out[name].dtype))
    for name, factor in factors.items():
        out[name] = (out[name] * factor).astype(out[name].dtype)
    return out


_narrow_inputs = second_inputs


def second_inputs(seed=0):

    out = dict(_narrow_inputs(seed))
    wider = {'g_out_mla': 3.7, 'g_out_dil': 3.8, 'g_ple': 12.0, 'g_final': 6.65}
    for name, times in wider.items():
        mean = out[name].mean()
        out[name] = (mean + times * (out[name] - mean)).astype(out[name].dtype)
    return out


def setup_inputs(seed=0):
    out = dict(first_inputs(seed))
    for name, value in second_inputs(seed + 1).items():
        if name != "x":
            out[name + "_2"] = value
    return out


def reference(
    x, c, ctx, c_ctx, w_ada, b_ada, norm_mix, norm_ffn, w_in, gla_lr_w, gla_lr_b, gla_norm,
    w_branch_gla, w_branch_ret, w_out, w_router_group, b_router_group, w_router_expert,
    b_router_expert, w_expert_gate, w_expert_up, w_expert_down, norm_final, p_2, g_mix_2,
    w_in_2, g_cq_2, w_uq_2, g_ckv_2, w_ukv_2, g_out_mla_2, g_out_dil_2, w_out_2, g_ffn_2,
    w_peer_q_2, peer_keys1_2, peer_keys2_2, peer_u_2, peer_v_2, g_ple_2, w_ple_gate_2,
    w_ple_proj_2, g_final_2,
):
    x = first_block(
        x, c, ctx, c_ctx, w_ada, b_ada, norm_mix, norm_ffn, w_in, gla_lr_w, gla_lr_b, gla_norm,
        w_branch_gla, w_branch_ret, w_out, w_router_group, b_router_group, w_router_expert,
        b_router_expert, w_expert_gate, w_expert_up, w_expert_down, norm_final,
    )
    return second_block(
        x, p_2, g_mix_2, w_in_2, g_cq_2, w_uq_2, g_ckv_2, w_ukv_2, g_out_mla_2, g_out_dil_2,
        w_out_2, g_ffn_2, w_peer_q_2, peer_keys1_2, peer_keys2_2, peer_u_2, peer_v_2, g_ple_2,
        w_ple_gate_2, w_ple_proj_2, g_final_2,
    )


_drawn_inputs = setup_inputs


def setup_inputs(seed=0):
    import zlib

    import numpy as np

    out = dict(_drawn_inputs(seed))
    spreads = {}
    factors = {}
    for name, (base, spread) in spreads.items():
        noise = np.random.default_rng([zlib.crc32(name.encode()), seed]).standard_normal(out[name].shape)
        drawn = base * np.exp(spread * noise) if base else spread * noise
        out[name] = __import__('jax').numpy.asarray(drawn.astype(out[name].dtype))
    for name, factor in factors.items():
        out[name] = (out[name] * factor).astype(out[name].dtype)
    return out
```

```python
from contextlib import ExitStack

import numpy as np
import concourse.bass as bass
from concourse import mybir

F32 = mybir.dt.float32
U32 = mybir.dt.uint32
I32 = mybir.dt.int32
ALU = mybir.AluOpType
ACT = mybir.ActivationFunctionType
AX = mybir.AxisListType

P = 128
D = 1024
KD = D // P
S = 512
NT = S // P
CT = 256
NCT = CT // P
TOK = S + CT
NCH = TOK // P
WBLK = 512
H1 = 4
DK = 128
DV = 256
EPS = 1e-6
NEG = -1e30

COLS = dict(norm_mix=8, norm_ffn=8, b_ada=48, gla_norm=2, gla_b=8, g_mix=8, g_cq=3, g_ckv=2, g_mla=4, g_dil=4,
            g_ffn=8, g_ple=8)
COL0 = {}
_at = 0
for _n, _w in COLS.items():
    COL0[_n] = _at
    _at += _w
NCOL = _at


class Env:

    def __init__(self, nc, ctx, dram):
        self.nc, self.ctx, self.dram = nc, ctx, dram
        self.turns = [0] * 8
        self.tile_no = 0
        self.blocks = []
        self.block_tile = {}
        self.issued = 0
        self.used = 0
        self.shared = {}

    def sb(self, name, shape, dt=F32):
        return self.ctx.enter_context(self.nc.sbuf_tensor(name, shape, dt))

    def sem(self, name):
        return self.ctx.enter_context(self.nc.semaphore(name))

    def again(self, name, n):
        if name not in self.shared:
            self.shared[name] = [self.sem(name), 0]
        sem, base = self.shared[name]
        self.shared[name][1] += n
        return sem, base

    def tile(self):
        b = self.tile_no % 8
        self.tile_no += 1
        n = self.turns[b]
        self.turns[b] += 1
        return b, n

    def tiles(self, n):
        return [self.tile() for _ in range(n)]

    def take_block(self, last_tile):
        b = self.used
        self.used += 1
        self.block_tile[b] = last_tile
        return b


def bank_ready(env, eng, t):
    if t[1] > 0:
        eng.wait_ge(env.bank_free[t[0]], t[1])


def product_done(env, eng, t):
    eng.wait_ge(env.bank_full[t[0]], t[1] + 1)


def evacuated(env, eng, t):
    eng.wait_ge(env.bank_free[t[0]], t[1] + 1)


def load_blocks(env, sp, ahead=2):
    nc = env.nc
    for b in range(env.issued, min(env.used + ahead, len(env.blocks))):
        if b >= 2:
            product_done(env, sp, env.block_tile[b - 2])
        nc.sync.dma_start(env.wring[:, b % 2, :], env.blocks[b]).then_inc(env.w_loaded[b % 2], 16)
        env.issued = b + 1


def block_view(env, pe, b):
    pe.wait_ge(env.w_loaded[b % 2], 16 * (b // 2 + 1))
    return env.wring[:, b % 2, :].rearrange("p (k n) -> p k n", k=KD)


class Chain:

    def __init__(self, sem):
        self.sem, self.n = sem, 0

    def __call__(self, eng, ins):
        self.n += 1
        ins.then_inc(self.sem, 1)
        eng.wait_ge(self.sem, self.n)


def col(env, name, j=0, n=1):
    return env.cols[:, COL0[name] + j:COL0[name] + j + n]


def stage_modulation(env):
    nc, dram = env.nc, env.dram
    tiles = env.tiles(12)
    blks = [env.take_block(t) for t in tiles]
    t_col = env.tile()
    t_bc = env.tiles(4)
    with ExitStack() as st:
        row = st.enter_context(nc.sbuf_tensor("ada_row", [2, 6 * D], F32))
        brow = st.enter_context(nc.sbuf_tensor("ada_brow", [1, 2 * D], F32))
        c2 = st.enter_context(nc.sbuf_tensor("c2", [P, KD, 2], F32))
        sc = st.enter_context(nc.sbuf_tensor("silu_c", [P, KD, 2], F32))
        c_in, c_act, b_in, cols_done = (env.sem(n) for n in ("c_in", "c_act", "b_in", "ada_cols_done"))
        with nc.Block() as block:
            @block.sync
            def _(sp):
                nc.sync.dma_start(c2[:], dram["c2"]).then_inc(c_in, 16)
                nc.sync.dma_start(env.ident[:], dram["ident"]).then_inc(env.const_in, 16)
                nc.sync.dma_start(env.cols[:], dram["cols"]).then_inc(env.const_in, 16)
                nc.sync.dma_start(env.h[:], dram["x"].rearrange("(t p) d -> p t d", p=P)).then_inc(env.x_in, 16)
                nc.sync.dma_start(env.hctx[:], dram["ctx"].rearrange("(t p) d -> p t d", p=P)).then_inc(env.x_in, 16)
                load_blocks(env, sp)
                nc.sync.dma_start(brow[:], dram["b_gates"]).then_inc(b_in, 16)

            @block.scalar
            def _(act):
                act.wait_ge(c_in, 16)
                nc.scalar.activation(sc[:], c2[:], ACT.Silu).then_inc(c_act, 1)
                for i, t in enumerate(tiles):
                    product_done(env, act, t)
                    nc.scalar.activation(row[:, i * WBLK:(i + 1) * WBLK], env.ps[0:2, t[0], :], ACT.Copy).then_inc(
                        env.bank_free[t[0]], 1)

            @block.vector
            def _(v):
                nc.vector.memset(env.ones[:], 1.0).then_inc(env.const_set, 1)
                nc.vector.memset(env.eps[:], EPS).then_inc(env.const_set, 1)
                v.wait_ge(env.const_in, 32)
                product_done(env, v, t_col)
                nc.vector.tensor_tensor(
                    env.ada[:], env.ps[:, t_col[0], 0:96].rearrange("p (j c) -> p j c", c=2),
                    col(env, "b_ada", 0, 48).unsqueeze(2).broadcast_to([P, 48, 2]), ALU.add).then_inc(
                    env.bank_free[t_col[0]], 1)
                evacuated(env, v, t_col)
                for n, (sc0, who, g) in enumerate(((8, 0, "norm_mix"), (8, 1, "norm_mix"), (32, 0, "norm_ffn"))):
                    nc.vector.scalar_tensor_tensor(env.gain[:, n, :], env.ada[:, sc0:sc0 + 8, who], 1.0,
                                                   col(env, g, 0, 8), ALU.add, ALU.mult).then_inc(cols_done, 1)
                for i, t in enumerate(t_bc):
                    product_done(env, v, t)
                    nc.vector.tensor_copy(env.gates[:, i // 2, (i % 2) * WBLK:(i % 2 + 1) * WBLK],
                                          env.ps[:, t[0], :]).then_inc(env.bank_free[t[0]], 1)
                v.wait_ge(cols_done, 3)

            @block.tensor
            def _(pe):
                pe.wait_ge(c_act, 1)
                for t, b in zip(tiles, blks):
                    w = block_view(env, pe, b)
                    bank_ready(env, pe, t)
                    for k in range(KD):
                        mm = nc.tensor.matmul(env.ps[0:2, t[0], :], sc[:, k, :], w[:, k, :],
                                              start=(k == 0), stop=(k == KD - 1))
                    mm.then_inc(env.bank_full[t[0]], 1)
                for t in tiles:
                    evacuated(env, pe, t)
                pe.wait_ge(env.const_in, 32)
                for j in range(48):
                    mm = nc.tensor.transpose(env.ps[:, t_col[0], 2 * j:2 * j + 2], row[:, j * P:(j + 1) * P],
                                             env.ident[0:2, 0:2])
                mm.then_inc(env.bank_full[t_col[0]], 1)
                pe.wait_ge(env.const_set, 2)
                pe.wait_ge(b_in, 16)
                for i, t in enumerate(t_bc):
                    bank_ready(env, pe, t)
                    at = (2 if i < 2 else 5) * D + (i % 2) * WBLK
                    nc.tensor.matmul(env.ps[:, t[0], :], env.ones[0:1, :], row[0:1, at:at + WBLK],
                                     start=True, stop=False)
                    nc.tensor.matmul(env.ps[:, t[0], :], env.ones[0:1, :], brow[0:1, i * WBLK:(i + 1) * WBLK],
                                     start=False, stop=True).then_inc(env.bank_full[t[0]], 1)


def stage_norm(env, name, src, parts, dst):
    nc = env.nc
    nt = sum(p[1] for p in parts)
    work = [(p, j, env.tile()) for p in parts for j in range(KD)]
    with ExitStack() as st:
        xn = st.enter_context(nc.sbuf_tensor(name + "_xn", [P, nt, D], F32))
        ss = st.enter_context(nc.sbuf_tensor(name + "_ss", [P, nt], F32))
        rs = st.enter_context(nc.sbuf_tensor(name + "_rs", [P, nt], F32))
        sq_done, sq0 = env.again("norm_sq", nt)
        rms_done, r0 = env.again("norm_rms", 1)
        inv_done, _ = env.again("norm_inv", 1)
        xn_done, xn0 = env.again("norm_xn", nt)
        with nc.Block() as block:
            @block.sync
            def _(sp):
                load_blocks(env, sp)

            @block.scalar
            def _(act):
                if name == "mix":
                    act.wait_ge(env.x_in, 32)
                for t in range(nt):
                    nc.scalar.activation(xn[:, t, :], src(t), ACT.Square, accum_out=ss[:, t:t + 1]).then_inc(sq_done, 1)
                act.wait_ge(sq_done, sq0 + nt)
                nc.scalar.activation(rs[:], ss[:], ACT.Sqrt, scale=1.0 / D, bias=env.eps[:, 0:1]).then_inc(rms_done, 1)

            @block.vector
            def _(v):
                v.wait_ge(rms_done, r0 + 1)
                nc.vector.reciprocal(ss[:], rs[:]).then_inc(inv_done, 1)
                v.wait_ge(inv_done, r0 + 1)
                for t in range(nt):
                    nc.vector.tensor_scalar(xn[:, t, :], src(t), ss[:, t:t + 1], None, ALU.mult).then_inc(xn_done, 1)
                for (t0, n, gain, shift), j, t in work:
                    product_done(env, v, t)
                    out, got = dst[:, j, t0 * P:(t0 + n) * P], env.ps[:, t[0], 0:n * P]
                    if shift is None:
                        ins = nc.vector.tensor_scalar(out, got, gain(j), None, ALU.mult)
                    else:
                        ins = nc.vector.tensor_scalar(out, got, gain(j), shift(j), ALU.mult, ALU.add)
                    ins.then_inc(env.bank_free[t[0]], 1)

            @block.tensor
            def _(pe):
                pe.wait_ge(env.const_in, 32)
                for (t0, n, _, _), j, t in work:
                    pe.wait_ge(xn_done, xn0 + t0 + n)
                    bank_ready(env, pe, t)
                    for i in range(n):
                        mm = nc.tensor.transpose(env.ps[:, t[0], i * P:(i + 1) * P],
                                                 xn[:, t0 + i, j * P:(j + 1) * P], env.ident[:])
                    mm.then_inc(env.bank_full[t[0]], 1)


def project(env, pe, t, out, w, lo, hi, rhs):
    bank_ready(env, pe, t)
    for k in range(KD):
        mm = env.nc.tensor.matmul(out, w[:, k, lo:hi], rhs(k), start=(k == 0), stop=(k == KD - 1))
    mm.then_inc(env.bank_full[t[0]], 1)


def chunks(ap):
    return ap.rearrange("p (c t) -> p c t", t=P)


def stage_gla_project(env, B):
    nc, dram = env.nc, env.dram
    hT = env.hT
    q_t = env.tiles(4)
    b_q = env.take_block(q_t[-1])
    k_t = [(j, lo, n, env.tile()) for j in range(4) for lo, n in ((0, S), (S, CT))]
    b_k = env.take_block(k_t[-1][3])
    v_t, b_v = [], []
    for half in range(2):
        v_t.append([(t, env.tile()) for t in range(NCH)])
        b_v.append(env.take_block(v_t[half][-1][1]))
    lr_t = [(d, lo, n, env.tile()) for d in range(2) for lo, n in ((0, S), (S, CT))]
    z_t = [(i, lo, n, env.tile()) for i in range(2 * H1) for lo, n in ((0, S), (S, CT))]
    lr_in, keep_set, e_done, ln_done, g_done, c_done = (
        env.sem(n) for n in ("lr_in", "keep_set", "gate_exp", "gate_ln", "gate_log", "gate_sum"))
    with ExitStack() as st:
        wlr = st.enter_context(nc.sbuf_tensor("wlr", [P, KD, 32], F32))
        lrw = st.enter_context(nc.sbuf_tensor("lrw", [16, 2, H1 * DK], F32))
        lr = st.enter_context(nc.sbuf_tensor("lr", [16, 2, TOK], F32))
        gate = st.enter_context(nc.sbuf_tensor("gate_log", [P, 2 * H1, TOK], F32))
        ea = B.sum
        keep = st.enter_context(nc.sbuf_tensor("keep", [P, TOK], F32))
        with nc.Block() as block:
            @block.sync
            def _(sp):
                nc.sync.dma_start(wlr[:], dram["w_lr"]).then_inc(lr_in, 16)
                nc.sync.dma_start(lrw[:], dram["gla_lr_w"].rearrange("d r n -> r d n")).then_inc(lr_in, 16)
                load_blocks(env, sp)

            @block.scalar
            def _(act):
                for j, t in enumerate(q_t):
                    product_done(env, act, t)
                    nc.scalar.activation(B.q[:, j, :], env.ps[:, t[0], :], ACT.Copy, scale=DK ** -0.5).then_inc(
                        env.bank_free[t[0]], 1)
                for half in range(2):
                    for i, t in v_t[half]:
                        product_done(env, act, t)
                        nc.scalar.activation(B.v[:, i, half * WBLK:(half + 1) * WBLK], env.ps[:, t[0], :],
                                             ACT.Copy).then_inc(env.bank_free[t[0]], 1)
                for n, (i, lo, w, t) in enumerate(z_t):
                    act.wait_ge(g_done, n + 1)
                    nc.scalar.activation(ea[:, i, lo:lo + w], env.ps[:, t[0], 0:w], ACT.Abs,
                                         bias=col(env, "gla_b", i)).then_inc(env.bank_free[t[0]], 1)
                for n, (i, lo, w, t) in enumerate(z_t):
                    evacuated(env, act, t)
                    nc.scalar.activation(ea[:, i, lo:lo + w], ea[:, i, lo:lo + w], ACT.Exp, scale=-1.0).then_inc(e_done, 1)
                act.wait_ge(e_done, len(z_t))
                for i in range(2 * H1):
                    nc.scalar.activation(ea[:, i, :], ea[:, i, :], ACT.Ln, bias=1.0).then_inc(ln_done, 1)

            @block.vector
            def _(v):
                nc.vector.memset(keep[:], 1.0).then_inc(keep_set, 1)
                v.wait_ge(keep_set, 1)
                nc.vector.memset(chunks(keep[:])[:, :, 0:1], 0.0).then_inc(keep_set, 1)
                for j, lo, n, t in k_t:
                    product_done(env, v, t)
                    nc.vector.tensor_copy(B.k[:, j, lo:lo + n], env.ps[:, t[0], 0:n]).then_inc(env.bank_free[t[0]], 1)
                for d, lo, n, t in lr_t:
                    product_done(env, v, t)
                    nc.vector.tensor_copy(lr[:, d, lo:lo + n], env.ps[0:16, t[0], 0:n]).then_inc(env.bank_free[t[0]], 1)
                m_done = 0
                for i, lo, n, t in z_t:
                    product_done(env, v, t)
                    b = col(env, "gla_b", i)
                    nc.vector.tensor_scalar(gate[:, i, lo:lo + n], env.ps[:, t[0], 0:n], b, 0.0,
                                            ALU.add, ALU.min).then_inc(g_done, 1)
                nz = len(z_t)
                v.wait_ge(g_done, nz)
                for i in range(2 * H1):
                    v.wait_ge(ln_done, i + 1)
                    nc.vector.tensor_tensor(gate[:, i, :], gate[:, i, :], ea[:, i, :], ALU.subtract).then_inc(g_done, 1)
                v.wait_ge(keep_set, 2)
                for i in range(2 * H1):
                    v.wait_ge(g_done, nz + i + 1)
                    nc.vector.tensor_tensor_scan(B.sum[:, i, :], keep[:], gate[:, i, :], 0.0,
                                                 ALU.mult, ALU.add).then_inc(c_done, 1)
                v.wait_ge(c_done, 2 * H1)
                ends = B.sum[:].rearrange("p i (c t) -> p i c t", t=P)[:, :, :, P - 1:P]
                nc.vector.tensor_copy(B.tot[:], ends.rearrange("p i c o -> p i (c o)")).then_inc(c_done, 1)
                v.wait_ge(c_done, 2 * H1 + 1)
                for i in range(H1, 2 * H1):
                    nc.vector.tensor_tensor(B.sum[:, i, :], gate[:, i, :], B.sum[:, i, :], ALU.subtract).then_inc(c_done, 1)

            @block.tensor
            def _(pe):
                w = block_view(env, pe, b_q)
                for j, t in enumerate(q_t):
                    project(env, pe, t, env.ps[:, t[0], :], w, j * P, (j + 1) * P, lambda k: hT[:, k, 0:S])
                w = block_view(env, pe, b_k)
                for j, lo, n, t in k_t:
                    project(env, pe, t, env.ps[:, t[0], 0:n], w, j * P, (j + 1) * P, lambda k: hT[:, k, lo:lo + n])
                for half in range(2):
                    w = block_view(env, pe, b_v[half])
                    for i, t in v_t[half]:
                        bank_ready(env, pe, t)
                        for k in range(KD):
                            mm = nc.tensor.matmul(env.ps[:, t[0], :], hT[:, k, i * P:(i + 1) * P], w[:, k, :],
                                                  start=(k == 0), stop=(k == KD - 1))
                        mm.then_inc(env.bank_full[t[0]], 1)
                pe.wait_ge(lr_in, 32)
                for d, lo, n, t in lr_t:
                    project(env, pe, t, env.ps[0:16, t[0], 0:n], wlr, 16 * d, 16 * d + 16, lambda k: hT[:, k, lo:lo + n])
                for _, _, _, t in lr_t:
                    evacuated(env, pe, t)
                for i, lo, n, t in z_t:
                    d, hd = i // H1, i % H1
                    bank_ready(env, pe, t)
                    nc.tensor.matmul(env.ps[:, t[0], 0:n], lrw[:, d, hd * DK:(hd + 1) * DK], lr[:, d, lo:lo + n],
                                     start=True, stop=True).then_inc(env.bank_full[t[0]], 1)


def stage_gla_core(env, B, oT):
    nc = env.nc
    G = 1.0 / 16.0
    walk = [[4, 5, 0, 1, 2], [5, 4, 3, 2, 1]]
    entry = [{0: 2, 1: 3, 2: 4, 3: 5}, {3: 2, 2: 3, 1: 4, 0: 5}]
    plan = []
    for hd in range(H1):
        tr = [env.tiles(2) for d in range(2)]
        up = [[env.tile() for _ in range(5)] for d in range(2)]
        sc = [env.tile() for _ in range(NT)]
        ov = [env.tile() for _ in range(NT)]
        plan.append((tr, up, sc, ov))
    fin = [env.tile() for _ in range(2 * H1)]
    names = ("g_arg", "g_exp", "g_mul", "g_dec", "g_zero", "g_sq", "g_rms", "g_inv", "g_nrm")
    arg_s, exp_s, mul_s, dec_s, zero_s, sq_s, rms_s, inv_s, nrm_s = (env.sem(n) for n in names)
    with ExitStack() as stk:
        T = lambda n, s: stk.enter_context(nc.sbuf_tensor("g_" + n, s, F32))
        arg = T("argt", [P, 2, S])
        e1, e3 = T("e1", [P, 2, S]), T("e3", [P, 2, S])
        e2 = arg
        e4 = T("e4", [P, 2, TOK])
        ktok = T("ktok", [P, 2, 5, DK])
        st = T("state", [P, 2, 6, DV])
        dec = T("decay", [P, 2 * H1, NCH])
        pm = T("pm", [P, 2, 2, P])
        o = T("o", [P, NT, H1, DV])
        sq = T("sqs", [P, DV])
        ss, rs = T("ss", [P, NT * H1]), T("rs", [P, NT * H1])
        mask = T("mask", [P, 2, P])
        mask_in = env.sem("g_mask_in")
        with nc.Block() as block:
            @block.sync
            def _(sp):
                nc.sync.dma_start(mask[:], env.dram["chunk_mask"]).then_inc(mask_in, 16)
                load_blocks(env, sp)

            @block.vector
            def _(v):
                nc.vector.memset(st[:, :, 0, :], 0.0).then_inc(zero_s, 1)
                v.wait_ge(dec_s, 1)
                v.wait_ge(zero_s, 1)
                for hd in range(H1):
                    tr, up, sc, ov = plan[hd]
                    if hd >= 1:
                        product_done(env, v, plan[hd - 1][3][-1])
                    for d in range(2):
                        c = B.sum[:, d * H1 + hd, :]
                        mid = chunks(c[:, 0:S])[:, :, 63 + d:64 + d].broadcast_to([P, NT, P])
                        nc.vector.tensor_tensor(chunks(arg[:, d, :]), chunks(c[:, 0:S]), mid, ALU.subtract).then_inc(arg_s, 1)
                        tot = B.tot[:, d * H1 + hd, :]
                        if d == 0:
                            nc.vector.tensor_tensor(chunks(e4[:, 0, :]), tot.unsqueeze(2).broadcast_to([P, NCH, P]),
                                                    chunks(c), ALU.subtract).then_inc(arg_s, 1)
                        else:
                            nc.vector.tensor_tensor(chunks(e3[:, 1, :]), chunks(c[:, 0:S]),
                                                    tot[:, 0:NT].unsqueeze(2).broadcast_to([P, NT, P]),
                                                    ALU.add).then_inc(arg_s, 1)
                    for d in range(2):
                        v.wait_ge(exp_s, 8 * hd + 4 * (d + 1))
                        for e, x in ((e1[:, d, :], B.q[:, hd, :]), (e2[:, d, :], B.k[:, hd, 0:S]),
                                     (e3[:, d, :], B.q[:, hd, :]), (e4[:, d, :], B.k[:, hd, :])):
                            nc.vector.tensor_tensor(e, e, x, ALU.mult).then_inc(mul_s, 1)
                    for d in range(2):
                        if hd >= 1:
                            product_done(env, v, plan[hd - 1][3][-1])
                        for n in range(5):
                            t = up[d][n]
                            product_done(env, v, t)
                            if n >= 1:
                                evacuated(env, v, up[d][n - 1])
                            i, ch = d * H1 + hd, walk[d][n]
                            nc.vector.scalar_tensor_tensor(st[:, d, n + 1, :], st[:, d, n, :], dec[:, i, ch:ch + 1],
                                                           env.ps[:, t[0], 0:DV], ALU.mult, ALU.add).then_inc(
                                env.bank_free[t[0]], 1)
                    v.wait_ge(mask_in, 16)
                    for ch in range(NT):
                        t = sc[ch]
                        product_done(env, v, t)
                        if hd * NT + ch >= 2:
                            pt = plan[hd][3][ch - 2] if ch >= 2 else plan[hd - 1][3][ch + 2]
                            product_done(env, v, pt)
                        nc.vector.tensor_tensor(pm[:, ch % 2, :, :],
                                                env.ps[:, t[0], 0:2 * P].rearrange("p (d t) -> p d t", d=2),
                                                mask[:], ALU.mult).then_inc(env.bank_free[t[0]], 1)
                v.wait_ge(rms_s, 1)
                nc.vector.reciprocal(ss[:], rs[:]).then_inc(inv_s, 1)
                v.wait_ge(inv_s, 1)
                for hd in range(H1):
                    for ch in range(NT):
                        n = hd * NT + ch
                        nc.vector.tensor_scalar(o[:, ch, hd, :], o[:, ch, hd, :], ss[:, n:n + 1], None,
                                                ALU.mult).then_inc(nrm_s, 1)
                for j, t in enumerate(fin):
                    product_done(env, v, t)
                    nc.vector.tensor_scalar(oT[:, j, :], env.ps[:, t[0], :], col(env, "gla_norm", j % 2), None,
                                            ALU.mult).then_inc(env.bank_free[t[0]], 1)

            @block.scalar
            def _(act):
                nc.scalar.activation(dec[:], B.tot[:], ACT.Exp, scale=G).then_inc(dec_s, 1)
                for hd in range(H1):
                    tr, up, sc, ov = plan[hd]
                    for d in range(2):
                        act.wait_ge(arg_s, 4 * hd + 2 * (d + 1))
                        c = B.sum[:, d * H1 + hd, :]
                        nc.scalar.activation(e1[:, d, :], arg[:, d, :], ACT.Exp, scale=G).then_inc(exp_s, 1)
                        nc.scalar.activation(e2[:, d, :], arg[:, d, :], ACT.Exp, scale=-G).then_inc(exp_s, 1)
                        if d == 0:
                            nc.scalar.activation(e3[:, 0, :], c[:, 0:S], ACT.Exp, scale=G).then_inc(exp_s, 1)
                            nc.scalar.activation(e4[:, 0, :], e4[:, 0, :], ACT.Exp, scale=G).then_inc(exp_s, 1)
                        else:
                            nc.scalar.activation(e3[:, 1, :], e3[:, 1, :], ACT.Exp, scale=G).then_inc(exp_s, 1)
                            nc.scalar.activation(e4[:, 1, :], c, ACT.Exp, scale=-G).then_inc(exp_s, 1)
                    for d in range(2):
                        for part, (lo, n) in enumerate(((0, 4), (4, 1))):
                            t = tr[d][part]
                            product_done(env, act, t)
                            if hd >= 1 and part == 0:
                                product_done(env, act, plan[hd - 1][1][d][4])
                            nc.scalar.activation(ktok[:, d, lo:lo + n, :],
                                                 env.ps[:, t[0], 0:n * P].rearrange("p (n k) -> p n k", k=DK),
                                                 ACT.Copy).then_inc(env.bank_free[t[0]], 1)
                    for ch in range(NT):
                        t = ov[ch]
                        n = hd * NT + ch
                        product_done(env, act, t)
                        if n >= 1:
                            act.wait_ge(sq_s, n)
                        nc.scalar.activation(sq[:], env.ps[:, t[0], 0:DV], ACT.Square, accum_out=ss[:, n:n + 1]).then_inc(sq_s, 1)
                        nc.scalar.activation(o[:, ch, hd, :], env.ps[:, t[0], 0:DV], ACT.Copy).then_inc(env.bank_free[t[0]], 1)
                act.wait_ge(sq_s, NT * H1)
                nc.scalar.activation(rs[:], ss[:], ACT.Sqrt, scale=1.0 / DV, bias=env.eps[:, 0:1]).then_inc(rms_s, 1)

            @block.tensor
            def _(pe):
                for hd in range(H1):
                    tr, up, sc, ov = plan[hd]
                    for d in range(2):
                        pe.wait_ge(mul_s, 8 * hd + 4 * (d + 1))
                        for part, (lo, n) in enumerate(((0, 4), (4, 1))):
                            t = tr[d][part]
                            bank_ready(env, pe, t)
                            for i in range(n):
                                ch = walk[d][lo + i]
                                mm = nc.tensor.transpose(env.ps[:, t[0], i * P:(i + 1) * P],
                                                         e4[:, d, ch * P:(ch + 1) * P], env.ident[:])
                            mm.then_inc(env.bank_full[t[0]], 1)
                    for d in range(2):
                        for n in range(5):
                            t, ch = up[d][n], walk[d][n]
                            evacuated(env, pe, tr[d][0 if n < 4 else 1])
                            bank_ready(env, pe, t)
                            nc.tensor.matmul(env.ps[:, t[0], 0:DV], ktok[:, d, n, :], B.v[:, ch, hd * DV:(hd + 1) * DV],
                                             start=True, stop=True).then_inc(env.bank_full[t[0]], 1)
                    for ch in range(NT):
                        t, cs = sc[ch], slice(ch * P, (ch + 1) * P)
                        bank_ready(env, pe, t)
                        for d in range(2):
                            mm = nc.tensor.matmul(env.ps[:, t[0], d * P:(d + 1) * P], e2[:, d, cs], e1[:, d, cs],
                                                  start=True, stop=True)
                        mm.then_inc(env.bank_full[t[0]], 1)
                    for ch in range(NT):
                        t, cs = ov[ch], slice(ch * P, (ch + 1) * P)
                        for d in range(2):
                            evacuated(env, pe, up[d][entry[d][ch] - 1])
                        evacuated(env, pe, sc[ch])
                        bank_ready(env, pe, t)
                        out = env.ps[:, t[0], 0:DV]
                        for d in range(2):
                            nc.tensor.matmul(out, e3[:, d, cs], st[:, d, entry[d][ch], :], start=(d == 0), stop=False)
                        for d in range(2):
                            mm = nc.tensor.matmul(out, pm[:, ch % 2, d, :], B.v[:, ch, hd * DV:(hd + 1) * DV],
                                                  start=False, stop=(d == 1))
                        mm.then_inc(env.bank_full[t[0]], 1)
                to_features(env, pe, fin, lambda ch, j: o[:, ch, j // 2, (j % 2) * P:(j % 2 + 1) * P],
                            lambda ch, j: pe.wait_ge(nrm_s, (j // 2) * NT + ch + 1))


def to_features(env, pe, tiles, src, wait):
    for j, t in enumerate(tiles):
        bank_ready(env, pe, t)
        for ch in range(NT):
            wait(ch, j)
            mm = env.nc.tensor.transpose(env.ps[:, t[0], ch * P:(ch + 1) * P], src(ch, j), env.ident[:])
        mm.then_inc(env.bank_full[t[0]], 1)


def stage_branch(env, name, oT, yT, first):
    nc, hT = env.nc, env.hT
    g_t = env.tiles(8)
    b_g = [env.take_block(g_t[3]), env.take_block(g_t[7])]
    m_t = env.tiles(8)
    b_m = [env.take_block(m_t[3]), env.take_block(m_t[7])]
    y_t = env.tiles(8)
    b_y = [env.take_block(y_t[3]), env.take_block(y_t[7])]
    mul_s, y_s = env.sem(name + "_gated"), env.sem(name + "_merged")
    with ExitStack() as st:
        gate = st.enter_context(nc.sbuf_tensor(name + "_gate", [P, KD, S], F32))
        merge = st.enter_context(nc.sbuf_tensor(name + "_merge", [P, KD, S], F32))
        with nc.Block() as block:
            @block.sync
            def _(sp):
                load_blocks(env, sp)

            @block.scalar
            def _(act):
                for j, t in enumerate(g_t):
                    product_done(env, act, t)
                    nc.scalar.activation(gate[:, j, :], env.ps[:, t[0], :], ACT.Silu).then_inc(env.bank_free[t[0]], 1)
                for j, t in enumerate(m_t):
                    product_done(env, act, t)
                    nc.scalar.activation(merge[:, j, :], env.ps[:, t[0], :], ACT.Sigmoid).then_inc(env.bank_free[t[0]], 1)

            @block.vector
            def _(v):
                for j, t in enumerate(g_t):
                    evacuated(env, v, t)
                    nc.vector.tensor_tensor(oT[:, j, :], oT[:, j, :], gate[:, j, :], ALU.mult).then_inc(mul_s, 1)
                for j, t in enumerate(y_t):
                    product_done(env, v, t)
                    evacuated(env, v, m_t[j])
                    out = yT[:, j, :] if first else merge[:, j, :]
                    nc.vector.tensor_tensor(out, merge[:, j, :], env.ps[:, t[0], :], ALU.mult).then_inc(
                        env.bank_free[t[0]], 1)
                    if not first:
                        evacuated(env, v, t)
                        nc.vector.tensor_tensor(yT[:, j, :], yT[:, j, :], merge[:, j, :], ALU.add).then_inc(y_s, 1)

            @block.tensor
            def _(pe):
                for tl, bl in ((g_t, b_g), (m_t, b_m)):
                    for i, b in enumerate(bl):
                        w = block_view(env, pe, b)
                        for j in range(4):
                            t = tl[4 * i + j]
                            project(env, pe, t, env.ps[:, t[0], :], w, j * P, (j + 1) * P, lambda k: hT[:, k, 0:S])
                pe.wait_ge(mul_s, KD)
                for i, b in enumerate(b_y):
                    w = block_view(env, pe, b)
                    for j in range(4):
                        t = y_t[4 * i + j]
                        project(env, pe, t, env.ps[:, t[0], :], w, j * P, (j + 1) * P, lambda k: oT[:, k, :])


def rope_mm(env, pe, tiles, perm, raw, ready):
    for j, t in enumerate(tiles):
        ready(j)
        bank_ready(env, pe, t)
        x = raw(j)
        env.nc.tensor.matmul(env.ps[0:x.shape[0], t[0], :], perm, x, start=True, stop=True).then_inc(env.bank_full[t[0]], 1)


def rope_dve(env, v, tiles, x, tab, sn, cos_s, rope_s):
    nc = env.nc
    for j, t in enumerate(tiles):
        a = x(j)
        rows = a.shape[0]
        product_done(env, v, t)
        nc.vector.tensor_tensor(a, a, tab[0:rows, 0, :], ALU.mult).then_inc(cos_s, 1)
        if j >= 2:
            v.wait_ge(rope_s, j - 1)
        nc.vector.tensor_tensor(sn[0:rows, j % 2, :], env.ps[0:rows, t[0], :], tab[0:rows, 1, :], ALU.mult).then_inc(
            env.bank_free[t[0]], 1)
        v.wait_ge(cos_s, j + 1)
        evacuated(env, v, t)
        nc.vector.tensor_tensor(a, a, sn[0:rows, j % 2, :], ALU.add).then_inc(rope_s, 1)


def stage_ret_project(env, R):
    nc, hT, dram = env.nc, env.hT, env.dram
    q_t = env.tiles(4)
    b_q = env.take_block(q_t[-1])
    k_t = env.tiles(4)
    kc_t = env.tiles(NCT)
    b_k = env.take_block(kc_t[-1])
    r_t = env.tiles(8)
    v_t, b_v = [], []
    for half in range(2):
        v_t.append(env.tiles(NCH))
        b_v.append(env.take_block(v_t[half][-1]))
    tab_in, cos_s, rope_s = env.sem("ret_tab_in"), env.sem("ret_cos"), env.sem("ret_rope")
    with ExitStack() as st:
        sn = st.enter_context(nc.sbuf_tensor("r_sn", [P, 2, S], F32))
        tab = st.enter_context(nc.sbuf_tensor("r_tab", [P, 2, S], F32))
        perm = st.enter_context(nc.sbuf_tensor("r_perm", [P, P], F32))
        with nc.Block() as block:
            @block.sync
            def _(sp):
                nc.sync.dma_start(tab[:], dram["rope_axial"]).then_inc(tab_in, 16)
                nc.sync.dma_start(perm[:], dram["perm_axial"]).then_inc(tab_in, 16)
                load_blocks(env, sp)

            @block.scalar
            def _(act):
                for j, t in enumerate(q_t + k_t):
                    product_done(env, act, t)
                    nc.scalar.activation(R.qk[:, j, :], env.ps[:, t[0], :], ACT.Copy).then_inc(env.bank_free[t[0]], 1)
                for i, t in enumerate(kc_t):
                    product_done(env, act, t)
                    nc.scalar.activation(R.kc[:, i, :], env.ps[:, t[0], :], ACT.Copy).then_inc(env.bank_free[t[0]], 1)
                for half in range(2):
                    for i, t in enumerate(v_t[half]):
                        product_done(env, act, t)
                        nc.scalar.activation(R.v[:, i, half * WBLK:(half + 1) * WBLK], env.ps[:, t[0], :],
                                             ACT.Copy).then_inc(env.bank_free[t[0]], 1)

            @block.vector
            def _(v):
                v.wait_ge(tab_in, 32)
                rope_dve(env, v, r_t, lambda j: R.qk[:, j, :], tab, sn, cos_s, rope_s)

            @block.tensor
            def _(pe):
                w = block_view(env, pe, b_q)
                for j, t in enumerate(q_t):
                    project(env, pe, t, env.ps[:, t[0], :], w, j * P, (j + 1) * P, lambda k: hT[:, k, 0:S])
                w = block_view(env, pe, b_k)
                for j, t in enumerate(k_t):
                    project(env, pe, t, env.ps[:, t[0], :], w, j * P, (j + 1) * P, lambda k: hT[:, k, 0:S])
                for i, t in enumerate(kc_t):
                    by_token(env, pe, t, WBLK, w, NT + i)
                pe.wait_ge(tab_in, 32)
                rope_mm(env, pe, r_t, perm[:], lambda j: R.qk[:, j, :], lambda j: evacuated(env, pe, (q_t + k_t)[j]))
                for half in range(2):
                    w = block_view(env, pe, b_v[half])
                    for i, t in enumerate(v_t[half]):
                        by_token(env, pe, t, WBLK, w, i)


def by_token(env, pe, t, n, w, i, lo=0):
    bank_ready(env, pe, t)
    for k in range(KD):
        mm = env.nc.tensor.matmul(env.ps[:, t[0], 0:n], env.hT[:, k, i * P:(i + 1) * P], w[:, k, lo:lo + n],
                                  start=(k == 0), stop=(k == KD - 1))
    mm.then_inc(env.bank_full[t[0]], 1)


def stage_ret_core(env, R, oT):
    nc, dram = env.nc, env.dram
    st_t = [[env.tile() for d in range(2)] for hd in range(H1)]
    plan = [([env.tile() for _ in range(NT)], [env.tile() for _ in range(NT)]) for hd in range(H1)]
    fin = env.tiles(2 * H1)
    in_s, kd_s, qd_s, bn_s, mv_s, rms_s, inv_s, nrm_s, o_s = (env.sem("rc_" + n) for n in (
        "in", "kd", "qd", "bn", "mv", "rms", "inv", "nrm", "o"))
    qdec_in = [env.sem(f"rc_qdec_in{i}") for i in range(2)]
    with ExitStack() as stk:
        T = lambda n, s: stk.enter_context(nc.sbuf_tensor("rc_" + n, s, F32))
        band = T("band", [P, H1, 896])
        qdec = T("qdec", [P, 2, 2, S])
        kdec = T("kdec", [P, 2 * H1, NCT])
        kd = T("kd", [P, 2, 2, NCT, DK])
        st = T("st", [P, H1, 2, DV])
        qd = T("qd", [P, 2, S])
        pm = T("pm", [P, NT, S])
        o = T("o", [P, NT, H1, DV])
        bn = T("bn", [P, NT * H1, 6])
        mv = T("mv", [P, NT * H1, 2])
        rs = T("rs", [P, NT * H1, 1])
        iv = T("iv", [P, NT * H1, 1])
        with nc.Block() as block:
            @block.sync
            def _(sp):
                nc.sync.dma_start(kdec[:], dram["ret_kdec"]).then_inc(in_s, 16)
                nc.sync.dma_start(band[:], dram["ret_band"]).then_inc(in_s, 16)
                for hd in range(H1):
                    if hd >= 2:
                        sp.wait_ge(qd_s, 2 * (hd - 1))
                    row = dram["ret_qdec"][hd:hd + 1].broadcast_to([P, 2, S])
                    nc.sync.dma_start(qdec[:, hd % 2], row).then_inc(qdec_in[hd % 2], 16)
                load_blocks(env, sp)

            @block.vector
            def _(v):
                v.wait_ge(in_s, 32)
                for hd in range(H1):
                    for d in range(2):
                        if hd >= 2:
                            product_done(env, v, st_t[hd - 2][d])
                        for i in range(NCT):
                            nc.vector.tensor_scalar(kd[:, hd % 2, d, i, :], R.kc[:, i, hd * DK:(hd + 1) * DK],
                                                    kdec[:, d * H1 + hd, i:i + 1], None, ALU.mult).then_inc(kd_s, 1)
                for hd in range(H1):
                    sc, ov = plan[hd]
                    if hd >= 1:
                        product_done(env, v, plan[hd - 1][1][-1])
                    v.wait_ge(qdec_in[hd % 2], 16 * (hd // 2 + 1))
                    for d in range(2):
                        nc.vector.tensor_tensor(qd[:, d, :], R.qk[:, hd, :], qdec[:, hd % 2, d, :], ALU.mult).then_inc(qd_s, 1)
                    for J, t in enumerate(sc):
                        product_done(env, v, t)
                        nc.vector.tensor_tensor(pm[:, J, :], env.ps[:, t[0], :], band[:, hd, 384 - J * P:384 - J * P + S],
                                                ALU.mult).then_inc(env.bank_free[t[0]], 1)
                    for I, t in enumerate(ov):
                        product_done(env, v, t)
                        nc.vector.bn_stats(bn[:, hd * NT + I, :], env.ps[:, t[0], 0:DV]).then_inc(bn_s, 1)
                for n in range(NT * H1):
                    v.wait_ge(bn_s, n + 1)
                    nc.vector.bn_aggr(mv[:, n, :], bn[:, n, :]).then_inc(mv_s, 1)
                v.wait_ge(rms_s, 1)
                nc.vector.reciprocal(iv[:], rs[:]).then_inc(inv_s, 1)
                v.wait_ge(inv_s, 1)
                v.wait_ge(o_s, NT * H1)
                for hd in range(H1):
                    for I in range(NT):
                        n = hd * NT + I
                        nc.vector.tensor_scalar(o[:, I, hd, :], o[:, I, hd, :], mv[:, n, 0:1], iv[:, n, :],
                                                ALU.subtract, ALU.mult).then_inc(nrm_s, 1)
                for j, t in enumerate(fin):
                    product_done(env, v, t)
                    nc.vector.tensor_copy(oT[:, j, :], env.ps[:, t[0], :]).then_inc(env.bank_free[t[0]], 1)

            @block.scalar
            def _(act):
                for hd in range(H1):
                    for d in range(2):
                        t = st_t[hd][d]
                        product_done(env, act, t)
                        nc.scalar.activation(st[:, hd, d, :], env.ps[:, t[0], 0:DV], ACT.Copy).then_inc(env.bank_free[t[0]], 1)
                for hd in range(H1):
                    for I, t in enumerate(plan[hd][1]):
                        act.wait_ge(bn_s, hd * NT + I + 1)
                        nc.scalar.activation(o[:, I, hd, :], env.ps[:, t[0], 0:DV], ACT.Copy).then_inc(env.bank_free[t[0]], 1)
                for hd in range(H1):
                    for t in plan[hd][1]:
                        evacuated(env, act, t)
                act.wait_ge(mv_s, NT * H1)
                nc.scalar.activation(rs[:], mv[:, :, 1:2], ACT.Sqrt, bias=env.eps[:, 0:1]).then_inc(rms_s, 1)
                nc.scalar.sem_inc(o_s, NT * H1)

            @block.tensor
            def _(pe):
                for hd in range(H1):
                    for d in range(2):
                        t = st_t[hd][d]
                        pe.wait_ge(kd_s, hd * 4 + d * 2 + 2)
                        bank_ready(env, pe, t)
                        for i in range(NCT):
                            mm = nc.tensor.matmul(env.ps[:, t[0], 0:DV], kd[:, hd % 2, d, i, :],
                                                  R.v[:, NT + i, hd * DV:(hd + 1) * DV], start=(i == 0), stop=(i == NCT - 1))
                        mm.then_inc(env.bank_full[t[0]], 1)
                for hd in range(H1):
                    sc, ov = plan[hd]
                    for J, t in enumerate(sc):
                        bank_ready(env, pe, t)
                        nc.tensor.matmul(env.ps[:, t[0], :], R.qk[:, 4 + hd, J * P:(J + 1) * P], R.qk[:, hd, :],
                                         start=True, stop=True).then_inc(env.bank_full[t[0]], 1)
                    pe.wait_ge(qd_s, 2 * (hd + 1))
                    for d in range(2):
                        evacuated(env, pe, st_t[hd][d])
                    for I, t in enumerate(ov):
                        bank_ready(env, pe, t)
                        out, ts = env.ps[:, t[0], 0:DV], slice(I * P, (I + 1) * P)
                        for d in range(2):
                            nc.tensor.matmul(out, qd[:, d, ts], st[:, hd, d, :], start=(d == 0), stop=False)
                        for J in range(NT):
                            evacuated(env, pe, sc[J])
                            mm = nc.tensor.matmul(out, pm[:, J, ts], R.v[:, J, hd * DV:(hd + 1) * DV],
                                                  start=False, stop=(J == NT - 1))
                        mm.then_inc(env.bank_full[t[0]], 1)
                to_features(env, pe, fin, lambda ch, j: o[:, ch, j // 2, (j % 2) * P:(j % 2 + 1) * P],
                            lambda ch, j: pe.wait_ge(nrm_s, (j // 2) * NT + ch + 1))


def stage_out(env, name, src, gate):
    nc = env.nc
    tl = [env.tiles(NT) for _ in range(2)]
    bl = [env.take_block(t[-1]) for t in tl]
    g_s = env.sem(name + "_sum")
    with ExitStack() as st:
        tmp = st.enter_context(nc.sbuf_tensor(name + "_tmp", [P, 2 * NT, WBLK], F32))
        with nc.Block() as block:
            @block.sync
            def _(sp):
                load_blocks(env, sp)

            @block.vector
            def _(v):
                for half in range(2):
                    cs = slice(half * WBLK, (half + 1) * WBLK)
                    for i, t in enumerate(tl[half]):
                        product_done(env, v, t)
                        got = env.ps[:, t[0], :]
                        if gate is None:
                            nc.vector.tensor_tensor(env.h[:, i, cs], env.h[:, i, cs], got, ALU.add).then_inc(
                                env.bank_free[t[0]], 1)
                        else:
                            x = tmp[:, half * NT + i, :]
                            nc.vector.tensor_tensor(x, env.gates[:, gate, cs], got, ALU.mult).then_inc(env.bank_free[t[0]], 1)
                            evacuated(env, v, t)
                            nc.vector.tensor_tensor(env.h[:, i, cs], env.h[:, i, cs], x, ALU.add).then_inc(g_s, 1)

            @block.tensor
            def _(pe):
                for half in range(2):
                    w = block_view(env, pe, bl[half])
                    for i, t in enumerate(tl[half]):
                        bank_ready(env, pe, t)
                        for k in range(KD):
                            mm = nc.tensor.matmul(env.ps[:, t[0], :], src[:, k, i * P:(i + 1) * P], w[:, k, :],
                                                  start=(k == 0), stop=(k == KD - 1))
                        mm.then_inc(env.bank_full[t[0]], 1)


def stage_rownorm(env, name, dst, row_name, store=None):
    nc = env.nc
    row_in, run16 = env.again("row_in", 16)
    run = run16 // 16
    sq_s, sq0 = env.again("row_sq", NT)
    rms_s, _ = env.again("row_rms", 1)
    inv_s, _ = env.again("row_inv", 1)
    done, d0 = env.again("row_done", NT)
    out_s, _ = env.again("row_out", 0)
    with ExitStack() as st:
        row = st.enter_context(nc.sbuf_tensor(name + "_row", [P, D], F32))
        sq = st.enter_context(nc.sbuf_tensor(name + "_sqs", [P, 2, D], F32))
        ss = st.enter_context(nc.sbuf_tensor(name + "_ss", [P, NT], F32))
        rs = st.enter_context(nc.sbuf_tensor(name + "_rs", [P, NT], F32))
        with nc.Block() as block:
            @block.sync
            def _(sp):
                nc.sync.dma_start(row[:], env.dram[row_name].broadcast_to([P, D])).then_inc(row_in, 16)
                load_blocks(env, sp)
                if store is not None:
                    rows = store.rearrange("(t p) d -> t p d", p=P)
                    for t in range(NT):
                        sp.wait_ge(done, d0 + t + 1)
                        nc.sync.dma_start(rows[t], dst[:, t, :]).then_inc(out_s, 16)
                    sp.wait_ge(out_s, 16 * NT)

            @block.scalar
            def _(act):
                for t in range(NT):
                    if t >= 2:
                        act.wait_ge(sq_s, sq0 + t - 1)
                    nc.scalar.activation(sq[:, t % 2, :], env.h[:, t, :], ACT.Square, accum_out=ss[:, t:t + 1]).then_inc(sq_s, 1)
                act.wait_ge(sq_s, sq0 + NT)
                nc.scalar.activation(rs[:], ss[:], ACT.Sqrt, scale=1.0 / D, bias=env.eps[:, 0:1]).then_inc(rms_s, 1)

            @block.vector
            def _(v):
                v.wait_ge(rms_s, run + 1)
                nc.vector.reciprocal(ss[:], rs[:]).then_inc(inv_s, 1)
                v.wait_ge(row_in, run16 + 16)
                v.wait_ge(inv_s, run + 1)
                for t in range(NT):
                    nc.vector.scalar_tensor_tensor(dst[:, t, :], env.h[:, t, :], ss[:, t:t + 1], row[:],
                                                   ALU.mult, ALU.mult).then_inc(done, 1)


NG, EPG = 4, 8
NE = NG * EPG
EF = 256
EFT = EF // P
NR = NG + NE
EW = KD * 2 * EF + EFT * D


def stage_router(env, wgt):
    nc, dram = env.nc, env.dram
    t_lg = env.tile()
    in_s, exp_s, ch_s, pair_s = (env.sem("rt_" + n) for n in ("in", "exp", "chain", "pair"))
    with ExitStack() as st:
        T = lambda n, s, d=F32: st.enter_context(nc.sbuf_tensor("rt_" + n, s, d))
        wr, br = T("w", [P, KD, NR]), T("b", [1, NR])
        idx = T("idx", [P, 2, NE])
        lg, gp = T("lg", [P, NT, NR]), T("gp", [P, NT, 8])
        gm, gi, gif = T("gm", [P, NT, 8]), T("gi", [P, NT, 8], U32), T("gif", [P, NT, 8])
        ng, gx, gs, gw = T("ng", [P, NT]), T("gx", [P, NT, 8]), T("gs", [P, NT]), T("gw", [P, NT])
        em, ev, ei, eif = T("em", [P, NT, NE]), T("ev", [P, NT, 8]), T("ei", [P, NT, 8], U32), T("eif", [P, NT, 8])
        df, dx, w0, w1, w2 = T("df", [P, NT]), T("dx", [P, NT]), T("w0", [P, NT]), T("w1", [P, NT]), T("w2", [P, NT, NE])
        with nc.Block() as block:
            @block.sync
            def _(sp):
                nc.sync.dma_start(wr[:], dram["w_router"]).then_inc(in_s, 16)
                nc.sync.dma_start(br[:], dram["b_router"]).then_inc(in_s, 16)
                nc.sync.dma_start(idx[:], dram["expert_numbers"]).then_inc(in_s, 16)
                load_blocks(env, sp)

            @block.tensor
            def _(pe):
                pe.wait_ge(in_s, 48)
                bank_ready(env, pe, t_lg)
                for t in range(NT):
                    out = env.ps[:, t_lg[0], t * NR:(t + 1) * NR]
                    for k in range(KD):
                        nc.tensor.matmul(out, env.hT[:, k, t * P:(t + 1) * P], wr[:, k, :], start=(k == 0), stop=False)
                    mm = nc.tensor.matmul(out, env.ones[0:1, :], br[:], start=False, stop=True)
                mm.then_inc(env.bank_full[t_lg[0]], 1)

            @block.scalar
            def _(act):
                for t in range(NT):
                    act.wait_ge(pair_s, 1)
                    nc.scalar.activation(gx[:, t, :], gp[:, t, :], ACT.Exp, bias=ng[:, t:t + 1],
                                         accum_out=gs[:, t:t + 1]).then_inc(exp_s, 1)
                act.wait_ge(pair_s, 2)
                nc.scalar.activation(dx[:], df[:], ACT.Exp).then_inc(exp_s, 1)

            @block.vector
            def _(v):
                step = Chain(ch_s)
                V = nc.vector
                step(v, V.memset(gp[:], NEG))
                v.wait_ge(in_s, 48)
                product_done(env, v, t_lg)
                V.tensor_copy(lg[:], env.ps[:, t_lg[0], 0:NT * NR].rearrange("p (t n) -> p t n", t=NT)).then_inc(
                    env.bank_free[t_lg[0]], 1)
                evacuated(env, v, t_lg)
                step(v, V.tensor_copy(gp[:, :, 0:NG], lg[:, :, 0:NG]))
                for t in range(NT):
                    step(v, V.max(gm[:, t, :], gp[:, t, :]))
                    step(v, V.max_index(gi[:, t, :], gm[:, t, :], gp[:, t, :]))
                V.tensor_scalar(ng[:], gm[:, :, 0], -1.0, None, ALU.mult).then_inc(pair_s, 1)
                step(v, V.tensor_copy(gif[:], gi[:]))
                for t in range(NT):
                    step(v, V.tensor_scalar(em[:, t, :], idx[:, 1, :], gif[:, t, 0:1], -NEG, ALU.is_equal, ALU.mult))
                    step(v, V.scalar_tensor_tensor(em[:, t, :], em[:, t, :], NEG, lg[:, t, NG:NR], ALU.add, ALU.add))
                    step(v, V.max(ev[:, t, :], em[:, t, :]))
                    step(v, V.max_index(ei[:, t, :], ev[:, t, :], em[:, t, :]))
                V.tensor_tensor(df[:], ev[:, :, 1], ev[:, :, 0], ALU.subtract).then_inc(pair_s, 1)
                step(v, V.tensor_copy(eif[:], ei[:]))
                v.wait_ge(exp_s, NT + 1)
                step(v, V.reciprocal(gw[:], gs[:]))
                step(v, V.tensor_scalar(w1[:], dx[:], 1.0, None, ALU.add))
                step(v, V.reciprocal(w0[:], w1[:]))
                step(v, V.tensor_tensor(w0[:], w0[:], gw[:], ALU.mult))
                step(v, V.tensor_tensor(w1[:], dx[:], w0[:], ALU.mult))
                for t in range(NT):
                    step(v, V.tensor_scalar(wgt[:, t, :], idx[:, 0, :], eif[:, t, 0:1], w0[:, t:t + 1], ALU.is_equal, ALU.mult))
                    step(v, V.tensor_scalar(w2[:, t, :], idx[:, 0, :], eif[:, t, 1:2], w1[:, t:t + 1], ALU.is_equal, ALU.mult))
                step(v, V.tensor_tensor(wgt[:], wgt[:], w2[:], ALU.add))


def stage_experts(env, wgt):
    nc, dram = env.nc, env.dram
    names = ("gu_full", "sg_done", "hid_done", "dn_full", "dn_free", "zero", "mix")
    gu_full, sg_done, hid_done, dn_full, dn_free, zero_s, mix_s = (env.sem("ex_" + n) for n in names)
    loaded = [env.sem(f"ex_loaded{s}") for s in range(2)]
    with ExitStack() as st:
        T = lambda n, s: st.enter_context(nc.sbuf_tensor("ex_" + n, s, F32))
        w = T("w", [P, 2, EW])
        acc = T("acc", [P, NT, D])
        sg, hid = T("sg", [P, EFT, S]), T("hid", [P, EFT, S])
        wg = [w[:, s, 0:KD * 2 * EF].rearrange("p (k n) -> p k n", k=KD) for s in range(2)]
        wd = [w[:, s, KD * 2 * EF:EW].rearrange("p (k n) -> p k n", k=EFT) for s in range(2)]
        GATE, UP = [0, 1], [2, 3]
        with nc.Block() as block:
            @block.sync
            def _(sp):
                load_blocks(env, sp)
                for s in range(2):
                    nc.sync.dma_start(w[:, s, :], dram["experts"][s]).then_inc(loaded[s], 16)
                with sp.Fori(0, NE // 2 - 1) as i:
                    for s in range(2):
                        sp.wait_ge(dn_full, 8 + 16 * i + 8 * (s + 1))
                        sp.nop(nofuse=True)
                        nc.sync.dma_start(w[:, s, :], dram["experts"][bass.ds(2 * i + s + 2, 1)].rearrange("o p n -> p (o n)")
                                          ).then_inc(loaded[s], 16)

            @block.tensor
            def _(pe):
                pe.sem_inc(dn_full, 8)
                with pe.Fori(0, NE // 2) as i:
                    for s in range(2):
                        e2 = 4 * i + 2 * s
                        pe.wait_ge(loaded[s], 16 * i + 16)
                        for j in range(EFT):
                            for bank, free, lo in ((GATE[j], sg_done, 0), (UP[j], hid_done, EF)):
                                pe.wait_ge(free, e2 + j + 1)
                                for k in range(KD):
                                    mm = nc.tensor.matmul(env.ps[:, bank, :], wg[s][:, k, lo + j * P:lo + (j + 1) * P],
                                                          env.hT[:, k, 0:S], start=(k == 0), stop=(k == KD - 1))
                                mm.then_inc(gu_full, 1)
                        pe.wait_ge(hid_done, e2 + 4)
                        for n in range(2 * NT):
                            t, half = n // 2, n % 2
                            pe.wait_ge(dn_free, 16 * i + 8 * s + n + 1)
                            for k in range(EFT):
                                mm = nc.tensor.matmul(env.ps[:, 4 + n % 4, :], hid[:, k, t * P:(t + 1) * P],
                                                      wd[s][:, k, half * WBLK:(half + 1) * WBLK],
                                                      start=(k == 0), stop=(k == EFT - 1))
                            mm.then_inc(dn_full, 1)

            @block.scalar
            def _(act):
                act.sem_inc(sg_done, 2)
                with act.Fori(0, NE // 2) as i:
                    for s in range(2):
                        for j in range(EFT):
                            act.wait_ge(hid_done, 4 * i + 2 * s + j + 1)
                            act.wait_ge(gu_full, 8 * i + 4 * s + 2 * j + 1)
                            nc.scalar.activation(sg[:, j, :], env.ps[:, GATE[j], :], ACT.Silu).then_inc(sg_done, 1)

            @block.vector
            def _(v):
                v.sem_inc(hid_done, 2)
                v.sem_inc(dn_free, 4)
                nc.vector.memset(acc[:], 0.0).then_inc(zero_s, 1)
                v.wait_ge(zero_s, 1)
                with v.Fori(0, NE // 2) as i:
                    for s in range(2):
                        for j in range(EFT):
                            v.wait_ge(sg_done, 2 + 4 * i + 2 * s + j + 1)
                            v.wait_ge(gu_full, 8 * i + 4 * s + 2 * j + 2)
                            v.wait_ge(dn_full, 8 + 16 * i + 8 * s)
                            nc.vector.tensor_tensor(hid[:, j, :], sg[:, j, :], env.ps[:, UP[j], :], ALU.mult).then_inc(hid_done, 1)
                        for n in range(2 * NT):
                            t, cs = n // 2, slice((n % 2) * WBLK, (n % 2 + 1) * WBLK)
                            v.wait_ge(dn_free, 4 + 16 * i + 8 * s + n)
                            v.wait_ge(dn_full, 8 + 16 * i + 8 * s + n + 1)
                            nc.vector.scalar_tensor_tensor(acc[:, t, cs], env.ps[:, 4 + n % 4, :],
                                                           wgt[:, t, bass.ds(2 * i + s, 1)], acc[:, t, cs],
                                                           ALU.mult, ALU.add).then_inc(dn_free, 1)
                v.wait_ge(dn_free, 4 + 8 * NE)
                for t in range(NT):
                    nc.vector.tensor_tensor(acc[:, t, :], acc[:, t, :], env.gates[:, 1, :], ALU.mult).then_inc(mix_s, 1)
                for t in range(NT):
                    v.wait_ge(mix_s, t + 1)
                    nc.vector.tensor_tensor(env.h[:, t, :], env.h[:, t, :], acc[:, t, :], ALU.add).then_inc(mix_s, 1)


AH = 8
QR, KVR = 384, 256
CQ, CKV = QR // P, KVR // P
NOPE, ROT, VH = 64, 32, 64
QH = NOPE + ROT
DH = 64


def stage_second_project(env, M):
    nc, dram = env.nc, env.dram
    q_t, k_t, r_t = env.tiles(4), env.tiles(4), env.tiles(8)
    v_t, c_t = env.tiles(NT), env.tiles(NT)
    e_t, kr_t = env.tiles(NT), env.tile()
    blks = [env.take_block(t) for t in (q_t[-1], k_t[-1], v_t[-1], c_t[-1], kr_t)]
    tab_in, cos_s, rope_s = (env.sem("sp_" + n) for n in ("tab", "cos", "rope"))
    with ExitStack() as st:
        sn = st.enter_context(nc.sbuf_tensor("sp_sn", [P, 2, S], F32))
        tab = st.enter_context(nc.sbuf_tensor("sp_tabs", [P, 2, S], F32))
        perm = st.enter_context(nc.sbuf_tensor("sp_perm", [P, P], F32))
        with nc.Block() as block:
            @block.sync
            def _(sp):
                nc.sync.dma_start(tab[:], dram["rope_dil"]).then_inc(tab_in, 16)
                nc.sync.dma_start(perm[:], dram["perm_dil"]).then_inc(tab_in, 16)
                load_blocks(env, sp)

            @block.scalar
            def _(act):
                for j, t in enumerate(q_t + k_t):
                    product_done(env, act, t)
                    nc.scalar.activation(M.dqk[:, j, :], env.ps[:, t[0], :], ACT.Copy,
                                         scale=DH ** -0.5 if j < 4 else 1.0).then_inc(env.bank_free[t[0]], 1)
                for tl, dst, n in ((v_t, M.dv, WBLK), (c_t, M.c, WBLK)):
                    for i, t in enumerate(tl):
                        product_done(env, act, t)
                        nc.scalar.activation(dst[:, i, 0:n], env.ps[:, t[0], 0:n], ACT.Copy).then_inc(env.bank_free[t[0]], 1)
                for i, t in enumerate(e_t):
                    product_done(env, act, t)
                    nc.scalar.activation(M.c[:, i, WBLK:WBLK + P], env.ps[:, t[0], 0:P], ACT.Copy).then_inc(env.bank_free[t[0]], 1)
                product_done(env, act, kr_t)
                nc.scalar.activation(M.kr[:], env.ps[0:QH, kr_t[0], :], ACT.Copy).then_inc(env.bank_free[kr_t[0]], 1)

            @block.vector
            def _(v):
                v.wait_ge(tab_in, 32)
                rope_dve(env, v, r_t, lambda j: M.dqk[:, j, :], tab, sn, cos_s, rope_s)

            @block.tensor
            def _(pe):
                for b, tl in zip(blks[:2], (q_t, k_t)):
                    w = block_view(env, pe, b)
                    for j, t in enumerate(tl):
                        project(env, pe, t, env.ps[:, t[0], :], w, j * P, (j + 1) * P, lambda k: env.hT[:, k, 0:S])
                pe.wait_ge(tab_in, 32)
                rope_mm(env, pe, r_t, perm[:], lambda j: M.dqk[:, j, :], lambda j: evacuated(env, pe, (q_t + k_t)[j]))
                for b, tl in zip(blks[2:4], (v_t, c_t)):
                    w = block_view(env, pe, b)
                    for i, t in enumerate(tl):
                        by_token(env, pe, t, WBLK, w, i)
                w = block_view(env, pe, blks[4])
                for i, t in enumerate(e_t):
                    by_token(env, pe, t, P, w, i)
                project(env, pe, kr_t, env.ps[0:QH, kr_t[0], :], w, P, P + QH, lambda k: env.hT[:, k, 0:S])


def stage_latent_expand(env, M):
    nc, dram = env.nc, env.dram
    c_t = env.tiles(CQ + CKV)
    q_t = env.tiles(AH)
    k_t = env.tiles(AH)
    r_t = env.tiles(AH + 1)
    v_t = env.tiles(NT)
    tab_in, sq_s, rms_s, inv_s, nrm_s, cos_s, rope_s = (env.sem("le_" + n) for n in (
        "tab", "sq", "rms", "inv", "nrm", "cos", "rope"))
    parts = ((0, QR), (QR, KVR))
    with ExitStack() as st:
        T = lambda n, s: st.enter_context(nc.sbuf_tensor("le_" + n, s, F32))
        sn, tab, perm = T("sn", [P, 2, S]), T("tabs", [P, 2, S]), T("perm", [P, P])
        wq, wkv = T("wq", [P, CQ, AH * QH]), T("wkv", [P, CKV, AH * (NOPE + VH)])
        cT = T("cT", [P, CQ + CKV, S])
        sq, ss, rs = T("sqs", [P, 2, QR]), T("ss", [P, 2, NT]), T("rs", [P, 2, NT])
        with nc.Block() as block:
            @block.sync
            def _(sp):
                nc.sync.dma_start(wq[:], dram["w_uq"]).then_inc(tab_in, 16)
                nc.sync.dma_start(wkv[:], dram["w_ukv"]).then_inc(tab_in, 16)
                nc.sync.dma_start(tab[0:QH], dram["rope_mla"]).then_inc(tab_in, 16)
                nc.sync.dma_start(perm[0:QH, 0:QH], dram["perm_mla"]).then_inc(tab_in, 16)
                load_blocks(env, sp)

            @block.scalar
            def _(act):
                n = 0
                for p, (lo, w) in enumerate(parts):
                    for t in range(NT):
                        if n >= 2:
                            act.wait_ge(sq_s, n - 1)
                        nc.scalar.activation(sq[:, n % 2, 0:w], M.c[:, t, lo:lo + w], ACT.Square,
                                             accum_out=ss[:, p, t:t + 1]).then_inc(sq_s, 1)
                        n += 1
                act.wait_ge(sq_s, n)
                for p, (lo, w) in enumerate(parts):
                    nc.scalar.activation(rs[:, p, :], ss[:, p, :], ACT.Sqrt, scale=1.0 / w, bias=env.eps[:, 0:1]).then_inc(rms_s, 1)
                for hd, t in enumerate(q_t):
                    product_done(env, act, t)
                    nc.scalar.activation(M.q[:, hd, :], env.ps[0:QH, t[0], :], ACT.Copy, scale=QH ** -0.5).then_inc(
                        env.bank_free[t[0]], 1)
                for hd, t in enumerate(k_t):
                    product_done(env, act, t)
                    nc.scalar.activation(M.k[0:NOPE, hd, :], env.ps[0:NOPE, t[0], :], ACT.Copy).then_inc(env.bank_free[t[0]], 1)
                for i, t in enumerate(v_t):
                    product_done(env, act, t)
                    nc.scalar.activation(M.v[:, i, :], env.ps[:, t[0], :], ACT.Copy).then_inc(env.bank_free[t[0]], 1)

            @block.vector
            def _(v):
                v.wait_ge(rms_s, 2)
                nc.vector.reciprocal(ss[:], rs[:]).then_inc(inv_s, 1)
                v.wait_ge(inv_s, 1)
                for p, (lo, w) in enumerate(parts):
                    for t in range(NT):
                        x = M.c[:, t, lo:lo + w]
                        nc.vector.tensor_scalar(x, x, ss[:, p, t:t + 1], None, ALU.mult).then_inc(nrm_s, 1)
                for j, t in enumerate(c_t):
                    product_done(env, v, t)
                    nc.vector.tensor_scalar(cT[:, j, :], env.ps[:, t[0], :], col(env, "g_cq", j), None, ALU.mult).then_inc(
                        env.bank_free[t[0]], 1)
                v.wait_ge(tab_in, 64)
                rope_dve(env, v, r_t, lambda j: M.q[:, j, :] if j < AH else M.kr[:], tab, sn, cos_s, rope_s)
                v.wait_ge(rope_s, AH + 1)
                nc.vector.tensor_copy(M.k[NOPE:QH, :, :], M.kr[NOPE:QH, :].unsqueeze(1).broadcast_to([ROT, AH, S])).then_inc(rope_s, 1)

            @block.tensor
            def _(pe):
                to_features(env, pe, c_t, lambda t, j: M.c[:, t, j * P:(j + 1) * P],
                            lambda t, j: pe.wait_ge(nrm_s, (t + 1) + (NT if j >= CQ else 0)))
                pe.wait_ge(tab_in, 64)
                for t in c_t:
                    evacuated(env, pe, t)
                for hd, t in enumerate(q_t):
                    bank_ready(env, pe, t)
                    for k in range(CQ):
                        mm = nc.tensor.matmul(env.ps[0:QH, t[0], :], wq[:, k, hd * QH:(hd + 1) * QH], cT[:, k, :],
                                              start=(k == 0), stop=(k == CQ - 1))
                    mm.then_inc(env.bank_full[t[0]], 1)
                for hd, t in enumerate(k_t):
                    bank_ready(env, pe, t)
                    for k in range(CKV):
                        mm = nc.tensor.matmul(env.ps[0:NOPE, t[0], :], wkv[:, k, hd * NOPE:(hd + 1) * NOPE], cT[:, CQ + k, :],
                                              start=(k == 0), stop=(k == CKV - 1))
                    mm.then_inc(env.bank_full[t[0]], 1)
                rope_mm(env, pe, r_t, perm[0:QH, 0:QH], lambda j: M.q[:, j, :] if j < AH else M.kr[:],
                        lambda j: evacuated(env, pe, q_t[j]) if j < AH else None)
                for i, t in enumerate(v_t):
                    bank_ready(env, pe, t)
                    for k in range(CKV):
                        mm = nc.tensor.matmul(env.ps[:, t[0], :], cT[:, CQ + k, i * P:(i + 1) * P], wkv[:, k, AH * NOPE:],
                                              start=(k == 0), stop=(k == CKV - 1))
                    mm.then_inc(env.bank_full[t[0]], 1)


def stage_attention(env, M, o):
    nc = env.nc
    units = []
    for hd in range(AH):
        for qt in range(NT):
            units += [(0, hd, qt), (1, hd, qt)]
    nu = len(units)
    sc, tr, pv = [None] * nu, [None] * nu, [None] * nu
    for s in range(nu + 2):
        if s < nu:
            sc[s] = env.tile()
        if 1 <= s <= nu:
            tr[s - 1] = env.tile()
        if s >= 2:
            pv[s - 2] = env.tile()
    mask_in, max_s, neg_s, ex_s, inv_s = (env.sem("at_" + n) for n in ("mask", "max", "neg", "exp", "inv"))

    def weights_ready(eng, u):
        if units[u][0] == 0:
            evacuated(env, eng, sc[u])
        else:
            eng.wait_ge(ex_s, u // 2 + 1)

    with ExitStack() as st:
        T = lambda n, s: st.enter_context(nc.sbuf_tensor("at_" + n, s, F32))
        mask = T("masks", [P, NT, S])
        sm = T("sm", [P, 2, S])
        pr, pt = T("pr", [P, 2, S]), T("pt", [P, 2, S])
        mx, nm, sums, inv = T("mx", [P, nu]), T("nm", [P, nu]), T("sums", [P, nu]), T("invs", [P, nu])
        with nc.Block() as block:
            @block.sync
            def _(sp):
                nc.sync.dma_start(mask[:], env.dram["dil_mask"]).then_inc(mask_in, 16)
                load_blocks(env, sp)

            @block.vector
            def _(v):
                v.wait_ge(mask_in, 16)
                for s in range(nu + 2):
                    if s < nu:
                        kind, hd, qt = units[s]
                        product_done(env, v, sc[s])
                        if kind == 0:
                            nc.vector.tensor_reduce(nm[:, s:s + 1], env.ps[:, sc[s][0], :], AX.X, ALU.max,
                                                    negate=True).then_inc(neg_s, 1)
                        else:
                            if s >= 4:
                                v.wait_ge(ex_s, s // 2 - 1)
                            nc.vector.tensor_tensor_reduce(sm[:, (s // 2) % 2, :], env.ps[:, sc[s][0], :], mask[:, qt, :],
                                                           1.0, NEG, ALU.add, ALU.max, mx[:, s:s + 1]).then_inc(
                                env.bank_free[sc[s][0]], 1)
                            evacuated(env, v, sc[s])
                            nc.vector.tensor_scalar(nm[:, s:s + 1], mx[:, s:s + 1], -1.0, None, ALU.mult).then_inc(neg_s, 1)
                    if s >= 2:
                        u = s - 2
                        kind, hd, qt = units[u]
                        weights_ready(v, u)
                        nc.vector.reciprocal(inv[:, u:u + 1], sums[:, u:u + 1]).then_inc(inv_s, 1)
                        product_done(env, v, pv[u])
                        v.wait_ge(inv_s, u + 1)
                        nc.vector.tensor_scalar(o[:, kind, qt, hd * VH:(hd + 1) * VH], env.ps[:, pv[u][0], 0:VH],
                                                inv[:, u:u + 1], None, ALU.mult).then_inc(env.bank_free[pv[u][0]], 1)

            @block.scalar
            def _(act):
                for s in range(nu + 1):
                    if s < nu:
                        kind, hd, qt = units[s]
                        act.wait_ge(neg_s, s + 1)
                        if s >= 2:
                            product_done(env, act, tr[s - 2])
                        if kind == 0:
                            nc.scalar.activation(pr[:, s % 2, :], env.ps[:, sc[s][0], :], ACT.Exp, bias=nm[:, s:s + 1],
                                                 accum_out=sums[:, s:s + 1]).then_inc(env.bank_free[sc[s][0]], 1)
                        else:
                            nc.scalar.activation(pr[:, s % 2, :], sm[:, (s // 2) % 2, :], ACT.Exp, bias=nm[:, s:s + 1],
                                                 accum_out=sums[:, s:s + 1]).then_inc(ex_s, 1)
                    if s >= 1:
                        u = s - 1
                        product_done(env, act, tr[u])
                        if u >= 2:
                            product_done(env, act, pv[u - 2])
                        nc.scalar.activation(pt[:, u % 2, :], env.ps[:, tr[u][0], :], ACT.Copy).then_inc(
                            env.bank_free[tr[u][0]], 1)

            @block.tensor
            def _(pe):
                for s in range(nu + 2):
                    if s < nu:
                        kind, hd, qt = units[s]
                        qs = slice(qt * P, (qt + 1) * P)
                        bank_ready(env, pe, sc[s])
                        if kind == 0:
                            q, k = M.q[:, hd, qs], M.k[:, hd, :]
                        else:
                            rows = slice(DH * (hd % 2), DH * (hd % 2 + 1))
                            q, k = M.dqk[rows, hd // 2, qs], M.dqk[rows, 4 + hd // 2, :]
                        nc.tensor.matmul(env.ps[:, sc[s][0], :], q, k, start=True, stop=True).then_inc(env.bank_full[sc[s][0]], 1)
                    if 1 <= s <= nu:
                        u = s - 1
                        weights_ready(pe, u)
                        bank_ready(env, pe, tr[u])
                        for kt in range(NT):
                            mm = nc.tensor.transpose(env.ps[:, tr[u][0], kt * P:(kt + 1) * P],
                                                     pr[:, u % 2, kt * P:(kt + 1) * P], env.ident[:])
                        mm.then_inc(env.bank_full[tr[u][0]], 1)
                    if s >= 2:
                        u = s - 2
                        kind, hd, qt = units[u]
                        evacuated(env, pe, tr[u])
                        bank_ready(env, pe, pv[u])
                        val = M.v if kind == 0 else M.dv
                        for kt in range(NT):
                            mm = nc.tensor.matmul(env.ps[:, pv[u][0], 0:VH], pt[:, u % 2, kt * P:(kt + 1) * P],
                                                  val[:, kt, hd * VH:(hd + 1) * VH], start=(kt == 0), stop=(kt == NT - 1))
                        mm.then_inc(env.bank_full[pv[u][0]], 1)


def stage_mix(env, o, mixT):
    nc = env.nc
    tl = env.tiles(KD)
    sq_s, rms_s, inv_s, nrm_s = (env.sem("mx_" + n) for n in ("sq", "rms", "inv", "nrm"))
    W = AH * VH
    with ExitStack() as st:
        T = lambda n, s: st.enter_context(nc.sbuf_tensor("mx_" + n, s, F32))
        sq, ss, rs = T("sqs", [P, 2, W]), T("ss", [P, 2, NT]), T("rs", [P, 2, NT])
        with nc.Block() as block:
            @block.sync
            def _(sp):
                load_blocks(env, sp)

            @block.scalar
            def _(act):
                for n in range(2 * NT):
                    if n >= 2:
                        act.wait_ge(sq_s, n - 1)
                    nc.scalar.activation(sq[:, n % 2, :], o[:, n // NT, n % NT, :], ACT.Square,
                                         accum_out=ss[:, n // NT, n % NT:n % NT + 1]).then_inc(sq_s, 1)
                act.wait_ge(sq_s, 2 * NT)
                nc.scalar.activation(rs[:], ss[:], ACT.Sqrt, scale=1.0 / W, bias=env.eps[:, 0:1]).then_inc(rms_s, 1)

            @block.vector
            def _(v):
                v.wait_ge(rms_s, 1)
                nc.vector.reciprocal(ss[:], rs[:]).then_inc(inv_s, 1)
                v.wait_ge(inv_s, 1)
                for n in range(2 * NT):
                    x = o[:, n // NT, n % NT, :]
                    nc.vector.tensor_scalar(x, x, ss[:, n // NT, n % NT:n % NT + 1], None, ALU.mult).then_inc(nrm_s, 1)
                for j, t in enumerate(tl):
                    product_done(env, v, t)
                    nc.vector.tensor_scalar(mixT[:, j, :], env.ps[:, t[0], :], col(env, "g_mla", j), None, ALU.mult).then_inc(
                        env.bank_free[t[0]], 1)

            @block.tensor
            def _(pe):
                to_features(env, pe, tl, lambda t, j: o[:, j // 4, t, (j % 4) * P:(j % 4 + 1) * P],
                            lambda t, j: pe.wait_ge(nrm_s, (j // 4) * NT + t + 1))


PH = 8
PK = 128
HALF = 64
TK = 16
SLOTS = PH * TK
RING = 8


class Group:

    def __init__(self, sem):
        self.sem, self.n = sem, 0

    def __call__(self, eng, steps):
        for ins in steps:
            ins.then_inc(self.sem, 1)
            self.n += 1
        eng.wait_ge(self.sem, self.n)


def stage_memory_route(env, rows, gate):
    nc, dram = env.nc, env.dram
    q_t = env.tiles(PH)
    blks = [env.take_block(q_t[3]), env.take_block(q_t[7])]
    s_t = [[[env.tile() for half in range(2)] for hg in range(2)] for t in range(NT)]
    in_s, grp_s, top_s, exp_s = (env.sem("pk_" + n) for n in ("in", "group", "top", "exp"))
    with ExitStack() as st:
        T = lambda n, s, d=F32: st.enter_context(nc.sbuf_tensor("pk_" + n, s, d))
        qp = T("qp", [P, PH, S])
        keys = T("keys", [P, PK])
        iota = T("iota", [P, TK])
        sc = T("sc", [P, 2, 2, PH, PK])
        rest = T("rest", [P, 2, PH, PK])
        v, ix, ixf = T("v", [P, 2, PH, TK]), T("ix", [P, 2, PH, TK], U32), T("ixf", [P, 2, PH, TK])
        cand, cand2 = T("cand", [P, PH, TK * TK]), T("cand2", [P, PH, TK * TK])
        top, pos = T("top", [P, PH, TK]), T("pos", [P, PH, TK], U32)
        ab, abf = T("ab", [P, 2, PH, TK], U32), T("abf", [P, 2, PH, TK])
        eq = T("eq", [P, 2, PH * TK, TK])
        pick = T("pick", [P, 2, PH * TK])
        ex, sm = T("ex", [P, 2, PH, TK]), T("sm", [P, 2, PH])
        with nc.Block() as block:
            @block.sync
            def _(sp):
                nc.sync.dma_start(keys[:], dram["peer_keys"]).then_inc(in_s, 16)
                nc.sync.dma_start(iota[:], dram["iota16"]).then_inc(in_s, 16)
                load_blocks(env, sp)

            @block.tensor
            def _(pe):
                for i, b in enumerate(blks):
                    w = block_view(env, pe, b)
                    for j in range(4):
                        t = q_t[4 * i + j]
                        project(env, pe, t, env.ps[:, t[0], :], w, j * P, (j + 1) * P, lambda k: env.hT[:, k, 0:S])
                pe.wait_ge(in_s, 32)
                for t in range(NT):
                    for hg in range(2):
                        for half in range(2):
                            tl, r = s_t[t][hg][half], slice(half * HALF, (half + 1) * HALF)
                            bank_ready(env, pe, tl)
                            for n in range(4):
                                hd = 4 * hg + n
                                evacuated(env, pe, q_t[hd])
                                mm = nc.tensor.matmul(env.ps[:, tl[0], n * PK:(n + 1) * PK], qp[r, hd, t * P:(t + 1) * P],
                                                      keys[r, :], start=True, stop=True)
                            mm.then_inc(env.bank_full[tl[0]], 1)

            @block.scalar
            def _(act):
                for hd, t in enumerate(q_t):
                    product_done(env, act, t)
                    nc.scalar.activation(qp[:, hd, :], env.ps[:, t[0], :], ACT.Copy).then_inc(env.bank_free[t[0]], 1)
                for t in range(NT):
                    if t >= 2:
                        act.wait_ge(top_s, t - 1)
                    for hg in range(2):
                        for half in range(2):
                            tl = s_t[t][hg][half]
                            product_done(env, act, tl)
                            nc.scalar.activation(sc[:, t % 2, half, 4 * hg:4 * hg + 4, :],
                                                 env.ps[:, tl[0], :].rearrange("p (h k) -> p h k", k=PK),
                                                 ACT.Copy).then_inc(env.bank_free[tl[0]], 1)
                    act.wait_ge(top_s, t + 1)
                    nc.scalar.activation(ex[:, t % 2], ex[:, t % 2], ACT.Exp).then_inc(exp_s, 1)

            @block.vector
            def _(ve):
                V = nc.vector
                group = Group(grp_s)
                ve.wait_ge(in_s, 32)
                pairs = [(half, hd) for half in range(2) for hd in range(PH)]

                def finish(t):
                    ve.wait_ge(exp_s, t + 1)
                    group(ve, [V.reduce_sum(sm[:, 0, :], ex[:, t % 2], axis=AX.X)])
                    group(ve, [V.reciprocal(sm[:, 1, :], sm[:, 0, :])])
                    group(ve, [V.tensor_tensor(gate[:, t, :].rearrange("p (h k) -> p h k", k=TK), ex[:, t % 2],
                                               sm[:, 1, :].unsqueeze(2).broadcast_to([P, PH, TK]), ALU.mult)])

                for t in range(NT):
                    for hg in range(2):
                        for half in range(2):
                            evacuated(env, ve, s_t[t][hg][half])
                    s = sc[:, t % 2]
                    group(ve, [V.max(v[:, a, h, 0:8], s[:, a, h, :]) for a, h in pairs])
                    group(ve, [V.max_index(ix[:, a, h, 0:8], v[:, a, h, 0:8], s[:, a, h, :]) for a, h in pairs] +
                          [V.match_replace(rest[:, a, h, :], v[:, a, h, 0:8], s[:, a, h, :], NEG) for a, h in pairs])
                    group(ve, [V.max(v[:, a, h, 8:16], rest[:, a, h, :]) for a, h in pairs])
                    group(ve, [V.max_index(ix[:, a, h, 8:16], v[:, a, h, 8:16], rest[:, a, h, :]) for a, h in pairs])
                    shape = [P, PH, TK, TK]
                    group(ve, [V.tensor_copy(ixf[:], ix[:]),
                               V.tensor_tensor(cand[:].rearrange("p h (a b) -> p h a b", b=TK),
                                               v[:, 0].unsqueeze(3).broadcast_to(shape), v[:, 1].unsqueeze(2).broadcast_to(shape),
                                               ALU.add)])
                    hs = range(PH)
                    group(ve, [V.max(top[:, h, 0:8], cand[:, h, :]) for h in hs])
                    group(ve, [V.max_index(pos[:, h, 0:8], top[:, h, 0:8], cand[:, h, :]) for h in hs] +
                          [V.match_replace(cand2[:, h, :], top[:, h, 0:8], cand[:, h, :], NEG) for h in hs])
                    group(ve, [V.max(top[:, h, 8:16], cand2[:, h, :]) for h in hs])
                    group(ve, [V.max_index(pos[:, h, 8:16], top[:, h, 8:16], cand2[:, h, :]) for h in hs])
                    V.tensor_tensor(ex[:, t % 2], top[:], top[:, :, 0:1].broadcast_to([P, PH, TK]), ALU.subtract).then_inc(top_s, 1)
                    group(ve, [V.tensor_scalar(ab[:, 0], pos[:], 4, None, ALU.logical_shift_right),
                               V.tensor_scalar(ab[:, 1], pos[:], 15, None, ALU.bitwise_and)])
                    group(ve, [V.tensor_copy(abf[:], ab[:])])
                    flat = [P, PH * TK, TK]
                    group(ve, [V.tensor_tensor(eq[:, a], iota[:].unsqueeze(1).broadcast_to(flat),
                                               abf[:, a].rearrange("p h k -> p (h k)").unsqueeze(2).broadcast_to(flat),
                                               ALU.is_equal) for a in range(2)])
                    group(ve, [V.tensor_tensor(eq[:, a].rearrange("p (h k) j -> p h k j", k=TK),
                                               eq[:, a].rearrange("p (h k) j -> p h k j", k=TK),
                                               ixf[:, a].unsqueeze(2).broadcast_to([P, PH, TK, TK]), ALU.mult) for a in range(2)])
                    group(ve, [V.reduce_sum(pick[:, a, :], eq[:, a], axis=AX.X) for a in range(2)])
                    group(ve, [V.scalar_tensor_tensor(pick[:, 0, :], pick[:, 0, :], float(PK), pick[:, 1, :], ALU.mult, ALU.add)])
                    group(ve, [V.tensor_copy(rows[:, t, :], pick[:, 0, :])])
                    if t >= 1:
                        finish(t - 1)
                finish(NT - 1)


def stage_memory(env, rows, gate, xg):
    nc, dram = env.nc, env.dram
    PER = 2 * RING
    TURNS = SLOTS // PER
    got = [env.sem(f"pm_got{r}") for r in range(RING)]
    used, idx_s, dot_s, act_s, coef_s, sum_s = (env.sem("pm_" + n) for n in (
        "used", "idx", "dot", "gelu", "coef", "sum"))
    with ExitStack() as st:
        T = lambda n, s, d=F32: st.enter_context(nc.sbuf_tensor("pm_" + n, s, d))
        ring = T("ring", [P, RING, D])
        idx = T("idxs", [P, 2, RING], U32)
        dots = T("dots", [P, PER])
        a, coef = T("a", [P, NT, SLOTS]), T("coefs", [P, NT, SLOTS])
        acc = T("acc", [P, 2, D])
        with nc.Block() as block:
            @block.sync
            def _(sp):
                load_blocks(env, sp)

            @block.gpsimd
            def _(pool):
                for t in range(NT):
                    for ph, table in enumerate(("peer_u", "peer_v")):
                        turn0 = (2 * t + ph) * TURNS
                        with pool.Fori(0, TURNS) as i:
                            for half in range(2):
                                n0 = (turn0 + i) * PER + half * RING
                                pool.wait_ge(used, n0 + 1)
                                pool.nop(nofuse=True)
                                nc.gpsimd.tensor_copy(idx[:, half, :], rows[:, t, bass.ds(i * PER + half * RING, RING)]
                                                      ).then_inc(idx_s, 1)
                                pool.wait_ge(idx_s, 2 * (turn0 + i) + half + 1)
                                for r in range(RING):
                                    pool.wait_ge(used, n0 + r + 1)
                                    pool.nop(nofuse=True)
                                    nc.gpsimd.indirect_dma_start(
                                        ring[:, r, :], None, dram[table],
                                        bass.IndirectOffsetOnAxis(ap=idx[:, half, r:r + 1], axis=0)).then_inc(got[r], 16)

            @block.scalar
            def _(act):
                for t in range(NT):
                    act.wait_ge(dot_s, 1 + (t + 1) * TURNS)
                    nc.scalar.activation(coef[:, t, :], a[:, t, :], ACT.Gelu).then_inc(act_s, 1)

            @block.vector
            def _(v):
                v.sem_inc(used, RING)
                v.sem_inc(dot_s, 1)
                for t in range(NT):
                    turn0 = 2 * t * TURNS
                    with v.Fori(0, TURNS) as i:
                        for n in range(PER):
                            r = n % RING
                            v.wait_ge(got[r], 32 * (turn0 + i) + 16 * (n // RING) + 16)
                            if n == 0:
                                v.wait_ge(dot_s, t * TURNS + i + 1)
                            nc.vector.tensor_tensor_reduce(ring[:, r, :], ring[:, r, :], xg[:, t, :], 1.0, 0.0,
                                                           ALU.mult, ALU.add, dots[:, n:n + 1]).then_inc(used, 1)
                        v.wait_ge(used, RING + (turn0 + i + 1) * PER)
                        nc.vector.tensor_copy(a[:, t, bass.ds(i * PER, PER)], dots[:]).then_inc(dot_s, 1)
                    v.wait_ge(act_s, t + 1)
                    nc.vector.tensor_tensor(coef[:, t, :], coef[:, t, :], gate[:, t, :], ALU.mult).then_inc(coef_s, 1)
                    if t >= 1:
                        v.wait_ge(sum_s, 2 * t)
                    nc.vector.memset(acc[:], 0.0).then_inc(coef_s, 1)
                    v.wait_ge(coef_s, 2 * (t + 1))
                    turn1 = turn0 + TURNS
                    with v.Fori(0, TURNS) as i:
                        for n in range(PER):
                            r = n % RING
                            v.wait_ge(got[r], 32 * (turn1 + i) + 16 * (n // RING) + 16)
                            v.wait_ge(used, RING + (turn1 + i) * PER + n - 1)
                            nc.vector.scalar_tensor_tensor(acc[:, n % 2, :], ring[:, r, :], coef[:, t, bass.ds(i * PER + n, 1)],
                                                           acc[:, n % 2, :], ALU.mult, ALU.add).then_inc(used, 1)
                    v.wait_ge(used, RING + (turn1 + TURNS) * PER)
                    for half in range(2):
                        if half:
                            v.wait_ge(sum_s, 2 * t + 1)
                        nc.vector.tensor_tensor(env.h[:, t, :], env.h[:, t, :], acc[:, half, :], ALU.add).then_inc(sum_s, 1)


PLE = 256


def stage_embedding(env):
    nc, dram = env.nc, env.dram
    g_t = [env.tiles(NT) for _ in range(2)]
    blks = [env.take_block(t[-1]) for t in g_t]
    p_t = [env.tiles(NT) for _ in range(2)]
    in_s, add_s = env.sem("pl_in"), env.sem("pl_add")
    with ExitStack() as st:
        T = lambda n, s: st.enter_context(nc.sbuf_tensor("pl_" + n, s, F32))
        gate = T("gate", [P, NT, D])
        pT, wp = T("pT", [P, PLE // P, S]), T("wp", [P, PLE // P, D])
        with nc.Block() as block:
            @block.sync
            def _(sp):
                nc.sync.dma_start(pT[:], dram["p_T"]).then_inc(in_s, 16)
                nc.sync.dma_start(wp[:], dram["w_ple_proj"]).then_inc(in_s, 16)
                load_blocks(env, sp)

            @block.scalar
            def _(act):
                for half in range(2):
                    for i, t in enumerate(g_t[half]):
                        product_done(env, act, t)
                        nc.scalar.activation(gate[:, i, half * WBLK:(half + 1) * WBLK], env.ps[:, t[0], :],
                                             ACT.Sigmoid).then_inc(env.bank_free[t[0]], 1)

            @block.vector
            def _(v):
                for half in range(2):
                    cs = slice(half * WBLK, (half + 1) * WBLK)
                    for i, t in enumerate(p_t[half]):
                        evacuated(env, v, g_t[half][i])
                        product_done(env, v, t)
                        nc.vector.tensor_tensor(gate[:, i, cs], gate[:, i, cs], env.ps[:, t[0], :], ALU.mult).then_inc(
                            env.bank_free[t[0]], 1)
                        evacuated(env, v, t)
                        nc.vector.tensor_tensor(env.h[:, i, cs], env.h[:, i, cs], gate[:, i, cs], ALU.add).then_inc(add_s, 1)

            @block.tensor
            def _(pe):
                for half in range(2):
                    w = block_view(env, pe, blks[half])
                    for i, t in enumerate(g_t[half]):
                        by_token(env, pe, t, WBLK, w, i)
                pe.wait_ge(in_s, 32)
                for half in range(2):
                    for i, t in enumerate(p_t[half]):
                        bank_ready(env, pe, t)
                        for k in range(PLE // P):
                            mm = nc.tensor.matmul(env.ps[:, t[0], :], pT[:, k, i * P:(i + 1) * P],
                                                  wp[:, k, half * WBLK:(half + 1) * WBLK], start=(k == 0), stop=(k == PLE // P - 1))
                        mm.then_inc(env.bank_full[t[0]], 1)


class Bufs:
    pass


def stream(env, *names):
    for n in names:
        a = env.dram[n]
        for i in range(a.shape[0]):
            env.blocks.append(a[i])


def load_tokens(env, name, src):
    nc = env.nc
    done = env.sem(name)
    with nc.Block() as block:
        @block.sync
        def _(sp):
            nc.sync.dma_start(env.h[:], src.rearrange("(t p) d -> p t d", p=P)).then_inc(done, 16)
            sp.wait_ge(done, 16)


def first_mixer(env):
    nc = env.nc
    gain = lambda n: (lambda j: env.gain[:, n, j:j + 1])
    shift = lambda c0, c: (lambda j: env.ada[:, c0 + j, c:c + 1])
    with ExitStack() as tok:
        env.h = tok.enter_context(nc.sbuf_tensor("x_tok", [P, NT, D], F32))
        env.hctx = tok.enter_context(nc.sbuf_tensor("ctx_tok", [P, NCT, D], F32))
        stage_modulation(env)
        stage_norm(env, "mix", lambda t: env.h[:, t, :] if t < NT else env.hctx[:, t - NT, :],
                   [(0, NT, gain(0), shift(0, 0)), (NT, NCT, gain(1), shift(0, 1))], env.hT)
    branch = ExitStack()
    oT = branch.enter_context(nc.sbuf_tensor("oT", [P, KD, S], F32))
    with ExitStack() as own:
        A = lambda n, s: own.enter_context(nc.sbuf_tensor(n, s, F32))
        B = Bufs()
        B.q, B.k, B.v = A("gla_q", [P, H1, S]), A("gla_k", [P, H1, TOK]), A("gla_v", [P, NCH, D])
        B.sum, B.tot = A("gla_sum", [P, 2 * H1, TOK]), A("gla_tot", [P, 2 * H1, NCH])
        stage_gla_project(env, B)
        stage_gla_core(env, B, oT)
    yT = branch.enter_context(nc.sbuf_tensor("yT", [P, KD, S], F32))
    stage_branch(env, "gla", oT, yT, True)
    with ExitStack() as own:
        A = lambda n, s: own.enter_context(nc.sbuf_tensor(n, s, F32))
        R = Bufs()
        R.qk, R.kc, R.v = A("ret_qk", [P, 2 * H1, S]), A("ret_kc", [P, NCT, H1 * DK]), A("ret_v", [P, NCH, D])
        stage_ret_project(env, R)
        stage_ret_core(env, R, oT)
    stage_branch(env, "ret", oT, yT, False)
    with ExitStack() as own:
        env.h = own.enter_context(nc.sbuf_tensor("h_mix", [P, NT, D], F32))
        load_tokens(env, "x_again", env.dram["x"])
        stage_out(env, "mix_out", yT, 0)
        save_tokens(env, "h_saved", env.dram["h_dram"])
    branch.close()


def first_experts(env):
    nc = env.nc
    env.h = env.sb("h_tok", [P, NT, D])
    load_tokens(env, "h_again", env.dram["h_dram"])
    stage_norm(env, "ffn", lambda t: env.h[:, t, :],
               [(0, NT, lambda j: env.gain[:, 2, j:j + 1], lambda j: env.ada[:, 24 + j, 0:1])], env.hT)
    with nc.sbuf_tensor("router_w", [P, NT, NE], F32) as wgt:
        stage_router(env, wgt)
        stage_experts(env, wgt)
    stage_rownorm(env, "fin1", env.h, "norm_final")


def second_block(env):
    nc = env.nc
    tok = lambda t: env.h[:, t, :]
    gain = lambda name: (lambda j: col(env, name, j))
    stage_norm(env, "mix2", tok, [(0, NT, gain("g_mix"), None)], env.hT)
    with ExitStack() as own:
        A = lambda n, s: own.enter_context(nc.sbuf_tensor(n, s, F32))
        M = Bufs()
        M.dqk, M.dv, M.kr = A("dil_qk", [P, 8, S]), A("dil_v", [P, NT, S]), A("mla_kr", [QH, S])
        M.q, M.k, M.v = A("mla_q", [QH, AH, S]), A("mla_k", [QH, AH, S]), A("mla_v", [P, NT, S])
        with nc.sbuf_tensor("mla_c", [P, NT, QR + KVR], F32) as c:
            M.c = c
            stage_second_project(env, M)
            stage_latent_expand(env, M)
        o = A("attn_o", [P, 2, NT, S])
        stage_attention(env, M, o)
        mixT = A("mixT", [P, KD, S])
        stage_mix(env, o, mixT)
        stage_out(env, "att_out", mixT, None)
    stage_norm(env, "ffn2", tok, [(0, NT, gain("g_ffn"), None)], env.hT)
    with ExitStack() as own:
        rows = own.enter_context(nc.sbuf_tensor("mem_rows", [P, NT, SLOTS], U32))
        gate = own.enter_context(nc.sbuf_tensor("mem_gate", [P, NT, SLOTS], F32))
        stage_memory_route(env, rows, gate)
        xg = own.enter_context(nc.sbuf_tensor("mem_x", [P, NT, D], F32))
        stage_rownorm(env, "ffn2_rows", xg, "g_ffn_row")
        stage_memory(env, rows, gate, xg)
    stage_norm(env, "ple", tok, [(0, NT, gain("g_ple"), None)], env.hT)
    stage_embedding(env)
    stage_rownorm(env, "fin2", env.h, "g_final_row", env.dram["out"])


def save_tokens(env, name, dst):
    nc = env.nc
    done = env.sem(name)
    with nc.Block() as block:
        @block.sync
        def _(sp):
            nc.sync.dma_start(dst.rearrange("(t p) d -> p t d", p=P), env.h[:]).then_inc(done, 16)
            sp.wait_ge(done, 16)


def program(nc, dram, stop=None):
    with ExitStack() as ctx:
        env = Env(nc, ctx, dram)
        env.ps = ctx.enter_context(nc.psum_tensor("ps", [P, 8, WBLK], F32))
        env.bank_full = [env.sem(f"bank_full{b}") for b in range(8)]
        env.bank_free = [env.sem(f"bank_free{b}") for b in range(8)]
        env.w_loaded = [env.sem(f"w_loaded{b}") for b in range(2)]
        env.const_in, env.const_set, env.x_in = env.sem("const_in"), env.sem("const_set"), env.sem("x_in")
        env.ident = env.sb("ident", [P, P])
        env.cols = env.sb("cols", [P, NCOL])
        env.ones = env.sb("ones", [P, P])
        env.eps = env.sb("eps", [P, 1])
        env.ada = env.sb("ada", [P, 48, 2])
        env.gain = env.sb("gain", [P, 3, 8])
        env.gates = env.sb("gates", [P, 2, D])
        env.hT = env.sb("hT", [P, KD, TOK])
        env.wring = env.sb("wring", [P, 2, KD * WBLK])
        stream(env, "w_ada")
        for b in (0, 1, 2, 3, 4, 5, 12, 13):
            env.blocks.append(dram["w_in"][b])
        stream(env, "w_branch_gla")
        for b in (6, 7, 8, 9, 10, 11, 14, 15):
            env.blocks.append(dram["w_in"][b])
        stream(env, "w_branch_ret", "w_out")
        stream(env, "w_in2", "w_out2", "w_peer_q", "w_ple_gate")
        first_mixer(env)
        first_experts(env)
        second_block(env)


def blocked(w):
    n = w.shape[1] // WBLK
    return w.reshape(KD, P, n, WBLK).transpose(2, 1, 0, 3).reshape(n, P, KD * WBLK)


def columns(a):
    return a.reshape(-1, P).T


def rope_table(seq_pos, inv, reps):
    ang = seq_pos[:, None].astype(np.float32) * inv[None, :]
    return np.cos(ang).T, np.sin(ang).T


def constants():
    f = np.float32
    c = {"ident": np.eye(P, dtype=f)}
    n = 32
    inv = (f(10000.0) ** (-np.arange(n, dtype=f) / f(n))).astype(f)
    tab = np.zeros((P, 2, S), f)
    perm = np.zeros((P, P), f)
    for half, pos in enumerate((np.repeat(np.arange(S // 64), 64), np.tile(np.arange(64), S // 64))):
        cs, sn = rope_table(pos, inv, 1)
        for part in range(2):
            r = half * 64 + part * 32
            tab[r:r + 32, 0], tab[r:r + 32, 1] = cs, sn
        for i in range(32):
            a, b = half * 64 + i, half * 64 + 32 + i
            perm[b, a] = -1.0
            perm[a, b] = 1.0
    c["rope_axial"], c["perm_axial"] = tab, perm
    h = np.arange(H1, dtype=np.float64)
    lg = [np.log1p(-np.exp2(-5.0 - h)), np.log1p(-np.exp2(-5.5 - h))]
    rel = np.arange(896)[None, :] - 384 - np.arange(P)[:, None]
    band = np.stack([np.where(rel >= 0, np.exp(np.maximum(rel, 0) * lg[0][i]), np.exp(np.maximum(-rel, 0) * lg[1][i]))
                     for i in range(H1)], 1)
    c["ret_band"] = (band * DK ** -0.5).astype(f)
    t = np.arange(S)
    c["ret_qdec"] = np.stack([np.stack([np.exp((t + 1) * lg[0][i]), np.exp((S - t) * lg[1][i])]) for i in range(H1)]).astype(f)
    s = np.arange(CT)
    kd = np.stack([np.exp((CT - 1 - s) * lg[0][i]) for i in range(H1)] + [np.exp(s * lg[1][i]) for i in range(H1)])
    c["ret_kdec"] = (kd * DK ** -0.5).reshape(2 * H1, NCT, P).transpose(2, 0, 1).astype(f)
    p = np.arange(P)
    c["chunk_mask"] = np.stack([p[:, None] <= p[None, :], p[:, None] > p[None, :]], 1).astype(f)
    e = np.arange(NE)
    c["iota16"] = np.broadcast_to(np.arange(TK, dtype=f), (P, TK))
    for name, rows, width, first, rot in (("mla", QH, QH, NOPE, ROT), ("dil", P, DH, 0, DH // 4)):
        half = rot // 2
        inv = (f(500000.0) ** (-np.arange(0, rot, 2, dtype=f) / f(rot))).astype(f)
        cs, sn = rope_table(np.arange(S), inv, 1)
        tab, perm = np.zeros((rows, 2, S), f), np.zeros((rows, rows), f)
        tab[:, 0] = 1.0
        for r0 in range(first, rows, width):
            for part in range(2):
                tab[r0 + part * half:r0 + (part + 1) * half, 0] = cs
                tab[r0 + part * half:r0 + (part + 1) * half, 1] = sn
            for i in range(half):
                perm[r0 + half + i, r0 + i] = -1.0
                perm[r0 + i, r0 + half + i] = 1.0
        c["rope_" + name], c["perm_" + name] = tab, perm
    q, k = np.arange(S)[:, None], np.arange(S)[None, :]
    count = sum(((q - k) % dil == 0) & (abs(q - k) <= win // 2) for win, dil in ((128, 1), (512, 4), (2048, 16)))
    mask = np.where(count > 0, np.log(np.maximum(count, 1)), NEG).astype(f)
    c["dil_mask"] = mask.reshape(NT, P, S).transpose(1, 0, 2)
    c["expert_numbers"] = np.broadcast_to(np.stack([e, e // EPG]), (P, 2, NE)).astype(f)
    return c


def layout(i):
    a = {k: np.asarray(v) for k, v in i.items()}
    d = constants()
    d["x"], d["ctx"] = a["x"][0], a["ctx"][0]
    d["c2"] = np.stack([a["c"][0].reshape(KD, P), a["c_ctx"].reshape(KD, P)], -1).transpose(1, 0, 2)
    vec = dict(norm_mix=a["norm_mix"][0], norm_ffn=a["norm_ffn"][0], b_ada=a["b_ada"][0], gla_norm=a["gla_norm"][0],
               gla_b=a["gla_lr_b"][0].reshape(-1), g_mix=a["g_mix_2"][0], g_cq=a["g_cq_2"][0], g_ckv=a["g_ckv_2"][0],
               g_mla=a["g_out_mla_2"][0], g_dil=a["g_out_dil_2"][0], g_ffn=a["g_ffn_2"][0], g_ple=a["g_ple_2"][0])
    d["cols"] = np.concatenate([columns(vec[n]) for n in COLS], 1)
    d["b_gates"] = np.concatenate([a["b_ada"][0, 2 * D:3 * D], a["b_ada"][0, 5 * D:6 * D]])[None]
    d["w_ada"] = blocked(a["w_ada"][0])
    w = a["w_in"][0]
    d["w_lr"] = w[:, 3072:3104].reshape(KD, P, 32).transpose(1, 0, 2)
    d["w_in"] = blocked(np.concatenate([w[:, :3072], w[:, 3104:]], 1))
    d["gla_lr_w"] = a["gla_lr_w"][0]
    d["w_router"] = np.concatenate([a["w_router_group"][0], a["w_router_expert"][0]], 1).reshape(KD, P, NR).transpose(1, 0, 2)
    d["b_router"] = np.concatenate([a["b_router_group"][0], a["b_router_expert"][0]])[None]
    gu = np.concatenate([a["w_expert_gate"][0], a["w_expert_up"][0]], 2).reshape(NE, KD, P, 2 * EF).transpose(0, 2, 1, 3)
    dn = a["w_expert_down"][0].reshape(NE, EFT, P, D).transpose(0, 2, 1, 3)
    d["experts"] = np.concatenate([gu.reshape(NE, P, -1), dn.reshape(NE, P, -1)], 2)
    w2 = a["w_in_2"][0]
    lat = QR + KVR
    pad = lambda n: np.zeros((D, n), np.float32)
    d["w_in2"] = blocked(np.concatenate([w2[:, lat + ROT:], w2[:, :lat], pad(NOPE), w2[:, lat:lat + ROT],
                                         pad(WBLK - P - QH)], 1))
    d["w_uq"] = a["w_uq_2"][0].reshape(CQ, P, AH * QH).transpose(1, 0, 2)
    kv = a["w_ukv_2"][0].reshape(KVR, AH, 2, NOPE).transpose(0, 2, 1, 3).reshape(KVR, -1)
    d["w_ukv"] = kv.reshape(CKV, P, -1).transpose(1, 0, 2)
    d["w_out2"], d["w_peer_q"], d["w_ple_gate"] = (blocked(a[n][0]) for n in ("w_out_2", "w_peer_q_2", "w_ple_gate_2"))
    d["peer_keys"] = np.concatenate([a["peer_keys1_2"][0].T, a["peer_keys2_2"][0].T], 0)
    d["peer_u"], d["peer_v"] = a["peer_u_2"][0], a["peer_v_2"][0]
    d["p_T"] = a["p_2"][0, 0].T.reshape(PLE // P, P, S).transpose(1, 0, 2)
    d["w_ple_proj"] = a["w_ple_proj_2"][0].reshape(PLE // P, P, D).transpose(1, 0, 2)
    d["g_ffn_row"], d["g_final_row"] = a["g_ffn_2"][0][None], a["g_final_2"][None]
    d["norm_final"] = a["norm_final"][None]
    for n in ("w_branch_gla", "w_branch_ret", "w_out"):
        d[n] = blocked(a[n][0])
    return d


def kernel(**inputs):
    import concourse.bacc as bacc
    from concourse.bass_utils import run_bass_kernel_spmd as run

    nc = bacc.Bacc("TRN2", target_bir_lowering=False, num_devices=1)
    arrays, dram = {}, {}
    for n, v in layout(inputs).items():
        arrays["in_" + n] = np.ascontiguousarray(v)
        dram[n] = nc.dram_tensor("in_" + n, v.shape, mybir.dt.from_np(v.dtype), kind="ExternalInput").ap()
    dram["out"] = nc.dram_tensor("out", (S, D), F32, kind="ExternalOutput").ap()
    dram["h_dram"] = nc.dram_tensor("h_dram_out", (S, D), F32, kind="ExternalOutput").ap()
    program(nc, dram)
    r = run(nc, [arrays], core_ids=[0])
    return r.results[0]["out"].reshape(1, S, D)
```

```python
from contextlib import ExitStack

import numpy as np
import concourse.bass as bass
from concourse import mybir

F32 = mybir.dt.float32
U32 = mybir.dt.uint32
I32 = mybir.dt.int32
ALU = mybir.AluOpType
ACT = mybir.ActivationFunctionType
AX = mybir.AxisListType

P = 128
D = 1024
KD = D // P
S = 512
NT = S // P
CT = 256
NCT = CT // P
TOK = S + CT
NCH = TOK // P
WBLK = 512
H1 = 4
DK = 128
DV = 256
EPS = 1e-6
NEG = -1e30

COLS = dict(norm_mix=8, norm_ffn=8, b_ada=48, gla_norm=2, gla_b=8, g_mix=8, g_cq=3, g_ckv=2, g_mla=4, g_dil=4,
            g_ffn=8, g_ple=8)
COL0 = {}
_at = 0
for _n, _w in COLS.items():
    COL0[_n] = _at
    _at += _w
NCOL = _at


class Env:

    def __init__(self, nc, ctx, dram):
        self.nc, self.ctx, self.dram = nc, ctx, dram
        self.turns = [0] * 8
        self.tile_no = 0
        self.blocks = []
        self.block_tile = {}
        self.issued = 0
        self.used = 0
        self.shared = {}

    def sb(self, name, shape, dt=F32):
        return self.ctx.enter_context(self.nc.sbuf_tensor(name, shape, dt))

    def sem(self, name):
        return self.ctx.enter_context(self.nc.semaphore(name))

    def again(self, name, n):
        if name not in self.shared:
            self.shared[name] = [self.sem(name), 0]
        sem, base = self.shared[name]
        self.shared[name][1] += n
        return sem, base

    def tile(self):
        b = self.tile_no % 8
        self.tile_no += 1
        n = self.turns[b]
        self.turns[b] += 1
        return b, n

    def tiles(self, n):
        return [self.tile() for _ in range(n)]

    def take_block(self, last_tile):
        b = self.used
        self.used += 1
        self.block_tile[b] = last_tile
        return b


def bank_ready(env, eng, t):
    if t[1] > 0:
        eng.wait_ge(env.bank_free[t[0]], t[1])


def product_done(env, eng, t):
    eng.wait_ge(env.bank_full[t[0]], t[1] + 1)


def evacuated(env, eng, t):
    eng.wait_ge(env.bank_free[t[0]], t[1] + 1)


def load_blocks(env, sp, ahead=2):
    nc = env.nc
    for b in range(env.issued, min(env.used + ahead, len(env.blocks))):
        if b >= 2:
            product_done(env, sp, env.block_tile[b - 2])
        nc.sync.dma_start(env.wring[:, b % 2, :], env.blocks[b]).then_inc(env.w_loaded[b % 2], 16)
        env.issued = b + 1


def block_view(env, pe, b):
    pe.wait_ge(env.w_loaded[b % 2], 16 * (b // 2 + 1))
    return env.wring[:, b % 2, :].rearrange("p (k n) -> p k n", k=KD)


class Chain:

    def __init__(self, sem):
        self.sem, self.n = sem, 0

    def __call__(self, eng, ins):
        self.n += 1
        ins.then_inc(self.sem, 1)
        eng.wait_ge(self.sem, self.n)


class Group:

    def __init__(self, sem):
        self.sem, self.n = sem, 0

    def __call__(self, eng, steps):
        for ins in steps:
            ins.then_inc(self.sem, 1)
            self.n += 1
        eng.wait_ge(self.sem, self.n)


def col(env, name, j=0, n=1):
    return env.cols[:, COL0[name] + j:COL0[name] + j + n]


def stage_modulation(env):
    nc, dram = env.nc, env.dram
    tiles = env.tiles(12)
    blks = [env.take_block(t) for t in tiles]
    t_col = env.tile()
    t_bc = env.tiles(4)
    with ExitStack() as st:
        row = st.enter_context(nc.sbuf_tensor("ada_row", [2, 6 * D], F32))
        brow = st.enter_context(nc.sbuf_tensor("ada_brow", [1, 2 * D], F32))
        c2 = st.enter_context(nc.sbuf_tensor("c2", [P, KD, 2], F32))
        sc = st.enter_context(nc.sbuf_tensor("silu_c", [P, KD, 2], F32))
        c_in, c_act, b_in, cols_done = (env.sem(n) for n in ("c_in", "c_act", "b_in", "ada_cols_done"))
        with nc.Block() as block:
            @block.sync
            def _(sp):
                nc.sync.dma_start(c2[:], dram["c2"]).then_inc(c_in, 16)
                nc.sync.dma_start(env.ident[:], dram["ident"]).then_inc(env.const_in, 16)
                nc.sync.dma_start(env.cols[:], dram["cols"]).then_inc(env.const_in, 16)
                nc.sync.dma_start(env.h[:], dram["x"].rearrange("(t p) d -> p t d", p=P)).then_inc(env.x_in, 16)
                nc.sync.dma_start(env.hctx[:], dram["ctx"].rearrange("(t p) d -> p t d", p=P)).then_inc(env.x_in, 16)
                load_blocks(env, sp)
                nc.sync.dma_start(brow[:], dram["b_gates"]).then_inc(b_in, 16)

            @block.scalar
            def _(act):
                act.wait_ge(c_in, 16)
                nc.scalar.activation(sc[:], c2[:], ACT.Silu).then_inc(c_act, 1)
                for i, t in enumerate(tiles):
                    product_done(env, act, t)
                    nc.scalar.activation(row[:, i * WBLK:(i + 1) * WBLK], env.ps[0:2, t[0], :], ACT.Copy).then_inc(
                        env.bank_free[t[0]], 1)

            @block.vector
            def _(v):
                nc.vector.memset(env.ones[:], 1.0).then_inc(env.const_set, 1)
                nc.vector.memset(env.eps[:], EPS).then_inc(env.const_set, 1)
                v.wait_ge(env.const_in, 32)
                product_done(env, v, t_col)
                nc.vector.tensor_tensor(
                    env.ada[:], env.ps[:, t_col[0], 0:96].rearrange("p (j c) -> p j c", c=2),
                    col(env, "b_ada", 0, 48).unsqueeze(2).broadcast_to([P, 48, 2]), ALU.add).then_inc(
                    env.bank_free[t_col[0]], 1)
                evacuated(env, v, t_col)
                for n, (sc0, who, g) in enumerate(((8, 0, "norm_mix"), (8, 1, "norm_mix"), (32, 0, "norm_ffn"))):
                    nc.vector.scalar_tensor_tensor(env.gain[:, n, :], env.ada[:, sc0:sc0 + 8, who], 1.0,
                                                   col(env, g, 0, 8), ALU.add, ALU.mult).then_inc(cols_done, 1)
                for i, t in enumerate(t_bc):
                    product_done(env, v, t)
                    nc.vector.tensor_copy(env.gates[:, i // 2, (i % 2) * WBLK:(i % 2 + 1) * WBLK],
                                          env.ps[:, t[0], :]).then_inc(env.bank_free[t[0]], 1)
                v.wait_ge(cols_done, 3)

            @block.tensor
            def _(pe):
                pe.wait_ge(c_act, 1)
                for t, b in zip(tiles, blks):
                    w = block_view(env, pe, b)
                    bank_ready(env, pe, t)
                    for k in range(KD):
                        mm = nc.tensor.matmul(env.ps[0:2, t[0], :], sc[:, k, :], w[:, k, :],
                                              start=(k == 0), stop=(k == KD - 1))
                    mm.then_inc(env.bank_full[t[0]], 1)
                for t in tiles:
                    evacuated(env, pe, t)
                pe.wait_ge(env.const_in, 32)
                for j in range(48):
                    mm = nc.tensor.transpose(env.ps[:, t_col[0], 2 * j:2 * j + 2], row[:, j * P:(j + 1) * P],
                                             env.ident[0:2, 0:2])
                mm.then_inc(env.bank_full[t_col[0]], 1)
                pe.wait_ge(env.const_set, 2)
                pe.wait_ge(b_in, 16)
                for i, t in enumerate(t_bc):
                    bank_ready(env, pe, t)
                    at = (2 if i < 2 else 5) * D + (i % 2) * WBLK
                    nc.tensor.matmul(env.ps[:, t[0], :], env.ones[0:1, :], row[0:1, at:at + WBLK],
                                     start=True, stop=False)
                    nc.tensor.matmul(env.ps[:, t[0], :], env.ones[0:1, :], brow[0:1, i * WBLK:(i + 1) * WBLK],
                                     start=False, stop=True).then_inc(env.bank_full[t[0]], 1)


def stage_norm(env, name, src, parts, dst, store=None):
    nc = env.nc
    nt = sum(p[1] for p in parts)
    work = [(p, j, env.tile()) for p in parts for j in range(KD)]
    with ExitStack() as st:
        xn = st.enter_context(nc.sbuf_tensor(name + "_xn", [P, nt, D], F32))
        ss = st.enter_context(nc.sbuf_tensor(name + "_ss", [P, nt], F32))
        rs = st.enter_context(nc.sbuf_tensor(name + "_rs", [P, nt], F32))
        sq_done, sq0 = env.again("norm_sq", nt)
        rms_done, r0 = env.again("norm_rms", 1)
        inv_done, _ = env.again("norm_inv", 1)
        xn_done, xn0 = env.again("norm_xn", nt)
        out_s, _ = env.again("row_out", 0)
        with nc.Block() as block:
            @block.sync
            def _(sp):
                load_blocks(env, sp)
                if store is not None:
                    for t in range(nt):
                        sp.wait_ge(xn_done, xn0 + t + 1)
                        nc.sync.dma_start(store[t * P:(t + 1) * P, :], xn[:, t, :]).then_inc(out_s, 16)
                    sp.wait_ge(out_s, 16 * nt)

            @block.scalar
            def _(act):
                if name == "mix":
                    act.wait_ge(env.x_in, 32)
                for t in range(nt):
                    nc.scalar.activation(xn[:, t, :], src(t), ACT.Square, accum_out=ss[:, t:t + 1]).then_inc(sq_done, 1)
                act.wait_ge(sq_done, sq0 + nt)
                nc.scalar.activation(rs[:], ss[:], ACT.Sqrt, scale=1.0 / D, bias=env.eps[:, 0:1]).then_inc(rms_done, 1)

            @block.vector
            def _(v):
                v.wait_ge(rms_done, r0 + 1)
                nc.vector.reciprocal(ss[:], rs[:]).then_inc(inv_done, 1)
                v.wait_ge(inv_done, r0 + 1)
                for t in range(nt):
                    nc.vector.tensor_scalar(xn[:, t, :], src(t), ss[:, t:t + 1], None, ALU.mult).then_inc(xn_done, 1)
                for (t0, n, gain, shift), j, t in work:
                    product_done(env, v, t)
                    out, got = dst[:, j, t0 * P:(t0 + n) * P], env.ps[:, t[0], 0:n * P]
                    if shift is None:
                        ins = nc.vector.tensor_scalar(out, got, gain(j), None, ALU.mult)
                    else:
                        ins = nc.vector.tensor_scalar(out, got, gain(j), shift(j), ALU.mult, ALU.add)
                    ins.then_inc(env.bank_free[t[0]], 1)

            @block.tensor
            def _(pe):
                pe.wait_ge(env.const_in, 32)
                for (t0, n, _, _), j, t in work:
                    pe.wait_ge(xn_done, xn0 + t0 + n)
                    bank_ready(env, pe, t)
                    for i in range(n):
                        mm = nc.tensor.transpose(env.ps[:, t[0], i * P:(i + 1) * P],
                                                 xn[:, t0 + i, j * P:(j + 1) * P], env.ident[:])
                    mm.then_inc(env.bank_full[t[0]], 1)


def project(env, pe, t, out, w, lo, hi, rhs):
    bank_ready(env, pe, t)
    for k in range(KD):
        mm = env.nc.tensor.matmul(out, w[:, k, lo:hi], rhs(k), start=(k == 0), stop=(k == KD - 1))
    mm.then_inc(env.bank_full[t[0]], 1)


def chunks(ap):
    return ap.rearrange("p (c t) -> p c t", t=P)


def stage_gla_project(env, B):
    nc, dram = env.nc, env.dram
    hT = env.hT
    q_t = env.tiles(4)
    b_q = env.take_block(q_t[-1])
    k_t = [(j, lo, n, env.tile()) for j in range(4) for lo, n in ((0, S), (S, CT))]
    b_k = env.take_block(k_t[-1][3])
    v_t, b_v = [], []
    for half in range(2):
        v_t.append([(t, env.tile()) for t in range(NCH)])
        b_v.append(env.take_block(v_t[half][-1][1]))
    lr_t = [(d, lo, n, env.tile()) for d in range(2) for lo, n in ((0, S), (S, CT))]
    z_t = [(i, lo, n, env.tile()) for i in range(2 * H1) for lo, n in ((0, S), (S, CT))]
    lr_in, keep_set, e_done, ln_done, g_done, c_done = (
        env.sem(n) for n in ("lr_in", "keep_set", "gate_exp", "gate_ln", "gate_log", "gate_sum"))
    with ExitStack() as st:
        wlr = st.enter_context(nc.sbuf_tensor("wlr", [P, KD, 32], F32))
        lrw = st.enter_context(nc.sbuf_tensor("lrw", [16, 2, H1 * DK], F32))
        lr = st.enter_context(nc.sbuf_tensor("lr", [16, 2, TOK], F32))
        gate = st.enter_context(nc.sbuf_tensor("gate_log", [P, 2 * H1, TOK], F32))
        ea = B.sum
        keep = st.enter_context(nc.sbuf_tensor("keep", [P, TOK], F32))
        with nc.Block() as block:
            @block.sync
            def _(sp):
                nc.sync.dma_start(wlr[:], dram["w_lr"]).then_inc(lr_in, 16)
                nc.sync.dma_start(lrw[:], dram["gla_lr_w"].rearrange("d r n -> r d n")).then_inc(lr_in, 16)
                load_blocks(env, sp)

            @block.scalar
            def _(act):
                for j, t in enumerate(q_t):
                    product_done(env, act, t)
                    nc.scalar.activation(B.q[:, j, :], env.ps[:, t[0], :], ACT.Copy, scale=DK ** -0.5).then_inc(
                        env.bank_free[t[0]], 1)
                for half in range(2):
                    for i, t in v_t[half]:
                        product_done(env, act, t)
                        nc.scalar.activation(B.v[:, i, half * WBLK:(half + 1) * WBLK], env.ps[:, t[0], :],
                                             ACT.Copy).then_inc(env.bank_free[t[0]], 1)
                for n, (i, lo, w, t) in enumerate(z_t):
                    act.wait_ge(g_done, n + 1)
                    nc.scalar.activation(ea[:, i, lo:lo + w], env.ps[:, t[0], 0:w], ACT.Abs,
                                         bias=col(env, "gla_b", i)).then_inc(env.bank_free[t[0]], 1)
                for n, (i, lo, w, t) in enumerate(z_t):
                    evacuated(env, act, t)
                    nc.scalar.activation(ea[:, i, lo:lo + w], ea[:, i, lo:lo + w], ACT.Exp, scale=-1.0).then_inc(e_done, 1)
                act.wait_ge(e_done, len(z_t))
                for i in range(2 * H1):
                    nc.scalar.activation(ea[:, i, :], ea[:, i, :], ACT.Ln, bias=1.0).then_inc(ln_done, 1)

            @block.vector
            def _(v):
                nc.vector.memset(keep[:], 1.0).then_inc(keep_set, 1)
                v.wait_ge(keep_set, 1)
                nc.vector.memset(chunks(keep[:])[:, :, 0:1], 0.0).then_inc(keep_set, 1)
                for j, lo, n, t in k_t:
                    product_done(env, v, t)
                    nc.vector.tensor_copy(B.k[:, j, lo:lo + n], env.ps[:, t[0], 0:n]).then_inc(env.bank_free[t[0]], 1)
                for d, lo, n, t in lr_t:
                    product_done(env, v, t)
                    nc.vector.tensor_copy(lr[:, d, lo:lo + n], env.ps[0:16, t[0], 0:n]).then_inc(env.bank_free[t[0]], 1)
                m_done = 0
                for i, lo, n, t in z_t:
                    product_done(env, v, t)
                    b = col(env, "gla_b", i)
                    nc.vector.tensor_scalar(gate[:, i, lo:lo + n], env.ps[:, t[0], 0:n], b, 0.0,
                                            ALU.add, ALU.min).then_inc(g_done, 1)
                nz = len(z_t)
                v.wait_ge(g_done, nz)
                for i in range(2 * H1):
                    v.wait_ge(ln_done, i + 1)
                    nc.vector.tensor_tensor(gate[:, i, :], gate[:, i, :], ea[:, i, :], ALU.subtract).then_inc(g_done, 1)
                v.wait_ge(keep_set, 2)
                for i in range(2 * H1):
                    v.wait_ge(g_done, nz + i + 1)
                    nc.vector.tensor_tensor_scan(B.sum[:, i, :], keep[:], gate[:, i, :], 0.0,
                                                 ALU.mult, ALU.add).then_inc(c_done, 1)
                v.wait_ge(c_done, 2 * H1)
                ends = B.sum[:].rearrange("p i (c t) -> p i c t", t=P)[:, :, :, P - 1:P]
                nc.vector.tensor_copy(B.tot[:], ends.rearrange("p i c o -> p i (c o)")).then_inc(c_done, 1)
                v.wait_ge(c_done, 2 * H1 + 1)
                for i in range(H1, 2 * H1):
                    nc.vector.tensor_tensor(B.sum[:, i, :], gate[:, i, :], B.sum[:, i, :], ALU.subtract).then_inc(c_done, 1)

            @block.tensor
            def _(pe):
                w = block_view(env, pe, b_q)
                for j, t in enumerate(q_t):
                    project(env, pe, t, env.ps[:, t[0], :], w, j * P, (j + 1) * P, lambda k: hT[:, k, 0:S])
                w = block_view(env, pe, b_k)
                for j, lo, n, t in k_t:
                    project(env, pe, t, env.ps[:, t[0], 0:n], w, j * P, (j + 1) * P, lambda k: hT[:, k, lo:lo + n])
                for half in range(2):
                    w = block_view(env, pe, b_v[half])
                    for i, t in v_t[half]:
                        bank_ready(env, pe, t)
                        for k in range(KD):
                            mm = nc.tensor.matmul(env.ps[:, t[0], :], hT[:, k, i * P:(i + 1) * P], w[:, k, :],
                                                  start=(k == 0), stop=(k == KD - 1))
                        mm.then_inc(env.bank_full[t[0]], 1)
                pe.wait_ge(lr_in, 32)
                for d, lo, n, t in lr_t:
                    project(env, pe, t, env.ps[0:16, t[0], 0:n], wlr, 16 * d, 16 * d + 16, lambda k: hT[:, k, lo:lo + n])
                for _, _, _, t in lr_t:
                    evacuated(env, pe, t)
                for i, lo, n, t in z_t:
                    d, hd = i // H1, i % H1
                    bank_ready(env, pe, t)
                    nc.tensor.matmul(env.ps[:, t[0], 0:n], lrw[:, d, hd * DK:(hd + 1) * DK], lr[:, d, lo:lo + n],
                                     start=True, stop=True).then_inc(env.bank_full[t[0]], 1)


def stage_gla_core(env, B, oT):
    nc = env.nc
    G = 1.0 / 16.0
    walk = [[4, 5, 0, 1, 2], [5, 4, 3, 2, 1]]
    entry = [{0: 2, 1: 3, 2: 4, 3: 5}, {3: 2, 2: 3, 1: 4, 0: 5}]
    plan = []
    for hd in range(H1):
        tr = [env.tiles(2) for d in range(2)]
        up = [[env.tile() for _ in range(5)] for d in range(2)]
        sc = [env.tile() for _ in range(NT)]
        ov = [env.tile() for _ in range(NT)]
        plan.append((tr, up, sc, ov))
    fin = [env.tile() for _ in range(2 * H1)]
    names = ("g_arg", "g_exp", "g_mul", "g_dec", "g_zero", "g_sq", "g_rms", "g_inv", "g_nrm")
    arg_s, exp_s, mul_s, dec_s, zero_s, sq_s, rms_s, inv_s, nrm_s = (env.sem(n) for n in names)
    with ExitStack() as stk:
        T = lambda n, s: stk.enter_context(nc.sbuf_tensor("g_" + n, s, F32))
        arg = T("argt", [P, 2, S])
        e1, e3 = T("e1", [P, 2, S]), T("e3", [P, 2, S])
        e2 = arg
        e4 = T("e4", [P, 2, TOK])
        ktok = T("ktok", [P, 2, 5, DK])
        st = T("state", [P, 2, 6, DV])
        dec = T("decay", [P, 2 * H1, NCH])
        pm = T("pm", [P, 2, 2, P])
        o = T("o", [P, NT, H1, DV])
        sq = T("sqs", [P, DV])
        ss, rs = T("ss", [P, NT * H1]), T("rs", [P, NT * H1])
        mask = T("mask", [P, 2, P])
        mask_in = env.sem("g_mask_in")
        with nc.Block() as block:
            @block.sync
            def _(sp):
                nc.sync.dma_start(mask[:], env.dram["chunk_mask"]).then_inc(mask_in, 16)
                load_blocks(env, sp)

            @block.vector
            def _(v):
                nc.vector.memset(st[:, :, 0, :], 0.0).then_inc(zero_s, 1)
                v.wait_ge(dec_s, 1)
                v.wait_ge(zero_s, 1)
                for hd in range(H1):
                    tr, up, sc, ov = plan[hd]
                    if hd >= 1:
                        product_done(env, v, plan[hd - 1][3][-1])
                    for d in range(2):
                        c = B.sum[:, d * H1 + hd, :]
                        mid = chunks(c[:, 0:S])[:, :, 63 + d:64 + d].broadcast_to([P, NT, P])
                        nc.vector.tensor_tensor(chunks(arg[:, d, :]), chunks(c[:, 0:S]), mid, ALU.subtract).then_inc(arg_s, 1)
                        tot = B.tot[:, d * H1 + hd, :]
                        if d == 0:
                            nc.vector.tensor_tensor(chunks(e4[:, 0, :]), tot.unsqueeze(2).broadcast_to([P, NCH, P]),
                                                    chunks(c), ALU.subtract).then_inc(arg_s, 1)
                        else:
                            nc.vector.tensor_tensor(chunks(e3[:, 1, :]), chunks(c[:, 0:S]),
                                                    tot[:, 0:NT].unsqueeze(2).broadcast_to([P, NT, P]),
                                                    ALU.add).then_inc(arg_s, 1)
                    for d in range(2):
                        v.wait_ge(exp_s, 8 * hd + 4 * (d + 1))
                        for e, x in ((e1[:, d, :], B.q[:, hd, :]), (e2[:, d, :], B.k[:, hd, 0:S]),
                                     (e3[:, d, :], B.q[:, hd, :]), (e4[:, d, :], B.k[:, hd, :])):
                            nc.vector.tensor_tensor(e, e, x, ALU.mult).then_inc(mul_s, 1)
                    for d in range(2):
                        if hd >= 1:
                            product_done(env, v, plan[hd - 1][3][-1])
                        for n in range(5):
                            t = up[d][n]
                            product_done(env, v, t)
                            if n >= 1:
                                evacuated(env, v, up[d][n - 1])
                            i, ch = d * H1 + hd, walk[d][n]
                            nc.vector.scalar_tensor_tensor(st[:, d, n + 1, :], st[:, d, n, :], dec[:, i, ch:ch + 1],
                                                           env.ps[:, t[0], 0:DV], ALU.mult, ALU.add).then_inc(
                                env.bank_free[t[0]], 1)
                    v.wait_ge(mask_in, 16)
                    for ch in range(NT):
                        t = sc[ch]
                        product_done(env, v, t)
                        if hd * NT + ch >= 2:
                            pt = plan[hd][3][ch - 2] if ch >= 2 else plan[hd - 1][3][ch + 2]
                            product_done(env, v, pt)
                        nc.vector.tensor_tensor(pm[:, ch % 2, :, :],
                                                env.ps[:, t[0], 0:2 * P].rearrange("p (d t) -> p d t", d=2),
                                                mask[:], ALU.mult).then_inc(env.bank_free[t[0]], 1)
                v.wait_ge(rms_s, 1)
                nc.vector.reciprocal(ss[:], rs[:]).then_inc(inv_s, 1)
                v.wait_ge(inv_s, 1)
                for hd in range(H1):
                    for ch in range(NT):
                        n = hd * NT + ch
                        nc.vector.tensor_scalar(o[:, ch, hd, :], o[:, ch, hd, :], ss[:, n:n + 1], None,
                                                ALU.mult).then_inc(nrm_s, 1)
                for j, t in enumerate(fin):
                    product_done(env, v, t)
                    nc.vector.tensor_scalar(oT[:, j, :], env.ps[:, t[0], :], col(env, "gla_norm", j % 2), None,
                                            ALU.mult).then_inc(env.bank_free[t[0]], 1)

            @block.scalar
            def _(act):
                nc.scalar.activation(dec[:], B.tot[:], ACT.Exp, scale=G).then_inc(dec_s, 1)
                for hd in range(H1):
                    tr, up, sc, ov = plan[hd]
                    for d in range(2):
                        act.wait_ge(arg_s, 4 * hd + 2 * (d + 1))
                        c = B.sum[:, d * H1 + hd, :]
                        nc.scalar.activation(e1[:, d, :], arg[:, d, :], ACT.Exp, scale=G).then_inc(exp_s, 1)
                        nc.scalar.activation(e2[:, d, :], arg[:, d, :], ACT.Exp, scale=-G).then_inc(exp_s, 1)
                        if d == 0:
                            nc.scalar.activation(e3[:, 0, :], c[:, 0:S], ACT.Exp, scale=G).then_inc(exp_s, 1)
                            nc.scalar.activation(e4[:, 0, :], e4[:, 0, :], ACT.Exp, scale=G).then_inc(exp_s, 1)
                        else:
                            nc.scalar.activation(e3[:, 1, :], e3[:, 1, :], ACT.Exp, scale=G).then_inc(exp_s, 1)
                            nc.scalar.activation(e4[:, 1, :], c, ACT.Exp, scale=-G).then_inc(exp_s, 1)
                    for d in range(2):
                        for part, (lo, n) in enumerate(((0, 4), (4, 1))):
                            t = tr[d][part]
                            product_done(env, act, t)
                            if hd >= 1 and part == 0:
                                product_done(env, act, plan[hd - 1][1][d][4])
                            nc.scalar.activation(ktok[:, d, lo:lo + n, :],
                                                 env.ps[:, t[0], 0:n * P].rearrange("p (n k) -> p n k", k=DK),
                                                 ACT.Copy).then_inc(env.bank_free[t[0]], 1)
                    for ch in range(NT):
                        t = ov[ch]
                        n = hd * NT + ch
                        product_done(env, act, t)
                        if n >= 1:
                            act.wait_ge(sq_s, n)
                        nc.scalar.activation(sq[:], env.ps[:, t[0], 0:DV], ACT.Square, accum_out=ss[:, n:n + 1]).then_inc(sq_s, 1)
                        nc.scalar.activation(o[:, ch, hd, :], env.ps[:, t[0], 0:DV], ACT.Copy).then_inc(env.bank_free[t[0]], 1)
                act.wait_ge(sq_s, NT * H1)
                nc.scalar.activation(rs[:], ss[:], ACT.Sqrt, scale=1.0 / DV, bias=env.eps[:, 0:1]).then_inc(rms_s, 1)

            @block.tensor
            def _(pe):
                for hd in range(H1):
                    tr, up, sc, ov = plan[hd]
                    for d in range(2):
                        pe.wait_ge(mul_s, 8 * hd + 4 * (d + 1))
                        for part, (lo, n) in enumerate(((0, 4), (4, 1))):
                            t = tr[d][part]
                            bank_ready(env, pe, t)
                            for i in range(n):
                                ch = walk[d][lo + i]
                                mm = nc.tensor.transpose(env.ps[:, t[0], i * P:(i + 1) * P],
                                                         e4[:, d, ch * P:(ch + 1) * P], env.ident[:])
                            mm.then_inc(env.bank_full[t[0]], 1)
                    for d in range(2):
                        for n in range(5):
                            t, ch = up[d][n], walk[d][n]
                            evacuated(env, pe, tr[d][0 if n < 4 else 1])
                            bank_ready(env, pe, t)
                            nc.tensor.matmul(env.ps[:, t[0], 0:DV], ktok[:, d, n, :], B.v[:, ch, hd * DV:(hd + 1) * DV],
                                             start=True, stop=True).then_inc(env.bank_full[t[0]], 1)
                    for ch in range(NT):
                        t, cs = sc[ch], slice(ch * P, (ch + 1) * P)
                        bank_ready(env, pe, t)
                        for d in range(2):
                            mm = nc.tensor.matmul(env.ps[:, t[0], d * P:(d + 1) * P], e2[:, d, cs], e1[:, d, cs],
                                                  start=True, stop=True)
                        mm.then_inc(env.bank_full[t[0]], 1)
                    for ch in range(NT):
                        t, cs = ov[ch], slice(ch * P, (ch + 1) * P)
                        for d in range(2):
                            evacuated(env, pe, up[d][entry[d][ch] - 1])
                        evacuated(env, pe, sc[ch])
                        bank_ready(env, pe, t)
                        out = env.ps[:, t[0], 0:DV]
                        for d in range(2):
                            nc.tensor.matmul(out, e3[:, d, cs], st[:, d, entry[d][ch], :], start=(d == 0), stop=False)
                        for d in range(2):
                            mm = nc.tensor.matmul(out, pm[:, ch % 2, d, :], B.v[:, ch, hd * DV:(hd + 1) * DV],
                                                  start=False, stop=(d == 1))
                        mm.then_inc(env.bank_full[t[0]], 1)
                to_features(env, pe, fin, lambda ch, j: o[:, ch, j // 2, (j % 2) * P:(j % 2 + 1) * P],
                            lambda ch, j: pe.wait_ge(nrm_s, (j // 2) * NT + ch + 1))


def to_features(env, pe, tiles, src, wait):
    for j, t in enumerate(tiles):
        bank_ready(env, pe, t)
        for ch in range(NT):
            wait(ch, j)
            mm = env.nc.tensor.transpose(env.ps[:, t[0], ch * P:(ch + 1) * P], src(ch, j), env.ident[:])
        mm.then_inc(env.bank_full[t[0]], 1)


def stage_branch(env, name, oT, yT, first):
    nc, hT = env.nc, env.hT
    g_t = env.tiles(8)
    b_g = [env.take_block(g_t[3]), env.take_block(g_t[7])]
    m_t = env.tiles(8)
    b_m = [env.take_block(m_t[3]), env.take_block(m_t[7])]
    y_t = env.tiles(8)
    b_y = [env.take_block(y_t[3]), env.take_block(y_t[7])]
    mul_s, y_s = env.sem(name + "_gated"), env.sem(name + "_merged")
    with ExitStack() as st:
        gate = st.enter_context(nc.sbuf_tensor(name + "_gate", [P, KD, S], F32))
        merge = st.enter_context(nc.sbuf_tensor(name + "_merge", [P, KD, S], F32))
        with nc.Block() as block:
            @block.sync
            def _(sp):
                load_blocks(env, sp)

            @block.scalar
            def _(act):
                for j, t in enumerate(g_t):
                    product_done(env, act, t)
                    nc.scalar.activation(gate[:, j, :], env.ps[:, t[0], :], ACT.Silu).then_inc(env.bank_free[t[0]], 1)
                for j, t in enumerate(m_t):
                    product_done(env, act, t)
                    nc.scalar.activation(merge[:, j, :], env.ps[:, t[0], :], ACT.Sigmoid).then_inc(env.bank_free[t[0]], 1)

            @block.vector
            def _(v):
                for j, t in enumerate(g_t):
                    evacuated(env, v, t)
                    nc.vector.tensor_tensor(oT[:, j, :], oT[:, j, :], gate[:, j, :], ALU.mult).then_inc(mul_s, 1)
                for j, t in enumerate(y_t):
                    product_done(env, v, t)
                    evacuated(env, v, m_t[j])
                    out = yT[:, j, :] if first else merge[:, j, :]
                    nc.vector.tensor_tensor(out, merge[:, j, :], env.ps[:, t[0], :], ALU.mult).then_inc(
                        env.bank_free[t[0]], 1)
                    if not first:
                        evacuated(env, v, t)
                        nc.vector.tensor_tensor(yT[:, j, :], yT[:, j, :], merge[:, j, :], ALU.add).then_inc(y_s, 1)

            @block.tensor
            def _(pe):
                for tl, bl in ((g_t, b_g), (m_t, b_m)):
                    for i, b in enumerate(bl):
                        w = block_view(env, pe, b)
                        for j in range(4):
                            t = tl[4 * i + j]
                            project(env, pe, t, env.ps[:, t[0], :], w, j * P, (j + 1) * P, lambda k: hT[:, k, 0:S])
                pe.wait_ge(mul_s, KD)
                for i, b in enumerate(b_y):
                    w = block_view(env, pe, b)
                    for j in range(4):
                        t = y_t[4 * i + j]
                        project(env, pe, t, env.ps[:, t[0], :], w, j * P, (j + 1) * P, lambda k: oT[:, k, :])


def rope_mm(env, pe, tiles, perm, raw, ready):
    for j, t in enumerate(tiles):
        ready(j)
        bank_ready(env, pe, t)
        x = raw(j)
        env.nc.tensor.matmul(env.ps[0:x.shape[0], t[0], :], perm, x, start=True, stop=True).then_inc(env.bank_full[t[0]], 1)


def rope_dve(env, v, tiles, x, tab, sn, cos_s, rope_s):
    nc = env.nc
    for j, t in enumerate(tiles):
        a = x(j)
        rows = a.shape[0]
        product_done(env, v, t)
        nc.vector.tensor_tensor(a, a, tab[0:rows, 0, :], ALU.mult).then_inc(cos_s, 1)
        if j >= 2:
            v.wait_ge(rope_s, j - 1)
        nc.vector.tensor_tensor(sn[0:rows, j % 2, :], env.ps[0:rows, t[0], :], tab[0:rows, 1, :], ALU.mult).then_inc(
            env.bank_free[t[0]], 1)
        v.wait_ge(cos_s, j + 1)
        evacuated(env, v, t)
        nc.vector.tensor_tensor(a, a, sn[0:rows, j % 2, :], ALU.add).then_inc(rope_s, 1)


def stage_ret_project(env, R):
    nc, hT, dram = env.nc, env.hT, env.dram
    q_t = env.tiles(4)
    b_q = env.take_block(q_t[-1])
    k_t = env.tiles(4)
    kc_t = env.tiles(NCT)
    b_k = env.take_block(kc_t[-1])
    r_t = env.tiles(8)
    v_t, b_v = [], []
    for half in range(2):
        v_t.append(env.tiles(NCH))
        b_v.append(env.take_block(v_t[half][-1]))
    tab_in, cos_s, rope_s = env.sem("ret_tab_in"), env.sem("ret_cos"), env.sem("ret_rope")
    with ExitStack() as st:
        sn = st.enter_context(nc.sbuf_tensor("r_sn", [P, 2, S], F32))
        tab = st.enter_context(nc.sbuf_tensor("r_tab", [P, 2, S], F32))
        perm = st.enter_context(nc.sbuf_tensor("r_perm", [P, P], F32))
        with nc.Block() as block:
            @block.sync
            def _(sp):
                nc.sync.dma_start(tab[:], dram["rope_axial"]).then_inc(tab_in, 16)
                nc.sync.dma_start(perm[:], dram["perm_axial"]).then_inc(tab_in, 16)
                load_blocks(env, sp)

            @block.scalar
            def _(act):
                for j, t in enumerate(q_t + k_t):
                    product_done(env, act, t)
                    nc.scalar.activation(R.qk[:, j, :], env.ps[:, t[0], :], ACT.Copy).then_inc(env.bank_free[t[0]], 1)
                for i, t in enumerate(kc_t):
                    product_done(env, act, t)
                    nc.scalar.activation(R.kc[:, i, :], env.ps[:, t[0], :], ACT.Copy).then_inc(env.bank_free[t[0]], 1)
                for half in range(2):
                    for i, t in enumerate(v_t[half]):
                        product_done(env, act, t)
                        nc.scalar.activation(R.v[:, i, half * WBLK:(half + 1) * WBLK], env.ps[:, t[0], :],
                                             ACT.Copy).then_inc(env.bank_free[t[0]], 1)

            @block.vector
            def _(v):
                v.wait_ge(tab_in, 32)
                rope_dve(env, v, r_t, lambda j: R.qk[:, j, :], tab, sn, cos_s, rope_s)

            @block.tensor
            def _(pe):
                w = block_view(env, pe, b_q)
                for j, t in enumerate(q_t):
                    project(env, pe, t, env.ps[:, t[0], :], w, j * P, (j + 1) * P, lambda k: hT[:, k, 0:S])
                w = block_view(env, pe, b_k)
                for j, t in enumerate(k_t):
                    project(env, pe, t, env.ps[:, t[0], :], w, j * P, (j + 1) * P, lambda k: hT[:, k, 0:S])
                for i, t in enumerate(kc_t):
                    by_token(env, pe, t, WBLK, w, NT + i)
                pe.wait_ge(tab_in, 32)
                rope_mm(env, pe, r_t, perm[:], lambda j: R.qk[:, j, :], lambda j: evacuated(env, pe, (q_t + k_t)[j]))
                for half in range(2):
                    w = block_view(env, pe, b_v[half])
                    for i, t in enumerate(v_t[half]):
                        by_token(env, pe, t, WBLK, w, i)


def by_token(env, pe, t, n, w, i, lo=0):
    bank_ready(env, pe, t)
    for k in range(KD):
        mm = env.nc.tensor.matmul(env.ps[:, t[0], 0:n], env.hT[:, k, i * P:(i + 1) * P], w[:, k, lo:lo + n],
                                  start=(k == 0), stop=(k == KD - 1))
    mm.then_inc(env.bank_full[t[0]], 1)


def stage_ret_core(env, R, oT):
    nc, dram = env.nc, env.dram
    st_t = [[env.tile() for d in range(2)] for hd in range(H1)]
    plan = [([env.tile() for _ in range(NT)], [env.tile() for _ in range(NT)]) for hd in range(H1)]
    fin = env.tiles(2 * H1)
    in_s, kd_s, qd_s, bn_s, mv_s, rms_s, inv_s, nrm_s, o_s = (env.sem("rc_" + n) for n in (
        "in", "kd", "qd", "bn", "mv", "rms", "inv", "nrm", "o"))
    qdec_in = [env.sem(f"rc_qdec_in{i}") for i in range(2)]
    with ExitStack() as stk:
        T = lambda n, s: stk.enter_context(nc.sbuf_tensor("rc_" + n, s, F32))
        band = T("band", [P, H1, 896])
        qdec = T("qdec", [P, 2, 2, S])
        kdec = T("kdec", [P, 2 * H1, NCT])
        kd = T("kd", [P, 2, 2, NCT, DK])
        st = T("st", [P, H1, 2, DV])
        qd = T("qd", [P, 2, S])
        pm = T("pm", [P, NT, S])
        o = T("o", [P, NT, H1, DV])
        bn = T("bn", [P, NT * H1, 6])
        mv = T("mv", [P, NT * H1, 2])
        rs = T("rs", [P, NT * H1, 1])
        iv = T("iv", [P, NT * H1, 1])
        with nc.Block() as block:
            @block.sync
            def _(sp):
                nc.sync.dma_start(kdec[:], dram["ret_kdec"]).then_inc(in_s, 16)
                nc.sync.dma_start(band[:], dram["ret_band"]).then_inc(in_s, 16)
                for hd in range(H1):
                    if hd >= 2:
                        sp.wait_ge(qd_s, 2 * (hd - 1))
                    row = dram["ret_qdec"][hd:hd + 1].broadcast_to([P, 2, S])
                    nc.sync.dma_start(qdec[:, hd % 2], row).then_inc(qdec_in[hd % 2], 16)
                load_blocks(env, sp)

            @block.vector
            def _(v):
                v.wait_ge(in_s, 32)
                for hd in range(H1):
                    for d in range(2):
                        if hd >= 2:
                            product_done(env, v, st_t[hd - 2][d])
                        for i in range(NCT):
                            nc.vector.tensor_scalar(kd[:, hd % 2, d, i, :], R.kc[:, i, hd * DK:(hd + 1) * DK],
                                                    kdec[:, d * H1 + hd, i:i + 1], None, ALU.mult).then_inc(kd_s, 1)
                for hd in range(H1):
                    sc, ov = plan[hd]
                    if hd >= 1:
                        product_done(env, v, plan[hd - 1][1][-1])
                    v.wait_ge(qdec_in[hd % 2], 16 * (hd // 2 + 1))
                    for d in range(2):
                        nc.vector.tensor_tensor(qd[:, d, :], R.qk[:, hd, :], qdec[:, hd % 2, d, :], ALU.mult).then_inc(qd_s, 1)
                    for J, t in enumerate(sc):
                        product_done(env, v, t)
                        nc.vector.tensor_tensor(pm[:, J, :], env.ps[:, t[0], :], band[:, hd, 384 - J * P:384 - J * P + S],
                                                ALU.mult).then_inc(env.bank_free[t[0]], 1)
                    for I, t in enumerate(ov):
                        product_done(env, v, t)
                        nc.vector.bn_stats(bn[:, hd * NT + I, :], env.ps[:, t[0], 0:DV]).then_inc(bn_s, 1)
                for n in range(NT * H1):
                    v.wait_ge(bn_s, n + 1)
                    nc.vector.bn_aggr(mv[:, n, :], bn[:, n, :]).then_inc(mv_s, 1)
                v.wait_ge(rms_s, 1)
                nc.vector.reciprocal(iv[:], rs[:]).then_inc(inv_s, 1)
                v.wait_ge(inv_s, 1)
                v.wait_ge(o_s, NT * H1)
                for hd in range(H1):
                    for I in range(NT):
                        n = hd * NT + I
                        nc.vector.tensor_scalar(o[:, I, hd, :], o[:, I, hd, :], mv[:, n, 0:1], iv[:, n, :],
                                                ALU.subtract, ALU.mult).then_inc(nrm_s, 1)
                for j, t in enumerate(fin):
                    product_done(env, v, t)
                    nc.vector.tensor_copy(oT[:, j, :], env.ps[:, t[0], :]).then_inc(env.bank_free[t[0]], 1)

            @block.scalar
            def _(act):
                for hd in range(H1):
                    for d in range(2):
                        t = st_t[hd][d]
                        product_done(env, act, t)
                        nc.scalar.activation(st[:, hd, d, :], env.ps[:, t[0], 0:DV], ACT.Copy).then_inc(env.bank_free[t[0]], 1)
                for hd in range(H1):
                    for I, t in enumerate(plan[hd][1]):
                        act.wait_ge(bn_s, hd * NT + I + 1)
                        nc.scalar.activation(o[:, I, hd, :], env.ps[:, t[0], 0:DV], ACT.Copy).then_inc(env.bank_free[t[0]], 1)
                for hd in range(H1):
                    for t in plan[hd][1]:
                        evacuated(env, act, t)
                act.wait_ge(mv_s, NT * H1)
                nc.scalar.activation(rs[:], mv[:, :, 1:2], ACT.Sqrt, bias=env.eps[:, 0:1]).then_inc(rms_s, 1)
                nc.scalar.sem_inc(o_s, NT * H1)

            @block.tensor
            def _(pe):
                for hd in range(H1):
                    for d in range(2):
                        t = st_t[hd][d]
                        pe.wait_ge(kd_s, hd * 4 + d * 2 + 2)
                        bank_ready(env, pe, t)
                        for i in range(NCT):
                            mm = nc.tensor.matmul(env.ps[:, t[0], 0:DV], kd[:, hd % 2, d, i, :],
                                                  R.v[:, NT + i, hd * DV:(hd + 1) * DV], start=(i == 0), stop=(i == NCT - 1))
                        mm.then_inc(env.bank_full[t[0]], 1)
                for hd in range(H1):
                    sc, ov = plan[hd]
                    for J, t in enumerate(sc):
                        bank_ready(env, pe, t)
                        nc.tensor.matmul(env.ps[:, t[0], :], R.qk[:, 4 + hd, J * P:(J + 1) * P], R.qk[:, hd, :],
                                         start=True, stop=True).then_inc(env.bank_full[t[0]], 1)
                    pe.wait_ge(qd_s, 2 * (hd + 1))
                    for d in range(2):
                        evacuated(env, pe, st_t[hd][d])
                    for I, t in enumerate(ov):
                        bank_ready(env, pe, t)
                        out, ts = env.ps[:, t[0], 0:DV], slice(I * P, (I + 1) * P)
                        for d in range(2):
                            nc.tensor.matmul(out, qd[:, d, ts], st[:, hd, d, :], start=(d == 0), stop=False)
                        for J in range(NT):
                            evacuated(env, pe, sc[J])
                            mm = nc.tensor.matmul(out, pm[:, J, ts], R.v[:, J, hd * DV:(hd + 1) * DV],
                                                  start=False, stop=(J == NT - 1))
                        mm.then_inc(env.bank_full[t[0]], 1)
                to_features(env, pe, fin, lambda ch, j: o[:, ch, j // 2, (j % 2) * P:(j % 2 + 1) * P],
                            lambda ch, j: pe.wait_ge(nrm_s, (j // 2) * NT + ch + 1))


def stage_out(env, name, src, gate):
    nc = env.nc
    tl = [env.tiles(NT) for _ in range(2)]
    bl = [env.take_block(t[-1]) for t in tl]
    g_s = env.sem(name + "_sum")
    with ExitStack() as st:
        tmp = st.enter_context(nc.sbuf_tensor(name + "_tmp", [P, 2 * NT, WBLK], F32))
        with nc.Block() as block:
            @block.sync
            def _(sp):
                load_blocks(env, sp)

            @block.vector
            def _(v):
                for half in range(2):
                    cs = slice(half * WBLK, (half + 1) * WBLK)
                    for i, t in enumerate(tl[half]):
                        product_done(env, v, t)
                        got = env.ps[:, t[0], :]
                        if gate is None:
                            nc.vector.tensor_tensor(env.h[:, i, cs], env.h[:, i, cs], got, ALU.add).then_inc(
                                env.bank_free[t[0]], 1)
                        else:
                            x = tmp[:, half * NT + i, :]
                            nc.vector.tensor_tensor(x, env.gates[:, gate, cs], got, ALU.mult).then_inc(env.bank_free[t[0]], 1)
                            evacuated(env, v, t)
                            nc.vector.tensor_tensor(env.h[:, i, cs], env.h[:, i, cs], x, ALU.add).then_inc(g_s, 1)

            @block.tensor
            def _(pe):
                for half in range(2):
                    w = block_view(env, pe, bl[half])
                    for i, t in enumerate(tl[half]):
                        bank_ready(env, pe, t)
                        for k in range(KD):
                            mm = nc.tensor.matmul(env.ps[:, t[0], :], src[:, k, i * P:(i + 1) * P], w[:, k, :],
                                                  start=(k == 0), stop=(k == KD - 1))
                        mm.then_inc(env.bank_full[t[0]], 1)


def stage_rownorm(env, name, dst, row_name, store=None, nt=NT, ahead=2):
    nc = env.nc
    row_in, run16 = env.again("row_in", 16)
    run = run16 // 16
    sq_s, sq0 = env.again("row_sq", nt)
    rms_s, _ = env.again("row_rms", 1)
    inv_s, _ = env.again("row_inv", 1)
    done, d0 = env.again("row_done", nt)
    out_s, _ = env.again("row_out", 0)
    with ExitStack() as st:
        row = st.enter_context(nc.sbuf_tensor(name + "_row", [P, D], F32))
        sq = st.enter_context(nc.sbuf_tensor(name + "_sqs", [P, 2, D], F32))
        ss = st.enter_context(nc.sbuf_tensor(name + "_ss", [P, nt], F32))
        rs = st.enter_context(nc.sbuf_tensor(name + "_rs", [P, nt], F32))
        with nc.Block() as block:
            @block.sync
            def _(sp):
                nc.sync.dma_start(row[:], env.dram[row_name].broadcast_to([P, D])).then_inc(row_in, 16)
                load_blocks(env, sp, ahead)
                if store is not None:
                    rows = store.rearrange("(t p) d -> t p d", p=P)
                    for t in range(nt):
                        sp.wait_ge(done, d0 + t + 1)
                        nc.sync.dma_start(rows[t], dst[:, t, :]).then_inc(out_s, 16)
                    sp.wait_ge(out_s, 2 * 16 * NT)

            @block.scalar
            def _(act):
                for t in range(nt):
                    if t >= 2:
                        act.wait_ge(sq_s, sq0 + t - 1)
                    nc.scalar.activation(sq[:, t % 2, :], env.h[:, t, :], ACT.Square, accum_out=ss[:, t:t + 1]).then_inc(sq_s, 1)
                act.wait_ge(sq_s, sq0 + nt)
                nc.scalar.activation(rs[:], ss[:], ACT.Sqrt, scale=1.0 / D, bias=env.eps[:, 0:1]).then_inc(rms_s, 1)

            @block.vector
            def _(v):
                v.wait_ge(rms_s, run + 1)
                nc.vector.reciprocal(ss[:], rs[:]).then_inc(inv_s, 1)
                v.wait_ge(row_in, run16 + 16)
                v.wait_ge(inv_s, run + 1)
                for t in range(nt):
                    nc.vector.scalar_tensor_tensor(dst[:, t, :], env.h[:, t, :], ss[:, t:t + 1], row[:],
                                                   ALU.mult, ALU.mult).then_inc(done, 1)


NG, EPG = 4, 8
NE = NG * EPG
EF = 256
EFT = EF // P
NR = NG + NE
EW = KD * 2 * EF + EFT * D


ROWB = P
PICKS = 2
NB = NE + (PICKS * S - NE) // ROWB
SLOT = 3
LAST = NB // SLOT


def stage_router(env, E):
    nc, dram = env.nc, env.dram
    t_lg, t_rank, t_rows = env.tile(), env.tile(), env.tile()
    in_s, exp_s, ch_s, pair_s = (env.sem("rt_" + n) for n in ("in", "exp", "chain", "pair"))
    with ExitStack() as st:
        T = lambda n, s, d=F32: st.enter_context(nc.sbuf_tensor("rt_" + n, s, d))
        wr, br = T("w", [P, KD, NR]), T("b", [1, NR])
        idx = T("idx", [P, 2, NE])
        before, row_no, block_no = T("before", [P, P]), T("row_no", [P, ROWB]), T("block_no", [P, NB])
        tok_no = T("tok_no", [P, NT])
        lg, gp = T("lg", [P, NT, NR]), T("gp", [P, NT, 8])
        gm, gi, gif = T("gm", [P, NT, 8]), T("gi", [P, NT, 8], U32), T("gif", [P, NT, 8])
        ng, gx, gs, gw = T("ng", [P, NT]), T("gx", [P, NT, 8]), T("gs", [P, NT]), T("gw", [P, NT])
        em, ev, ei, eif = T("em", [P, NT, NE]), T("ev", [P, NT, 8]), T("ei", [P, NT, 8], U32), T("eif", [P, NT, 8])
        df, dx, one_dx = T("df", [P, NT]), T("dx", [P, NT]), T("one_dx", [P, NT])
        picked, both = T("picked", [P, PICKS, NT, NE]), T("both", [P, NT, NE])
        count, count_u, blocks, ends = T("count", [P, NE]), T("count_u", [P, NE], U32), T("blocks", [P, NE]), T("ends", [P, NE])
        starts, at = T("starts", [P, NE]), T("at", [P, NT, NE])
        pos, split, splitf = T("pos", [P, PICKS, NT]), T("split", [P, 2, PICKS, NT], U32), T("splitf", [P, 2, PICKS, NT])
        in_row, in_block = T("in_row", [P, PICKS, NT, ROWB]), T("in_block", [P, PICKS, NT, NB])
        past, block_e = T("past", [P, NB, NE]), T("block_e", [P, NB])
        with nc.Block() as block:
            @block.sync
            def _(sp):
                loads = ((wr, "w_router"), (br, "b_router"), (idx, "expert_numbers"), (before, "token_before"),
                         (row_no, "row_numbers"), (block_no, "block_numbers"), (tok_no, "token_numbers"))
                for dst, name in loads:
                    nc.sync.dma_start(dst[:], dram[name]).then_inc(in_s, 16)
                load_blocks(env, sp)

            @block.tensor
            def _(pe):
                pe.wait_ge(in_s, 112)
                bank_ready(env, pe, t_lg)
                for t in range(NT):
                    out = env.ps[:, t_lg[0], t * NR:(t + 1) * NR]
                    for k in range(KD):
                        nc.tensor.matmul(out, env.hT[:, k, t * P:(t + 1) * P], wr[:, k, :], start=(k == 0), stop=False)
                    mm = nc.tensor.matmul(out, env.ones[0:1, :], br[:], start=False, stop=True)
                mm.then_inc(env.bank_full[t_lg[0]], 1)
                bank_ready(env, pe, t_rank)
                pe.wait_ge(pair_s, 3)
                for t in range(NT + 1):
                    out = env.ps[:, t_rank[0], t * NE:(t + 1) * NE]
                    for u in range(min(t + 1, NT)):
                        mm = nc.tensor.matmul(out, before[:] if u == t else env.ones[:], both[:, u, :],
                                              start=(u == 0), stop=(u == min(t, NT - 1)))
                mm.then_inc(env.bank_full[t_rank[0]], 1)
                bank_ready(env, pe, t_rows)
                pe.wait_ge(pair_s, 4)
                for n in range(PICKS * NT):
                    mm = nc.tensor.matmul(env.ps[:, t_rows[0], 0:NB], in_row[:, n // NT, n % NT, :],
                                          in_block[:, n // NT, n % NT, :], start=(n == 0), stop=(n == PICKS * NT - 1))
                mm.then_inc(env.bank_full[t_rows[0]], 1)

            @block.scalar
            def _(act):
                for t in range(NT):
                    act.wait_ge(pair_s, 1)
                    nc.scalar.activation(gx[:, t, :], gp[:, t, :], ACT.Exp, bias=ng[:, t:t + 1],
                                         accum_out=gs[:, t:t + 1]).then_inc(exp_s, 1)
                act.wait_ge(pair_s, 2)
                nc.scalar.activation(dx[:], df[:], ACT.Exp).then_inc(exp_s, 1)

            @block.vector
            def _(v):
                step = Group(ch_s)
                V = nc.vector
                ts = range(NT)
                step(v, [V.memset(gp[:], NEG)])
                v.wait_ge(in_s, 112)
                product_done(env, v, t_lg)
                V.tensor_copy(lg[:], env.ps[:, t_lg[0], 0:NT * NR].rearrange("p (t n) -> p t n", t=NT)).then_inc(
                    env.bank_free[t_lg[0]], 1)
                evacuated(env, v, t_lg)
                step(v, [V.tensor_copy(gp[:, :, 0:NG], lg[:, :, 0:NG])])
                step(v, [V.max(gm[:, t, :], gp[:, t, :]) for t in ts])
                V.tensor_scalar(ng[:], gm[:, :, 0], -1.0, None, ALU.mult).then_inc(pair_s, 1)
                step(v, [V.max_index(gi[:, t, :], gm[:, t, :], gp[:, t, :]) for t in ts])
                step(v, [V.tensor_copy(gif[:], gi[:])])
                step(v, [V.tensor_scalar(em[:, t, :], idx[:, 1, :], gif[:, t, 0:1], -NEG, ALU.is_equal, ALU.mult) for t in ts])
                step(v, [V.scalar_tensor_tensor(em[:, t, :], em[:, t, :], NEG, lg[:, t, NG:NR], ALU.add, ALU.add) for t in ts])
                step(v, [V.max(ev[:, t, :], em[:, t, :]) for t in ts])
                step(v, [V.max_index(ei[:, t, :], ev[:, t, :], em[:, t, :]) for t in ts])
                V.tensor_tensor(df[:], ev[:, :, 1], ev[:, :, 0], ALU.subtract).then_inc(pair_s, 1)
                step(v, [V.tensor_copy(eif[:], ei[:])])
                step(v, [V.tensor_scalar(picked[:, k, t, :], idx[:, 0, :], eif[:, t, k:k + 1], None, ALU.is_equal)
                         for k in range(PICKS) for t in ts])
                V.tensor_tensor(both[:], picked[:, 0], picked[:, 1], ALU.add).then_inc(pair_s, 1)
                v.wait_ge(exp_s, NT + 1)
                step(v, [V.reciprocal(gw[:], gs[:]), V.tensor_scalar(one_dx[:], dx[:], 1.0, None, ALU.add)])
                step(v, [V.reciprocal(E.weight[:, 0, :], one_dx[:])])
                step(v, [V.tensor_tensor(E.weight[:, 0, :], E.weight[:, 0, :], gw[:], ALU.mult)])
                step(v, [V.tensor_tensor(E.weight[:, 1, :], dx[:], E.weight[:, 0, :], ALU.mult)])
                product_done(env, v, t_rank)
                step(v, [V.tensor_scalar(count[:], env.ps[:, t_rank[0], NT * NE:(NT + 1) * NE], ROWB - 1.0, None, ALU.add)])
                step(v, [V.tensor_copy(count_u[:], count[:])])
                step(v, [V.tensor_scalar(count_u[:], count_u[:], 7, None, ALU.logical_shift_right)])
                step(v, [V.tensor_copy(blocks[:], count_u[:])])
                step(v, [V.tensor_tensor_scan(ends[:], env.ones[:, 0:NE], blocks[:], 0.0, ALU.mult, ALU.add)])
                step(v, [V.tensor_tensor(starts[:], ends[:], blocks[:], ALU.subtract)])
                V.scalar_tensor_tensor(at[:], starts[:].unsqueeze(1).broadcast_to([P, NT, NE]), float(ROWB),
                                       env.ps[:, t_rank[0], 0:NT * NE].rearrange("p (t e) -> p t e", t=NT),
                                       ALU.mult, ALU.add).then_inc(env.bank_free[t_rank[0]], 1)
                evacuated(env, v, t_rank)
                step(v, [V.tensor_tensor(picked[:, k], picked[:, k], at[:], ALU.mult) for k in range(PICKS)])
                step(v, [V.reduce_sum(pos[:, k], picked[:, k], axis=AX.X) for k in range(PICKS)])
                step(v, [V.tensor_copy(E.pos[:], pos[:])])
                step(v, [V.tensor_scalar(split[:, 0], E.pos[:], 127, None, ALU.bitwise_and),
                         V.tensor_scalar(split[:, 1], E.pos[:], 7, None, ALU.logical_shift_right)])
                step(v, [V.tensor_copy(splitf[:], split[:])])
                both_kt = [(k, t) for k in range(PICKS) for t in ts]
                step(v, [V.tensor_scalar(in_row[:, k, t, :], row_no[:], splitf[:, 0, k, t:t + 1], None, ALU.is_equal)
                         for k, t in both_kt] +
                        [V.tensor_scalar(in_block[:, k, t, :], block_no[:], splitf[:, 1, k, t:t + 1], tok_no[:, t:t + 1],
                                         ALU.is_equal, ALU.mult) for k, t in both_kt[:-1]])
                k, t = both_kt[-1]
                V.tensor_scalar(in_block[:, k, t, :], block_no[:], splitf[:, 1, k, t:t + 1], tok_no[:, t:t + 1],
                                ALU.is_equal, ALU.mult).then_inc(pair_s, 1)
                step(v, [V.tensor_tensor(past[:], ends[:].unsqueeze(1).broadcast_to([P, NB, NE]),
                                         block_no[:].unsqueeze(2).broadcast_to([P, NB, NE]), ALU.is_le)])
                step(v, [V.reduce_sum(block_e[:], past[:], axis=AX.X)])
                step(v, [V.tensor_scalar(block_e[:], block_e[:], float(NE - 1), None, ALU.min)])
                step(v, [V.tensor_copy(E.block_expert[:], block_e[:])])
                product_done(env, v, t_rows)
                V.tensor_copy(E.row_token[:], env.ps[:, t_rows[0], 0:NB]).then_inc(env.bank_free[t_rows[0]], 1)
                evacuated(env, v, t_rows)


def stage_experts(env, E):
    nc, dram = env.nc, env.dram
    names = ("idx", "rows_full", "xT_done", "gu_full", "silu_done", "hid_done", "hidT_full", "hidT_done", "dn_full", "y_done")
    idx_s, rows_full, xT_done, gu_full, silu_done, hid_done, hidT_full, hidT_done, dn_full, y_done = (
        env.sem("ex_" + n) for n in names)
    x_got, w_got, y_out = ([env.sem(f"ex_{n}{s}") for s in range(SLOT)] for n in ("x_got", "w_got", "y_out"))
    gain, shift = (lambda j: env.gain[:, 2, j:j + 1]), (lambda j: env.ada[:, 24 + j, 0:1])
    ROWS, GU, HID, DOWN = [0, 1], [2, 3, 4], 5, [6, 7]
    y_rows = dram["y_dram"].rearrange("(b p) d -> b p d", p=ROWB)
    with ExitStack() as st:
        T = lambda n, s, d=F32: st.enter_context(nc.sbuf_tensor("ex_" + n, s, d))
        idx = T("idx", [P, SLOT], U32)
        x, xT = T("x", [P, SLOT, D]), T("xT", [P, SLOT, KD, P])
        w = T("w", [P, SLOT, EW])
        silu, hid, hidT = T("silu", [P, SLOT, EF]), T("hid", [P, SLOT, EF]), T("hidT", [P, SLOT, EFT, P])
        y = T("y", [P, SLOT, D])
        wg = [w[:, s, 0:KD * 2 * EF].rearrange("p (k n) -> p k n", k=KD) for s in range(SLOT)]
        wd = [w[:, s, KD * 2 * EF:EW].rearrange("p (k n) -> p k n", k=EFT) for s in range(SLOT)]

        def after(i, s):
            return (i, s + 1) if s + 1 < SLOT else (i + 1, 0)

        with nc.Block() as block:
            @block.gpsimd
            def _(pool):
                with pool.Fori(0, LAST) as i:
                    for s in range(SLOT):
                        b = SLOT * i + s
                        pool.wait_ge(rows_full, 2 * b + 2)
                        pool.nop(nofuse=True)
                        nc.gpsimd.tensor_copy(idx[:, s:s + 1], E.row_token[:, bass.ds(b, 1)]).then_inc(idx_s, 1)
                        pool.wait_ge(idx_s, b + 1)
                        pool.nop(nofuse=True)
                        nc.gpsimd.indirect_dma_start(x[:, s, :], None, dram["xn_dram"], bass.IndirectOffsetOnAxis(
                            ap=idx[:, s:s + 1], axis=0)).then_inc(x_got[s], 16)

            @block.sync
            def _(sp):
                def load(b, s):
                    e = nc.sync.value_load(E.block_expert[0:1, bass.ds(b, 1)], min_val=0, max_val=NE - 1)
                    nc.sync.dma_start(w[:, s, :], dram["experts"][bass.ds(e, 1)].rearrange("o p n -> p (o n)")
                                      ).then_inc(w_got[s], 16)

                def store(b, s):
                    sp.wait_ge(y_done, 2 + 2 * b + 2)
                    sp.nop(nofuse=True)
                    nc.sync.dma_start(y_rows[bass.ds(b, 1)].rearrange("o p d -> p (o d)"), y[:, s, :]).then_inc(y_out[s], 16)

                for s in range(SLOT):
                    sp.sem_inc(y_out[s], 16)
                    load(s, s)
                with sp.Fori(0, LAST - 1) as i:
                    for s in range(SLOT):
                        sp.wait_ge(dn_full, 2 * (SLOT * i + s) + 2)
                        sp.nop(nofuse=True)
                        load(SLOT * i + SLOT + s, s)
                        store(SLOT * i + s, s)
                for s in range(SLOT):
                    store(SLOT * (LAST - 1) + s, s)
                load_blocks(env, sp)
                for s in range(SLOT):
                    sp.wait_ge(y_out[s], 16 + 16 * LAST)

            @block.tensor
            def _(pe):
                def rows(i, s, first=False):
                    b = SLOT * i + s
                    pe.wait_ge(x_got[s], 16 * i + 16)
                    for n in range(2):
                        if not first:
                            pe.wait_ge(xT_done, KD * b - KD // 2 * (1 - n))
                        for j in range(KD // 2):
                            mm = nc.tensor.transpose(env.ps[:, ROWS[n], j * P:(j + 1) * P],
                                                     x[:, s, (n * KD // 2 + j) * P:(n * KD // 2 + j + 1) * P], env.ident[:])
                        mm.then_inc(rows_full, 1)

                def gate_up(i, s):
                    b = SLOT * i + s
                    pe.wait_ge(w_got[s], 16 * i + 16)
                    pe.wait_ge(xT_done, KD * b + KD)
                    for k in range(KD):
                        mm = nc.tensor.matmul(env.ps[:, GU[s], :], xT[:, s, k, :], wg[s][:, k, :],
                                              start=(k == 0), stop=(k == KD - 1))
                    mm.then_inc(gu_full, 1)

                def hidden(i, s):
                    pe.wait_ge(hid_done, SLOT * i + s + 1)
                    for k in range(EFT):
                        mm = nc.tensor.transpose(env.ps[:, HID, k * P:(k + 1) * P], hid[:, s, k * P:(k + 1) * P], env.ident[:])
                    mm.then_inc(hidT_full, 1)

                def down(i, s):
                    b = SLOT * i + s
                    pe.wait_ge(hidT_done, b + 1)
                    for n in range(2):
                        pe.wait_ge(y_done, 2 * b + n + 1)
                        for k in range(EFT):
                            mm = nc.tensor.matmul(env.ps[:, DOWN[n], :], hidT[:, s, k, :],
                                                  wd[s][:, k, n * WBLK:(n + 1) * WBLK], start=(k == 0), stop=(k == EFT - 1))
                        mm.then_inc(dn_full, 1)

                pe.sem_inc(rows_full, 2 * SLOT)
                rows(0, 0, first=True)
                gate_up(0, 0)
                rows(0, 1)
                with pe.Fori(0, LAST - 1) as i:
                    for s in range(SLOT):
                        now = after(i, s)
                        gate_up(*now)
                        hidden(i, s)
                        rows(*after(*now))
                        down(i, s)
                for s in range(SLOT):
                    now = after(LAST - 1, s)
                    if s + 1 < SLOT:
                        gate_up(*now)
                    hidden(LAST - 1, s)
                    if s + 2 < SLOT:
                        rows(*after(*now))
                    down(LAST - 1, s)

            @block.scalar
            def _(act):
                def gate(i, s):
                    act.wait_ge(gu_full, SLOT * i + s + 1)
                    nc.scalar.activation(silu[:, s, :], env.ps[:, GU[s], 0:EF], ACT.Silu).then_inc(silu_done, 1)

                def finish(i, s):
                    b = SLOT * i + s
                    act.wait_ge(hidT_full, b + 1)
                    nc.scalar.activation(hidT[:, s].rearrange("p k t -> p (k t)"), env.ps[:, HID, 0:EF],
                                         ACT.Copy).then_inc(hidT_done, 1)
                    act.wait_ge(y_out[s], 16 * i + 16)
                    for n in range(2):
                        act.wait_ge(dn_full, 2 * b + n + 1)
                        nc.scalar.activation(y[:, s, n * WBLK:(n + 1) * WBLK], env.ps[:, DOWN[n], :],
                                             ACT.Copy).then_inc(y_done, 1)

                act.sem_inc(y_done, 2)
                gate(0, 0)
                with act.Fori(0, LAST - 1) as i:
                    for s in range(SLOT):
                        gate(*after(i, s))
                        finish(i, s)
                for s in range(SLOT):
                    if s + 1 < SLOT:
                        gate(*after(LAST - 1, s))
                    finish(LAST - 1, s)

            @block.vector
            def _(v):
                def features(i, s):
                    b = SLOT * i + s
                    for n in range(2):
                        v.wait_ge(rows_full, 2 * SLOT + 2 * b + n + 1)
                        for j in range(KD // 2):
                            k = n * KD // 2 + j
                            nc.vector.tensor_scalar(xT[:, s, k, :], env.ps[:, ROWS[n], j * P:(j + 1) * P], gain(k), shift(k),
                                                    ALU.mult, ALU.add).then_inc(xT_done, 1)

                def product(i, s):
                    v.wait_ge(silu_done, SLOT * i + s + 1)
                    nc.vector.tensor_tensor(hid[:, s, :], silu[:, s, :], env.ps[:, GU[s], EF:2 * EF],
                                            ALU.mult).then_inc(hid_done, 1)

                features(0, 0)
                with v.Fori(0, LAST - 1) as i:
                    for s in range(SLOT):
                        product(i, s)
                        features(*after(i, s))
                for s in range(SLOT):
                    product(LAST - 1, s)
                    if s + 1 < SLOT:
                        features(*after(LAST - 1, s))


def stage_expert_sum(env, E):
    nc, dram = env.nc, env.dram
    got = [env.sem(f"es_got{t}") for t in range(NT)]
    first_s, sum_s = env.sem("es_first"), env.sem("es_sum")
    with nc.sbuf_tensor("es_y", [P, NT, PICKS, D], F32) as y:
        with nc.Block() as block:
            @block.gpsimd
            def _(pool):
                for t in range(NT):
                    for k in range(PICKS):
                        nc.gpsimd.indirect_dma_start(y[:, t, k, :], None, dram["y_dram"], bass.IndirectOffsetOnAxis(
                            ap=E.pos[:, k, t:t + 1], axis=0)).then_inc(got[t], 16)

            @block.scalar
            def _(act):
                for t in range(NT):
                    act.wait_ge(got[t], 16 * PICKS)
                    nc.scalar.activation(y[:, t, 0, :], y[:, t, 0, :], ACT.Copy, scale=E.weight[:, 0, t:t + 1]).then_inc(first_s, 1)

            @block.vector
            def _(v):
                step = Chain(sum_s)
                for t in range(NT):
                    v.wait_ge(first_s, t + 1)
                    step(v, nc.vector.scalar_tensor_tensor(y[:, t, 1, :], y[:, t, 1, :], E.weight[:, 1, t:t + 1], y[:, t, 0, :],
                                                           ALU.mult, ALU.add))
                    step(v, nc.vector.tensor_tensor(y[:, t, 1, :], y[:, t, 1, :], env.gates[:, 1, :], ALU.mult))
                    step(v, nc.vector.tensor_tensor(env.h[:, t, :], env.h[:, t, :], y[:, t, 1, :], ALU.add))


AH = 8
QR, KVR = 384, 256
CQ, CKV = QR // P, KVR // P
NOPE, ROT, VH = 64, 32, 64
QH = NOPE + ROT
DH = 64


def stage_second_project(env, M):
    nc, dram = env.nc, env.dram
    q_t, k_t, r_t = env.tiles(4), env.tiles(4), env.tiles(8)
    v_t, c_t = env.tiles(NT), env.tiles(NT)
    e_t, kr_t = env.tiles(NT), env.tile()
    blks = [env.take_block(t) for t in (q_t[-1], k_t[-1], v_t[-1], c_t[-1], kr_t)]
    tab_in, cos_s, rope_s = (env.sem("sp_" + n) for n in ("tab", "cos", "rope"))
    with ExitStack() as st:
        sn = st.enter_context(nc.sbuf_tensor("sp_sn", [P, 2, S], F32))
        tab = st.enter_context(nc.sbuf_tensor("sp_tabs", [P, 2, S], F32))
        perm = st.enter_context(nc.sbuf_tensor("sp_perm", [P, P], F32))
        with nc.Block() as block:
            @block.sync
            def _(sp):
                nc.sync.dma_start(tab[:], dram["rope_dil"]).then_inc(tab_in, 16)
                nc.sync.dma_start(perm[:], dram["perm_dil"]).then_inc(tab_in, 16)
                load_blocks(env, sp)

            @block.scalar
            def _(act):
                for j, t in enumerate(q_t + k_t):
                    product_done(env, act, t)
                    nc.scalar.activation(M.dqk[:, j, :], env.ps[:, t[0], :], ACT.Copy,
                                         scale=DH ** -0.5 if j < 4 else 1.0).then_inc(env.bank_free[t[0]], 1)
                for tl, dst, n in ((v_t, M.dv, WBLK), (c_t, M.c, WBLK)):
                    for i, t in enumerate(tl):
                        product_done(env, act, t)
                        nc.scalar.activation(dst[:, i, 0:n], env.ps[:, t[0], 0:n], ACT.Copy).then_inc(env.bank_free[t[0]], 1)
                for i, t in enumerate(e_t):
                    product_done(env, act, t)
                    nc.scalar.activation(M.c[:, i, WBLK:WBLK + P], env.ps[:, t[0], 0:P], ACT.Copy).then_inc(env.bank_free[t[0]], 1)
                product_done(env, act, kr_t)
                nc.scalar.activation(M.kr[:], env.ps[0:QH, kr_t[0], :], ACT.Copy).then_inc(env.bank_free[kr_t[0]], 1)

            @block.vector
            def _(v):
                v.wait_ge(tab_in, 32)
                rope_dve(env, v, r_t, lambda j: M.dqk[:, j, :], tab, sn, cos_s, rope_s)

            @block.tensor
            def _(pe):
                for b, tl in zip(blks[:2], (q_t, k_t)):
                    w = block_view(env, pe, b)
                    for j, t in enumerate(tl):
                        project(env, pe, t, env.ps[:, t[0], :], w, j * P, (j + 1) * P, lambda k: env.hT[:, k, 0:S])
                pe.wait_ge(tab_in, 32)
                rope_mm(env, pe, r_t, perm[:], lambda j: M.dqk[:, j, :], lambda j: evacuated(env, pe, (q_t + k_t)[j]))
                for b, tl in zip(blks[2:4], (v_t, c_t)):
                    w = block_view(env, pe, b)
                    for i, t in enumerate(tl):
                        by_token(env, pe, t, WBLK, w, i)
                w = block_view(env, pe, blks[4])
                for i, t in enumerate(e_t):
                    by_token(env, pe, t, P, w, i)
                project(env, pe, kr_t, env.ps[0:QH, kr_t[0], :], w, P, P + QH, lambda k: env.hT[:, k, 0:S])


def stage_latent_expand(env, M):
    nc, dram = env.nc, env.dram
    c_t = env.tiles(CQ + CKV)
    q_t = env.tiles(AH)
    k_t = env.tiles(AH)
    r_t = env.tiles(AH + 1)
    v_t = env.tiles(NT)
    tab_in, sq_s, rms_s, inv_s, nrm_s, cos_s, rope_s = (env.sem("le_" + n) for n in (
        "tab", "sq", "rms", "inv", "nrm", "cos", "rope"))
    parts = ((0, QR), (QR, KVR))
    with ExitStack() as st:
        T = lambda n, s: st.enter_context(nc.sbuf_tensor("le_" + n, s, F32))
        sn, tab, perm = T("sn", [P, 2, S]), T("tabs", [P, 2, S]), T("perm", [P, P])
        wq, wkv = T("wq", [P, CQ, AH * QH]), T("wkv", [P, CKV, AH * (NOPE + VH)])
        cT = T("cT", [P, CQ + CKV, S])
        sq, ss, rs = T("sqs", [P, 2, QR]), T("ss", [P, 2, NT]), T("rs", [P, 2, NT])
        with nc.Block() as block:
            @block.sync
            def _(sp):
                nc.sync.dma_start(wq[:], dram["w_uq"]).then_inc(tab_in, 16)
                nc.sync.dma_start(wkv[:], dram["w_ukv"]).then_inc(tab_in, 16)
                nc.sync.dma_start(tab[0:QH], dram["rope_mla"]).then_inc(tab_in, 16)
                nc.sync.dma_start(perm[0:QH, 0:QH], dram["perm_mla"]).then_inc(tab_in, 16)
                load_blocks(env, sp)

            @block.scalar
            def _(act):
                n = 0
                for p, (lo, w) in enumerate(parts):
                    for t in range(NT):
                        if n >= 2:
                            act.wait_ge(sq_s, n - 1)
                        nc.scalar.activation(sq[:, n % 2, 0:w], M.c[:, t, lo:lo + w], ACT.Square,
                                             accum_out=ss[:, p, t:t + 1]).then_inc(sq_s, 1)
                        n += 1
                act.wait_ge(sq_s, n)
                for p, (lo, w) in enumerate(parts):
                    nc.scalar.activation(rs[:, p, :], ss[:, p, :], ACT.Sqrt, scale=1.0 / w, bias=env.eps[:, 0:1]).then_inc(rms_s, 1)
                for hd, t in enumerate(q_t):
                    product_done(env, act, t)
                    nc.scalar.activation(M.q[:, hd, :], env.ps[0:QH, t[0], :], ACT.Copy, scale=QH ** -0.5).then_inc(
                        env.bank_free[t[0]], 1)
                for hd, t in enumerate(k_t):
                    product_done(env, act, t)
                    nc.scalar.activation(M.k[0:NOPE, hd, :], env.ps[0:NOPE, t[0], :], ACT.Copy).then_inc(env.bank_free[t[0]], 1)
                for i, t in enumerate(v_t):
                    product_done(env, act, t)
                    nc.scalar.activation(M.v[:, i, :], env.ps[:, t[0], :], ACT.Copy).then_inc(env.bank_free[t[0]], 1)

            @block.vector
            def _(v):
                v.wait_ge(rms_s, 2)
                nc.vector.reciprocal(ss[:], rs[:]).then_inc(inv_s, 1)
                v.wait_ge(inv_s, 1)
                for p, (lo, w) in enumerate(parts):
                    for t in range(NT):
                        x = M.c[:, t, lo:lo + w]
                        nc.vector.tensor_scalar(x, x, ss[:, p, t:t + 1], None, ALU.mult).then_inc(nrm_s, 1)
                for j, t in enumerate(c_t):
                    product_done(env, v, t)
                    nc.vector.tensor_scalar(cT[:, j, :], env.ps[:, t[0], :], col(env, "g_cq", j), None, ALU.mult).then_inc(
                        env.bank_free[t[0]], 1)
                v.wait_ge(tab_in, 64)
                rope_dve(env, v, r_t, lambda j: M.q[:, j, :] if j < AH else M.kr[:], tab, sn, cos_s, rope_s)
                v.wait_ge(rope_s, AH + 1)
                nc.vector.tensor_copy(M.k[NOPE:QH, :, :], M.kr[NOPE:QH, :].unsqueeze(1).broadcast_to([ROT, AH, S])).then_inc(rope_s, 1)

            @block.tensor
            def _(pe):
                to_features(env, pe, c_t, lambda t, j: M.c[:, t, j * P:(j + 1) * P],
                            lambda t, j: pe.wait_ge(nrm_s, (t + 1) + (NT if j >= CQ else 0)))
                pe.wait_ge(tab_in, 64)
                for t in c_t:
                    evacuated(env, pe, t)
                for hd, t in enumerate(q_t):
                    bank_ready(env, pe, t)
                    for k in range(CQ):
                        mm = nc.tensor.matmul(env.ps[0:QH, t[0], :], wq[:, k, hd * QH:(hd + 1) * QH], cT[:, k, :],
                                              start=(k == 0), stop=(k == CQ - 1))
                    mm.then_inc(env.bank_full[t[0]], 1)
                for hd, t in enumerate(k_t):
                    bank_ready(env, pe, t)
                    for k in range(CKV):
                        mm = nc.tensor.matmul(env.ps[0:NOPE, t[0], :], wkv[:, k, hd * NOPE:(hd + 1) * NOPE], cT[:, CQ + k, :],
                                              start=(k == 0), stop=(k == CKV - 1))
                    mm.then_inc(env.bank_full[t[0]], 1)
                rope_mm(env, pe, r_t, perm[0:QH, 0:QH], lambda j: M.q[:, j, :] if j < AH else M.kr[:],
                        lambda j: evacuated(env, pe, q_t[j]) if j < AH else None)
                for i, t in enumerate(v_t):
                    bank_ready(env, pe, t)
                    for k in range(CKV):
                        mm = nc.tensor.matmul(env.ps[:, t[0], :], cT[:, CQ + k, i * P:(i + 1) * P], wkv[:, k, AH * NOPE:],
                                              start=(k == 0), stop=(k == CKV - 1))
                    mm.then_inc(env.bank_full[t[0]], 1)


def stage_attention(env, M, o):
    nc = env.nc
    units = []
    for hd in range(AH):
        for qt in range(NT):
            units += [(0, hd, qt), (1, hd, qt)]
    nu = len(units)
    sc, tr, pv = [None] * nu, [None] * nu, [None] * nu
    for s in range(nu + 2):
        if s < nu:
            sc[s] = env.tile()
        if 1 <= s <= nu:
            tr[s - 1] = env.tile()
        if s >= 2:
            pv[s - 2] = env.tile()
    mask_in, max_s, neg_s, ex_s, inv_s = (env.sem("at_" + n) for n in ("mask", "max", "neg", "exp", "inv"))

    def weights_ready(eng, u):
        if units[u][0] == 0:
            evacuated(env, eng, sc[u])
        else:
            eng.wait_ge(ex_s, u // 2 + 1)

    with ExitStack() as st:
        T = lambda n, s: st.enter_context(nc.sbuf_tensor("at_" + n, s, F32))
        mask = T("masks", [P, NT, S])
        sm = T("sm", [P, 2, S])
        pr, pt = T("pr", [P, 2, S]), T("pt", [P, 2, S])
        mx, nm, sums, inv = T("mx", [P, nu]), T("nm", [P, nu]), T("sums", [P, nu]), T("invs", [P, nu])
        with nc.Block() as block:
            @block.sync
            def _(sp):
                nc.sync.dma_start(mask[:], env.dram["dil_mask"]).then_inc(mask_in, 16)
                load_blocks(env, sp)

            @block.vector
            def _(v):
                v.wait_ge(mask_in, 16)
                for s in range(nu + 2):
                    if s < nu:
                        kind, hd, qt = units[s]
                        product_done(env, v, sc[s])
                        if kind == 0:
                            nc.vector.tensor_reduce(nm[:, s:s + 1], env.ps[:, sc[s][0], :], AX.X, ALU.max,
                                                    negate=True).then_inc(neg_s, 1)
                        else:
                            if s >= 4:
                                v.wait_ge(ex_s, s // 2 - 1)
                            nc.vector.tensor_tensor_reduce(sm[:, (s // 2) % 2, :], env.ps[:, sc[s][0], :], mask[:, qt, :],
                                                           1.0, NEG, ALU.add, ALU.max, mx[:, s:s + 1]).then_inc(
                                env.bank_free[sc[s][0]], 1)
                            evacuated(env, v, sc[s])
                            nc.vector.tensor_scalar(nm[:, s:s + 1], mx[:, s:s + 1], -1.0, None, ALU.mult).then_inc(neg_s, 1)
                    if s >= 2:
                        u = s - 2
                        kind, hd, qt = units[u]
                        weights_ready(v, u)
                        nc.vector.reciprocal(inv[:, u:u + 1], sums[:, u:u + 1]).then_inc(inv_s, 1)
                        product_done(env, v, pv[u])
                        v.wait_ge(inv_s, u + 1)
                        nc.vector.tensor_scalar(o[:, kind, qt, hd * VH:(hd + 1) * VH], env.ps[:, pv[u][0], 0:VH],
                                                inv[:, u:u + 1], None, ALU.mult).then_inc(env.bank_free[pv[u][0]], 1)

            @block.scalar
            def _(act):
                for s in range(nu + 1):
                    if s < nu:
                        kind, hd, qt = units[s]
                        act.wait_ge(neg_s, s + 1)
                        if s >= 2:
                            product_done(env, act, tr[s - 2])
                        if kind == 0:
                            nc.scalar.activation(pr[:, s % 2, :], env.ps[:, sc[s][0], :], ACT.Exp, bias=nm[:, s:s + 1],
                                                 accum_out=sums[:, s:s + 1]).then_inc(env.bank_free[sc[s][0]], 1)
                        else:
                            nc.scalar.activation(pr[:, s % 2, :], sm[:, (s // 2) % 2, :], ACT.Exp, bias=nm[:, s:s + 1],
                                                 accum_out=sums[:, s:s + 1]).then_inc(ex_s, 1)
                    if s >= 1:
                        u = s - 1
                        product_done(env, act, tr[u])
                        if u >= 2:
                            product_done(env, act, pv[u - 2])
                        nc.scalar.activation(pt[:, u % 2, :], env.ps[:, tr[u][0], :], ACT.Copy).then_inc(
                            env.bank_free[tr[u][0]], 1)

            @block.tensor
            def _(pe):
                for s in range(nu + 2):
                    if s < nu:
                        kind, hd, qt = units[s]
                        qs = slice(qt * P, (qt + 1) * P)
                        bank_ready(env, pe, sc[s])
                        if kind == 0:
                            q, k = M.q[:, hd, qs], M.k[:, hd, :]
                        else:
                            rows = slice(DH * (hd % 2), DH * (hd % 2 + 1))
                            q, k = M.dqk[rows, hd // 2, qs], M.dqk[rows, 4 + hd // 2, :]
                        nc.tensor.matmul(env.ps[:, sc[s][0], :], q, k, start=True, stop=True).then_inc(env.bank_full[sc[s][0]], 1)
                    if 1 <= s <= nu:
                        u = s - 1
                        weights_ready(pe, u)
                        bank_ready(env, pe, tr[u])
                        for kt in range(NT):
                            mm = nc.tensor.transpose(env.ps[:, tr[u][0], kt * P:(kt + 1) * P],
                                                     pr[:, u % 2, kt * P:(kt + 1) * P], env.ident[:])
                        mm.then_inc(env.bank_full[tr[u][0]], 1)
                    if s >= 2:
                        u = s - 2
                        kind, hd, qt = units[u]
                        evacuated(env, pe, tr[u])
                        bank_ready(env, pe, pv[u])
                        val = M.v if kind == 0 else M.dv
                        for kt in range(NT):
                            mm = nc.tensor.matmul(env.ps[:, pv[u][0], 0:VH], pt[:, u % 2, kt * P:(kt + 1) * P],
                                                  val[:, kt, hd * VH:(hd + 1) * VH], start=(kt == 0), stop=(kt == NT - 1))
                        mm.then_inc(env.bank_full[pv[u][0]], 1)


def stage_mix(env, o, mixT):
    nc = env.nc
    tl = env.tiles(KD)
    sq_s, rms_s, inv_s, nrm_s = (env.sem("mx_" + n) for n in ("sq", "rms", "inv", "nrm"))
    W = AH * VH
    with ExitStack() as st:
        T = lambda n, s: st.enter_context(nc.sbuf_tensor("mx_" + n, s, F32))
        sq, ss, rs = T("sqs", [P, 2, W]), T("ss", [P, 2, NT]), T("rs", [P, 2, NT])
        with nc.Block() as block:
            @block.sync
            def _(sp):
                load_blocks(env, sp)

            @block.scalar
            def _(act):
                for n in range(2 * NT):
                    if n >= 2:
                        act.wait_ge(sq_s, n - 1)
                    nc.scalar.activation(sq[:, n % 2, :], o[:, n // NT, n % NT, :], ACT.Square,
                                         accum_out=ss[:, n // NT, n % NT:n % NT + 1]).then_inc(sq_s, 1)
                act.wait_ge(sq_s, 2 * NT)
                nc.scalar.activation(rs[:], ss[:], ACT.Sqrt, scale=1.0 / W, bias=env.eps[:, 0:1]).then_inc(rms_s, 1)

            @block.vector
            def _(v):
                v.wait_ge(rms_s, 1)
                nc.vector.reciprocal(ss[:], rs[:]).then_inc(inv_s, 1)
                v.wait_ge(inv_s, 1)
                for n in range(2 * NT):
                    x = o[:, n // NT, n % NT, :]
                    nc.vector.tensor_scalar(x, x, ss[:, n // NT, n % NT:n % NT + 1], None, ALU.mult).then_inc(nrm_s, 1)
                for j, t in enumerate(tl):
                    product_done(env, v, t)
                    nc.vector.tensor_scalar(mixT[:, j, :], env.ps[:, t[0], :], col(env, "g_mla", j), None, ALU.mult).then_inc(
                        env.bank_free[t[0]], 1)

            @block.tensor
            def _(pe):
                to_features(env, pe, tl, lambda t, j: o[:, j // 4, t, (j % 4) * P:(j % 4 + 1) * P],
                            lambda t, j: pe.wait_ge(nrm_s, (j // 4) * NT + t + 1))


PH = 8
PK = 128
HALF = 64
TK = 16
SLOTS = PH * TK
RING = 8
GT = 2
DT = NT - GT
DS = DT * P
PER = 2 * RING
TURNS = SLOTS // PER
STEP = 4
PARTS = 2 * GT
PB = PK // PARTS
GRP = KD


def stage_memory_route(env, rows, pairs, gate):
    nc, dram = env.nc, env.dram
    q_t = env.tiles(PH)
    blks = [env.take_block(q_t[3]), env.take_block(q_t[7])]
    s_t = [[[env.tile() for half in range(2)] for hg in range(2)] for t in range(NT)]
    in_s, grp_s, top_s, exp_s = (env.sem("pk_" + n) for n in ("in", "group", "top", "exp"))
    with ExitStack() as st:
        T = lambda n, s, d=F32: st.enter_context(nc.sbuf_tensor("pk_" + n, s, d))
        qp = T("qp", [P, PH, S])
        keys = T("keys", [P, PK])
        iota = T("iota", [P, TK])
        sc = T("sc", [P, 2, 2, PH, PK])
        rest = T("rest", [P, 2, PH, PK])
        v, ix, ixf = T("v", [P, 2, PH, TK]), T("ix", [P, 2, PH, TK], U32), T("ixf", [P, 2, PH, TK])
        cand, cand2 = T("cand", [P, PH, TK * TK]), T("cand2", [P, PH, TK * TK])
        top, pos = T("top", [P, PH, TK]), T("pos", [P, PH, TK], U32)
        ab, abf = T("ab", [P, 2, PH, TK], U32), T("abf", [P, 2, PH, TK])
        eq = T("eq", [P, 2, PH * TK, TK])
        pick = T("pick", [P, 2, PH * TK])
        ex, sm = T("ex", [P, 2, PH, TK]), T("sm", [P, 2, PH])
        with nc.Block() as block:
            @block.sync
            def _(sp):
                nc.sync.dma_start(keys[:], dram["peer_keys"]).then_inc(in_s, 16)
                nc.sync.dma_start(iota[:], dram["iota16"]).then_inc(in_s, 16)
                load_blocks(env, sp, 0)

            @block.tensor
            def _(pe):
                for i, b in enumerate(blks):
                    w = block_view(env, pe, b)
                    for j in range(4):
                        t = q_t[4 * i + j]
                        project(env, pe, t, env.ps[:, t[0], :], w, j * P, (j + 1) * P, lambda k: env.hT[:, k, 0:S])
                pe.wait_ge(in_s, 32)
                for t in range(NT):
                    for hg in range(2):
                        for half in range(2):
                            tl, r = s_t[t][hg][half], slice(half * HALF, (half + 1) * HALF)
                            bank_ready(env, pe, tl)
                            for n in range(4):
                                hd = 4 * hg + n
                                evacuated(env, pe, q_t[hd])
                                mm = nc.tensor.matmul(env.ps[:, tl[0], n * PK:(n + 1) * PK], qp[r, hd, t * P:(t + 1) * P],
                                                      keys[r, :], start=True, stop=True)
                            mm.then_inc(env.bank_full[tl[0]], 1)

            @block.scalar
            def _(act):
                for hd, t in enumerate(q_t):
                    product_done(env, act, t)
                    nc.scalar.activation(qp[:, hd, :], env.ps[:, t[0], :], ACT.Copy).then_inc(env.bank_free[t[0]], 1)
                for t in range(NT):
                    if t >= 2:
                        act.wait_ge(top_s, t - 1)
                    for hg in range(2):
                        for half in range(2):
                            tl = s_t[t][hg][half]
                            product_done(env, act, tl)
                            nc.scalar.activation(sc[:, t % 2, half, 4 * hg:4 * hg + 4, :],
                                                 env.ps[:, tl[0], :].rearrange("p (h k) -> p h k", k=PK),
                                                 ACT.Copy).then_inc(env.bank_free[tl[0]], 1)
                    act.wait_ge(top_s, t + 1)
                    nc.scalar.activation(ex[:, t % 2], ex[:, t % 2], ACT.Exp).then_inc(exp_s, 1)

            @block.vector
            def _(ve):
                V = nc.vector
                group = Group(grp_s)
                ve.wait_ge(in_s, 32)
                halves = [(half, hd) for half in range(2) for hd in range(PH)]

                def finish(t):
                    ve.wait_ge(exp_s, t + 1)
                    group(ve, [V.reduce_sum(sm[:, 0, :], ex[:, t % 2], axis=AX.X)])
                    group(ve, [V.reciprocal(sm[:, 1, :], sm[:, 0, :])])
                    group(ve, [V.tensor_tensor(gate[:, t, :].rearrange("p (h k) -> p h k", k=TK), ex[:, t % 2],
                                               sm[:, 1, :].unsqueeze(2).broadcast_to([P, PH, TK]), ALU.mult)])

                for t in range(NT):
                    for hg in range(2):
                        for half in range(2):
                            evacuated(env, ve, s_t[t][hg][half])
                    s = sc[:, t % 2]
                    group(ve, [V.max(v[:, a, h, 0:8], s[:, a, h, :]) for a, h in halves])
                    group(ve, [V.max_index(ix[:, a, h, 0:8], v[:, a, h, 0:8], s[:, a, h, :]) for a, h in halves] +
                          [V.match_replace(rest[:, a, h, :], v[:, a, h, 0:8], s[:, a, h, :], NEG) for a, h in halves])
                    group(ve, [V.max(v[:, a, h, 8:16], rest[:, a, h, :]) for a, h in halves])
                    group(ve, [V.max_index(ix[:, a, h, 8:16], v[:, a, h, 8:16], rest[:, a, h, :]) for a, h in halves])
                    shape = [P, PH, TK, TK]
                    group(ve, [V.tensor_copy(ixf[:], ix[:]),
                               V.tensor_tensor(cand[:].rearrange("p h (a b) -> p h a b", b=TK),
                                               v[:, 0].unsqueeze(3).broadcast_to(shape), v[:, 1].unsqueeze(2).broadcast_to(shape),
                                               ALU.add)])
                    hs = range(PH)
                    group(ve, [V.max(top[:, h, 0:8], cand[:, h, :]) for h in hs])
                    group(ve, [V.max_index(pos[:, h, 0:8], top[:, h, 0:8], cand[:, h, :]) for h in hs] +
                          [V.match_replace(cand2[:, h, :], top[:, h, 0:8], cand[:, h, :], NEG) for h in hs])
                    group(ve, [V.max(top[:, h, 8:16], cand2[:, h, :]) for h in hs])
                    group(ve, [V.max_index(pos[:, h, 8:16], top[:, h, 8:16], cand2[:, h, :]) for h in hs])
                    V.tensor_tensor(ex[:, t % 2], top[:], top[:, :, 0:1].broadcast_to([P, PH, TK]), ALU.subtract).then_inc(top_s, 1)
                    group(ve, [V.tensor_scalar(ab[:, 0], pos[:], 4, None, ALU.logical_shift_right),
                               V.tensor_scalar(ab[:, 1], pos[:], 15, None, ALU.bitwise_and)])
                    group(ve, [V.tensor_copy(abf[:], ab[:])])
                    flat = [P, PH * TK, TK]
                    group(ve, [V.tensor_tensor(eq[:, a], iota[:].unsqueeze(1).broadcast_to(flat),
                                               abf[:, a].rearrange("p h k -> p (h k)").unsqueeze(2).broadcast_to(flat),
                                               ALU.is_equal) for a in range(2)])
                    group(ve, [V.tensor_tensor(eq[:, a].rearrange("p (h k) j -> p h k j", k=TK),
                                               eq[:, a].rearrange("p (h k) j -> p h k j", k=TK),
                                               ixf[:, a].unsqueeze(2).broadcast_to([P, PH, TK, TK]), ALU.mult) for a in range(2)])
                    group(ve, [V.reduce_sum(pick[:, a, :], eq[:, a], axis=AX.X) for a in range(2)])
                    if t < GT:
                        group(ve, [V.scalar_tensor_tensor(pick[:, 0, :], pick[:, 0, :], float(PK), pick[:, 1, :],
                                                          ALU.mult, ALU.add)])
                        group(ve, [V.tensor_copy(rows[:, t, :], pick[:, 0, :])])
                    else:
                        group(ve, [V.tensor_copy(pairs[:, t - GT], pick[:])])
                    if t >= 1:
                        finish(t - 1)
                finish(NT - 1)


def stage_memory(env, rows, pairs, gate, xg):
    nc, dram = env.nc, env.dram
    assert PB == TURNS * STEP == DS // GRP and PER % STEP == 0
    got = [env.sem(f"pm_got{r}") for r in range(RING)]
    table_got = [env.sem(f"pm_table{s}") for s in range(STEP)]
    used, idx_s, dot_s, act_s, coef_s, sum_s = (env.sem("pm_" + n) for n in (
        "used", "idx", "dot", "gelu", "coef", "sum"))
    names = ("const", "zero", "keyT_full", "keyT_done", "score_full", "gelu_done", "w_done", "out_done", "ab_done",
             "c_full", "c_done")
    const_in, zero_s, keyT_full, keyT_done, score_full, gelu_done, w_done, out_done, ab_done, c_full, c_done = (
        env.sem("pd_" + n) for n in names)
    SCORE, OUT, CB, KT = [4, 5], [0, 1, 2, 3], [6, 7], [6, 7]
    u_blocks, v_blocks = dram["peer_uT"], dram["peer_v"].rearrange("(a b) d -> b a d", b=PK)
    uT = [env.wring[:, 0, s * D:(s + 1) * D] for s in range(STEP)]
    vr = [env.wring[:, 1, s * D:(s + 1) * D] for s in range(STEP)]

    def A(n, j):
        return env.hT[:, j, S + n * P:S + (n + 1) * P]

    def after(turn, s):
        return (turn, s + 1) if s + 1 < STEP else (turn + 1, 0)

    with ExitStack() as st:
        T = lambda n, s, d=F32: st.enter_context(nc.sbuf_tensor("pm_" + n, s, d))
        ring = T("ring", [P, RING, D])
        idx = T("idxs", [P, 2, RING], U32)
        dots = T("dots", [P, PER])
        coef = T("coefs", [P, SLOTS])
        acc = T("acc", [P, 2, D])
        iota, zeros = T("iota", [P, PK]), T("zeros", [P, P])
        keyT = T("keyT", [P, 3, DS])
        B = T("onehot", [P, 2, GRP, PB])
        C = T("coef_part", [P, 2, DS, PB])
        W = T("weighted", [P, 2, DS])
        with nc.Block() as block:
            @block.sync
            def _(sp):
                nc.sync.dma_start(iota[:], dram["row_numbers"]).then_inc(const_in, 16)
                with sp.Fori(0, PK // STEP) as i:
                    for s in range(STEP):
                        m = STEP * i + s
                        sp.wait_ge(out_done, m + 1)
                        sp.nop(nofuse=True)
                        nc.sync.dma_start(uT[s], u_blocks[bass.ds(m, 1)].rearrange("o p n -> p (o n)")).then_inc(table_got[s], 16)
                        nc.sync.dma_start(vr[s], v_blocks[bass.ds(m, 1)].rearrange("o p n -> p (o n)")).then_inc(table_got[s], 16)

            @block.gpsimd
            def _(pool):
                for t in range(GT):
                    for ph, table in enumerate(("peer_u", "peer_v")):
                        turn0 = (2 * t + ph) * TURNS
                        with pool.Fori(0, TURNS) as i:
                            for half in range(2):
                                n0 = (turn0 + i) * PER + half * RING
                                pool.wait_ge(used, n0 + 1)
                                pool.nop(nofuse=True)
                                nc.gpsimd.tensor_copy(idx[:, half, :], rows[:, t, bass.ds(i * PER + half * RING, RING)]
                                                      ).then_inc(idx_s, 1)
                                pool.wait_ge(idx_s, 2 * (turn0 + i) + half + 1)
                                for r in range(RING):
                                    pool.wait_ge(used, n0 + r + 1)
                                    pool.nop(nofuse=True)
                                    nc.gpsimd.indirect_dma_start(
                                        ring[:, r, :], None, dram[table],
                                        bass.IndirectOffsetOnAxis(ap=idx[:, half, r:r + 1], axis=0)).then_inc(got[r], 16)

            @block.tensor
            def _(pe):
                def scores(turn, s):
                    pe.wait_ge(table_got[s], 32 * turn + 32)
                    for k in range(KD):
                        mm = nc.tensor.matmul(env.ps[:, SCORE[s % 2], 0:DS], uT[s][:, k * P:(k + 1) * P],
                                              env.hT[:, k, GT * P:S], start=(k == 0), stop=(k == KD - 1))
                    mm.then_inc(score_full, 1)

                def coefficients(part, i, s):
                    g = PB * part + STEP * i + s
                    pe.wait_ge(ab_done, (GRP + 1) * g + GRP + 1)
                    pe.wait_ge(c_done, g + 1)
                    for j in range(GRP):
                        mm = nc.tensor.matmul(env.ps[:, CB[s % 2], j * PB:(j + 1) * PB], A(s % 2, j), B[:, s % 2, j, :],
                                              start=True, stop=True)
                    mm.then_inc(c_full, 1)

                def outputs(turn, s, stop=False):
                    pe.wait_ge(w_done, STEP * turn + s + 1)
                    for n in range(2 * DT):
                        t, half = n // 2, n % 2
                        mm = nc.tensor.matmul(env.ps[:, OUT[n], :], W[:, s % 2, t * P:(t + 1) * P],
                                              vr[s][:, half * WBLK:(half + 1) * WBLK], start=False, stop=stop)
                    mm.then_inc(out_done, 1)

                pe.sem_inc(out_done, STEP)
                pe.sem_inc(c_full, 2)
                for n, src in enumerate((pairs[:, :, 0, :], pairs[:, :, 1, :], gate[:, GT:, :])):
                    for t in range(DT):
                        mm = nc.tensor.transpose(env.ps[:, KT[n // 2], (n % 2) * DS + t * P:(n % 2) * DS + (t + 1) * P],
                                                 src[:, t, :], env.ident[:])
                    if n:
                        mm.then_inc(keyT_full, 1)
                pe.wait_ge(zero_s, 1)
                for b in OUT:
                    nc.tensor.matmul(env.ps[:, b, :], zeros[:], env.hT[:, 0, 0:S], start=True, stop=False)
                scores(0, 0)
                pe.wait_ge(keyT_done, 2)
                with pe.Fori(0, TURNS) as i:
                    for s in range(STEP):
                        coefficients(0, i, s)
                for part in range(PARTS - 1):
                    with pe.Fori(0, TURNS) as i:
                        for s in range(STEP):
                            scores(*after(part * TURNS + i, s))
                            coefficients(part + 1, i, s)
                            outputs(part * TURNS + i, s)
                with pe.Fori((PARTS - 1) * TURNS, PARTS * TURNS - 1) as turn:
                    for s in range(STEP):
                        scores(*after(turn, s))
                        outputs(turn, s)
                for s in range(STEP):
                    if s + 1 < STEP:
                        scores(PARTS * TURNS - 1, s + 1)
                    outputs(PARTS * TURNS - 1, s, stop=(s + 1 == STEP))

            @block.scalar
            def _(act):
                def gelu(turn, s):
                    m = STEP * turn + s
                    act.wait_ge(out_done, STEP + m - 1)
                    act.wait_ge(score_full, m + 1)
                    nc.scalar.activation(W[:, s % 2, :], env.ps[:, SCORE[s % 2], 0:DS], ACT.Gelu).then_inc(gelu_done, 1)

                def keep(part, i, s):
                    n = STEP * i + s
                    act.wait_ge(c_full, 2 + PB * part + n + 1)
                    act.nop(nofuse=True)
                    nc.scalar.activation(C[:, part % 2, bass.ds(n * GRP, GRP), :],
                                         env.ps[:, CB[s % 2], 0:GRP * PB].rearrange("p (t m) -> p t m", t=GRP),
                                         ACT.Copy).then_inc(c_done, 1)

                act.sem_inc(c_done, 2)
                act.wait_ge(keyT_full, 2)
                nc.scalar.activation(keyT[:, 0:2, :], env.ps[:, KT[0], :].rearrange("p (k t) -> p k t", k=2),
                                     ACT.Copy).then_inc(keyT_done, 1)
                nc.scalar.activation(keyT[:, 2, :], env.ps[:, KT[1], 0:DS], ACT.Copy).then_inc(keyT_done, 1)
                gelu(0, 0)
                with act.Fori(0, TURNS) as i:
                    for s in range(STEP):
                        keep(0, i, s)
                for part in range(PARTS):
                    if 1 <= part < PARTS - 1:
                        act.wait_ge(w_done, PB * part)
                    last = part == PARTS - 1
                    with act.Fori(0, TURNS - 1 if last else TURNS) as i:
                        for s in range(STEP):
                            gelu(*after(part * TURNS + i, s))
                            if not last:
                                keep(part + 1, i, s)
                    if last:
                        for s in range(1, STEP):
                            gelu(PARTS * TURNS - 1, s)
                    if part % 2 == 0:
                        act.wait_ge(dot_s, 1 + (part // 2 + 1) * TURNS)
                        nc.scalar.activation(coef[:], coef[:], ACT.Gelu).then_inc(act_s, 1)

            @block.vector
            def _(v):
                def one_hot(part, i, s):
                    n = STEP * i + s
                    v.wait_ge(c_full, PB * part + n + 1)
                    nc.vector.tensor_tensor(B[:, s % 2], iota[:, part * PB:(part + 1) * PB].unsqueeze(1).broadcast_to([P, GRP, PB]),
                                            keyT[:, 1, bass.ds(n * GRP, GRP)].unsqueeze(2).broadcast_to([P, GRP, PB]),
                                            ALU.is_equal).then_inc(ab_done, 1)
                    for j in range(GRP):
                        nc.vector.tensor_scalar(A(s % 2, j), iota[:], keyT[:, 0, bass.ds(n * GRP + j, 1)],
                                                keyT[:, 2, bass.ds(n * GRP + j, 1)], ALU.is_equal, ALU.mult).then_inc(ab_done, 1)

                def weigh(part, i, s):
                    n = STEP * i + s
                    v.wait_ge(gelu_done, PB * part + n + 1)
                    nc.vector.tensor_tensor(W[:, s % 2, :], W[:, s % 2, :], C[:, part % 2, :, bass.ds(n, 1)].rearrange("p t o -> p (t o)"),
                                            ALU.mult).then_inc(w_done, 1)

                v.sem_inc(used, RING)
                v.sem_inc(dot_s, 1)
                nc.vector.memset(zeros[:], 0.0).then_inc(zero_s, 1)
                v.wait_ge(const_in, 16)
                v.wait_ge(keyT_done, 2)
                with v.Fori(0, TURNS) as i:
                    for s in range(STEP):
                        one_hot(0, i, s)
                for t in range(GT):
                    turn0 = 2 * t * TURNS
                    v.wait_ge(c_done, 2 + PB * (2 * t + 1))
                    with v.Fori(0, TURNS) as i:
                        for n in range(PER):
                            r = n % RING
                            v.wait_ge(got[r], 32 * (turn0 + i) + 16 * (n // RING) + 16)
                            if n == 0:
                                v.wait_ge(dot_s, t * TURNS + i + 1)
                            nc.vector.tensor_tensor_reduce(ring[:, r, :], ring[:, r, :], xg[:, t, :], 1.0, 0.0,
                                                           ALU.mult, ALU.add, dots[:, n:n + 1]).then_inc(used, 1)
                            if n % (PER // STEP) == PER // STEP - 1:
                                one_hot(2 * t + 1, i, n // (PER // STEP))
                                weigh(2 * t, i, n // (PER // STEP))
                        v.wait_ge(used, RING + (turn0 + i + 1) * PER)
                        nc.vector.tensor_copy(coef[:, bass.ds(i * PER, PER)], dots[:]).then_inc(dot_s, 1)
                    v.wait_ge(act_s, t + 1)
                    nc.vector.tensor_tensor(coef[:], coef[:], gate[:, t, :], ALU.mult).then_inc(coef_s, 1)
                    if t >= 1:
                        v.wait_ge(sum_s, 2 * t)
                    nc.vector.memset(acc[:], 0.0).then_inc(coef_s, 1)
                    v.wait_ge(coef_s, 2 * (t + 1))
                    v.wait_ge(c_done, 2 + PB * (2 * t + 2))
                    turn1 = turn0 + TURNS
                    with v.Fori(0, TURNS) as i:
                        for n in range(PER):
                            r = n % RING
                            v.wait_ge(got[r], 32 * (turn1 + i) + 16 * (n // RING) + 16)
                            v.wait_ge(used, RING + (turn1 + i) * PER + n - 1)
                            nc.vector.scalar_tensor_tensor(acc[:, n % 2, :], ring[:, r, :], coef[:, bass.ds(i * PER + n, 1)],
                                                           acc[:, n % 2, :], ALU.mult, ALU.add).then_inc(used, 1)
                            if n % (PER // STEP) == PER // STEP - 1:
                                if t + 1 < GT:
                                    one_hot(2 * t + 2, i, n // (PER // STEP))
                                weigh(2 * t + 1, i, n // (PER // STEP))
                    v.wait_ge(used, RING + (turn1 + TURNS) * PER)
                    for half in range(2):
                        if half:
                            v.wait_ge(sum_s, 2 * t + 1)
                        nc.vector.tensor_tensor(env.h[:, t, :], env.h[:, t, :], acc[:, half, :], ALU.add).then_inc(sum_s, 1)
                v.wait_ge(out_done, STEP + PK)
                for n in range(2 * DT):
                    t, cs = GT + n // 2, slice((n % 2) * WBLK, (n % 2 + 1) * WBLK)
                    nc.vector.tensor_tensor(env.h[:, t, cs], env.h[:, t, cs], env.ps[:, OUT[n], :], ALU.add).then_inc(sum_s, 1)


PLE = 256


def stage_embedding(env):
    nc, dram = env.nc, env.dram
    g_t = [env.tiles(NT) for _ in range(2)]
    blks = [env.take_block(t[-1]) for t in g_t]
    p_t = [env.tiles(NT) for _ in range(2)]
    in_s, add_s = env.sem("pl_in"), env.sem("pl_add")
    with ExitStack() as st:
        T = lambda n, s: st.enter_context(nc.sbuf_tensor("pl_" + n, s, F32))
        gate = T("gate", [P, NT, D])
        pT, wp = T("pT", [P, PLE // P, S]), T("wp", [P, PLE // P, D])
        with nc.Block() as block:
            @block.sync
            def _(sp):
                nc.sync.dma_start(pT[:], dram["p_T"]).then_inc(in_s, 16)
                nc.sync.dma_start(wp[:], dram["w_ple_proj"]).then_inc(in_s, 16)
                load_blocks(env, sp)

            @block.scalar
            def _(act):
                for half in range(2):
                    for i, t in enumerate(g_t[half]):
                        product_done(env, act, t)
                        nc.scalar.activation(gate[:, i, half * WBLK:(half + 1) * WBLK], env.ps[:, t[0], :],
                                             ACT.Sigmoid).then_inc(env.bank_free[t[0]], 1)

            @block.vector
            def _(v):
                for half in range(2):
                    cs = slice(half * WBLK, (half + 1) * WBLK)
                    for i, t in enumerate(p_t[half]):
                        evacuated(env, v, g_t[half][i])
                        product_done(env, v, t)
                        nc.vector.tensor_tensor(gate[:, i, cs], gate[:, i, cs], env.ps[:, t[0], :], ALU.mult).then_inc(
                            env.bank_free[t[0]], 1)
                        evacuated(env, v, t)
                        nc.vector.tensor_tensor(env.h[:, i, cs], env.h[:, i, cs], gate[:, i, cs], ALU.add).then_inc(add_s, 1)

            @block.tensor
            def _(pe):
                for half in range(2):
                    w = block_view(env, pe, blks[half])
                    for i, t in enumerate(g_t[half]):
                        by_token(env, pe, t, WBLK, w, i)
                pe.wait_ge(in_s, 32)
                for half in range(2):
                    for i, t in enumerate(p_t[half]):
                        bank_ready(env, pe, t)
                        for k in range(PLE // P):
                            mm = nc.tensor.matmul(env.ps[:, t[0], :], pT[:, k, i * P:(i + 1) * P],
                                                  wp[:, k, half * WBLK:(half + 1) * WBLK], start=(k == 0), stop=(k == PLE // P - 1))
                        mm.then_inc(env.bank_full[t[0]], 1)


class Bufs:
    pass


def stream(env, *names):
    for n in names:
        a = env.dram[n]
        for i in range(a.shape[0]):
            env.blocks.append(a[i])


def load_tokens(env, name, src):
    nc = env.nc
    done = env.sem(name)
    with nc.Block() as block:
        @block.sync
        def _(sp):
            nc.sync.dma_start(env.h[:], src.rearrange("(t p) d -> p t d", p=P)).then_inc(done, 16)
            sp.wait_ge(done, 16)


def first_mixer(env):
    nc = env.nc
    gain = lambda n: (lambda j: env.gain[:, n, j:j + 1])
    shift = lambda c0, c: (lambda j: env.ada[:, c0 + j, c:c + 1])
    with ExitStack() as tok:
        env.h = tok.enter_context(nc.sbuf_tensor("x_tok", [P, NT, D], F32))
        env.hctx = tok.enter_context(nc.sbuf_tensor("ctx_tok", [P, NCT, D], F32))
        stage_modulation(env)
        stage_norm(env, "mix", lambda t: env.h[:, t, :] if t < NT else env.hctx[:, t - NT, :],
                   [(0, NT, gain(0), shift(0, 0)), (NT, NCT, gain(1), shift(0, 1))], env.hT)
    branch = ExitStack()
    oT = branch.enter_context(nc.sbuf_tensor("oT", [P, KD, S], F32))
    with ExitStack() as own:
        A = lambda n, s: own.enter_context(nc.sbuf_tensor(n, s, F32))
        B = Bufs()
        B.q, B.k, B.v = A("gla_q", [P, H1, S]), A("gla_k", [P, H1, TOK]), A("gla_v", [P, NCH, D])
        B.sum, B.tot = A("gla_sum", [P, 2 * H1, TOK]), A("gla_tot", [P, 2 * H1, NCH])
        stage_gla_project(env, B)
        stage_gla_core(env, B, oT)
    yT = branch.enter_context(nc.sbuf_tensor("yT", [P, KD, S], F32))
    stage_branch(env, "gla", oT, yT, True)
    with ExitStack() as own:
        A = lambda n, s: own.enter_context(nc.sbuf_tensor(n, s, F32))
        R = Bufs()
        R.qk, R.kc, R.v = A("ret_qk", [P, 2 * H1, S]), A("ret_kc", [P, NCT, H1 * DK]), A("ret_v", [P, NCH, D])
        stage_ret_project(env, R)
        stage_ret_core(env, R, oT)
    stage_branch(env, "ret", oT, yT, False)
    with ExitStack() as own:
        env.h = own.enter_context(nc.sbuf_tensor("h_mix", [P, NT, D], F32))
        load_tokens(env, "x_again", env.dram["x"])
        stage_out(env, "mix_out", yT, 0)
        save_tokens(env, "h_saved", env.dram["h_dram"])
    branch.close()


def first_experts(env):
    nc = env.nc
    env.h = env.sb("h_tok", [P, NT, D])
    load_tokens(env, "h_again", env.dram["h_dram"])
    stage_norm(env, "ffn", lambda t: env.h[:, t, :],
               [(0, NT, lambda j: env.gain[:, 2, j:j + 1], lambda j: env.ada[:, 24 + j, 0:1])], env.hT,
               env.dram["xn_dram"])
    with ExitStack() as own:
        E = Bufs()
        E.weight = own.enter_context(nc.sbuf_tensor("pick_weight", [P, PICKS, NT], F32))
        E.pos = own.enter_context(nc.sbuf_tensor("pick_row", [P, PICKS, NT], U32))
        E.row_token = own.enter_context(nc.sbuf_tensor("row_token", [P, NB], U32))
        E.block_expert = own.enter_context(nc.sbuf_tensor("block_expert", [P, NB], I32))
        stage_router(env, E)
        stage_experts(env, E)
        stage_expert_sum(env, E)
    stage_rownorm(env, "fin1", env.h, "norm_final")


def second_block(env):
    nc = env.nc
    tok = lambda t: env.h[:, t, :]
    gain = lambda name: (lambda j: col(env, name, j))
    stage_norm(env, "mix2", tok, [(0, NT, gain("g_mix"), None)], env.hT)
    with ExitStack() as own:
        A = lambda n, s: own.enter_context(nc.sbuf_tensor(n, s, F32))
        M = Bufs()
        M.dqk, M.dv, M.kr = A("dil_qk", [P, 8, S]), A("dil_v", [P, NT, S]), A("mla_kr", [QH, S])
        M.q, M.k, M.v = A("mla_q", [QH, AH, S]), A("mla_k", [QH, AH, S]), A("mla_v", [P, NT, S])
        with nc.sbuf_tensor("mla_c", [P, NT, QR + KVR], F32) as c:
            M.c = c
            stage_second_project(env, M)
            stage_latent_expand(env, M)
        o = A("attn_o", [P, 2, NT, S])
        stage_attention(env, M, o)
        mixT = A("mixT", [P, KD, S])
        stage_mix(env, o, mixT)
        stage_out(env, "att_out", mixT, None)
    stage_norm(env, "ffn2", tok, [(0, NT, gain("g_ffn"), None)], env.hT)
    with ExitStack() as own:
        rows = own.enter_context(nc.sbuf_tensor("mem_rows", [P, GT, SLOTS], U32))
        pairs = own.enter_context(nc.sbuf_tensor("mem_pairs", [P, DT, 2, SLOTS], F32))
        gate = own.enter_context(nc.sbuf_tensor("mem_gate", [P, NT, SLOTS], F32))
        stage_memory_route(env, rows, pairs, gate)
        xg = own.enter_context(nc.sbuf_tensor("mem_x", [P, GT, D], F32))
        stage_rownorm(env, "ffn2_rows", xg, "g_ffn_row", nt=GT, ahead=0)
        stage_memory(env, rows, pairs, gate, xg)
    stage_norm(env, "ple", tok, [(0, NT, gain("g_ple"), None)], env.hT)
    stage_embedding(env)
    stage_rownorm(env, "fin2", env.h, "g_final_row", env.dram["out"])


def save_tokens(env, name, dst):
    nc = env.nc
    done = env.sem(name)
    with nc.Block() as block:
        @block.sync
        def _(sp):
            nc.sync.dma_start(dst.rearrange("(t p) d -> p t d", p=P), env.h[:]).then_inc(done, 16)
            sp.wait_ge(done, 16)


def program(nc, dram):
    with ExitStack() as ctx:
        env = Env(nc, ctx, dram)
        env.ps = ctx.enter_context(nc.psum_tensor("ps", [P, 8, WBLK], F32))
        env.bank_full = [env.sem(f"bank_full{b}") for b in range(8)]
        env.bank_free = [env.sem(f"bank_free{b}") for b in range(8)]
        env.w_loaded = [env.sem(f"w_loaded{b}") for b in range(2)]
        env.const_in, env.const_set, env.x_in = env.sem("const_in"), env.sem("const_set"), env.sem("x_in")
        env.ident = env.sb("ident", [P, P])
        env.cols = env.sb("cols", [P, NCOL])
        env.ones = env.sb("ones", [P, P])
        env.eps = env.sb("eps", [P, 1])
        env.ada = env.sb("ada", [P, 48, 2])
        env.gain = env.sb("gain", [P, 3, 8])
        env.gates = env.sb("gates", [P, 2, D])
        env.hT = env.sb("hT", [P, KD, TOK])
        env.wring = env.sb("wring", [P, 2, KD * WBLK])
        stream(env, "w_ada")
        for b in (0, 1, 2, 3, 4, 5, 12, 13):
            env.blocks.append(dram["w_in"][b])
        stream(env, "w_branch_gla")
        for b in (6, 7, 8, 9, 10, 11, 14, 15):
            env.blocks.append(dram["w_in"][b])
        stream(env, "w_branch_ret", "w_out")
        stream(env, "w_in2", "w_out2", "w_peer_q", "w_ple_gate")
        first_mixer(env)
        first_experts(env)
        second_block(env)


def blocked(w):
    n = w.shape[1] // WBLK
    return w.reshape(KD, P, n, WBLK).transpose(2, 1, 0, 3).reshape(n, P, KD * WBLK)


def columns(a):
    return a.reshape(-1, P).T


def rope_table(seq_pos, inv, reps):
    ang = seq_pos[:, None].astype(np.float32) * inv[None, :]
    return np.cos(ang).T, np.sin(ang).T


def constants():
    f = np.float32
    c = {"ident": np.eye(P, dtype=f)}
    n = 32
    inv = (f(10000.0) ** (-np.arange(n, dtype=f) / f(n))).astype(f)
    tab = np.zeros((P, 2, S), f)
    perm = np.zeros((P, P), f)
    for half, pos in enumerate((np.repeat(np.arange(S // 64), 64), np.tile(np.arange(64), S // 64))):
        cs, sn = rope_table(pos, inv, 1)
        for part in range(2):
            r = half * 64 + part * 32
            tab[r:r + 32, 0], tab[r:r + 32, 1] = cs, sn
        for i in range(32):
            a, b = half * 64 + i, half * 64 + 32 + i
            perm[b, a] = -1.0
            perm[a, b] = 1.0
    c["rope_axial"], c["perm_axial"] = tab, perm
    h = np.arange(H1, dtype=np.float64)
    lg = [np.log1p(-np.exp2(-5.0 - h)), np.log1p(-np.exp2(-5.5 - h))]
    rel = np.arange(896)[None, :] - 384 - np.arange(P)[:, None]
    band = np.stack([np.where(rel >= 0, np.exp(np.maximum(rel, 0) * lg[0][i]), np.exp(np.maximum(-rel, 0) * lg[1][i]))
                     for i in range(H1)], 1)
    c["ret_band"] = (band * DK ** -0.5).astype(f)
    t = np.arange(S)
    c["ret_qdec"] = np.stack([np.stack([np.exp((t + 1) * lg[0][i]), np.exp((S - t) * lg[1][i])]) for i in range(H1)]).astype(f)
    s = np.arange(CT)
    kd = np.stack([np.exp((CT - 1 - s) * lg[0][i]) for i in range(H1)] + [np.exp(s * lg[1][i]) for i in range(H1)])
    c["ret_kdec"] = (kd * DK ** -0.5).reshape(2 * H1, NCT, P).transpose(2, 0, 1).astype(f)
    p = np.arange(P)
    c["chunk_mask"] = np.stack([p[:, None] <= p[None, :], p[:, None] > p[None, :]], 1).astype(f)
    e = np.arange(NE)
    c["iota16"] = np.broadcast_to(np.arange(TK, dtype=f), (P, TK))
    for name, rows, width, first, rot in (("mla", QH, QH, NOPE, ROT), ("dil", P, DH, 0, DH // 4)):
        half = rot // 2
        inv = (f(500000.0) ** (-np.arange(0, rot, 2, dtype=f) / f(rot))).astype(f)
        cs, sn = rope_table(np.arange(S), inv, 1)
        tab, perm = np.zeros((rows, 2, S), f), np.zeros((rows, rows), f)
        tab[:, 0] = 1.0
        for r0 in range(first, rows, width):
            for part in range(2):
                tab[r0 + part * half:r0 + (part + 1) * half, 0] = cs
                tab[r0 + part * half:r0 + (part + 1) * half, 1] = sn
            for i in range(half):
                perm[r0 + half + i, r0 + i] = -1.0
                perm[r0 + i, r0 + half + i] = 1.0
        c["rope_" + name], c["perm_" + name] = tab, perm
    q, k = np.arange(S)[:, None], np.arange(S)[None, :]
    count = sum(((q - k) % dil == 0) & (abs(q - k) <= win // 2) for win, dil in ((128, 1), (512, 4), (2048, 16)))
    mask = np.where(count > 0, np.log(np.maximum(count, 1)), NEG).astype(f)
    c["dil_mask"] = mask.reshape(NT, P, S).transpose(1, 0, 2)
    c["token_before"] = (p[:, None] < p[None, :]).astype(f)
    c["row_numbers"] = np.broadcast_to(p, (P, ROWB)).astype(f)
    c["block_numbers"] = np.broadcast_to(np.arange(NB), (P, NB)).astype(f)
    c["token_numbers"] = (np.arange(NT)[None, :] * P + p[:, None]).astype(f)
    c["expert_numbers"] = np.broadcast_to(np.stack([e, e // EPG]), (P, 2, NE)).astype(f)
    return c


def layout(i):
    a = {k: np.asarray(v) for k, v in i.items()}
    d = constants()
    d["x"], d["ctx"] = a["x"][0], a["ctx"][0]
    d["c2"] = np.stack([a["c"][0].reshape(KD, P), a["c_ctx"].reshape(KD, P)], -1).transpose(1, 0, 2)
    vec = dict(norm_mix=a["norm_mix"][0], norm_ffn=a["norm_ffn"][0], b_ada=a["b_ada"][0], gla_norm=a["gla_norm"][0],
               gla_b=a["gla_lr_b"][0].reshape(-1), g_mix=a["g_mix_2"][0], g_cq=a["g_cq_2"][0], g_ckv=a["g_ckv_2"][0],
               g_mla=a["g_out_mla_2"][0], g_dil=a["g_out_dil_2"][0], g_ffn=a["g_ffn_2"][0], g_ple=a["g_ple_2"][0])
    d["cols"] = np.concatenate([columns(vec[n]) for n in COLS], 1)
    d["b_gates"] = np.concatenate([a["b_ada"][0, 2 * D:3 * D], a["b_ada"][0, 5 * D:6 * D]])[None]
    d["w_ada"] = blocked(a["w_ada"][0])
    w = a["w_in"][0]
    d["w_lr"] = w[:, 3072:3104].reshape(KD, P, 32).transpose(1, 0, 2)
    d["w_in"] = blocked(np.concatenate([w[:, :3072], w[:, 3104:]], 1))
    d["gla_lr_w"] = a["gla_lr_w"][0]
    d["w_router"] = np.concatenate([a["w_router_group"][0], a["w_router_expert"][0]], 1).reshape(KD, P, NR).transpose(1, 0, 2)
    d["b_router"] = np.concatenate([a["b_router_group"][0], a["b_router_expert"][0]])[None]
    gu = np.concatenate([a["w_expert_gate"][0], a["w_expert_up"][0]], 2).reshape(NE, KD, P, 2 * EF).transpose(0, 2, 1, 3)
    dn = a["w_expert_down"][0].reshape(NE, EFT, P, D).transpose(0, 2, 1, 3)
    d["experts"] = np.concatenate([gu.reshape(NE, P, -1), dn.reshape(NE, P, -1)], 2)
    w2 = a["w_in_2"][0]
    lat = QR + KVR
    pad = lambda n: np.zeros((D, n), np.float32)
    d["w_in2"] = blocked(np.concatenate([w2[:, lat + ROT:], w2[:, :lat], pad(NOPE), w2[:, lat:lat + ROT],
                                         pad(WBLK - P - QH)], 1))
    d["w_uq"] = a["w_uq_2"][0].reshape(CQ, P, AH * QH).transpose(1, 0, 2)
    kv = a["w_ukv_2"][0].reshape(KVR, AH, 2, NOPE).transpose(0, 2, 1, 3).reshape(KVR, -1)
    d["w_ukv"] = kv.reshape(CKV, P, -1).transpose(1, 0, 2)
    d["w_out2"], d["w_peer_q"], d["w_ple_gate"] = (blocked(a[n][0]) for n in ("w_out_2", "w_peer_q_2", "w_ple_gate_2"))
    d["peer_keys"] = np.concatenate([a["peer_keys1_2"][0].T, a["peer_keys2_2"][0].T], 0)
    d["peer_u"], d["peer_v"] = a["peer_u_2"][0], a["peer_v_2"][0]
    d["peer_uT"] = d["peer_u"].reshape(PK, PK, KD, P).transpose(1, 3, 2, 0).reshape(PK, P, D)
    d["p_T"] = a["p_2"][0, 0].T.reshape(PLE // P, P, S).transpose(1, 0, 2)
    d["w_ple_proj"] = a["w_ple_proj_2"][0].reshape(PLE // P, P, D).transpose(1, 0, 2)
    d["g_ffn_row"], d["g_final_row"] = a["g_ffn_2"][0][None], a["g_final_2"][None]
    d["norm_final"] = a["norm_final"][None]
    for n in ("w_branch_gla", "w_branch_ret", "w_out"):
        d[n] = blocked(a[n][0])
    return d


def kernel(**inputs):
    import concourse.bacc as bacc
    from concourse.bass_utils import run_bass_kernel_spmd as run

    nc = bacc.Bacc("TRN2", target_bir_lowering=False, num_devices=1)
    arrays, dram = {}, {}
    for n, v in layout(inputs).items():
        arrays["in_" + n] = np.ascontiguousarray(v)
        dram[n] = nc.dram_tensor("in_" + n, v.shape, mybir.dt.from_np(v.dtype), kind="ExternalInput").ap()
    dram["out"] = nc.dram_tensor("out", (S, D), F32, kind="ExternalOutput").ap()
    dram["h_dram"] = nc.dram_tensor("h_dram_out", (S, D), F32, kind="ExternalOutput").ap()
    dram["xn_dram"] = nc.dram_tensor("xn_dram_out", (S, D), F32, kind="ExternalOutput").ap()
    dram["y_dram"] = nc.dram_tensor("y_dram_out", (NB * ROWB, D), F32, kind="ExternalOutput").ap()
    program(nc, dram)
    r = run(nc, [arrays], core_ids=[0])
    return r.results[0]["out"].reshape(1, S, D)
```

```python
from contextlib import ExitStack

import numpy as np
import concourse.bass as bass
from concourse import mybir

F32 = mybir.dt.float32
U32 = mybir.dt.uint32
I32 = mybir.dt.int32
ALU = mybir.AluOpType
ACT = mybir.ActivationFunctionType
AX = mybir.AxisListType

P = 128
D = 1024
KD = D // P
S = 512
NT = S // P
CT = 256
NCT = CT // P
TOK = S + CT
NCH = TOK // P
WBLK = 512
H1 = 4
DK = 128
DV = 256
EPS = 1e-6
NEG = -1e30

COLS = dict(norm_mix=8, norm_ffn=8, b_ada=48, gla_norm=2, gla_b=8, g_mix=8, g_cq=3, g_ckv=2, g_mla=4, g_dil=4,
            g_ffn=8, g_ple=8)
COL0 = {}
_at = 0
for _n, _w in COLS.items():
    COL0[_n] = _at
    _at += _w
NCOL = _at


class Env:

    def __init__(self, nc, ctx, dram):
        self.nc, self.ctx, self.dram = nc, ctx, dram
        self.turns = [0] * 8
        self.tile_no = 0
        self.blocks = []
        self.block_tile = {}
        self.issued = 0
        self.used = 0
        self.shared = {}

    def sb(self, name, shape, dt=F32):
        return self.ctx.enter_context(self.nc.sbuf_tensor(name, shape, dt))

    def sem(self, name):
        return self.ctx.enter_context(self.nc.semaphore(name))

    def again(self, name, n):
        if name not in self.shared:
            self.shared[name] = [self.sem(name), 0]
        sem, base = self.shared[name]
        self.shared[name][1] += n
        return sem, base

    def tile(self):
        b = self.tile_no % 8
        self.tile_no += 1
        n = self.turns[b]
        self.turns[b] += 1
        return b, n

    def tiles(self, n):
        return [self.tile() for _ in range(n)]

    def take_block(self, last_tile):
        b = self.used
        self.used += 1
        self.block_tile[b] = last_tile
        return b


def bank_ready(env, eng, t):
    if t[1] > 0:
        eng.wait_ge(env.bank_free[t[0]], t[1])


def product_done(env, eng, t):
    eng.wait_ge(env.bank_full[t[0]], t[1] + 1)


def evacuated(env, eng, t):
    eng.wait_ge(env.bank_free[t[0]], t[1] + 1)


def load_blocks(env, sp, ahead=2):
    nc = env.nc
    for b in range(env.issued, min(env.used + ahead, len(env.blocks))):
        if b >= 2:
            product_done(env, sp, env.block_tile[b - 2])
        nc.sync.dma_start(env.wring[:, b % 2, :], env.blocks[b]).then_inc(env.w_loaded[b % 2], 16)
        env.issued = b + 1


def block_view(env, pe, b):
    pe.wait_ge(env.w_loaded[b % 2], 16 * (b // 2 + 1))
    return env.wring[:, b % 2, :].rearrange("p (k n) -> p k n", k=KD)


class Chain:

    def __init__(self, sem):
        self.sem, self.n = sem, 0

    def __call__(self, eng, ins):
        self.n += 1
        ins.then_inc(self.sem, 1)
        eng.wait_ge(self.sem, self.n)


class Group:

    def __init__(self, sem):
        self.sem, self.n = sem, 0

    def __call__(self, eng, steps):
        for ins in steps:
            ins.then_inc(self.sem, 1)
            self.n += 1
        eng.wait_ge(self.sem, self.n)


def col(env, name, j=0, n=1):
    return env.cols[:, COL0[name] + j:COL0[name] + j + n]


def stage_modulation(env, rows):
    nc, dram = env.nc, env.dram
    tiles = env.tiles(12)
    blks = [env.take_block(t) for t in tiles]
    t_col = env.tile()
    t_bc = env.tiles(4)
    with ExitStack() as st:
        row = st.enter_context(nc.sbuf_tensor("ada_row", [2, 6 * D], F32))
        brow = st.enter_context(nc.sbuf_tensor("ada_brow", [1, 2 * D], F32))
        c2 = st.enter_context(nc.sbuf_tensor("c2", [P, KD, 2], F32))
        sc = st.enter_context(nc.sbuf_tensor("silu_c", [P, KD, 2], F32))
        c_in, c_act, b_in, cols_done = (env.sem(n) for n in ("c_in", "c_act", "b_in", "ada_cols_done"))
        with nc.Block() as block:
            @block.sync
            def _(sp):
                nc.sync.dma_start(c2[:], dram["c2"]).then_inc(c_in, 16)
                nc.sync.dma_start(env.ident[:], dram["ident"]).then_inc(env.const_in, 16)
                nc.sync.dma_start(env.cols[:], dram["cols"]).then_inc(env.const_in, 16)
                load_blocks(env, sp)
                nc.sync.dma_start(brow[:], dram["b_gates"]).then_inc(b_in, 16)

            @block.scalar
            def _(act):
                act.wait_ge(c_in, 16)
                nc.scalar.activation(sc[:], c2[:], ACT.Silu).then_inc(c_act, 1)
                act.wait_ge(env.w_loaded[0], 16)
                nc.scalar.dma_start(env.h[:], dram["x"].rearrange("(t p) d -> p t d", p=P)).then_inc(env.x_in, 16)
                nc.scalar.dma_start(env.hctx[:], dram["ctx"].rearrange("(t p) d -> p t d", p=P)).then_inc(env.x_in, 16)
                act.wait_ge(env.x_in, 32)
                act.wait_ge(env.const_set, 2)
                rows.on_scalar(act)
                for i, t in enumerate(tiles):
                    product_done(env, act, t)
                    nc.scalar.activation(row[:, i * WBLK:(i + 1) * WBLK], env.ps[0:2, t[0], :], ACT.Copy).then_inc(
                        env.bank_free[t[0]], 1)

            @block.vector
            def _(v):
                nc.vector.memset(env.ones[:], 1.0).then_inc(env.const_set, 1)
                nc.vector.memset(env.eps[:], EPS).then_inc(env.const_set, 1)
                rows.on_vector(v)
                v.wait_ge(env.const_in, 32)
                product_done(env, v, t_col)
                nc.vector.tensor_tensor(
                    env.ada[:], env.ps[:, t_col[0], 0:96].rearrange("p (j c) -> p j c", c=2),
                    col(env, "b_ada", 0, 48).unsqueeze(2).broadcast_to([P, 48, 2]), ALU.add).then_inc(
                    env.bank_free[t_col[0]], 1)
                evacuated(env, v, t_col)
                for n, (sc0, who, g) in enumerate(((8, 0, "norm_mix"), (8, 1, "norm_mix"), (32, 0, "norm_ffn"))):
                    nc.vector.scalar_tensor_tensor(env.gain[:, n, :], env.ada[:, sc0:sc0 + 8, who], 1.0,
                                                   col(env, g, 0, 8), ALU.add, ALU.mult).then_inc(cols_done, 1)
                for i, t in enumerate(t_bc):
                    product_done(env, v, t)
                    nc.vector.tensor_copy(env.gates[:, i // 2, (i % 2) * WBLK:(i % 2 + 1) * WBLK],
                                          env.ps[:, t[0], :]).then_inc(env.bank_free[t[0]], 1)
                v.wait_ge(cols_done, 3)

            @block.tensor
            def _(pe):
                pe.wait_ge(c_act, 1)
                for t, b in zip(tiles, blks):
                    w = block_view(env, pe, b)
                    bank_ready(env, pe, t)
                    for k in range(KD):
                        mm = nc.tensor.matmul(env.ps[0:2, t[0], :], sc[:, k, :], w[:, k, :],
                                              start=(k == 0), stop=(k == KD - 1))
                    mm.then_inc(env.bank_full[t[0]], 1)
                for t in tiles:
                    evacuated(env, pe, t)
                pe.wait_ge(env.const_in, 32)
                for j in range(48):
                    mm = nc.tensor.transpose(env.ps[:, t_col[0], 2 * j:2 * j + 2], row[:, j * P:(j + 1) * P],
                                             env.ident[0:2, 0:2])
                mm.then_inc(env.bank_full[t_col[0]], 1)
                pe.wait_ge(env.const_set, 2)
                pe.wait_ge(b_in, 16)
                for i, t in enumerate(t_bc):
                    bank_ready(env, pe, t)
                    at = (2 if i < 2 else 5) * D + (i % 2) * WBLK
                    nc.tensor.matmul(env.ps[:, t[0], :], env.ones[0:1, :], row[0:1, at:at + WBLK],
                                     start=True, stop=False)
                    nc.tensor.matmul(env.ps[:, t[0], :], env.ones[0:1, :], brow[0:1, i * WBLK:(i + 1) * WBLK],
                                     start=False, stop=True).then_inc(env.bank_full[t[0]], 1)


class NormRows:

    def __init__(self, env, st, name, src, nt, xn):
        self.env, self.src, self.nt, self.xn = env, src, nt, xn
        self.ss = st.enter_context(env.nc.sbuf_tensor(name + "_ss", [P, nt], F32))
        self.rs = st.enter_context(env.nc.sbuf_tensor(name + "_rs", [P, nt], F32))
        self.sq_done, self.sq0 = env.again("norm_sq", nt)
        self.rms_done, self.r0 = env.again("norm_rms", 1)
        self.inv_done, _ = env.again("norm_inv", 1)
        self.done, self.done0 = env.again("norm_xn", nt)

    def on_scalar(self, act):
        nc = self.env.nc
        for t in range(self.nt):
            nc.scalar.activation(self.xn[:, t, :], self.src(t), ACT.Square,
                                 accum_out=self.ss[:, t:t + 1]).then_inc(self.sq_done, 1)
        act.wait_ge(self.sq_done, self.sq0 + self.nt)
        nc.scalar.activation(self.rs[:], self.ss[:], ACT.Sqrt, scale=1.0 / D, bias=self.env.eps[:, 0:1]).then_inc(self.rms_done, 1)
        act.wait_ge(self.inv_done, self.r0 + 1)
        for t in range(1, self.nt, 2):
            nc.scalar.activation(self.xn[:, t, :], self.src(t), ACT.Copy, scale=self.ss[:, t:t + 1]).then_inc(self.done, 1)

    def on_vector(self, v):
        nc = self.env.nc
        v.wait_ge(self.rms_done, self.r0 + 1)
        nc.vector.reciprocal(self.ss[:], self.rs[:]).then_inc(self.inv_done, 1)
        v.wait_ge(self.inv_done, self.r0 + 1)
        v.wait_ge(self.sq_done, self.sq0 + self.nt)
        for t in range(0, self.nt, 2):
            nc.vector.tensor_scalar(self.xn[:, t, :], self.src(t), self.ss[:, t:t + 1], None, ALU.mult).then_inc(self.done, 1)


def stage_norm(env, name, src, parts, dst, store=None, made=None):
    nc = env.nc
    nt = sum(p[1] for p in parts)
    work = [(p, j, env.tile()) for p in parts for j in range(KD)]
    with ExitStack() as st:
        rows = made or NormRows(env, st, name, src, nt, st.enter_context(nc.sbuf_tensor(name + "_xn", [P, nt, D], F32)))
        xn = rows.xn
        out_s, out0 = env.again("row_out", 16 * nt if store is not None else 0)
        with nc.Block() as block:
            @block.sync
            def _(sp):
                load_blocks(env, sp)
                if store is not None:
                    sp.wait_ge(rows.done, rows.done0 + nt)
                    for t in range(nt):
                        nc.sync.dma_start(store[t * P:(t + 1) * P, :], xn[:, t, :]).then_inc(out_s, 16)
                    sp.wait_ge(out_s, out0 + 16 * nt)

            @block.scalar
            def _(act):
                if made is None:
                    rows.on_scalar(act)
                for (t0, n, gain, shift), j, t in work[1::2]:
                    product_done(env, act, t)
                    out, got = dst[:, j, t0 * P:(t0 + n) * P], env.ps[:, t[0], 0:n * P]
                    if shift is None:
                        ins = nc.scalar.activation(out, got, ACT.Copy, scale=gain(j))
                    else:
                        ins = nc.scalar.activation(out, got, ACT.Identity, scale=gain(j), bias=shift(j))
                    ins.then_inc(env.bank_free[t[0]], 1)

            @block.vector
            def _(v):
                if made is None:
                    rows.on_vector(v)
                for (t0, n, gain, shift), j, t in work[0::2]:
                    product_done(env, v, t)
                    out, got = dst[:, j, t0 * P:(t0 + n) * P], env.ps[:, t[0], 0:n * P]
                    if shift is None:
                        ins = nc.vector.tensor_scalar(out, got, gain(j), None, ALU.mult)
                    else:
                        ins = nc.vector.tensor_scalar(out, got, gain(j), shift(j), ALU.mult, ALU.add)
                    ins.then_inc(env.bank_free[t[0]], 1)

            @block.tensor
            def _(pe):
                pe.wait_ge(env.const_in, 32)
                pe.wait_ge(rows.done, rows.done0 + nt)
                for (t0, n, _, _), j, t in work:
                    bank_ready(env, pe, t)
                    for i in range(n):
                        mm = nc.tensor.transpose(env.ps[:, t[0], i * P:(i + 1) * P],
                                                 xn[:, t0 + i, j * P:(j + 1) * P], env.ident[:])
                    mm.then_inc(env.bank_full[t[0]], 1)


def project(env, pe, t, out, w, lo, hi, rhs):
    bank_ready(env, pe, t)
    for k in range(KD):
        mm = env.nc.tensor.matmul(out, w[:, k, lo:hi], rhs(k), start=(k == 0), stop=(k == KD - 1))
    mm.then_inc(env.bank_full[t[0]], 1)


def chunks(ap):
    return ap.rearrange("p (c t) -> p c t", t=P)


def stage_gla_project(env, B):
    nc, dram = env.nc, env.dram
    hT = env.hT
    q_t = env.tiles(4)
    b_q = env.take_block(q_t[-1])
    k_t = [(j, lo, n, env.tile()) for j in range(4) for lo, n in ((0, S), (S, CT))]
    b_k = env.take_block(k_t[-1][3])
    lr_t = [(d, lo, n, env.tile()) for d in range(2) for lo, n in ((0, S), (S, CT))]
    z_t = [(i, lo, n, env.tile()) for i in range(2 * H1) for lo, n in ((0, S), (S, CT))]
    v_t, b_v = [], []
    for half in range(2):
        v_t.append([(t, env.tile()) for t in range(NCH)])
        b_v.append(env.take_block(v_t[half][-1][1]))
    lr_in, keep_set, e_done, ln_done, g_done, c_done = (
        env.sem(n) for n in ("lr_in", "keep_set", "gate_exp", "gate_ln", "gate_log", "gate_sum"))
    with ExitStack() as st:
        wlr = st.enter_context(nc.sbuf_tensor("wlr", [P, KD, 32], F32))
        lrw = st.enter_context(nc.sbuf_tensor("lrw", [16, 2, H1 * DK], F32))
        lr = st.enter_context(nc.sbuf_tensor("lr", [16, 2, TOK], F32))
        gate = st.enter_context(nc.sbuf_tensor("gate_log", [P, 2 * H1, TOK], F32))
        ea = B.sum
        keep = st.enter_context(nc.sbuf_tensor("keep", [P, TOK], F32))
        with nc.Block() as block:
            @block.sync
            def _(sp):
                nc.sync.dma_start(wlr[:], dram["w_lr"]).then_inc(lr_in, 16)
                nc.sync.dma_start(lrw[:], dram["gla_lr_w"].rearrange("d r n -> r d n")).then_inc(lr_in, 16)
                load_blocks(env, sp)

            @block.scalar
            def _(act):
                for j, t in enumerate(q_t):
                    product_done(env, act, t)
                    nc.scalar.activation(B.q[:, j, :], env.ps[:, t[0], :], ACT.Copy, scale=DK ** -0.5).then_inc(
                        env.bank_free[t[0]], 1)
                for n, (i, lo, w, t) in enumerate(z_t):
                    act.wait_ge(g_done, n + 1)
                    nc.scalar.activation(ea[:, i, lo:lo + w], env.ps[:, t[0], 0:w], ACT.Abs,
                                         bias=col(env, "gla_b", i)).then_inc(env.bank_free[t[0]], 1)
                for n, (i, lo, w, t) in enumerate(z_t):
                    evacuated(env, act, t)
                    nc.scalar.activation(ea[:, i, lo:lo + w], ea[:, i, lo:lo + w], ACT.Exp, scale=-1.0).then_inc(e_done, 1)
                act.wait_ge(e_done, len(z_t))
                for i in range(2 * H1):
                    nc.scalar.activation(ea[:, i, :], ea[:, i, :], ACT.Ln, bias=1.0).then_inc(ln_done, 1)
                for half in range(2):
                    for i, t in v_t[half]:
                        product_done(env, act, t)
                        nc.scalar.activation(B.v[:, i, half * WBLK:(half + 1) * WBLK], env.ps[:, t[0], :],
                                             ACT.Copy).then_inc(env.bank_free[t[0]], 1)

            @block.vector
            def _(v):
                nc.vector.memset(keep[:], 1.0).then_inc(keep_set, 1)
                v.wait_ge(keep_set, 1)
                nc.vector.memset(chunks(keep[:])[:, :, 0:1], 0.0).then_inc(keep_set, 1)
                for j, lo, n, t in k_t:
                    product_done(env, v, t)
                    nc.vector.tensor_copy(B.k[:, j, lo:lo + n], env.ps[:, t[0], 0:n]).then_inc(env.bank_free[t[0]], 1)
                for d, lo, n, t in lr_t:
                    product_done(env, v, t)
                    nc.vector.tensor_copy(lr[:, d, lo:lo + n], env.ps[0:16, t[0], 0:n]).then_inc(env.bank_free[t[0]], 1)
                for i, lo, n, t in z_t:
                    product_done(env, v, t)
                    b = col(env, "gla_b", i)
                    nc.vector.tensor_scalar(gate[:, i, lo:lo + n], env.ps[:, t[0], 0:n], b, 0.0,
                                            ALU.add, ALU.min).then_inc(g_done, 1)
                nz = len(z_t)
                v.wait_ge(g_done, nz)
                for i in range(2 * H1):
                    v.wait_ge(ln_done, i + 1)
                    nc.vector.tensor_tensor(gate[:, i, :], gate[:, i, :], ea[:, i, :], ALU.subtract).then_inc(g_done, 1)
                v.wait_ge(keep_set, 2)
                for i in range(2 * H1):
                    v.wait_ge(g_done, nz + i + 1)
                    nc.vector.tensor_tensor_scan(B.sum[:, i, :], keep[:], gate[:, i, :], 0.0,
                                                 ALU.mult, ALU.add).then_inc(c_done, 1)
                v.wait_ge(c_done, 2 * H1)
                ends = B.sum[:].rearrange("p i (c t) -> p i c t", t=P)[:, :, :, P - 1:P]
                nc.vector.tensor_copy(B.tot[:], ends.rearrange("p i c o -> p i (c o)")).then_inc(c_done, 1)
                v.wait_ge(c_done, 2 * H1 + 1)
                for i in range(H1, 2 * H1):
                    nc.vector.tensor_tensor(B.sum[:, i, :], gate[:, i, :], B.sum[:, i, :], ALU.subtract).then_inc(c_done, 1)

            @block.tensor
            def _(pe):
                w = block_view(env, pe, b_q)
                for j, t in enumerate(q_t):
                    project(env, pe, t, env.ps[:, t[0], :], w, j * P, (j + 1) * P, lambda k: hT[:, k, 0:S])
                w = block_view(env, pe, b_k)
                for j, lo, n, t in k_t:
                    project(env, pe, t, env.ps[:, t[0], 0:n], w, j * P, (j + 1) * P, lambda k: hT[:, k, lo:lo + n])
                pe.wait_ge(lr_in, 32)
                for d, lo, n, t in lr_t:
                    project(env, pe, t, env.ps[0:16, t[0], 0:n], wlr, 16 * d, 16 * d + 16, lambda k: hT[:, k, lo:lo + n])
                for _, _, _, t in lr_t:
                    evacuated(env, pe, t)
                for i, lo, n, t in z_t:
                    d, hd = i // H1, i % H1
                    bank_ready(env, pe, t)
                    nc.tensor.matmul(env.ps[:, t[0], 0:n], lrw[:, d, hd * DK:(hd + 1) * DK], lr[:, d, lo:lo + n],
                                     start=True, stop=True).then_inc(env.bank_full[t[0]], 1)
                for half in range(2):
                    w = block_view(env, pe, b_v[half])
                    for i, t in v_t[half]:
                        bank_ready(env, pe, t)
                        for k in range(KD):
                            mm = nc.tensor.matmul(env.ps[:, t[0], :], hT[:, k, i * P:(i + 1) * P], w[:, k, :],
                                                  start=(k == 0), stop=(k == KD - 1))
                        mm.then_inc(env.bank_full[t[0]], 1)


def stage_gla_core(env, B, oT):
    nc = env.nc
    G = 1.0 / 16.0
    walk = [[4, 5, 0, 1, 2], [5, 4, 3, 2, 1]]
    entry = [{0: 2, 1: 3, 2: 4, 3: 5}, {3: 2, 2: 3, 1: 4, 0: 5}]
    plan = []
    turned = lambda: [env.tiles(2) for d in range(2)]
    tr_next = turned()
    for hd in range(H1):
        tr = tr_next
        up = [[env.tile() for _ in range(5)] for d in range(2)]
        sc = env.tiles(NT)
        tr_next = turned() if hd + 1 < H1 else None
        plan.append((tr, up, sc, env.tiles(NT)))
    fin = [env.tile() for _ in range(2 * H1)]
    names = ("g_arg", "g_exp", "g_mul", "g_dec", "g_zero", "g_sq", "g_rms", "g_inv", "g_nrm")
    arg_s, exp_s, mul_s, dec_s, zero_s, sq_s, rms_s, inv_s, nrm_s = (env.sem(n) for n in names)
    with ExitStack() as stk:
        T = lambda n, s: stk.enter_context(nc.sbuf_tensor("g_" + n, s, F32))
        both = lambda n, w: [T(f"{n}{i}", [P, 2, w]) for i in range(2)]
        args, e1s, e3s, e4s = both("arg", S), both("e1", S), both("e3", S), both("e4", TOK)
        ktok = T("ktok", [P, 2, 5, DK])
        st = T("state", [P, 2, 6, DV])
        dec = T("decay", [P, 2 * H1, NCH])
        pm = T("pm", [P, 2, 2, P])
        o = B.v[:, 0:NT, :].rearrange("p t (h v) -> p t h v", h=H1)
        sq = T("sqs", [P, DV])
        ss, rs = T("ss", [P, NT * H1]), T("rs", [P, NT * H1])
        mask = T("mask", [P, 2, P])
        mask_in = env.sem("g_mask_in")
        with nc.Block() as block:
            @block.sync
            def _(sp):
                nc.sync.dma_start(mask[:], env.dram["chunk_mask"]).then_inc(mask_in, 16)
                load_blocks(env, sp)

            @block.vector
            def _(v):
                nc.vector.memset(st[:, :, 0, :], 0.0).then_inc(zero_s, 1)
                v.wait_ge(dec_s, 1)
                v.wait_ge(zero_s, 1)
                def arguments(hd):
                    arg, e3, e4 = args[hd % 2], e3s[hd % 2], e4s[hd % 2]
                    if hd >= 2:
                        product_done(env, v, plan[hd - 2][3][-1])
                    for d in range(2):
                        c = B.sum[:, d * H1 + hd, :]
                        mid = chunks(c[:, 0:S])[:, :, 63 + d:64 + d].broadcast_to([P, NT, P])
                        nc.vector.tensor_tensor(chunks(arg[:, d, :]), chunks(c[:, 0:S]), mid, ALU.subtract).then_inc(arg_s, 1)
                        tot = B.tot[:, d * H1 + hd, :]
                        if d == 0:
                            nc.vector.tensor_tensor(chunks(e4[:, 0, :]), tot.unsqueeze(2).broadcast_to([P, NCH, P]),
                                                    chunks(c), ALU.subtract).then_inc(arg_s, 1)
                        else:
                            nc.vector.tensor_tensor(chunks(e3[:, 1, :]), chunks(c[:, 0:S]),
                                                    tot[:, 0:NT].unsqueeze(2).broadcast_to([P, NT, P]),
                                                    ALU.add).then_inc(arg_s, 1)

                def scaled(hd):
                    e1, e2, e3, e4 = e1s[hd % 2], args[hd % 2], e3s[hd % 2], e4s[hd % 2]
                    for d in range(2):
                        v.wait_ge(exp_s, 8 * hd + 4 * (d + 1))
                        for e, x in ((e4[:, d, :], B.k[:, hd, :]), (e1[:, d, :], B.q[:, hd, :]),
                                     (e2[:, d, :], B.k[:, hd, 0:S]), (e3[:, d, :], B.q[:, hd, :])):
                            nc.vector.tensor_tensor(e, e, x, ALU.mult).then_inc(mul_s, 1)

                arguments(0)
                scaled(0)
                for hd in range(H1):
                    tr, up, sc, ov = plan[hd]
                    if hd + 1 < H1:
                        arguments(hd + 1)
                    for d in range(2):
                        if hd >= 1:
                            product_done(env, v, plan[hd - 1][3][-1])
                        for n in range(5):
                            t = up[d][n]
                            product_done(env, v, t)
                            if n >= 1:
                                evacuated(env, v, up[d][n - 1])
                            i, ch = d * H1 + hd, walk[d][n]
                            nc.vector.scalar_tensor_tensor(st[:, d, n + 1, :], st[:, d, n, :], dec[:, i, ch:ch + 1],
                                                           env.ps[:, t[0], 0:DV], ALU.mult, ALU.add).then_inc(
                                env.bank_free[t[0]], 1)
                    if hd + 1 < H1:
                        scaled(hd + 1)
                    v.wait_ge(mask_in, 16)
                    for ch in range(NT):
                        t = sc[ch]
                        product_done(env, v, t)
                        if hd * NT + ch >= 2:
                            pt = plan[hd][3][ch - 2] if ch >= 2 else plan[hd - 1][3][ch + 2]
                            product_done(env, v, pt)
                        nc.vector.tensor_tensor(pm[:, ch % 2, :, :],
                                                env.ps[:, t[0], 0:2 * P].rearrange("p (d t) -> p d t", d=2),
                                                mask[:], ALU.mult).then_inc(env.bank_free[t[0]], 1)
                v.wait_ge(rms_s, 1)
                nc.vector.reciprocal(ss[:], rs[:]).then_inc(inv_s, 1)
                v.wait_ge(inv_s, 1)
                for hd in range(H1):
                    for ch in range(NT):
                        n = hd * NT + ch
                        nc.vector.tensor_scalar(o[:, ch, hd, :], o[:, ch, hd, :], ss[:, n:n + 1], None,
                                                ALU.mult).then_inc(nrm_s, 1)
                for j, t in enumerate(fin):
                    product_done(env, v, t)
                    nc.vector.tensor_scalar(oT[:, j, :], env.ps[:, t[0], :], col(env, "gla_norm", j % 2), None,
                                            ALU.mult).then_inc(env.bank_free[t[0]], 1)

            @block.scalar
            def _(act):
                nc.scalar.activation(dec[:], B.tot[:], ACT.Exp, scale=G).then_inc(dec_s, 1)
                def exponentials(hd):
                    arg, e1, e3, e4 = args[hd % 2], e1s[hd % 2], e3s[hd % 2], e4s[hd % 2]
                    for d in range(2):
                        act.wait_ge(arg_s, 4 * hd + 2 * (d + 1))
                        c = B.sum[:, d * H1 + hd, :]
                        nc.scalar.activation(e1[:, d, :], arg[:, d, :], ACT.Exp, scale=G).then_inc(exp_s, 1)
                        nc.scalar.activation(arg[:, d, :], arg[:, d, :], ACT.Exp, scale=-G).then_inc(exp_s, 1)
                        if d == 0:
                            nc.scalar.activation(e3[:, 0, :], c[:, 0:S], ACT.Exp, scale=G).then_inc(exp_s, 1)
                            nc.scalar.activation(e4[:, 0, :], e4[:, 0, :], ACT.Exp, scale=G).then_inc(exp_s, 1)
                        else:
                            nc.scalar.activation(e3[:, 1, :], e3[:, 1, :], ACT.Exp, scale=G).then_inc(exp_s, 1)
                            nc.scalar.activation(e4[:, 1, :], c, ACT.Exp, scale=-G).then_inc(exp_s, 1)

                def k_by_token(hd):
                    for d in range(2):
                        for part, (lo, n) in enumerate(((0, 4), (4, 1))):
                            t = plan[hd][0][d][part]
                            product_done(env, act, t)
                            if hd >= 1 and part == 0:
                                product_done(env, act, plan[hd - 1][1][d][4])
                            nc.scalar.activation(ktok[:, d, lo:lo + n, :],
                                                 env.ps[:, t[0], 0:n * P].rearrange("p (n k) -> p n k", k=DK),
                                                 ACT.Copy).then_inc(env.bank_free[t[0]], 1)

                exponentials(0)
                k_by_token(0)
                for hd in range(H1):
                    ov = plan[hd][3]
                    if hd + 1 < H1:
                        exponentials(hd + 1)
                        k_by_token(hd + 1)
                    for ch in range(NT):
                        t = ov[ch]
                        n = hd * NT + ch
                        product_done(env, act, t)
                        if n >= 1:
                            act.wait_ge(sq_s, n)
                        nc.scalar.activation(sq[:], env.ps[:, t[0], 0:DV], ACT.Square, accum_out=ss[:, n:n + 1]).then_inc(sq_s, 1)
                        nc.scalar.activation(o[:, ch, hd, :], env.ps[:, t[0], 0:DV], ACT.Copy).then_inc(env.bank_free[t[0]], 1)
                act.wait_ge(sq_s, NT * H1)
                nc.scalar.activation(rs[:], ss[:], ACT.Sqrt, scale=1.0 / DV, bias=env.eps[:, 0:1]).then_inc(rms_s, 1)

            @block.tensor
            def _(pe):
                def k_turned(hd):
                    for d in range(2):
                        pe.wait_ge(mul_s, 8 * hd + 4 * d + 1)
                        for part, (lo, n) in enumerate(((0, 4), (4, 1))):
                            t = plan[hd][0][d][part]
                            bank_ready(env, pe, t)
                            for i in range(n):
                                ch = walk[d][lo + i]
                                mm = nc.tensor.transpose(env.ps[:, t[0], i * P:(i + 1) * P],
                                                         e4s[hd % 2][:, d, ch * P:(ch + 1) * P], env.ident[:])
                            mm.then_inc(env.bank_full[t[0]], 1)

                k_turned(0)
                for hd in range(H1):
                    tr, up, sc, ov = plan[hd]
                    e1, e2, e3 = e1s[hd % 2], args[hd % 2], e3s[hd % 2]
                    for d in range(2):
                        for n in range(5):
                            t, ch = up[d][n], walk[d][n]
                            evacuated(env, pe, tr[d][0 if n < 4 else 1])
                            bank_ready(env, pe, t)
                            nc.tensor.matmul(env.ps[:, t[0], 0:DV], ktok[:, d, n, :], B.v[:, ch, hd * DV:(hd + 1) * DV],
                                             start=True, stop=True).then_inc(env.bank_full[t[0]], 1)
                    pe.wait_ge(mul_s, 8 * hd + 8)
                    for ch in range(NT):
                        t, cs = sc[ch], slice(ch * P, (ch + 1) * P)
                        bank_ready(env, pe, t)
                        for d in range(2):
                            mm = nc.tensor.matmul(env.ps[:, t[0], d * P:(d + 1) * P], e2[:, d, cs], e1[:, d, cs],
                                                  start=True, stop=True)
                        mm.then_inc(env.bank_full[t[0]], 1)
                    if hd + 1 < H1:
                        k_turned(hd + 1)
                    for ch in range(NT):
                        t, cs = ov[ch], slice(ch * P, (ch + 1) * P)
                        for d in range(2):
                            evacuated(env, pe, up[d][entry[d][ch] - 1])
                        evacuated(env, pe, sc[ch])
                        bank_ready(env, pe, t)
                        out = env.ps[:, t[0], 0:DV]
                        for d in range(2):
                            nc.tensor.matmul(out, e3[:, d, cs], st[:, d, entry[d][ch], :], start=(d == 0), stop=False)
                        for d in range(2):
                            mm = nc.tensor.matmul(out, pm[:, ch % 2, d, :], B.v[:, ch, hd * DV:(hd + 1) * DV],
                                                  start=False, stop=(d == 1))
                        mm.then_inc(env.bank_full[t[0]], 1)
                to_features(env, pe, fin, lambda ch, j: o[:, ch, j // 2, (j % 2) * P:(j % 2 + 1) * P],
                            lambda ch, j: pe.wait_ge(nrm_s, (j // 2) * NT + ch + 1))


def to_features(env, pe, tiles, src, wait):
    for j, t in enumerate(tiles):
        bank_ready(env, pe, t)
        for ch in range(NT):
            wait(ch, j)
            mm = env.nc.tensor.transpose(env.ps[:, t[0], ch * P:(ch + 1) * P], src(ch, j), env.ident[:])
        mm.then_inc(env.bank_full[t[0]], 1)


def stage_branch(env, name, oT, yT, first):
    nc, hT = env.nc, env.hT
    g_t = env.tiles(8)
    b_g = [env.take_block(g_t[3]), env.take_block(g_t[7])]
    m_t = env.tiles(8)
    b_m = [env.take_block(m_t[3]), env.take_block(m_t[7])]
    y_t = env.tiles(8)
    b_y = [env.take_block(y_t[3]), env.take_block(y_t[7])]
    mul_s, y_s = env.sem(name + "_gated"), env.sem(name + "_merged")
    with ExitStack() as st:
        gate = st.enter_context(nc.sbuf_tensor(name + "_gate", [P, KD, S], F32))
        merge = st.enter_context(nc.sbuf_tensor(name + "_merge", [P, KD, S], F32))
        with nc.Block() as block:
            @block.sync
            def _(sp):
                load_blocks(env, sp)

            @block.scalar
            def _(act):
                for j, t in enumerate(g_t):
                    product_done(env, act, t)
                    nc.scalar.activation(gate[:, j, :], env.ps[:, t[0], :], ACT.Silu).then_inc(env.bank_free[t[0]], 1)
                for j, t in enumerate(m_t):
                    product_done(env, act, t)
                    nc.scalar.activation(merge[:, j, :], env.ps[:, t[0], :], ACT.Sigmoid).then_inc(env.bank_free[t[0]], 1)

            @block.vector
            def _(v):
                for j, t in enumerate(g_t):
                    evacuated(env, v, t)
                    nc.vector.tensor_tensor(oT[:, j, :], oT[:, j, :], gate[:, j, :], ALU.mult).then_inc(mul_s, 1)
                for j, t in enumerate(y_t):
                    product_done(env, v, t)
                    evacuated(env, v, m_t[j])
                    out = yT[:, j, :] if first else merge[:, j, :]
                    nc.vector.tensor_tensor(out, merge[:, j, :], env.ps[:, t[0], :], ALU.mult).then_inc(
                        env.bank_free[t[0]], 1)
                    if not first:
                        evacuated(env, v, t)
                        nc.vector.tensor_tensor(yT[:, j, :], yT[:, j, :], merge[:, j, :], ALU.add).then_inc(y_s, 1)

            @block.tensor
            def _(pe):
                for tl, bl in ((g_t, b_g), (m_t, b_m)):
                    for i, b in enumerate(bl):
                        w = block_view(env, pe, b)
                        for j in range(4):
                            t = tl[4 * i + j]
                            project(env, pe, t, env.ps[:, t[0], :], w, j * P, (j + 1) * P, lambda k: hT[:, k, 0:S])
                pe.wait_ge(mul_s, KD)
                for i, b in enumerate(b_y):
                    w = block_view(env, pe, b)
                    for j in range(4):
                        t = y_t[4 * i + j]
                        project(env, pe, t, env.ps[:, t[0], :], w, j * P, (j + 1) * P, lambda k: oT[:, k, :])


def rope_mm(env, pe, tiles, perm, raw, ready):
    for j, t in enumerate(tiles):
        ready(j)
        bank_ready(env, pe, t)
        x = raw(j)
        env.nc.tensor.matmul(env.ps[0:x.shape[0], t[0], :], perm, x, start=True, stop=True).then_inc(env.bank_full[t[0]], 1)


def rope_dve(env, v, tiles, x, tab, sn, cos_s, rope_s):
    nc = env.nc
    for j, t in enumerate(tiles):
        a = x(j)
        rows = a.shape[0]
        product_done(env, v, t)
        nc.vector.tensor_tensor(a, a, tab[0:rows, 0, :], ALU.mult).then_inc(cos_s, 1)
        if j >= 2:
            v.wait_ge(rope_s, j - 1)
        nc.vector.tensor_tensor(sn[0:rows, j % 2, :], env.ps[0:rows, t[0], :], tab[0:rows, 1, :], ALU.mult).then_inc(
            env.bank_free[t[0]], 1)
        v.wait_ge(cos_s, j + 1)
        evacuated(env, v, t)
        nc.vector.tensor_tensor(a, a, sn[0:rows, j % 2, :], ALU.add).then_inc(rope_s, 1)


def stage_ret_project(env, R):
    nc, hT, dram = env.nc, env.hT, env.dram
    q_t = env.tiles(4)
    b_q = env.take_block(q_t[-1])
    k_t = env.tiles(4)
    kc_t = env.tiles(NCT)
    b_k = env.take_block(kc_t[-1])
    r_t = env.tiles(8)
    v_t, b_v = [], []
    for half in range(2):
        v_t.append(env.tiles(NCH))
        b_v.append(env.take_block(v_t[half][-1]))
    tab_in, cos_s, rope_s = env.sem("ret_tab_in"), env.sem("ret_cos"), env.sem("ret_rope")
    with ExitStack() as st:
        sn = st.enter_context(nc.sbuf_tensor("r_sn", [P, 2, S], F32))
        tab = st.enter_context(nc.sbuf_tensor("r_tab", [P, 2, S], F32))
        perm = st.enter_context(nc.sbuf_tensor("r_perm", [P, P], F32))
        with nc.Block() as block:
            @block.sync
            def _(sp):
                nc.sync.dma_start(tab[:], dram["rope_axial"]).then_inc(tab_in, 16)
                nc.sync.dma_start(perm[:], dram["perm_axial"]).then_inc(tab_in, 16)
                load_blocks(env, sp)

            @block.scalar
            def _(act):
                for j, t in enumerate(q_t + k_t):
                    product_done(env, act, t)
                    nc.scalar.activation(R.qk[:, j, :], env.ps[:, t[0], :], ACT.Copy).then_inc(env.bank_free[t[0]], 1)
                for i, t in enumerate(kc_t):
                    product_done(env, act, t)
                    nc.scalar.activation(R.kc[:, i, :], env.ps[:, t[0], :], ACT.Copy).then_inc(env.bank_free[t[0]], 1)
                for half in range(2):
                    for i, t in enumerate(v_t[half]):
                        product_done(env, act, t)
                        nc.scalar.activation(R.v[:, i, half * WBLK:(half + 1) * WBLK], env.ps[:, t[0], :],
                                             ACT.Copy).then_inc(env.bank_free[t[0]], 1)

            @block.vector
            def _(v):
                v.wait_ge(tab_in, 32)
                rope_dve(env, v, r_t, lambda j: R.qk[:, j, :], tab, sn, cos_s, rope_s)

            @block.tensor
            def _(pe):
                w = block_view(env, pe, b_q)
                for j, t in enumerate(q_t):
                    project(env, pe, t, env.ps[:, t[0], :], w, j * P, (j + 1) * P, lambda k: hT[:, k, 0:S])
                w = block_view(env, pe, b_k)
                for j, t in enumerate(k_t):
                    project(env, pe, t, env.ps[:, t[0], :], w, j * P, (j + 1) * P, lambda k: hT[:, k, 0:S])
                for i, t in enumerate(kc_t):
                    by_token(env, pe, t, WBLK, w, NT + i)
                pe.wait_ge(tab_in, 32)
                rope_mm(env, pe, r_t, perm[:], lambda j: R.qk[:, j, :], lambda j: evacuated(env, pe, (q_t + k_t)[j]))
                for half in range(2):
                    w = block_view(env, pe, b_v[half])
                    for i, t in enumerate(v_t[half]):
                        by_token(env, pe, t, WBLK, w, i)


def by_token(env, pe, t, n, w, i, lo=0):
    bank_ready(env, pe, t)
    for k in range(KD):
        mm = env.nc.tensor.matmul(env.ps[:, t[0], 0:n], env.hT[:, k, i * P:(i + 1) * P], w[:, k, lo:lo + n],
                                  start=(k == 0), stop=(k == KD - 1))
    mm.then_inc(env.bank_full[t[0]], 1)


def stage_ret_core(env, R, oT):
    nc, dram = env.nc, env.dram
    st_t = [[env.tile() for d in range(2)] for hd in range(H1)]
    plan = [([env.tile() for _ in range(NT)], [env.tile() for _ in range(NT)]) for hd in range(H1)]
    fin = env.tiles(2 * H1)
    in_s, kd_s, qd_s, bn_s, mv_s, rms_s, inv_s, nrm_s, o_s = (env.sem("rc_" + n) for n in (
        "in", "kd", "qd", "bn", "mv", "rms", "inv", "nrm", "o"))
    qdec_in = [env.sem(f"rc_qdec_in{i}") for i in range(2)]
    with ExitStack() as stk:
        T = lambda n, s: stk.enter_context(nc.sbuf_tensor("rc_" + n, s, F32))
        band = T("band", [P, H1, 896])
        qdec = T("qdec", [P, 2, 2, S])
        kdec = T("kdec", [P, 2 * H1, NCT])
        kd = T("kd", [P, 2, 2, NCT, DK])
        st = T("st", [P, H1, 2, DV])
        qd = T("qd", [P, 2, S])
        pm = T("pm", [P, NT, S])
        o = T("o", [P, NT, H1, DV])
        bn = T("bn", [P, NT * H1, 6])
        mv = T("mv", [P, NT * H1, 2])
        rs = T("rs", [P, NT * H1, 1])
        iv = T("iv", [P, NT * H1, 1])
        with nc.Block() as block:
            @block.sync
            def _(sp):
                nc.sync.dma_start(kdec[:], dram["ret_kdec"]).then_inc(in_s, 16)
                nc.sync.dma_start(band[:], dram["ret_band"]).then_inc(in_s, 16)
                for hd in range(H1):
                    if hd >= 2:
                        sp.wait_ge(qd_s, 2 * (hd - 1))
                    row = dram["ret_qdec"][hd:hd + 1].broadcast_to([P, 2, S])
                    nc.sync.dma_start(qdec[:, hd % 2], row).then_inc(qdec_in[hd % 2], 16)
                load_blocks(env, sp)

            @block.vector
            def _(v):
                v.wait_ge(in_s, 32)
                for hd in range(H1):
                    for d in range(2):
                        if hd >= 2:
                            product_done(env, v, st_t[hd - 2][d])
                        for i in range(NCT):
                            nc.vector.tensor_scalar(kd[:, hd % 2, d, i, :], R.kc[:, i, hd * DK:(hd + 1) * DK],
                                                    kdec[:, d * H1 + hd, i:i + 1], None, ALU.mult).then_inc(kd_s, 1)
                for hd in range(H1):
                    sc, ov = plan[hd]
                    if hd >= 1:
                        product_done(env, v, plan[hd - 1][1][-1])
                    v.wait_ge(qdec_in[hd % 2], 16 * (hd // 2 + 1))
                    for d in range(2):
                        nc.vector.tensor_tensor(qd[:, d, :], R.qk[:, hd, :], qdec[:, hd % 2, d, :], ALU.mult).then_inc(qd_s, 1)
                    for J, t in enumerate(sc):
                        product_done(env, v, t)
                        nc.vector.tensor_tensor(pm[:, J, :], env.ps[:, t[0], :], band[:, hd, 384 - J * P:384 - J * P + S],
                                                ALU.mult).then_inc(env.bank_free[t[0]], 1)
                    for I, t in enumerate(ov):
                        product_done(env, v, t)
                        nc.vector.bn_stats(bn[:, hd * NT + I, :], env.ps[:, t[0], 0:DV]).then_inc(bn_s, 1)
                for n in range(NT * H1):
                    v.wait_ge(bn_s, n + 1)
                    nc.vector.bn_aggr(mv[:, n, :], bn[:, n, :]).then_inc(mv_s, 1)
                v.wait_ge(rms_s, 1)
                nc.vector.reciprocal(iv[:], rs[:]).then_inc(inv_s, 1)
                v.wait_ge(inv_s, 1)
                v.wait_ge(o_s, NT * H1)
                for hd in range(H1):
                    for I in range(NT):
                        n = hd * NT + I
                        nc.vector.tensor_scalar(o[:, I, hd, :], o[:, I, hd, :], mv[:, n, 0:1], iv[:, n, :],
                                                ALU.subtract, ALU.mult).then_inc(nrm_s, 1)
                for j, t in enumerate(fin):
                    product_done(env, v, t)
                    nc.vector.tensor_copy(oT[:, j, :], env.ps[:, t[0], :]).then_inc(env.bank_free[t[0]], 1)

            @block.scalar
            def _(act):
                for hd in range(H1):
                    for d in range(2):
                        t = st_t[hd][d]
                        product_done(env, act, t)
                        nc.scalar.activation(st[:, hd, d, :], env.ps[:, t[0], 0:DV], ACT.Copy).then_inc(env.bank_free[t[0]], 1)
                for hd in range(H1):
                    for I, t in enumerate(plan[hd][1]):
                        act.wait_ge(bn_s, hd * NT + I + 1)
                        nc.scalar.activation(o[:, I, hd, :], env.ps[:, t[0], 0:DV], ACT.Copy).then_inc(env.bank_free[t[0]], 1)
                for hd in range(H1):
                    for t in plan[hd][1]:
                        evacuated(env, act, t)
                act.wait_ge(mv_s, NT * H1)
                nc.scalar.activation(rs[:], mv[:, :, 1:2], ACT.Sqrt, bias=env.eps[:, 0:1]).then_inc(rms_s, 1)
                nc.scalar.sem_inc(o_s, NT * H1)

            @block.tensor
            def _(pe):
                for hd in range(H1):
                    for d in range(2):
                        t = st_t[hd][d]
                        pe.wait_ge(kd_s, hd * 4 + d * 2 + 2)
                        bank_ready(env, pe, t)
                        for i in range(NCT):
                            mm = nc.tensor.matmul(env.ps[:, t[0], 0:DV], kd[:, hd % 2, d, i, :],
                                                  R.v[:, NT + i, hd * DV:(hd + 1) * DV], start=(i == 0), stop=(i == NCT - 1))
                        mm.then_inc(env.bank_full[t[0]], 1)
                for hd in range(H1):
                    sc, ov = plan[hd]
                    for J, t in enumerate(sc):
                        bank_ready(env, pe, t)
                        nc.tensor.matmul(env.ps[:, t[0], :], R.qk[:, 4 + hd, J * P:(J + 1) * P], R.qk[:, hd, :],
                                         start=True, stop=True).then_inc(env.bank_full[t[0]], 1)
                    pe.wait_ge(qd_s, 2 * (hd + 1))
                    for d in range(2):
                        evacuated(env, pe, st_t[hd][d])
                    for I, t in enumerate(ov):
                        bank_ready(env, pe, t)
                        out, ts = env.ps[:, t[0], 0:DV], slice(I * P, (I + 1) * P)
                        for d in range(2):
                            nc.tensor.matmul(out, qd[:, d, ts], st[:, hd, d, :], start=(d == 0), stop=False)
                        for J in range(NT):
                            evacuated(env, pe, sc[J])
                            mm = nc.tensor.matmul(out, pm[:, J, ts], R.v[:, J, hd * DV:(hd + 1) * DV],
                                                  start=False, stop=(J == NT - 1))
                        mm.then_inc(env.bank_full[t[0]], 1)
                to_features(env, pe, fin, lambda ch, j: o[:, ch, j // 2, (j % 2) * P:(j % 2 + 1) * P],
                            lambda ch, j: pe.wait_ge(nrm_s, (j // 2) * NT + ch + 1))


def stage_out(env, name, src, gate):
    nc = env.nc
    tl = [env.tiles(NT) for _ in range(2)]
    bl = [env.take_block(t[-1]) for t in tl]
    g_s = env.sem(name + "_sum")
    with ExitStack() as st:
        tmp = st.enter_context(nc.sbuf_tensor(name + "_tmp", [P, 2 * NT, WBLK], F32))
        with nc.Block() as block:
            @block.sync
            def _(sp):
                load_blocks(env, sp)

            @block.vector
            def _(v):
                for half in range(2):
                    cs = slice(half * WBLK, (half + 1) * WBLK)
                    for i, t in enumerate(tl[half]):
                        product_done(env, v, t)
                        got = env.ps[:, t[0], :]
                        if gate is None:
                            nc.vector.tensor_tensor(env.h[:, i, cs], env.h[:, i, cs], got, ALU.add).then_inc(
                                env.bank_free[t[0]], 1)
                        else:
                            x = tmp[:, half * NT + i, :]
                            nc.vector.tensor_tensor(x, env.gates[:, gate, cs], got, ALU.mult).then_inc(env.bank_free[t[0]], 1)
                            evacuated(env, v, t)
                            nc.vector.tensor_tensor(env.h[:, i, cs], env.h[:, i, cs], x, ALU.add).then_inc(g_s, 1)

            @block.tensor
            def _(pe):
                for half in range(2):
                    w = block_view(env, pe, bl[half])
                    for i, t in enumerate(tl[half]):
                        bank_ready(env, pe, t)
                        for k in range(KD):
                            mm = nc.tensor.matmul(env.ps[:, t[0], :], src[:, k, i * P:(i + 1) * P], w[:, k, :],
                                                  start=(k == 0), stop=(k == KD - 1))
                        mm.then_inc(env.bank_full[t[0]], 1)


def stage_rownorm(env, name, dst, row_name, store=None, stored=None):
    nc = env.nc
    row_in, run16 = env.again("row_in", 16)
    sq_s, sq0 = env.again("row_sq", NT)
    rms_s, run = env.again("row_rms", 1)
    inv_s, _ = env.again("row_inv", 1)
    done, d0 = env.again("row_done", NT)
    out_s, out0 = env.again("row_out", 16 * NT if store is not None else 0)
    with ExitStack() as st:
        row = st.enter_context(nc.sbuf_tensor(name + "_row", [P, D], F32))
        sq = st.enter_context(nc.sbuf_tensor(name + "_sqs", [P, 2, D], F32))
        ss = st.enter_context(nc.sbuf_tensor(name + "_ss", [P, NT], F32))
        rs = st.enter_context(nc.sbuf_tensor(name + "_rs", [P, NT], F32))
        with nc.Block() as block:
            @block.sync
            def _(sp):
                nc.sync.dma_start(row[:], env.dram[row_name].broadcast_to([P, D])).then_inc(row_in, 16)
                load_blocks(env, sp)
                if stored is not None:
                    sp.wait_ge(*stored)
                if store is not None:
                    rows = store.rearrange("(t p) d -> t p d", p=P)
                    for t in range(NT):
                        sp.wait_ge(done, d0 + t + 1)
                        nc.sync.dma_start(rows[t], dst[:, t, :]).then_inc(out_s, 16)
                    sp.wait_ge(out_s, out0 + 16 * NT)

            @block.scalar
            def _(act):
                for t in range(NT):
                    if t >= 2:
                        act.wait_ge(sq_s, sq0 + t - 1)
                    nc.scalar.activation(sq[:, t % 2, :], env.h[:, t, :], ACT.Square, accum_out=ss[:, t:t + 1]).then_inc(sq_s, 1)
                act.wait_ge(sq_s, sq0 + NT)
                nc.scalar.activation(rs[:], ss[:], ACT.Sqrt, scale=1.0 / D, bias=env.eps[:, 0:1]).then_inc(rms_s, 1)

            @block.vector
            def _(v):
                v.wait_ge(rms_s, run + 1)
                nc.vector.reciprocal(ss[:], rs[:]).then_inc(inv_s, 1)
                v.wait_ge(row_in, run16 + 16)
                v.wait_ge(inv_s, run + 1)
                for t in range(NT):
                    nc.vector.scalar_tensor_tensor(dst[:, t, :], env.h[:, t, :], ss[:, t:t + 1], row[:],
                                                   ALU.mult, ALU.mult).then_inc(done, 1)


PLE = 256
NG, EPG = 4, 8
NE = NG * EPG
EF = 256
EFT = EF // P
NR = NG + NE
EW = KD * 2 * EF + EFT * D


ROWB = P
PICKS = 2
NB = NE + (PICKS * S - NE) // ROWB
SLOT = 3
LAST = NB // SLOT


def stage_router(env, E):
    nc, dram = env.nc, env.dram
    t_lg, t_rank, t_rows = env.tile(), env.tile(), env.tile()
    in_s, exp_s, ch_s, pair_s = (env.sem("rt_" + n) for n in ("in", "exp", "chain", "pair"))
    with ExitStack() as st:
        T = lambda n, s, d=F32: st.enter_context(nc.sbuf_tensor("rt_" + n, s, d))
        wr, br = T("w", [P, KD, NR]), T("b", [1, NR])
        idx = T("idx", [P, 2, NE])
        before, row_no, block_no = T("before", [P, P]), T("row_no", [P, ROWB]), T("block_no", [P, NB])
        tok_no = T("tok_no", [P, NT])
        lg, gp = T("lg", [P, NT, NR]), T("gp", [P, NT, 8])
        gm, gi, gif = T("gm", [P, NT, 8]), T("gi", [P, NT, 8], U32), T("gif", [P, NT, 8])
        ng, gx, gs, gw = T("ng", [P, NT]), T("gx", [P, NT, 8]), T("gs", [P, NT]), T("gw", [P, NT])
        em, ev, ei, eif = T("em", [P, NT, NE]), T("ev", [P, NT, 8]), T("ei", [P, NT, 8], U32), T("eif", [P, NT, 8])
        df, dx, one_dx = T("df", [P, NT]), T("dx", [P, NT]), T("one_dx", [P, NT])
        picked, both = T("picked", [P, PICKS, NT, NE]), T("both", [P, NT, NE])
        count, count_u, blocks, ends = T("count", [P, NE]), T("count_u", [P, NE], U32), T("blocks", [P, NE]), T("ends", [P, NE])
        starts, at = T("starts", [P, NE]), T("at", [P, NT, NE])
        pos, split, splitf = T("pos", [P, PICKS, NT]), T("split", [P, 2, PICKS, NT], U32), T("splitf", [P, 2, PICKS, NT])
        in_row, in_block = T("in_row", [P, PICKS, NT, ROWB]), T("in_block", [P, PICKS, NT, NB])
        past, block_e = T("past", [P, NB, NE]), T("block_e", [P, NB])
        with nc.Block() as block:
            @block.sync
            def _(sp):
                loads = ((wr, "w_router"), (br, "b_router"), (idx, "expert_numbers"), (before, "token_before"),
                         (row_no, "row_numbers"), (block_no, "block_numbers"), (tok_no, "token_numbers"))
                for dst, name in loads:
                    nc.sync.dma_start(dst[:], dram[name]).then_inc(in_s, 16)
                load_blocks(env, sp)

            @block.tensor
            def _(pe):
                pe.wait_ge(in_s, 112)
                bank_ready(env, pe, t_lg)
                for t in range(NT):
                    out = env.ps[:, t_lg[0], t * NR:(t + 1) * NR]
                    for k in range(KD):
                        nc.tensor.matmul(out, env.hT[:, k, t * P:(t + 1) * P], wr[:, k, :], start=(k == 0), stop=False)
                    mm = nc.tensor.matmul(out, env.ones[0:1, :], br[:], start=False, stop=True)
                mm.then_inc(env.bank_full[t_lg[0]], 1)
                bank_ready(env, pe, t_rank)
                pe.wait_ge(pair_s, 3)
                for t in range(NT + 1):
                    out = env.ps[:, t_rank[0], t * NE:(t + 1) * NE]
                    for u in range(min(t + 1, NT)):
                        mm = nc.tensor.matmul(out, before[:] if u == t else env.ones[:], both[:, u, :],
                                              start=(u == 0), stop=(u == min(t, NT - 1)))
                mm.then_inc(env.bank_full[t_rank[0]], 1)
                bank_ready(env, pe, t_rows)
                pe.wait_ge(pair_s, 4)
                for n in range(PICKS * NT):
                    mm = nc.tensor.matmul(env.ps[:, t_rows[0], 0:NB], in_row[:, n // NT, n % NT, :],
                                          in_block[:, n // NT, n % NT, :], start=(n == 0), stop=(n == PICKS * NT - 1))
                mm.then_inc(env.bank_full[t_rows[0]], 1)

            @block.scalar
            def _(act):
                for t in range(NT):
                    act.wait_ge(pair_s, 1)
                    nc.scalar.activation(gx[:, t, :], gp[:, t, :], ACT.Exp, bias=ng[:, t:t + 1],
                                         accum_out=gs[:, t:t + 1]).then_inc(exp_s, 1)
                act.wait_ge(pair_s, 2)
                nc.scalar.activation(dx[:], df[:], ACT.Exp).then_inc(exp_s, 1)

            @block.vector
            def _(v):
                step = Group(ch_s)
                V = nc.vector
                ts = range(NT)
                step(v, [V.memset(gp[:], NEG)])
                v.wait_ge(in_s, 112)
                product_done(env, v, t_lg)
                V.tensor_copy(lg[:], env.ps[:, t_lg[0], 0:NT * NR].rearrange("p (t n) -> p t n", t=NT)).then_inc(
                    env.bank_free[t_lg[0]], 1)
                evacuated(env, v, t_lg)
                step(v, [V.tensor_copy(gp[:, :, 0:NG], lg[:, :, 0:NG])])
                step(v, [V.max(gm[:, t, :], gp[:, t, :]) for t in ts])
                V.tensor_scalar(ng[:], gm[:, :, 0], -1.0, None, ALU.mult).then_inc(pair_s, 1)
                step(v, [V.max_index(gi[:, t, :], gm[:, t, :], gp[:, t, :]) for t in ts])
                step(v, [V.tensor_copy(gif[:], gi[:])])
                step(v, [V.tensor_scalar(em[:, t, :], idx[:, 1, :], gif[:, t, 0:1], -NEG, ALU.is_equal, ALU.mult) for t in ts])
                step(v, [V.scalar_tensor_tensor(em[:, t, :], em[:, t, :], NEG, lg[:, t, NG:NR], ALU.add, ALU.add) for t in ts])
                step(v, [V.max(ev[:, t, :], em[:, t, :]) for t in ts])
                step(v, [V.max_index(ei[:, t, :], ev[:, t, :], em[:, t, :]) for t in ts])
                V.tensor_tensor(df[:], ev[:, :, 1], ev[:, :, 0], ALU.subtract).then_inc(pair_s, 1)
                step(v, [V.tensor_copy(eif[:], ei[:])])
                step(v, [V.tensor_scalar(picked[:, k, t, :], idx[:, 0, :], eif[:, t, k:k + 1], None, ALU.is_equal)
                         for k in range(PICKS) for t in ts])
                V.tensor_tensor(both[:], picked[:, 0], picked[:, 1], ALU.add).then_inc(pair_s, 1)
                v.wait_ge(exp_s, NT + 1)
                step(v, [V.reciprocal(gw[:], gs[:]), V.tensor_scalar(one_dx[:], dx[:], 1.0, None, ALU.add)])
                step(v, [V.reciprocal(E.weight[:, 0, :], one_dx[:])])
                step(v, [V.tensor_tensor(E.weight[:, 0, :], E.weight[:, 0, :], gw[:], ALU.mult)])
                step(v, [V.tensor_tensor(E.weight[:, 1, :], dx[:], E.weight[:, 0, :], ALU.mult)])
                product_done(env, v, t_rank)
                step(v, [V.tensor_scalar(count[:], env.ps[:, t_rank[0], NT * NE:(NT + 1) * NE], ROWB - 1.0, None, ALU.add)])
                step(v, [V.tensor_copy(count_u[:], count[:])])
                step(v, [V.tensor_scalar(count_u[:], count_u[:], 7, None, ALU.logical_shift_right)])
                step(v, [V.tensor_copy(blocks[:], count_u[:])])
                step(v, [V.tensor_tensor_scan(ends[:], env.ones[:, 0:NE], blocks[:], 0.0, ALU.mult, ALU.add)])
                step(v, [V.tensor_tensor(starts[:], ends[:], blocks[:], ALU.subtract)])
                V.scalar_tensor_tensor(at[:], starts[:].unsqueeze(1).broadcast_to([P, NT, NE]), float(ROWB),
                                       env.ps[:, t_rank[0], 0:NT * NE].rearrange("p (t e) -> p t e", t=NT),
                                       ALU.mult, ALU.add).then_inc(env.bank_free[t_rank[0]], 1)
                evacuated(env, v, t_rank)
                step(v, [V.tensor_tensor(picked[:, k], picked[:, k], at[:], ALU.mult) for k in range(PICKS)])
                step(v, [V.reduce_sum(pos[:, k], picked[:, k], axis=AX.X) for k in range(PICKS)])
                step(v, [V.tensor_copy(E.pos[:], pos[:])])
                step(v, [V.tensor_scalar(split[:, 0], E.pos[:], 127, None, ALU.bitwise_and),
                         V.tensor_scalar(split[:, 1], E.pos[:], 7, None, ALU.logical_shift_right)])
                step(v, [V.tensor_copy(splitf[:], split[:])])
                both_kt = [(k, t) for k in range(PICKS) for t in ts]
                step(v, [V.tensor_scalar(in_row[:, k, t, :], row_no[:], splitf[:, 0, k, t:t + 1], None, ALU.is_equal)
                         for k, t in both_kt] +
                        [V.tensor_scalar(in_block[:, k, t, :], block_no[:], splitf[:, 1, k, t:t + 1], tok_no[:, t:t + 1],
                                         ALU.is_equal, ALU.mult) for k, t in both_kt[:-1]])
                k, t = both_kt[-1]
                V.tensor_scalar(in_block[:, k, t, :], block_no[:], splitf[:, 1, k, t:t + 1], tok_no[:, t:t + 1],
                                ALU.is_equal, ALU.mult).then_inc(pair_s, 1)
                step(v, [V.tensor_tensor(past[:], ends[:].unsqueeze(1).broadcast_to([P, NB, NE]),
                                         block_no[:].unsqueeze(2).broadcast_to([P, NB, NE]), ALU.is_le)])
                step(v, [V.reduce_sum(block_e[:], past[:], axis=AX.X)])
                step(v, [V.tensor_scalar(block_e[:], block_e[:], float(NE - 1), None, ALU.min)])
                step(v, [V.tensor_copy(E.block_expert[:], block_e[:])])
                product_done(env, v, t_rows)
                V.tensor_copy(E.row_token[:], env.ps[:, t_rows[0], 0:NB]).then_inc(env.bank_free[t_rows[0]], 1)
                evacuated(env, v, t_rows)


def stage_experts(env, E):
    nc, dram = env.nc, env.dram
    names = ("idx", "rows_full", "xT_done", "gu_full", "silu_done", "hid_done", "hidT_full", "hidT_done", "dn_full", "y_done")
    idx_s, rows_full, xT_done, gu_full, silu_done, hid_done, hidT_full, hidT_done, dn_full, y_done = (
        env.sem("ex_" + n) for n in names)
    x_got, w_got, y_out = ([env.sem(f"ex_{n}{s}") for s in range(SLOT)] for n in ("x_got", "w_got", "y_out"))
    gain, shift = (lambda j: env.gain[:, 2, j:j + 1]), (lambda j: env.ada[:, 24 + j, 0:1])
    ROWS, GU, HID, DOWN = [0, 1], [2, 3, 4], 5, [6, 7]
    y_rows = dram["y_dram"].rearrange("(b p) d -> b p d", p=ROWB)
    with ExitStack() as st:
        T = lambda n, s, d=F32: st.enter_context(nc.sbuf_tensor("ex_" + n, s, d))
        idx = T("idx", [P, SLOT], U32)
        x, xT = T("x", [P, SLOT, D]), T("xT", [P, SLOT, KD, P])
        w = T("w", [P, SLOT, EW])
        silu, hid, hidT = T("silu", [P, SLOT, EF]), T("hid", [P, SLOT, EF]), T("hidT", [P, SLOT, EFT, P])
        y = T("y", [P, SLOT, D])
        wg = [w[:, s, 0:KD * 2 * EF].rearrange("p (k n) -> p k n", k=KD) for s in range(SLOT)]
        wd = [w[:, s, KD * 2 * EF:EW].rearrange("p (k n) -> p k n", k=EFT) for s in range(SLOT)]

        def after(i, s):
            return (i, s + 1) if s + 1 < SLOT else (i + 1, 0)

        with nc.Block() as block:
            @block.gpsimd
            def _(pool):
                with pool.Fori(0, LAST) as i:
                    for s in range(SLOT):
                        b = SLOT * i + s
                        pool.wait_ge(rows_full, 2 * b + 2)
                        pool.nop(nofuse=True)
                        nc.gpsimd.tensor_copy(idx[:, s:s + 1], E.row_token[:, bass.ds(b, 1)]).then_inc(idx_s, 1)
                        pool.wait_ge(idx_s, b + 1)
                        pool.nop(nofuse=True)
                        nc.gpsimd.indirect_dma_start(x[:, s, :], None, dram["xn_dram"], bass.IndirectOffsetOnAxis(
                            ap=idx[:, s:s + 1], axis=0)).then_inc(x_got[s], 16)

            @block.sync
            def _(sp):
                def load(b, s):
                    e = nc.sync.value_load(E.block_expert[0:1, bass.ds(b, 1)], min_val=0, max_val=NE - 1)
                    nc.sync.dma_start(w[:, s, :], dram["experts"][bass.ds(e, 1)].rearrange("o p n -> p (o n)")
                                      ).then_inc(w_got[s], 16)

                def store(b, s):
                    sp.wait_ge(y_done, 2 + 2 * b + 2)
                    sp.nop(nofuse=True)
                    nc.sync.dma_start(y_rows[bass.ds(b, 1)].rearrange("o p d -> p (o d)"), y[:, s, :]).then_inc(y_out[s], 16)

                for s in range(SLOT):
                    sp.sem_inc(y_out[s], 16)
                    load(s, s)
                with sp.Fori(0, LAST - 1) as i:
                    for s in range(SLOT):
                        sp.wait_ge(dn_full, 2 * (SLOT * i + s) + 2)
                        sp.nop(nofuse=True)
                        load(SLOT * i + SLOT + s, s)
                        store(SLOT * i + s, s)
                for s in range(SLOT):
                    store(SLOT * (LAST - 1) + s, s)
                load_blocks(env, sp)
                for s in range(SLOT):
                    sp.wait_ge(y_out[s], 16 + 16 * LAST)

            @block.tensor
            def _(pe):
                def rows(i, s, first=False):
                    b = SLOT * i + s
                    pe.wait_ge(x_got[s], 16 * i + 16)
                    for n in range(2):
                        if not first:
                            pe.wait_ge(xT_done, KD * b - KD // 2 * (1 - n))
                        for j in range(KD // 2):
                            mm = nc.tensor.transpose(env.ps[:, ROWS[n], j * P:(j + 1) * P],
                                                     x[:, s, (n * KD // 2 + j) * P:(n * KD // 2 + j + 1) * P], env.ident[:])
                        mm.then_inc(rows_full, 1)

                def gate_up(i, s):
                    b = SLOT * i + s
                    pe.wait_ge(w_got[s], 16 * i + 16)
                    pe.wait_ge(xT_done, KD * b + KD)
                    for k in range(KD):
                        mm = nc.tensor.matmul(env.ps[:, GU[s], :], xT[:, s, k, :], wg[s][:, k, :],
                                              start=(k == 0), stop=(k == KD - 1))
                    mm.then_inc(gu_full, 1)

                def hidden(i, s):
                    pe.wait_ge(hid_done, SLOT * i + s + 1)
                    for k in range(EFT):
                        mm = nc.tensor.transpose(env.ps[:, HID, k * P:(k + 1) * P], hid[:, s, k * P:(k + 1) * P], env.ident[:])
                    mm.then_inc(hidT_full, 1)

                def down(i, s):
                    b = SLOT * i + s
                    pe.wait_ge(hidT_done, b + 1)
                    for n in range(2):
                        pe.wait_ge(y_done, 2 * b + n + 1)
                        for k in range(EFT):
                            mm = nc.tensor.matmul(env.ps[:, DOWN[n], :], hidT[:, s, k, :],
                                                  wd[s][:, k, n * WBLK:(n + 1) * WBLK], start=(k == 0), stop=(k == EFT - 1))
                        mm.then_inc(dn_full, 1)

                pe.sem_inc(rows_full, 2 * SLOT)
                rows(0, 0, first=True)
                gate_up(0, 0)
                rows(0, 1)
                with pe.Fori(0, LAST - 1) as i:
                    for s in range(SLOT):
                        now = after(i, s)
                        gate_up(*now)
                        hidden(i, s)
                        rows(*after(*now))
                        down(i, s)
                for s in range(SLOT):
                    now = after(LAST - 1, s)
                    if s + 1 < SLOT:
                        gate_up(*now)
                    hidden(LAST - 1, s)
                    if s + 2 < SLOT:
                        rows(*after(*now))
                    down(LAST - 1, s)

            @block.scalar
            def _(act):
                def gate(i, s):
                    act.wait_ge(gu_full, SLOT * i + s + 1)
                    nc.scalar.activation(silu[:, s, :], env.ps[:, GU[s], 0:EF], ACT.Silu).then_inc(silu_done, 1)

                def finish(i, s):
                    b = SLOT * i + s
                    act.wait_ge(hidT_full, b + 1)
                    nc.scalar.activation(hidT[:, s].rearrange("p k t -> p (k t)"), env.ps[:, HID, 0:EF],
                                         ACT.Copy).then_inc(hidT_done, 1)
                    act.wait_ge(y_out[s], 16 * i + 16)
                    for n in range(2):
                        act.wait_ge(dn_full, 2 * b + n + 1)
                        nc.scalar.activation(y[:, s, n * WBLK:(n + 1) * WBLK], env.ps[:, DOWN[n], :],
                                             ACT.Copy).then_inc(y_done, 1)

                act.sem_inc(y_done, 2)
                gate(0, 0)
                with act.Fori(0, LAST - 1) as i:
                    for s in range(SLOT):
                        gate(*after(i, s))
                        finish(i, s)
                for s in range(SLOT):
                    if s + 1 < SLOT:
                        gate(*after(LAST - 1, s))
                    finish(LAST - 1, s)

            @block.vector
            def _(v):
                def features(i, s):
                    b = SLOT * i + s
                    for n in range(2):
                        v.wait_ge(rows_full, 2 * SLOT + 2 * b + n + 1)
                        for j in range(KD // 2):
                            k = n * KD // 2 + j
                            nc.vector.tensor_scalar(xT[:, s, k, :], env.ps[:, ROWS[n], j * P:(j + 1) * P], gain(k), shift(k),
                                                    ALU.mult, ALU.add).then_inc(xT_done, 1)

                def product(i, s):
                    v.wait_ge(silu_done, SLOT * i + s + 1)
                    nc.vector.tensor_tensor(hid[:, s, :], silu[:, s, :], env.ps[:, GU[s], EF:2 * EF],
                                            ALU.mult).then_inc(hid_done, 1)

                features(0, 0)
                with v.Fori(0, LAST - 1) as i:
                    for s in range(SLOT):
                        product(i, s)
                        features(*after(i, s))
                for s in range(SLOT):
                    product(LAST - 1, s)
                    if s + 1 < SLOT:
                        features(*after(LAST - 1, s))


def stage_expert_sum(env, E):
    nc, dram = env.nc, env.dram
    got = [env.again(f"gathered{t}", 16 * PICKS)[0] for t in range(NT)]
    first_s, sum_s = env.sem("es_first"), env.sem("es_sum")
    p_t = env.tiles(2 * NT)
    p_in = env.again("proj_in", 32)[0]
    p_out, out0 = env.again("row_out", 16 * NT)
    with ExitStack() as st:
        T = lambda n, s: st.enter_context(nc.sbuf_tensor("es_" + n, s, F32))
        y = T("y", [P, NT, PICKS, D])
        pT, wp, proj = T("pT", [P, PLE // P, S]), T("wp", [P, PLE // P, D]), E.proj
        with nc.Block() as block:
            @block.sync
            def _(sp):
                nc.sync.dma_start(pT[:], dram["p_T"]).then_inc(p_in, 16)
                nc.sync.dma_start(wp[:], dram["w_ple_proj"]).then_inc(p_in, 16)
                for t in range(NT):
                    for n in range(2):
                        evacuated(env, sp, p_t[2 * t + n])
                    nc.sync.dma_start(dram["p_dram"][t * P:(t + 1) * P, :], proj[:, t, :]).then_inc(p_out, 16)

            @block.tensor
            def _(pe):
                pe.wait_ge(p_in, 32)
                for i, t in enumerate(p_t):
                    bank_ready(env, pe, t)
                    for k in range(PLE // P):
                        mm = nc.tensor.matmul(env.ps[:, t[0], :], pT[:, k, i // 2 * P:(i // 2 + 1) * P],
                                              wp[:, k, i % 2 * WBLK:(i % 2 + 1) * WBLK], start=(k == 0), stop=(k == PLE // P - 1))
                    mm.then_inc(env.bank_full[t[0]], 1)

            @block.gpsimd
            def _(pool):
                for t in range(NT):
                    for k in range(PICKS):
                        nc.gpsimd.indirect_dma_start(y[:, t, k, :], None, dram["y_dram"], bass.IndirectOffsetOnAxis(
                            ap=E.pos[:, k, t:t + 1], axis=0)).then_inc(got[t], 16)

            @block.scalar
            def _(act):
                for t in range(NT):
                    act.wait_ge(got[t], 16 * PICKS)
                    nc.scalar.activation(y[:, t, 0, :], y[:, t, 0, :], ACT.Copy, scale=E.weight[:, 0, t:t + 1]).then_inc(first_s, 1)
                for i, t in enumerate(p_t):
                    product_done(env, act, t)
                    nc.scalar.activation(proj[:, i // 2, i % 2 * WBLK:(i % 2 + 1) * WBLK], env.ps[:, t[0], :],
                                         ACT.Copy).then_inc(env.bank_free[t[0]], 1)

            @block.vector
            def _(v):
                step = Chain(sum_s)
                for t in range(NT):
                    v.wait_ge(first_s, t + 1)
                    step(v, nc.vector.scalar_tensor_tensor(y[:, t, 1, :], y[:, t, 1, :], E.weight[:, 1, t:t + 1], y[:, t, 0, :],
                                                           ALU.mult, ALU.add))
                    step(v, nc.vector.tensor_tensor(y[:, t, 1, :], y[:, t, 1, :], env.gates[:, 1, :], ALU.mult))
                    step(v, nc.vector.tensor_tensor(env.h[:, t, :], env.h[:, t, :], y[:, t, 1, :], ALU.add))
    return p_out, out0 + 16 * NT


AH = 8
QR, KVR = 384, 256
CQ, CKV = QR // P, KVR // P
NOPE, ROT, VH = 64, 32, 64
QH = NOPE + ROT
DH = 64


def stage_second_project(env, M):
    nc, dram = env.nc, env.dram
    q_t, k_t, r_t = env.tiles(4), env.tiles(4), env.tiles(8)
    v_t, c_t = env.tiles(NT), env.tiles(NT)
    e_t, kr_t = env.tiles(NT), env.tile()
    blks = [env.take_block(t) for t in (q_t[-1], k_t[-1], v_t[-1], c_t[-1], kr_t)]
    tab_in, cos_s, rope_s = (env.sem("sp_" + n) for n in ("tab", "cos", "rope"))
    with ExitStack() as st:
        sn = st.enter_context(nc.sbuf_tensor("sp_sn", [P, 2, S], F32))
        tab = st.enter_context(nc.sbuf_tensor("sp_tabs", [P, 2, S], F32))
        perm = st.enter_context(nc.sbuf_tensor("sp_perm", [P, P], F32))
        with nc.Block() as block:
            @block.sync
            def _(sp):
                nc.sync.dma_start(tab[:], dram["rope_dil"]).then_inc(tab_in, 16)
                nc.sync.dma_start(perm[:], dram["perm_dil"]).then_inc(tab_in, 16)
                load_blocks(env, sp)

            @block.scalar
            def _(act):
                for j, t in enumerate(q_t + k_t):
                    product_done(env, act, t)
                    nc.scalar.activation(M.dqk[:, j, :], env.ps[:, t[0], :], ACT.Copy,
                                         scale=DH ** -0.5 if j < 4 else 1.0).then_inc(env.bank_free[t[0]], 1)
                for tl, dst, n in ((v_t, M.dv, WBLK), (c_t, M.c, WBLK)):
                    for i, t in enumerate(tl):
                        product_done(env, act, t)
                        nc.scalar.activation(dst[:, i, 0:n], env.ps[:, t[0], 0:n], ACT.Copy).then_inc(env.bank_free[t[0]], 1)
                for i, t in enumerate(e_t):
                    product_done(env, act, t)
                    nc.scalar.activation(M.c[:, i, WBLK:WBLK + P], env.ps[:, t[0], 0:P], ACT.Copy).then_inc(env.bank_free[t[0]], 1)
                product_done(env, act, kr_t)
                nc.scalar.activation(M.kr[:], env.ps[0:QH, kr_t[0], :], ACT.Copy).then_inc(env.bank_free[kr_t[0]], 1)

            @block.vector
            def _(v):
                v.wait_ge(tab_in, 32)
                rope_dve(env, v, r_t, lambda j: M.dqk[:, j, :], tab, sn, cos_s, rope_s)

            @block.tensor
            def _(pe):
                for b, tl in zip(blks[:2], (q_t, k_t)):
                    w = block_view(env, pe, b)
                    for j, t in enumerate(tl):
                        project(env, pe, t, env.ps[:, t[0], :], w, j * P, (j + 1) * P, lambda k: env.hT[:, k, 0:S])
                pe.wait_ge(tab_in, 32)
                rope_mm(env, pe, r_t, perm[:], lambda j: M.dqk[:, j, :], lambda j: evacuated(env, pe, (q_t + k_t)[j]))
                for b, tl in zip(blks[2:4], (v_t, c_t)):
                    w = block_view(env, pe, b)
                    for i, t in enumerate(tl):
                        by_token(env, pe, t, WBLK, w, i)
                w = block_view(env, pe, blks[4])
                for i, t in enumerate(e_t):
                    by_token(env, pe, t, P, w, i)
                project(env, pe, kr_t, env.ps[0:QH, kr_t[0], :], w, P, P + QH, lambda k: env.hT[:, k, 0:S])


def stage_latent_expand(env, M):
    nc, dram = env.nc, env.dram
    c_t = env.tiles(CQ + CKV)
    q_t = env.tiles(AH)
    k_t = env.tiles(AH)
    r_t = env.tiles(AH + 1)
    v_t = env.tiles(NT)
    tab_in, sq_s, rms_s, inv_s, nrm_s, cos_s, rope_s = (env.sem("le_" + n) for n in (
        "tab", "sq", "rms", "inv", "nrm", "cos", "rope"))
    parts = ((0, QR), (QR, KVR))
    with ExitStack() as st:
        T = lambda n, s: st.enter_context(nc.sbuf_tensor("le_" + n, s, F32))
        sn, tab, perm = T("sn", [P, 2, S]), T("tabs", [P, 2, S]), T("perm", [P, P])
        wq, wkv = T("wq", [P, CQ, AH * QH]), T("wkv", [P, CKV, AH * (NOPE + VH)])
        cT = T("cT", [P, CQ + CKV, S])
        sq, ss, rs = T("sqs", [P, 2, QR]), T("ss", [P, 2, NT]), T("rs", [P, 2, NT])
        with nc.Block() as block:
            @block.sync
            def _(sp):
                nc.sync.dma_start(wq[:], dram["w_uq"]).then_inc(tab_in, 16)
                nc.sync.dma_start(wkv[:], dram["w_ukv"]).then_inc(tab_in, 16)
                nc.sync.dma_start(tab[0:QH], dram["rope_mla"]).then_inc(tab_in, 16)
                nc.sync.dma_start(perm[0:QH, 0:QH], dram["perm_mla"]).then_inc(tab_in, 16)
                load_blocks(env, sp)

            @block.scalar
            def _(act):
                n = 0
                for p, (lo, w) in enumerate(parts):
                    for t in range(NT):
                        if n >= 2:
                            act.wait_ge(sq_s, n - 1)
                        nc.scalar.activation(sq[:, n % 2, 0:w], M.c[:, t, lo:lo + w], ACT.Square,
                                             accum_out=ss[:, p, t:t + 1]).then_inc(sq_s, 1)
                        n += 1
                act.wait_ge(sq_s, n)
                for p, (lo, w) in enumerate(parts):
                    nc.scalar.activation(rs[:, p, :], ss[:, p, :], ACT.Sqrt, scale=1.0 / w, bias=env.eps[:, 0:1]).then_inc(rms_s, 1)
                for hd, t in enumerate(q_t):
                    product_done(env, act, t)
                    nc.scalar.activation(M.q[:, hd, :], env.ps[0:QH, t[0], :], ACT.Copy, scale=QH ** -0.5).then_inc(
                        env.bank_free[t[0]], 1)
                for hd, t in enumerate(k_t):
                    product_done(env, act, t)
                    nc.scalar.activation(M.k[0:NOPE, hd, :], env.ps[0:NOPE, t[0], :], ACT.Copy).then_inc(env.bank_free[t[0]], 1)
                for i, t in enumerate(v_t):
                    product_done(env, act, t)
                    nc.scalar.activation(M.v[:, i, :], env.ps[:, t[0], :], ACT.Copy).then_inc(env.bank_free[t[0]], 1)

            @block.vector
            def _(v):
                v.wait_ge(rms_s, 2)
                nc.vector.reciprocal(ss[:], rs[:]).then_inc(inv_s, 1)
                v.wait_ge(inv_s, 1)
                for p, (lo, w) in enumerate(parts):
                    for t in range(NT):
                        x = M.c[:, t, lo:lo + w]
                        nc.vector.tensor_scalar(x, x, ss[:, p, t:t + 1], None, ALU.mult).then_inc(nrm_s, 1)
                for j, t in enumerate(c_t):
                    product_done(env, v, t)
                    nc.vector.tensor_scalar(cT[:, j, :], env.ps[:, t[0], :], col(env, "g_cq", j), None, ALU.mult).then_inc(
                        env.bank_free[t[0]], 1)
                v.wait_ge(tab_in, 64)
                rope_dve(env, v, r_t, lambda j: M.q[:, j, :] if j < AH else M.kr[:], tab, sn, cos_s, rope_s)
                v.wait_ge(rope_s, AH + 1)
                nc.vector.tensor_copy(M.k[NOPE:QH, :, :], M.kr[NOPE:QH, :].unsqueeze(1).broadcast_to([ROT, AH, S])).then_inc(rope_s, 1)

            @block.tensor
            def _(pe):
                to_features(env, pe, c_t, lambda t, j: M.c[:, t, j * P:(j + 1) * P],
                            lambda t, j: pe.wait_ge(nrm_s, (t + 1) + (NT if j >= CQ else 0)))
                pe.wait_ge(tab_in, 64)
                for t in c_t:
                    evacuated(env, pe, t)
                for hd, t in enumerate(q_t):
                    bank_ready(env, pe, t)
                    for k in range(CQ):
                        mm = nc.tensor.matmul(env.ps[0:QH, t[0], :], wq[:, k, hd * QH:(hd + 1) * QH], cT[:, k, :],
                                              start=(k == 0), stop=(k == CQ - 1))
                    mm.then_inc(env.bank_full[t[0]], 1)
                for hd, t in enumerate(k_t):
                    bank_ready(env, pe, t)
                    for k in range(CKV):
                        mm = nc.tensor.matmul(env.ps[0:NOPE, t[0], :], wkv[:, k, hd * NOPE:(hd + 1) * NOPE], cT[:, CQ + k, :],
                                              start=(k == 0), stop=(k == CKV - 1))
                    mm.then_inc(env.bank_full[t[0]], 1)
                rope_mm(env, pe, r_t, perm[0:QH, 0:QH], lambda j: M.q[:, j, :] if j < AH else M.kr[:],
                        lambda j: evacuated(env, pe, q_t[j]) if j < AH else None)
                for i, t in enumerate(v_t):
                    bank_ready(env, pe, t)
                    for k in range(CKV):
                        mm = nc.tensor.matmul(env.ps[:, t[0], :], cT[:, CQ + k, i * P:(i + 1) * P], wkv[:, k, AH * NOPE:],
                                              start=(k == 0), stop=(k == CKV - 1))
                    mm.then_inc(env.bank_full[t[0]], 1)


def stage_attention(env, M, o):
    nc = env.nc
    units = []
    for hd in range(AH):
        for qt in range(NT):
            units += [(0, hd, qt), (1, hd, qt)]
    nu = len(units)
    sc, tr, pv = [None] * nu, [None] * nu, [None] * nu
    for s in range(nu + 2):
        if s < nu:
            sc[s] = env.tile()
        if 1 <= s <= nu:
            tr[s - 1] = env.tile()
        if s >= 2:
            pv[s - 2] = env.tile()
    mask_in, neg_s, ex_s, inv_s = (env.sem("at_" + n) for n in ("mask", "neg", "exp", "inv"))

    def weights_ready(eng, u):
        if units[u][0] == 0:
            evacuated(env, eng, sc[u])
        else:
            eng.wait_ge(ex_s, u // 2 + 1)

    with ExitStack() as st:
        T = lambda n, s: st.enter_context(nc.sbuf_tensor("at_" + n, s, F32))
        mask = T("masks", [P, NT, S])
        sm = T("sm", [P, 2, S])
        pr, pt = T("pr", [P, 2, S]), T("pt", [P, 2, S])
        mx, nm, sums, inv = T("mx", [P, nu]), T("nm", [P, nu]), T("sums", [P, nu]), T("invs", [P, nu])
        with nc.Block() as block:
            @block.sync
            def _(sp):
                nc.sync.dma_start(mask[:], env.dram["dil_mask"]).then_inc(mask_in, 16)
                load_blocks(env, sp)

            @block.vector
            def _(v):
                v.wait_ge(mask_in, 16)
                for s in range(nu + 2):
                    if s < nu:
                        kind, hd, qt = units[s]
                        product_done(env, v, sc[s])
                        if kind == 0:
                            nc.vector.tensor_reduce(nm[:, s:s + 1], env.ps[:, sc[s][0], :], AX.X, ALU.max,
                                                    negate=True).then_inc(neg_s, 1)
                        else:
                            if s >= 4:
                                v.wait_ge(ex_s, s // 2 - 1)
                            nc.vector.tensor_tensor_reduce(sm[:, (s // 2) % 2, :], env.ps[:, sc[s][0], :], mask[:, qt, :],
                                                           1.0, NEG, ALU.add, ALU.max, mx[:, s:s + 1]).then_inc(
                                env.bank_free[sc[s][0]], 1)
                            evacuated(env, v, sc[s])
                            nc.vector.tensor_scalar(nm[:, s:s + 1], mx[:, s:s + 1], -1.0, None, ALU.mult).then_inc(neg_s, 1)
                    if s >= 2:
                        u = s - 2
                        kind, hd, qt = units[u]
                        weights_ready(v, u)
                        nc.vector.reciprocal(inv[:, u:u + 1], sums[:, u:u + 1]).then_inc(inv_s, 1)
                        product_done(env, v, pv[u])
                        v.wait_ge(inv_s, u + 1)
                        nc.vector.tensor_scalar(o[:, kind, qt, hd * VH:(hd + 1) * VH], env.ps[:, pv[u][0], 0:VH],
                                                inv[:, u:u + 1], None, ALU.mult).then_inc(env.bank_free[pv[u][0]], 1)

            @block.scalar
            def _(act):
                for s in range(nu + 1):
                    if s < nu:
                        kind, hd, qt = units[s]
                        act.wait_ge(neg_s, s + 1)
                        if s >= 2:
                            product_done(env, act, tr[s - 2])
                        if kind == 0:
                            nc.scalar.activation(pr[:, s % 2, :], env.ps[:, sc[s][0], :], ACT.Exp, bias=nm[:, s:s + 1],
                                                 accum_out=sums[:, s:s + 1]).then_inc(env.bank_free[sc[s][0]], 1)
                        else:
                            nc.scalar.activation(pr[:, s % 2, :], sm[:, (s // 2) % 2, :], ACT.Exp, bias=nm[:, s:s + 1],
                                                 accum_out=sums[:, s:s + 1]).then_inc(ex_s, 1)
                    if s >= 1:
                        u = s - 1
                        product_done(env, act, tr[u])
                        if u >= 2:
                            product_done(env, act, pv[u - 2])
                        nc.scalar.activation(pt[:, u % 2, :], env.ps[:, tr[u][0], :], ACT.Copy).then_inc(
                            env.bank_free[tr[u][0]], 1)

            @block.tensor
            def _(pe):
                for s in range(nu + 2):
                    if s < nu:
                        kind, hd, qt = units[s]
                        qs = slice(qt * P, (qt + 1) * P)
                        bank_ready(env, pe, sc[s])
                        if kind == 0:
                            q, k = M.q[:, hd, qs], M.k[:, hd, :]
                        else:
                            rows = slice(DH * (hd % 2), DH * (hd % 2 + 1))
                            q, k = M.dqk[rows, hd // 2, qs], M.dqk[rows, 4 + hd // 2, :]
                        nc.tensor.matmul(env.ps[:, sc[s][0], :], q, k, start=True, stop=True).then_inc(env.bank_full[sc[s][0]], 1)
                    if 1 <= s <= nu:
                        u = s - 1
                        weights_ready(pe, u)
                        bank_ready(env, pe, tr[u])
                        for kt in range(NT):
                            mm = nc.tensor.transpose(env.ps[:, tr[u][0], kt * P:(kt + 1) * P],
                                                     pr[:, u % 2, kt * P:(kt + 1) * P], env.ident[:])
                        mm.then_inc(env.bank_full[tr[u][0]], 1)
                    if s >= 2:
                        u = s - 2
                        kind, hd, qt = units[u]
                        evacuated(env, pe, tr[u])
                        bank_ready(env, pe, pv[u])
                        val = M.v if kind == 0 else M.dv
                        for kt in range(NT):
                            mm = nc.tensor.matmul(env.ps[:, pv[u][0], 0:VH], pt[:, u % 2, kt * P:(kt + 1) * P],
                                                  val[:, kt, hd * VH:(hd + 1) * VH], start=(kt == 0), stop=(kt == NT - 1))
                        mm.then_inc(env.bank_full[pv[u][0]], 1)


def stage_mix(env, o, mixT):
    nc = env.nc
    tl = env.tiles(KD)
    sq_s, rms_s, inv_s, nrm_s = (env.sem("mx_" + n) for n in ("sq", "rms", "inv", "nrm"))
    W = AH * VH
    with ExitStack() as st:
        T = lambda n, s: st.enter_context(nc.sbuf_tensor("mx_" + n, s, F32))
        sq, ss, rs = T("sqs", [P, 2, W]), T("ss", [P, 2, NT]), T("rs", [P, 2, NT])
        with nc.Block() as block:
            @block.sync
            def _(sp):
                load_blocks(env, sp)

            @block.scalar
            def _(act):
                for n in range(2 * NT):
                    if n >= 2:
                        act.wait_ge(sq_s, n - 1)
                    nc.scalar.activation(sq[:, n % 2, :], o[:, n // NT, n % NT, :], ACT.Square,
                                         accum_out=ss[:, n // NT, n % NT:n % NT + 1]).then_inc(sq_s, 1)
                act.wait_ge(sq_s, 2 * NT)
                nc.scalar.activation(rs[:], ss[:], ACT.Sqrt, scale=1.0 / W, bias=env.eps[:, 0:1]).then_inc(rms_s, 1)

            @block.vector
            def _(v):
                v.wait_ge(rms_s, 1)
                nc.vector.reciprocal(ss[:], rs[:]).then_inc(inv_s, 1)
                v.wait_ge(inv_s, 1)
                for n in range(2 * NT):
                    x = o[:, n // NT, n % NT, :]
                    nc.vector.tensor_scalar(x, x, ss[:, n // NT, n % NT:n % NT + 1], None, ALU.mult).then_inc(nrm_s, 1)
                for j, t in enumerate(tl):
                    product_done(env, v, t)
                    nc.vector.tensor_scalar(mixT[:, j, :], env.ps[:, t[0], :], col(env, "g_mla", j), None, ALU.mult).then_inc(
                        env.bank_free[t[0]], 1)

            @block.tensor
            def _(pe):
                to_features(env, pe, tl, lambda t, j: o[:, j // 4, t, (j % 4) * P:(j % 4 + 1) * P],
                            lambda t, j: pe.wait_ge(nrm_s, (j // 4) * NT + t + 1))


PH = 8
PK = 128
HALF = 64
TK = 16
SLOTS = PH * TK
STAIRS = ((0, 1, 16, 0), (1, 3, 8, 16), (4, 4, 4, 40), (8, 8, 1, 56))
NCAND = 64
RING = 8
GT = 2
DT = NT - GT
DS = DT * P
PER = 2 * RING
TURNS = SLOTS // PER
STEP = 4
PARTS = 2 * GT
PB = PK // PARTS
GRP = KD
MIDDLE = PB * 5 // 8
EARLY = PB
LATE = (SLOTS - EARLY) * RING // PB


def stage_memory_route(env, rows, pairs, gate, xg):
    nc, dram = env.nc, env.dram
    pair_tiles = lambda: env.tiles(PH)
    score_tiles = lambda: [[env.tile() for half in range(2)] for hg in range(2)]
    q_t, s_t = [pair_tiles()], [score_tiles(), score_tiles()]
    q_t.append(pair_tiles())
    s_t.append(score_tiles())
    u_t = env.tiles(MIDDLE)
    s_t.append(score_tiles())
    u_t += env.tiles(PB - MIDDLE)
    blks = [env.take_block(q_t[1][3]), env.take_block(q_t[1][7])]
    rounds = PB // STEP
    u_in = [env.again(f"table_in{n}", 16 * rounds)[0] for n in range(STEP)]
    g_out = [env.sem(f"pk_g_out{n}") for n in range(STEP)]
    in_s, grp_s, top_s, exp_s, place_s, match_s = (env.sem("pk_" + n) for n in (
        "in", "group", "top", "exp", "place", "match"))
    with ExitStack() as st:
        T = lambda n, s, d=F32: st.enter_context(nc.sbuf_tensor("pk_" + n, s, d))
        qp = T("qp", [P, PH, S])
        keys = T("keys", [P, PK])
        iota = T("iota", [P, TK])
        sc = T("sc", [P, 2, 2, PH, PK])
        rest = T("rest", [P, 2, PH, PK])
        v, ix, ixf = T("v", [P, 2, PH, TK]), T("ix", [P, 2, PH, TK], U32), T("ixf", [P, 2, PH, TK])
        cand, cand2 = T("cand", [P, PH, NCAND]), T("cand2", [P, PH, NCAND])
        top, pos = T("top", [P, PH, TK]), T("pos", [P, PH, TK], U32)
        ab, abf = T("ab", [P, 2, PH, TK], U32), T("abf", [P, 2, PH, TK])
        posf, runs, place = T("posf", [P, PH, TK]), T("runs", [P, 3, PH, TK]), T("place", [P, 2, PH, TK])
        eq = T("eq", [P, 2, PH * TK, TK])
        pick = T("pick", [P, 2, PH * TK])
        ex, sm = T("ex", [P, 2, PH, TK]), T("sm", [P, 2, PH])
        u, g = T("u", [P, STEP, D]), T("g", [P, STEP, DS])
        row = T("row", [P, D])
        token_rows = NormRows(env, st, "ffn2_rows", lambda t: env.h[:, t, :], GT, xg)
        row_in, row0 = env.again("row_in", 16)
        row_done, _ = env.again("row_done", GT)
        flat = [P, PH * TK, TK]

        def match(a):
            return nc.vector.tensor_tensor(eq[:, a], iota[:].unsqueeze(1).broadcast_to(flat),
                                           place[:, a].rearrange("p h k -> p (h k)").unsqueeze(2).broadcast_to(flat), ALU.is_equal)

        def number(E, a):
            by_head = eq[:, a].rearrange("p (h k) j -> p h k j", k=TK)
            return E.tensor_tensor(by_head, by_head, ixf[:, a].unsqueeze(2).broadcast_to([P, PH, TK, TK]), ALU.mult)

        with nc.Block() as block:
            @block.gpsimd
            def _(pool):
                for t in range(NT):
                    pool.wait_ge(place_s, t + 1)
                    number(nc.gpsimd, 1).then_inc(match_s, 1)

            @block.sync
            def _(sp):
                nc.sync.dma_start(keys[:], dram["peer_keys"]).then_inc(in_s, 16)
                nc.sync.dma_start(iota[:], dram["iota16"]).then_inc(in_s, 16)
                nc.sync.dma_start(row[:], dram["g_ffn_row"].broadcast_to([P, D])).then_inc(row_in, 16)
                load_blocks(env, sp, 0)

                def store(m):
                    evacuated(env, sp, u_t[m])
                    nc.sync.dma_start(dram["g_dram"][m], g[:, m % STEP, :]).then_inc(g_out[m % STEP], 16)

                for m in range(PB):
                    if m >= STEP:
                        product_done(env, sp, u_t[m - STEP])
                    nc.sync.dma_start(u[:, m % STEP, :], dram["peer_uT"][m]).then_inc(u_in[m % STEP], 16)
                    if m >= STEP:
                        store(m - STEP)
                for m in range(PB - STEP, PB):
                    store(m)
                for n in range(STEP):
                    sp.wait_ge(g_out[n], 16 * rounds)

            @block.tensor
            def _(pe):
                w = [block_view(env, pe, b) for b in blks]
                pe.wait_ge(in_s, 32)

                def queries(pair):
                    lo, hi = 2 * pair * P, 2 * (pair + 1) * P
                    for hd, tl in enumerate(q_t[pair]):
                        project(env, pe, tl, env.ps[:, tl[0], 0:2 * P], w[hd // 4], hd % 4 * P, (hd % 4 + 1) * P,
                                lambda k: env.hT[:, k, lo:hi])

                def key_scores(t):
                    for hg in range(2):
                        for half in range(2):
                            tl, r = s_t[t][hg][half], slice(half * HALF, (half + 1) * HALF)
                            bank_ready(env, pe, tl)
                            for n in range(4):
                                hd = 4 * hg + n
                                evacuated(env, pe, q_t[t // 2][hd])
                                mm = nc.tensor.matmul(env.ps[:, tl[0], n * PK:(n + 1) * PK], qp[r, hd, t * P:(t + 1) * P],
                                                      keys[r, :], start=True, stop=True)
                            mm.then_inc(env.bank_full[tl[0]], 1)

                def table(first, last):
                    for m in range(first, last):
                        tl = u_t[m]
                        pe.wait_ge(u_in[m % STEP], 16 * (m // STEP + 1))
                        project(env, pe, tl, env.ps[:, tl[0], 0:DS], u[:, m % STEP, :].rearrange("p (k i) -> p k i", k=KD), 0, P,
                                lambda k: env.hT[:, k, GT * P:S])

                queries(0)
                key_scores(0)
                key_scores(1)
                queries(1)
                key_scores(2)
                table(0, MIDDLE)
                key_scores(3)
                table(MIDDLE, PB)

            @block.scalar
            def _(act):
                def queries(pair):
                    for hd, tl in enumerate(q_t[pair]):
                        product_done(env, act, tl)
                        nc.scalar.activation(qp[:, hd, 2 * pair * P:2 * (pair + 1) * P], env.ps[:, tl[0], 0:2 * P],
                                             ACT.Copy).then_inc(env.bank_free[tl[0]], 1)

                def key_scores(t):
                    if t >= 2:
                        act.wait_ge(top_s, t - 1)
                    for hg in range(2):
                        for half in range(2):
                            tl = s_t[t][hg][half]
                            product_done(env, act, tl)
                            nc.scalar.activation(sc[:, t % 2, half, 4 * hg:4 * hg + 4, :],
                                                 env.ps[:, tl[0], :].rearrange("p (h k) -> p h k", k=PK),
                                                 ACT.Copy).then_inc(env.bank_free[tl[0]], 1)

                def exponentials(t):
                    act.wait_ge(top_s, t + 1)
                    nc.scalar.activation(ex[:, t % 2], ex[:, t % 2], ACT.Exp).then_inc(exp_s, 1)

                def table(first, last):
                    for m in range(first, last):
                        if m >= STEP:
                            act.wait_ge(g_out[m % STEP], 16 * (m // STEP))
                        product_done(env, act, u_t[m])
                        nc.scalar.activation(g[:, m % STEP, :], env.ps[:, u_t[m][0], 0:DS], ACT.Gelu).then_inc(
                            env.bank_free[u_t[m][0]], 1)

                token_rows.on_scalar(act)
                queries(0)
                key_scores(0)
                key_scores(1)
                queries(1)
                exponentials(0)
                key_scores(2)
                table(0, MIDDLE // 2)
                exponentials(1)
                table(MIDDLE // 2, MIDDLE)
                key_scores(3)
                exponentials(2)
                table(MIDDLE, PB)
                exponentials(3)

            @block.vector
            def _(ve):
                V = nc.vector
                group = Group(grp_s)
                token_rows.on_vector(ve)
                ve.wait_ge(token_rows.done, token_rows.done0 + GT)
                ve.wait_ge(row_in, row0 + 16)
                for t in range(GT):
                    V.tensor_tensor(xg[:, t, :], xg[:, t, :], row[:], ALU.mult).then_inc(row_done, 1)
                ve.wait_ge(in_s, 32)
                halves = [(half, hd) for half in range(2) for hd in range(PH)]

                def finish(t):
                    ve.wait_ge(exp_s, t + 1)
                    group(ve, [V.reduce_sum(sm[:, 0, :], ex[:, t % 2], axis=AX.X)])
                    group(ve, [V.reciprocal(sm[:, 1, :], sm[:, 0, :])])
                    group(ve, [V.tensor_tensor(gate[:, t, :].rearrange("p (h k) -> p h k", k=TK), ex[:, t % 2],
                                               sm[:, 1, :].unsqueeze(2).broadcast_to([P, PH, TK]), ALU.mult)])

                for t in range(NT):
                    for hg in range(2):
                        for half in range(2):
                            evacuated(env, ve, s_t[t][hg][half])
                    s = sc[:, t % 2]
                    group(ve, [V.max(v[:, a, h, 0:8], s[:, a, h, :]) for a, h in halves])
                    group(ve, [V.max_index(ix[:, a, h, 0:8], v[:, a, h, 0:8], s[:, a, h, :]) for a, h in halves] +
                          [V.match_replace(rest[:, a, h, :], v[:, a, h, 0:8], s[:, a, h, :], NEG) for a, h in halves])
                    group(ve, [V.max(v[:, a, h, 8:16], rest[:, a, h, :]) for a, h in halves])
                    group(ve, [V.max_index(ix[:, a, h, 8:16], v[:, a, h, 8:16], rest[:, a, h, :]) for a, h in halves])
                    group(ve, [V.tensor_copy(ixf[:], ix[:])] +
                          [V.tensor_tensor(cand[:, :, at:at + na * nb].rearrange("p h (a b) -> p h a b", b=nb),
                                           v[:, 0, :, a0:a0 + na].unsqueeze(3).broadcast_to([P, PH, na, nb]),
                                           v[:, 1, :, 0:nb].unsqueeze(2).broadcast_to([P, PH, na, nb]), ALU.add)
                           for a0, na, nb, at in STAIRS])
                    hs = range(PH)
                    group(ve, [V.max(top[:, h, 0:8], cand[:, h, :]) for h in hs])
                    group(ve, [V.max_index(pos[:, h, 0:8], top[:, h, 0:8], cand[:, h, :]) for h in hs] +
                          [V.match_replace(cand2[:, h, :], top[:, h, 0:8], cand[:, h, :], NEG) for h in hs])
                    group(ve, [V.max(top[:, h, 8:16], cand2[:, h, :]) for h in hs])
                    group(ve, [V.max_index(pos[:, h, 8:16], top[:, h, 8:16], cand2[:, h, :]) for h in hs])
                    V.tensor_tensor(ex[:, t % 2], top[:], top[:, :, 0:1].broadcast_to([P, PH, TK]), ALU.subtract).then_inc(top_s, 1)
                    group(ve, [V.tensor_scalar(ab[:, 0], pos[:], 3, None, ALU.logical_shift_right),
                               V.tensor_scalar(ab[:, 1], pos[:], 2, None, ALU.logical_shift_right),
                               V.tensor_copy(posf[:], pos[:])])
                    group(ve, [V.tensor_copy(abf[:], ab[:])])
                    by8, by4, stt = abf[:, 0], abf[:, 1], V.scalar_tensor_tensor
                    group(ve, [V.tensor_scalar(place[:, 0], by8, -1.0, 0.0, ALU.add, ALU.max),
                               stt(runs[:, 0], by8, 2.0, by8, ALU.is_ge, ALU.mult),
                               stt(runs[:, 1], by4, 10.0, by4, ALU.is_ge, ALU.mult),
                               stt(runs[:, 2], posf[:], 56.0, posf[:], ALU.is_ge, ALU.mult)])
                    group(ve, [stt(place[:, 0], by4, -6.0, place[:, 0], ALU.add, ALU.max),
                               stt(runs[:, 1], runs[:, 0], 2.0, runs[:, 1], ALU.mult, ALU.max)])
                    group(ve, [stt(place[:, 0], posf[:], -48.0, place[:, 0], ALU.add, ALU.max),
                               stt(runs[:, 2], runs[:, 1], 4.0, runs[:, 2], ALU.mult, ALU.max)])
                    group(ve, [V.tensor_tensor(place[:, 1], posf[:], runs[:, 2], ALU.subtract)])
                    match(1).then_inc(place_s, 1)
                    group(ve, [match(0)])
                    group(ve, [number(V, 0)])
                    ve.wait_ge(match_s, t + 1)
                    group(ve, [V.reduce_sum(pick[:, a, :], eq[:, a], axis=AX.X) for a in range(2)])
                    if t < GT:
                        group(ve, [V.scalar_tensor_tensor(pick[:, 0, :], pick[:, 0, :], float(PK), pick[:, 1, :],
                                                          ALU.mult, ALU.add)])
                        group(ve, [V.tensor_copy(rows[:, t, :], pick[:, 0, :])])
                    else:
                        group(ve, [V.tensor_copy(pairs[:, t - GT], pick[:])])
                    if t >= 1:
                        finish(t - 1)
                finish(NT - 1)


def stage_memory(env, rows, pairs, gate, xg):
    nc, dram = env.nc, env.dram
    assert PB == TURNS * STEP == DS // GRP and PER % STEP == 0 and EARLY // RING + PB // RING == TURNS
    got, got0 = zip(*(env.again(f"gathered{r}", 16 * 2 * GT * SLOTS // RING) for r in range(RING)))
    table_got, table0 = [], 0
    for n in range(STEP):
        sem, table0 = env.again(f"table_in{n}", 32 * PK // STEP)
        table_got.append(sem)
    used, idx_s, dot_s, act_s, coef_s, sum_s = (env.sem("pm_" + n) for n in (
        "used", "idx", "dot", "gelu", "coef", "sum"))
    names = ("const", "zero", "keyT_full", "keyT_done", "score_full", "gelu_done", "w_done", "out_done", "ab_done",
             "c_full", "c_done")
    const_in, zero_s, keyT_full, keyT_done, score_full, gelu_done, w_done, out_done, ab_done, c_full, c_done = (
        env.sem("pd_" + n) for n in names)
    SCORE, OUT, CB, KT = [4, 5], [0, 1, 2, 3], [6, 7], [6, 7]
    u_blocks, v_blocks = dram["peer_uT"], dram["peer_v"].rearrange("(a b) d -> b a d", b=PK)
    uT = [env.wring[:, 0, s * D:(s + 1) * D] for s in range(STEP)]
    vr = [env.wring[:, 1, s * D:(s + 1) * D] for s in range(STEP)]

    def A(n):
        return env.hT[:, :, S + n * P:S + (n + 1) * P]

    def after(turn, s):
        return (turn, s + 1) if s + 1 < STEP else (turn + 1, 0)

    with ExitStack() as st:
        T = lambda n, s, d=F32: st.enter_context(nc.sbuf_tensor("pm_" + n, s, d))
        ring = T("ring", [P, RING, D])
        idx = T("idxs", [P, 2, RING], U32)
        dots = T("dots", [P, LATE])
        coef = T("coefs", [P, SLOTS])
        acc = T("acc", [P, 2, D])
        iota, zeros = T("iota", [P, PK]), T("zeros", [P, P])
        keyT = T("keyT", [P, 3, DS])
        B = T("onehot", [P, 2, GRP, PB])
        C = T("coef_part", [P, 2, DS, PB])
        W = T("weighted", [P, 2, DS])
        with nc.Block() as block:
            @block.sync
            def _(sp):
                nc.sync.dma_start(iota[:], dram["row_numbers"]).then_inc(const_in, 16)
                with sp.Fori(0, TURNS) as i:
                    for s in range(STEP):
                        m = STEP * i + s
                        sp.wait_ge(out_done, STEP - 1 + m)
                        sp.nop(nofuse=True)
                        nc.sync.dma_start(W[:, s % 2, :], dram["g_dram"][bass.ds(m, 1)].rearrange("o p n -> p (o n)")
                                          ).then_inc(table_got[s], 16)
                        nc.sync.dma_start(vr[s], v_blocks[bass.ds(m, 1)].rearrange("o p n -> p (o n)")).then_inc(table_got[s], 16)
                with sp.Fori(TURNS, PARTS * TURNS) as i:
                    for s in range(STEP):
                        m = STEP * i + s
                        sp.wait_ge(out_done, m + 1)
                        sp.nop(nofuse=True)
                        nc.sync.dma_start(uT[s], u_blocks[bass.ds(m, 1)].rearrange("o p n -> p (o n)")).then_inc(table_got[s], 16)
                        nc.sync.dma_start(vr[s], v_blocks[bass.ds(m, 1)].rearrange("o p n -> p (o n)")).then_inc(table_got[s], 16)

            @block.gpsimd
            def _(pool):
                for t in range(GT):
                    for ph, table in enumerate(("peer_u", "peer_v")):
                        turn0 = (2 * t + ph) * TURNS
                        with pool.Fori(0, TURNS) as i:
                            for half in range(2):
                                n0 = (turn0 + i) * PER + half * RING
                                pool.wait_ge(used, n0 + 1)
                                pool.nop(nofuse=True)
                                nc.gpsimd.tensor_copy(idx[:, half, :], rows[:, t, bass.ds(i * PER + half * RING, RING)]
                                                      ).then_inc(idx_s, 1)
                                pool.wait_ge(idx_s, 2 * (turn0 + i) + half + 1)
                                for r in range(RING):
                                    pool.wait_ge(used, n0 + r + 1)
                                    pool.nop(nofuse=True)
                                    nc.gpsimd.indirect_dma_start(
                                        ring[:, r, :], None, dram[table],
                                        bass.IndirectOffsetOnAxis(ap=idx[:, half, r:r + 1], axis=0)).then_inc(got[r], 16)

            @block.tensor
            def _(pe):
                def scores(turn, s):
                    pe.wait_ge(table_got[s], table0 + 32 * turn + 32)
                    for k in range(KD):
                        mm = nc.tensor.matmul(env.ps[:, SCORE[s % 2], 0:DS], uT[s][:, k * P:(k + 1) * P],
                                              env.hT[:, k, GT * P:S], start=(k == 0), stop=(k == KD - 1))
                    mm.then_inc(score_full, 1)

                def coefficients(part, i, s):
                    g = PB * part + STEP * i + s
                    pe.wait_ge(ab_done, 3 * g + 3)
                    pe.wait_ge(c_done, g + 1)
                    for j in range(GRP):
                        mm = nc.tensor.matmul(env.ps[:, CB[s % 2], j * PB:(j + 1) * PB], A(s % 2)[:, j, :], B[:, s % 2, j, :],
                                              start=True, stop=True)
                    mm.then_inc(c_full, 1)

                def outputs(turn, s, stop=False):
                    pe.wait_ge(w_done, STEP * turn + s + 1)
                    for n in range(2 * DT):
                        t, half = n // 2, n % 2
                        mm = nc.tensor.matmul(env.ps[:, OUT[n], :], W[:, s % 2, t * P:(t + 1) * P],
                                              vr[s][:, half * WBLK:(half + 1) * WBLK], start=False, stop=stop)
                    mm.then_inc(out_done, 1)

                pe.sem_inc(out_done, STEP)
                pe.sem_inc(c_full, 2)
                for n, src in enumerate((pairs[:, :, 0, :], pairs[:, :, 1, :], gate[:, GT:, :])):
                    for t in range(DT):
                        mm = nc.tensor.transpose(env.ps[:, KT[n // 2], (n % 2) * DS + t * P:(n % 2) * DS + (t + 1) * P],
                                                 src[:, t, :], env.ident[:])
                    if n:
                        mm.then_inc(keyT_full, 1)
                pe.wait_ge(zero_s, 1)
                for b in OUT:
                    nc.tensor.matmul(env.ps[:, b, :], zeros[:], env.hT[:, 0, 0:S], start=True, stop=False)
                pe.wait_ge(keyT_done, 2)
                with pe.Fori(0, TURNS) as i:
                    for s in range(STEP):
                        coefficients(0, i, s)
                with pe.Fori(0, TURNS) as i:
                    for s in range(STEP):
                        outputs(i, s)
                        coefficients(1, i, s)
                scores(TURNS, 0)
                for part in range(1, PARTS - 1):
                    with pe.Fori(0, TURNS) as i:
                        for s in range(STEP):
                            scores(*after(part * TURNS + i, s))
                            outputs(part * TURNS + i, s)
                            coefficients(part + 1, i, s)
                with pe.Fori((PARTS - 1) * TURNS, PARTS * TURNS - 1) as turn:
                    for s in range(STEP):
                        scores(*after(turn, s))
                        outputs(turn, s)
                for s in range(STEP):
                    if s + 1 < STEP:
                        scores(PARTS * TURNS - 1, s + 1)
                    outputs(PARTS * TURNS - 1, s, stop=(s + 1 == STEP))

            @block.scalar
            def _(act):
                def gelu(turn, s):
                    m = STEP * turn + s
                    act.wait_ge(out_done, STEP + m - 1)
                    act.wait_ge(score_full, m - PB + 1)
                    nc.scalar.activation(W[:, s % 2, :], env.ps[:, SCORE[s % 2], 0:DS], ACT.Gelu).then_inc(gelu_done, 1)

                def keep(part, i, s):
                    n = STEP * i + s
                    act.wait_ge(c_full, 2 + PB * part + n + 1)
                    act.nop(nofuse=True)
                    nc.scalar.activation(C[:, part % 2, bass.ds(n * GRP, GRP), :],
                                         env.ps[:, CB[s % 2], 0:GRP * PB].rearrange("p (t m) -> p t m", t=GRP),
                                         ACT.Copy).then_inc(c_done, 1)

                act.sem_inc(c_done, 2)
                act.wait_ge(keyT_full, 2)
                nc.scalar.activation(keyT[:, 0:2, :], env.ps[:, KT[0], :].rearrange("p (k t) -> p k t", k=2),
                                     ACT.Copy).then_inc(keyT_done, 1)
                nc.scalar.activation(keyT[:, 2, :], env.ps[:, KT[1], 0:DS], ACT.Copy).then_inc(keyT_done, 1)
                with act.Fori(0, TURNS) as i:
                    for s in range(STEP):
                        keep(0, i, s)
                for part in range(PARTS):
                    if 1 <= part < PARTS - 1:
                        act.wait_ge(w_done, PB * part)
                    last = part == PARTS - 1
                    with act.Fori(0, TURNS - 1 if last else TURNS) as i:
                        for s in range(STEP):
                            if part:
                                gelu(*after(part * TURNS + i, s))
                            if not last:
                                keep(part + 1, i, s)
                    if part == 0:
                        gelu(TURNS, 0)
                    if last:
                        for s in range(1, STEP):
                            gelu(PARTS * TURNS - 1, s)
                    if part % 2 == 0:
                        act.wait_ge(dot_s, 1 + (part // 2 + 1) * TURNS)
                        nc.scalar.activation(coef[:], coef[:], ACT.Gelu).then_inc(act_s, 1)

            @block.vector
            def _(v):
                def one_hot(part, i, s):
                    n = STEP * i + s
                    v.wait_ge(c_full, PB * part + n + 1)
                    g, ts = PB * part + n, bass.ds(n * GRP, GRP)
                    nc.vector.tensor_tensor(B[:, s % 2], iota[:, part * PB:(part + 1) * PB].unsqueeze(1).broadcast_to([P, GRP, PB]),
                                            keyT[:, 1, ts].unsqueeze(2).broadcast_to([P, GRP, PB]), ALU.is_equal).then_inc(ab_done, 1)
                    nc.vector.tensor_tensor(A(s % 2), iota[:].unsqueeze(1).broadcast_to([P, GRP, PK]),
                                            keyT[:, 0, ts].unsqueeze(2).broadcast_to([P, GRP, PK]), ALU.is_equal).then_inc(ab_done, 1)
                    v.wait_ge(ab_done, 3 * g + 1)
                    nc.vector.tensor_tensor(B[:, s % 2], B[:, s % 2], keyT[:, 2, ts].unsqueeze(2).broadcast_to([P, GRP, PB]),
                                            ALU.mult).then_inc(ab_done, 1)

                def weigh(part, i, s):
                    n = STEP * i + s
                    if part == 0:
                        v.wait_ge(table_got[s], table0 + 32 * i + 32)
                    else:
                        v.wait_ge(gelu_done, PB * (part - 1) + n + 1)
                    nc.vector.tensor_tensor(W[:, s % 2, :], W[:, s % 2, :], C[:, part % 2, :, bass.ds(n, 1)].rearrange("p t o -> p (t o)"),
                                            ALU.mult).then_inc(w_done, 1)

                v.sem_inc(used, RING)
                v.sem_inc(dot_s, 1)
                nc.vector.memset(zeros[:], 0.0).then_inc(zero_s, 1)
                v.wait_ge(const_in, 16)
                v.wait_ge(keyT_done, 2)

                def dot(t, fills, n):
                    r = n % RING
                    v.wait_ge(got[r], got0[r] + 16 * (fills + n // RING) + 16)
                    nc.vector.tensor_tensor_reduce(ring[:, r, :], ring[:, r, :], xg[:, t, :], 1.0, 0.0,
                                                   ALU.mult, ALU.add, dots[:, n:n + 1]).then_inc(used, 1)

                def keep_dots(fills, at, n):
                    v.wait_ge(used, RING * (fills + 1) + n)
                    nc.vector.tensor_copy(coef[:, bass.ds(at, n)], dots[:, 0:n]).then_inc(dot_s, 1)

                with v.Fori(0, EARLY // RING) as i:
                    v.wait_ge(dot_s, i + 1)
                    for n in range(RING):
                        one_hot(0, RING // STEP * i + n // STEP, n % STEP)
                        dot(0, i, n)
                    keep_dots(i, i * RING, RING)
                v.wait_ge(c_done, 2 + PB)
                with v.Fori(0, PB // RING) as i:
                    fills = EARLY // RING + LATE // RING * i
                    v.wait_ge(dot_s, EARLY // RING + i + 1)
                    for n in range(LATE):
                        m = n // (LATE // RING)
                        if n % (LATE // RING) == 0:
                            weigh(0, RING // STEP * i + m // STEP, m % STEP)
                            one_hot(1, RING // STEP * i + m // STEP, m % STEP)
                        dot(0, fills, n)
                    keep_dots(fills, EARLY + i * LATE, LATE)
                for t in range(GT):
                    turn0 = 2 * t * TURNS
                    if t >= 1:
                        v.wait_ge(c_done, 2 + PB * (2 * t + 1))
                        with v.Fori(0, TURNS) as i:
                            v.wait_ge(dot_s, t * TURNS + i + 1)
                            for n in range(PER):
                                if n % (PER // STEP) == 0:
                                    weigh(2 * t, i, n // (PER // STEP))
                                    one_hot(2 * t + 1, i, n // (PER // STEP))
                                dot(t, 2 * (turn0 + i), n)
                            keep_dots(2 * (turn0 + i), i * PER, PER)
                    v.wait_ge(act_s, t + 1)
                    nc.vector.tensor_tensor(coef[:], coef[:], gate[:, t, :], ALU.mult).then_inc(coef_s, 1)
                    if t >= 1:
                        v.wait_ge(sum_s, 2 * t)
                    nc.vector.memset(acc[:], 0.0).then_inc(coef_s, 1)
                    v.wait_ge(coef_s, 2 * (t + 1))
                    v.wait_ge(c_done, 2 + PB * (2 * t + 2))
                    turn1 = turn0 + TURNS
                    with v.Fori(0, TURNS) as i:
                        for n in range(PER):
                            r = n % RING
                            if n % (PER // STEP) == 0:
                                weigh(2 * t + 1, i, n // (PER // STEP))
                                if t + 1 < GT:
                                    one_hot(2 * t + 2, i, n // (PER // STEP))
                            v.wait_ge(got[r], got0[r] + 32 * (turn1 + i) + 16 * (n // RING) + 16)
                            v.wait_ge(used, RING + (turn1 + i) * PER + n - 1)
                            nc.vector.scalar_tensor_tensor(acc[:, n % 2, :], ring[:, r, :], coef[:, bass.ds(i * PER + n, 1)],
                                                           acc[:, n % 2, :], ALU.mult, ALU.add).then_inc(used, 1)
                    v.wait_ge(used, RING + (turn1 + TURNS) * PER)
                    for half in range(2):
                        if half:
                            v.wait_ge(sum_s, 2 * t + 1)
                        nc.vector.tensor_tensor(env.h[:, t, :], env.h[:, t, :], acc[:, half, :], ALU.add).then_inc(sum_s, 1)
                v.wait_ge(out_done, STEP + PK)
                for n in range(2 * DT):
                    t, cs = GT + n // 2, slice((n % 2) * WBLK, (n % 2 + 1) * WBLK)
                    nc.vector.tensor_tensor(env.h[:, t, cs], env.h[:, t, cs], env.ps[:, OUT[n], :], ALU.add).then_inc(sum_s, 1)


def stage_embedding(env):
    nc, dram = env.nc, env.dram
    g_t = [env.tiles(NT) for _ in range(2)]
    blks = [env.take_block(t[-1]) for t in g_t]
    in_s, in0 = env.again("proj_in", 16)
    add_s = env.sem("pl_add")
    with ExitStack() as st:
        T = lambda n, s: st.enter_context(nc.sbuf_tensor("pl_" + n, s, F32))
        gate = T("gate", [P, NT, D])
        proj = T("proj", [P, NT, D])
        with nc.Block() as block:
            @block.sync
            def _(sp):
                nc.sync.dma_start(proj[:], dram["p_dram"].rearrange("(t p) d -> p t d", p=P)).then_inc(in_s, 16)
                load_blocks(env, sp)

            @block.scalar
            def _(act):
                for half in range(2):
                    for i, t in enumerate(g_t[half]):
                        product_done(env, act, t)
                        nc.scalar.activation(gate[:, i, half * WBLK:(half + 1) * WBLK], env.ps[:, t[0], :],
                                             ACT.Sigmoid).then_inc(env.bank_free[t[0]], 1)

            @block.vector
            def _(v):
                v.wait_ge(in_s, in0 + 16)
                step = Chain(add_s)
                for half in range(2):
                    cs = slice(half * WBLK, (half + 1) * WBLK)
                    for i, t in enumerate(g_t[half]):
                        evacuated(env, v, t)
                        step(v, nc.vector.tensor_tensor(gate[:, i, cs], gate[:, i, cs], proj[:, i, cs], ALU.mult))
                        step(v, nc.vector.tensor_tensor(env.h[:, i, cs], env.h[:, i, cs], gate[:, i, cs], ALU.add))

            @block.tensor
            def _(pe):
                for half in range(2):
                    w = block_view(env, pe, blks[half])
                    for i, t in enumerate(g_t[half]):
                        by_token(env, pe, t, WBLK, w, i)


class Bufs:
    pass


def stream(env, *names):
    for n in names:
        a = env.dram[n]
        for i in range(a.shape[0]):
            env.blocks.append(a[i])


def load_tokens(env, name, src):
    nc = env.nc
    done = env.sem(name)
    with nc.Block() as block:
        @block.sync
        def _(sp):
            nc.sync.dma_start(env.h[:], src.rearrange("(t p) d -> p t d", p=P)).then_inc(done, 16)
            sp.wait_ge(done, 16)


def first_mixer(env):
    nc = env.nc
    gain = lambda n: (lambda j: env.gain[:, n, j:j + 1])
    shift = lambda c0, c: (lambda j: env.ada[:, c0 + j, c:c + 1])
    with ExitStack() as tok:
        env.hctx = tok.enter_context(nc.sbuf_tensor("ctx_tok", [P, NCT, D], F32))
        xn = tok.enter_context(nc.sbuf_tensor("mix_xn", [P, NT + NCT, D], F32))
        src = lambda t: env.h[:, t, :] if t < NT else env.hctx[:, t - NT, :]
        rows = NormRows(env, tok, "mix", src, NT + NCT, xn)
        stage_modulation(env, rows)
        stage_norm(env, "mix", src, [(0, NT, gain(0), shift(0, 0)), (NT, NCT, gain(1), shift(0, 1))], env.hT, made=rows)
    branch = ExitStack()
    oT = env.h[:].rearrange("p t d -> p (t d)").rearrange("p (k s) -> p k s", k=KD)
    with ExitStack() as own:
        A = lambda n, s: own.enter_context(nc.sbuf_tensor(n, s, F32))
        B = Bufs()
        B.q, B.k, B.v = A("gla_q", [P, H1, S]), A("gla_k", [P, H1, TOK]), A("gla_v", [P, NCH, D])
        B.sum, B.tot = A("gla_sum", [P, 2 * H1, TOK]), A("gla_tot", [P, 2 * H1, NCH])
        stage_gla_project(env, B)
        stage_gla_core(env, B, oT)
    yT = branch.enter_context(nc.sbuf_tensor("yT", [P, KD, S], F32))
    stage_branch(env, "gla", oT, yT, True)
    with ExitStack() as own:
        A = lambda n, s: own.enter_context(nc.sbuf_tensor(n, s, F32))
        R = Bufs()
        R.qk, R.kc, R.v = A("ret_qk", [P, 2 * H1, S]), A("ret_kc", [P, NCT, H1 * DK]), A("ret_v", [P, NCH, D])
        stage_ret_project(env, R)
        stage_ret_core(env, R, oT)
    stage_branch(env, "ret", oT, yT, False)
    load_tokens(env, "x_again", env.dram["x"])
    stage_out(env, "mix_out", yT, 0)
    branch.close()


def first_experts(env):
    nc = env.nc
    stage_norm(env, "ffn", lambda t: env.h[:, t, :],
               [(0, NT, lambda j: env.gain[:, 2, j:j + 1], lambda j: env.ada[:, 24 + j, 0:1])], env.hT,
               env.dram["xn_dram"])
    with ExitStack() as own:
        E = Bufs()
        E.weight = own.enter_context(nc.sbuf_tensor("pick_weight", [P, PICKS, NT], F32))
        E.pos = own.enter_context(nc.sbuf_tensor("pick_row", [P, PICKS, NT], U32))
        E.row_token = own.enter_context(nc.sbuf_tensor("row_token", [P, NB], U32))
        E.block_expert = own.enter_context(nc.sbuf_tensor("block_expert", [P, NB], I32))
        stage_router(env, E)
        stage_experts(env, E)
        E.proj = own.enter_context(nc.sbuf_tensor("ple_proj", [P, NT, D], F32))
        proj_stored = stage_expert_sum(env, E)
        stage_rownorm(env, "fin1", env.h, "norm_final", stored=proj_stored)


def second_block(env):
    nc = env.nc
    tok = lambda t: env.h[:, t, :]
    gain = lambda name: (lambda j: col(env, name, j))
    stage_norm(env, "mix2", tok, [(0, NT, gain("g_mix"), None)], env.hT)
    with ExitStack() as own:
        A = lambda n, s: own.enter_context(nc.sbuf_tensor(n, s, F32))
        M = Bufs()
        M.dqk, M.dv, M.kr = A("dil_qk", [P, 8, S]), A("dil_v", [P, NT, S]), A("mla_kr", [QH, S])
        M.q, M.k, M.v = A("mla_q", [QH, AH, S]), A("mla_k", [QH, AH, S]), A("mla_v", [P, NT, S])
        with nc.sbuf_tensor("mla_c", [P, NT, QR + KVR], F32) as c:
            M.c = c
            stage_second_project(env, M)
            stage_latent_expand(env, M)
        o = A("attn_o", [P, 2, NT, S])
        stage_attention(env, M, o)
        mixT = A("mixT", [P, KD, S])
        stage_mix(env, o, mixT)
        stage_out(env, "att_out", mixT, None)
    stage_norm(env, "ffn2", tok, [(0, NT, gain("g_ffn"), None)], env.hT)
    with ExitStack() as own:
        rows = own.enter_context(nc.sbuf_tensor("mem_rows", [P, GT, SLOTS], U32))
        pairs = own.enter_context(nc.sbuf_tensor("mem_pairs", [P, DT, 2, SLOTS], F32))
        gate = own.enter_context(nc.sbuf_tensor("mem_gate", [P, NT, SLOTS], F32))
        xg = own.enter_context(nc.sbuf_tensor("mem_x", [P, GT, D], F32))
        stage_memory_route(env, rows, pairs, gate, xg)
        stage_memory(env, rows, pairs, gate, xg)
    stage_norm(env, "ple", tok, [(0, NT, gain("g_ple"), None)], env.hT)
    stage_embedding(env)
    stage_rownorm(env, "fin2", env.h, "g_final_row", env.dram["out"])


def program(nc, dram):
    with ExitStack() as ctx:
        env = Env(nc, ctx, dram)
        env.ps = ctx.enter_context(nc.psum_tensor("ps", [P, 8, WBLK], F32))
        env.bank_full = [env.sem(f"bank_full{b}") for b in range(8)]
        env.bank_free = [env.sem(f"bank_free{b}") for b in range(8)]
        env.w_loaded = [env.sem(f"w_loaded{b}") for b in range(2)]
        env.const_in, env.const_set, env.x_in = env.sem("const_in"), env.sem("const_set"), env.sem("x_in")
        env.ident = env.sb("ident", [P, P])
        env.cols = env.sb("cols", [P, NCOL])
        env.ones = env.sb("ones", [P, P])
        env.eps = env.sb("eps", [P, 1])
        env.ada = env.sb("ada", [P, 48, 2])
        env.gain = env.sb("gain", [P, 3, 8])
        env.gates = env.sb("gates", [P, 2, D])
        env.hT = env.sb("hT", [P, KD, TOK])
        env.h = env.sb("h_tok", [P, NT, D])
        env.wring = env.sb("wring", [P, 2, KD * WBLK])
        stream(env, "w_ada")
        for b in (0, 1, 2, 3, 4, 5, 12, 13):
            env.blocks.append(dram["w_in"][b])
        stream(env, "w_branch_gla")
        for b in (6, 7, 8, 9, 10, 11, 14, 15):
            env.blocks.append(dram["w_in"][b])
        stream(env, "w_branch_ret", "w_out")
        stream(env, "w_in2", "w_out2", "w_peer_q", "w_ple_gate")
        first_mixer(env)
        first_experts(env)
        second_block(env)


def blocked(w):
    n = w.shape[1] // WBLK
    return w.reshape(KD, P, n, WBLK).transpose(2, 1, 0, 3).reshape(n, P, KD * WBLK)


def columns(a):
    return a.reshape(-1, P).T


def rope_table(seq_pos, inv):
    ang = seq_pos[:, None].astype(np.float32) * inv[None, :]
    return np.cos(ang).T, np.sin(ang).T


def constants():
    f = np.float32
    c = {"ident": np.eye(P, dtype=f)}
    n = 32
    inv = (f(10000.0) ** (-np.arange(n, dtype=f) / f(n))).astype(f)
    tab = np.zeros((P, 2, S), f)
    perm = np.zeros((P, P), f)
    for half, pos in enumerate((np.repeat(np.arange(S // 64), 64), np.tile(np.arange(64), S // 64))):
        cs, sn = rope_table(pos, inv)
        for part in range(2):
            r = half * 64 + part * 32
            tab[r:r + 32, 0], tab[r:r + 32, 1] = cs, sn
        for i in range(32):
            a, b = half * 64 + i, half * 64 + 32 + i
            perm[b, a] = -1.0
            perm[a, b] = 1.0
    c["rope_axial"], c["perm_axial"] = tab, perm
    h = np.arange(H1, dtype=np.float64)
    lg = [np.log1p(-np.exp2(-5.0 - h)), np.log1p(-np.exp2(-5.5 - h))]
    rel = np.arange(896)[None, :] - 384 - np.arange(P)[:, None]
    band = np.stack([np.where(rel >= 0, np.exp(np.maximum(rel, 0) * lg[0][i]), np.exp(np.maximum(-rel, 0) * lg[1][i]))
                     for i in range(H1)], 1)
    c["ret_band"] = (band * DK ** -0.5).astype(f)
    t = np.arange(S)
    c["ret_qdec"] = np.stack([np.stack([np.exp((t + 1) * lg[0][i]), np.exp((S - t) * lg[1][i])]) for i in range(H1)]).astype(f)
    s = np.arange(CT)
    kd = np.stack([np.exp((CT - 1 - s) * lg[0][i]) for i in range(H1)] + [np.exp(s * lg[1][i]) for i in range(H1)])
    c["ret_kdec"] = (kd * DK ** -0.5).reshape(2 * H1, NCT, P).transpose(2, 0, 1).astype(f)
    p = np.arange(P)
    c["chunk_mask"] = np.stack([p[:, None] <= p[None, :], p[:, None] > p[None, :]], 1).astype(f)
    e = np.arange(NE)
    c["iota16"] = np.broadcast_to(np.arange(TK, dtype=f), (P, TK))
    for name, rows, width, first, rot in (("mla", QH, QH, NOPE, ROT), ("dil", P, DH, 0, DH // 4)):
        half = rot // 2
        inv = (f(500000.0) ** (-np.arange(0, rot, 2, dtype=f) / f(rot))).astype(f)
        cs, sn = rope_table(np.arange(S), inv)
        tab, perm = np.zeros((rows, 2, S), f), np.zeros((rows, rows), f)
        tab[:, 0] = 1.0
        for r0 in range(first, rows, width):
            for part in range(2):
                tab[r0 + part * half:r0 + (part + 1) * half, 0] = cs
                tab[r0 + part * half:r0 + (part + 1) * half, 1] = sn
            for i in range(half):
                perm[r0 + half + i, r0 + i] = -1.0
                perm[r0 + i, r0 + half + i] = 1.0
        c["rope_" + name], c["perm_" + name] = tab, perm
    q, k = np.arange(S)[:, None], np.arange(S)[None, :]
    count = sum(((q - k) % dil == 0) & (abs(q - k) <= win // 2) for win, dil in ((128, 1), (512, 4), (2048, 16)))
    mask = np.where(count > 0, np.log(np.maximum(count, 1)), NEG).astype(f)
    c["dil_mask"] = mask.reshape(NT, P, S).transpose(1, 0, 2)
    c["token_before"] = (p[:, None] < p[None, :]).astype(f)
    c["row_numbers"] = np.broadcast_to(p, (P, ROWB)).astype(f)
    c["block_numbers"] = np.broadcast_to(np.arange(NB), (P, NB)).astype(f)
    c["token_numbers"] = (np.arange(NT)[None, :] * P + p[:, None]).astype(f)
    c["expert_numbers"] = np.broadcast_to(np.stack([e, e // EPG]), (P, 2, NE)).astype(f)
    return c


def layout(i):
    a = {k: np.asarray(v) for k, v in i.items()}
    d = constants()
    d["x"], d["ctx"] = a["x"][0], a["ctx"][0]
    d["c2"] = np.stack([a["c"][0].reshape(KD, P), a["c_ctx"].reshape(KD, P)], -1).transpose(1, 0, 2)
    vec = dict(norm_mix=a["norm_mix"][0], norm_ffn=a["norm_ffn"][0], b_ada=a["b_ada"][0], gla_norm=a["gla_norm"][0],
               gla_b=a["gla_lr_b"][0].reshape(-1), g_mix=a["g_mix_2"][0], g_cq=a["g_cq_2"][0], g_ckv=a["g_ckv_2"][0],
               g_mla=a["g_out_mla_2"][0], g_dil=a["g_out_dil_2"][0], g_ffn=a["g_ffn_2"][0], g_ple=a["g_ple_2"][0])
    d["cols"] = np.concatenate([columns(vec[n]) for n in COLS], 1)
    d["b_gates"] = np.concatenate([a["b_ada"][0, 2 * D:3 * D], a["b_ada"][0, 5 * D:6 * D]])[None]
    d["w_ada"] = blocked(a["w_ada"][0])
    w = a["w_in"][0]
    d["w_lr"] = w[:, 3072:3104].reshape(KD, P, 32).transpose(1, 0, 2)
    d["w_in"] = blocked(np.concatenate([w[:, :3072], w[:, 3104:]], 1))
    d["gla_lr_w"] = a["gla_lr_w"][0]
    d["w_router"] = np.concatenate([a["w_router_group"][0], a["w_router_expert"][0]], 1).reshape(KD, P, NR).transpose(1, 0, 2)
    d["b_router"] = np.concatenate([a["b_router_group"][0], a["b_router_expert"][0]])[None]
    gu = np.concatenate([a["w_expert_gate"][0], a["w_expert_up"][0]], 2).reshape(NE, KD, P, 2 * EF).transpose(0, 2, 1, 3)
    dn = a["w_expert_down"][0].reshape(NE, EFT, P, D).transpose(0, 2, 1, 3)
    d["experts"] = np.concatenate([gu.reshape(NE, P, -1), dn.reshape(NE, P, -1)], 2)
    w2 = a["w_in_2"][0]
    lat = QR + KVR
    pad = lambda n: np.zeros((D, n), np.float32)
    d["w_in2"] = blocked(np.concatenate([w2[:, lat + ROT:], w2[:, :lat], pad(NOPE), w2[:, lat:lat + ROT],
                                         pad(WBLK - P - QH)], 1))
    d["w_uq"] = a["w_uq_2"][0].reshape(CQ, P, AH * QH).transpose(1, 0, 2)
    kv = a["w_ukv_2"][0].reshape(KVR, AH, 2, NOPE).transpose(0, 2, 1, 3).reshape(KVR, -1)
    d["w_ukv"] = kv.reshape(CKV, P, -1).transpose(1, 0, 2)
    d["w_out2"], d["w_peer_q"], d["w_ple_gate"] = (blocked(a[n][0]) for n in ("w_out_2", "w_peer_q_2", "w_ple_gate_2"))
    d["peer_keys"] = np.concatenate([a["peer_keys1_2"][0].T, a["peer_keys2_2"][0].T], 0)
    d["peer_u"], d["peer_v"] = a["peer_u_2"][0], a["peer_v_2"][0]
    d["peer_uT"] = d["peer_u"].reshape(PK, PK, KD, P).transpose(1, 3, 2, 0).reshape(PK, P, D)
    d["p_T"] = a["p_2"][0, 0].T.reshape(PLE // P, P, S).transpose(1, 0, 2)
    d["w_ple_proj"] = a["w_ple_proj_2"][0].reshape(PLE // P, P, D).transpose(1, 0, 2)
    d["g_ffn_row"], d["g_final_row"] = a["g_ffn_2"][0][None], a["g_final_2"][None]
    d["norm_final"] = a["norm_final"][None]
    for n in ("w_branch_gla", "w_branch_ret", "w_out"):
        d[n] = blocked(a[n][0])
    return d


def kernel(**inputs):
    import concourse.bacc as bacc
    from concourse.bass_utils import run_bass_kernel_spmd as run

    nc = bacc.Bacc("TRN2", target_bir_lowering=False, num_devices=1)
    arrays, dram = {}, {}
    for n, v in layout(inputs).items():
        arrays["in_" + n] = np.ascontiguousarray(v)
        dram[n] = nc.dram_tensor("in_" + n, v.shape, mybir.dt.from_np(v.dtype), kind="ExternalInput").ap()
    dram["out"] = nc.dram_tensor("out", (S, D), F32, kind="ExternalOutput").ap()
    dram["xn_dram"] = nc.dram_tensor("xn_dram_out", (S, D), F32, kind="ExternalOutput").ap()
    dram["p_dram"] = nc.dram_tensor("p_dram_out", (S, D), F32, kind="ExternalOutput").ap()
    dram["g_dram"] = nc.dram_tensor("g_dram_out", (PB, P, DS), F32, kind="ExternalOutput").ap()
    dram["y_dram"] = nc.dram_tensor("y_dram_out", (NB * ROWB, D), F32, kind="ExternalOutput").ap()
    program(nc, dram)
    r = run(nc, [arrays], core_ids=[0])
    return r.results[0]["out"].reshape(1, S, D)
```
